# Optimizing a Trainium2 kernel written in Bass

```python
import math
import jax, jax.numpy as jnp
from jax import lax
import numpy as np

D_MODEL = 1024
BATCH = 1
SEQ = 1024
DEPTH = 1

MLA_HEADS = 8
QK_NOPE = 64
QK_ROPE = 32
V_DIM = 64
Q_LORA = 384
KV_LORA = 256
ROPE_BASE = 10000.0
Q_BLOCK = 128
MLA_OUT = MLA_HEADS * V_DIM
RWKV_HEADS = 8
RWKV_HEAD = 64
RWKV_DIM = RWKV_HEADS * RWKV_HEAD
DECAY_LORA = 64
AAA_LORA = 64
GATE_LORA = 128
LNX_EPS = 64e-5
N_DIR = 2
N_BRANCH = 2
MLA_IN = Q_LORA + KV_LORA + QK_ROPE
RWKV_IN = 3 * RWKV_DIM + N_DIR * DECAY_LORA + N_DIR * AAA_LORA + GATE_LORA
GATE_IN = N_BRANCH * D_MODEL
IN_DIM = MLA_IN + RWKV_IN + GATE_IN
N_GROUPS = 4
EXPERTS_PER_GROUP = 8
N_EXPERTS = N_GROUPS * EXPERTS_PER_GROUP
TOP_K = 2
D_EXPERT = 256
MOE_BLOCK = 128
NORM_EPS = 1e-6


def rms_norm(x, g, eps=NORM_EPS):
    xf = x.astype(jnp.float32)
    y = xf * lax.rsqrt(jnp.mean(xf * xf, axis=-1, keepdims=True) + eps)
    return (y * g.astype(jnp.float32)).astype(x.dtype)

def apply_rope(x, cos, sin):
    half = x.shape[-1] // 2
    x1 = x[..., :half].astype(jnp.float32)
    x2 = x[..., half:].astype(jnp.float32)
    out = jnp.concatenate([x1 * cos - x2 * sin, x1 * sin + x2 * cos], axis=-1)
    return out.astype(x.dtype)

def mla_branch(z, q_norm_g, kv_norm_g, w_uq, w_ukv):
    B, S, _ = z.shape
    c_q = rms_norm(z[..., :Q_LORA], q_norm_g)
    c_kv = rms_norm(z[..., Q_LORA:Q_LORA + KV_LORA], kv_norm_g)
    k_rope = z[..., Q_LORA + KV_LORA:]
    q = (c_q @ w_uq).reshape(B, S, MLA_HEADS, QK_NOPE + QK_ROPE)
    kv = (c_kv @ w_ukv).reshape(B, S, MLA_HEADS, QK_NOPE + V_DIM)
    q_nope, q_rope = q[..., :QK_NOPE], q[..., QK_NOPE:]
    k_nope, v = kv[..., :QK_NOPE], kv[..., QK_NOPE:]
    pos = jnp.arange(S, dtype=jnp.float32)
    inv_freq = ROPE_BASE ** (-jnp.arange(0, QK_ROPE, 2, dtype=jnp.float32) / QK_ROPE)
    ang = pos[:, None] * inv_freq[None, :]
    cos, sin = jnp.cos(ang), jnp.sin(ang)
    q_rope = apply_rope(q_rope, cos[:, None, :], sin[:, None, :])
    k_rope = apply_rope(k_rope, cos, sin)
    scale = (QK_NOPE + QK_ROPE) ** -0.5
    nb = S // Q_BLOCK
    qn_b = q_nope.reshape(B, nb, Q_BLOCK, MLA_HEADS, QK_NOPE).transpose(1, 0, 2, 3, 4)
    qr_b = q_rope.reshape(B, nb, Q_BLOCK, MLA_HEADS, QK_ROPE).transpose(1, 0, 2, 3, 4)

    def attend(blk):
        qn, qr = blk
        s = (jnp.einsum('bqhd,bkhd->bhqk', qn, k_nope)
             + jnp.einsum('bqhd,bkd->bhqk', qr, k_rope))
        p = jax.nn.softmax(s.astype(jnp.float32) * scale, axis=-1).astype(v.dtype)
        return jnp.einsum('bhqk,bkhd->bqhd', p, v)

    o = lax.map(attend, (qn_b, qr_b))
    return o.transpose(1, 0, 2, 3, 4).reshape(B, S, MLA_OUT)

def token_shift_centred(z, mu_prev, mu_next):
    z_prev = jnp.pad(z[:, :-1], ((0, 0), (1, 0), (0, 0)))
    z_next = jnp.pad(z[:, 1:], ((0, 0), (0, 1), (0, 0)))
    return z + mu_prev * (z_prev - z) + mu_next * (z_next - z)

def wkv7_scan(r, w, k, v, a_vec, b_vec):
    B, S, H, N = r.shape

    def step(state, inp):
        r_t, w_t, k_t, v_t, a_t, b_t = inp
        sa = jnp.einsum('bhvk,bhk->bhv', state, a_t)
        state = (state * w_t[:, :, None, :] + sa[..., None] * b_t[:, :, None, :]
                 + v_t[..., None] * k_t[:, :, None, :])
        return state, jnp.einsum('bhvk,bhk->bhv', state, r_t)

    xs = tuple(jnp.moveaxis(t, 1, 0) for t in (r, w, k, v, a_vec, b_vec))
    s0 = jnp.zeros((B, H, N, N), jnp.float32)
    _, y = lax.scan(step, s0, xs)
    return jnp.moveaxis(y, 0, 1)

def rwkv_branch(z, mu_prev, mu_next, w0, w_up, a0, a_up, g_up, k_k, k_a, r_k, lnx_g, lnx_b):
    B, S, _ = z.shape
    C, H, N = RWKV_DIM, RWKV_HEADS, RWKV_HEAD
    f32 = jnp.float32
    zf = token_shift_centred(z.astype(f32), mu_prev.astype(f32), mu_next.astype(f32))
    r, k, v = zf[..., :C], zf[..., C:2 * C], zf[..., 2 * C:3 * C]
    o = 3 * C
    wd = zf[..., o:o + N_DIR * DECAY_LORA].reshape(B, S, N_DIR, DECAY_LORA)
    o += N_DIR * DECAY_LORA
    ad = zf[..., o:o + N_DIR * AAA_LORA].reshape(B, S, N_DIR, AAA_LORA)
    o += N_DIR * AAA_LORA
    gd = zf[..., o:]
    w_logit = w0.astype(f32) + jnp.einsum('bsdr,drc->bsdc', jnp.tanh(wd), w_up.astype(f32))
    decay = jnp.exp(-jnp.exp(-jax.nn.softplus(-w_logit) - 0.5))
    a = jax.nn.sigmoid(a0.astype(f32) + jnp.einsum('bsdr,drc->bsdc', ad, a_up.astype(f32)))
    g = jax.nn.sigmoid(gd) @ g_up.astype(f32)

    def heads(t):
        return t.reshape(t.shape[:-1] + (H, N))

    kk = heads(k * k_k.astype(f32))
    kk = kk / jnp.maximum(jnp.sqrt(jnp.sum(kk * kk, axis=-1, keepdims=True)), 1e-12)
    k_dir = heads(k[:, :, None, :] * (1.0 + (a - 1.0) * k_a.astype(f32)))
    a_h, decay_h = heads(a), heads(decay)
    r_h, v_h = heads(r), heads(v)
    y_f = wkv7_scan(r_h, decay_h[:, :, 0], k_dir[:, :, 0], v_h, -kk, kk * a_h[:, :, 0])
    fl = lambda t: jnp.flip(t, axis=1)
    y_b = fl(wkv7_scan(fl(r_h), fl(decay_h[:, :, 1]), fl(k_dir[:, :, 1]), fl(v_h),
                       fl(-kk), fl(kk * a_h[:, :, 1])))
    y = y_f + y_b
    mu = jnp.mean(y, axis=-1, keepdims=True)
    var = jnp.mean(jnp.square(y - mu), axis=-1, keepdims=True)
    y = ((y - mu) * lax.rsqrt(var + LNX_EPS)).reshape(B, S, C)
    y = y * lnx_g.astype(f32) + lnx_b.astype(f32)
    bonus = jnp.sum(r_h[:, :, None] * k_dir * heads(r_k.astype(f32)), axis=-1, keepdims=True) * v_h[:, :, None]
    y = y + jnp.sum(bonus, axis=2).reshape(B, S, C)
    return (y * g).astype(z.dtype)

def hier_moe(h, rg_w, rg_b, re_w, re_b, w1, w3, w2):
    B, S, D = h.shape
    T = B * S
    ht = h.reshape(T, D)
    group_p = jax.nn.softmax((ht @ rg_w + rg_b).astype(jnp.float32), axis=-1)
    gp, gi = lax.top_k(group_p, 1)
    gp, gi = gp[:, 0], gi[:, 0]
    e_logits = (ht @ re_w + re_b).astype(jnp.float32).reshape(T, N_GROUPS, EXPERTS_PER_GROUP)
    sel = jnp.take_along_axis(e_logits, gi[:, None, None], axis=1)[:, 0]
    ep = jax.nn.softmax(sel, axis=-1)
    tp, ti = lax.top_k(ep, TOP_K)
    tp = tp / jnp.sum(tp, axis=-1, keepdims=True)
    weight = gp[:, None] * tp
    expert = gi[:, None] * EXPERTS_PER_GROUP + ti
    A = T * TOP_K
    flat_e = expert.reshape(A)
    flat_w = weight.reshape(A)
    flat_tok = jnp.repeat(jnp.arange(T, dtype=jnp.int32), TOP_K)
    order = jnp.argsort(flat_e)
    se, stok, sw = flat_e[order], flat_tok[order], flat_w[order]
    counts = jnp.bincount(flat_e, length=N_EXPERTS)
    padded = ((counts + MOE_BLOCK - 1) // MOE_BLOCK) * MOE_BLOCK
    start = jnp.cumsum(counts) - counts
    pend = jnp.cumsum(padded)
    pstart = pend - padded
    dest = pstart[se] + (jnp.arange(A, dtype=jnp.int32) - start[se])
    n_blocks = -(-A // MOE_BLOCK) + N_EXPERTS
    cap = n_blocks * MOE_BLOCK
    slot_tok = jnp.full((cap,), T, jnp.int32).at[dest].set(stok)
    slot_w = jnp.zeros((cap,), h.dtype).at[dest].set(sw.astype(h.dtype))
    block_e = jnp.minimum(jnp.searchsorted(pend, jnp.arange(n_blocks) * MOE_BLOCK, side='right'),
                          N_EXPERTS - 1)
    h_pad = jnp.concatenate([ht, jnp.zeros((1, D), ht.dtype)], axis=0)
    xb = h_pad[slot_tok].reshape(n_blocks, MOE_BLOCK, D)

    def expert_block(args):
        xblk, e = args
        hid = jax.nn.silu(xblk @ w1[e]) * (xblk @ w3[e])
        return hid @ w2[e]

    yb = lax.map(expert_block, (xb, block_e)).reshape(cap, D)
    y = jax.ops.segment_sum(yb * slot_w[:, None], slot_tok, num_segments=T + 1)[:T]
    return y.reshape(B, S, D)

def first_inputs(seed: int = 0) -> dict:
    key = jax.random.key(seed)
    ks = iter(jax.random.split(key, 48))
    L, D, C = DEPTH, D_MODEL, RWKV_DIM
    f32 = jnp.float32
    nrm = lambda shape, s: jax.random.normal(next(ks), shape, f32) * s
    uni = lambda shape, lo, hi: jax.random.uniform(next(ks), shape, f32, lo, hi)
    return {
        'x': nrm((BATCH, SEQ, D), 1.0),
        'norm_mix_g': 1.0 + nrm((L, D), 0.02),
        'w_in': nrm((L, D, IN_DIM), D ** -0.5),
        'q_norm_g': 1.0 + nrm((L, Q_LORA), 0.02),
        'kv_norm_g': 1.0 + nrm((L, KV_LORA), 0.02),
        'w_uq': nrm((L, Q_LORA, MLA_HEADS * (QK_NOPE + QK_ROPE)), Q_LORA ** -0.5),
        'w_ukv': nrm((L, KV_LORA, MLA_HEADS * (QK_NOPE + V_DIM)), KV_LORA ** -0.5),
        'w_br_mla': nrm((L, MLA_OUT, D), MLA_OUT ** -0.5),
        'mu_prev': uni((L, RWKV_IN), 0.0, 0.5),
        'mu_next': uni((L, RWKV_IN), 0.0, 0.5),
        'w0': uni((L, N_DIR, C), -3.0, 1.0),
        'w_up': nrm((L, N_DIR, DECAY_LORA, C), 0.5 * DECAY_LORA ** -0.5),
        'a0': nrm((L, N_DIR, C), 0.1),
        'a_up': nrm((L, N_DIR, AAA_LORA, C), 0.5 * AAA_LORA ** -0.5),
        'g_up': nrm((L, GATE_LORA, C), GATE_LORA ** -0.5),
        'k_k': 0.85 + nrm((L, C), 0.02),
        'k_a': 1.0 + nrm((L, C), 0.02),
        'r_k': nrm((L, C), 0.1),
        'lnx_g': 1.0 + nrm((L, C), 0.02),
        'lnx_b': nrm((L, C), 0.01),
        'w_br_rwkv': nrm((L, C, D), C ** -0.5),
        'gate_b': nrm((L, N_BRANCH, D), 0.01),
        'w_out': nrm((L, D, D), D ** -0.5),
        'norm_ffn_g': 1.0 + nrm((L, D), 0.02),
        'router_group_w': nrm((L, D, N_GROUPS), D ** -0.5),
        'router_group_b': nrm((L, N_GROUPS), 0.01),
        'router_expert_w': nrm((L, D, N_EXPERTS), D ** -0.5),
        'router_expert_b': nrm((L, N_EXPERTS), 0.01),
        'w1': nrm((L, N_EXPERTS, D, D_EXPERT), D ** -0.5),
        'w3': nrm((L, N_EXPERTS, D, D_EXPERT), D ** -0.5),
        'w2': nrm((L, N_EXPERTS, D_EXPERT, D), D_EXPERT ** -0.5),
        'norm_final_g': 1.0 + nrm((D,), 0.02),
    }

def first_block(x, norm_mix_g, w_in, q_norm_g, kv_norm_g, w_uq, w_ukv, w_br_mla,
              mu_prev, mu_next, w0, w_up, a0, a_up, g_up, k_k, k_a, r_k, lnx_g, lnx_b,
              w_br_rwkv, gate_b, w_out, norm_ffn_g, router_group_w, router_group_b,
              router_expert_w, router_expert_b, w1, w3, w2, norm_final_g):
    B, S, D = x.shape
    for l in range(DEPTH):
        h = rms_norm(x, norm_mix_g[l])
        z = h @ w_in[l]
        z_mla = z[..., :MLA_IN]
        z_rwkv = z[..., MLA_IN:MLA_IN + RWKV_IN]
        z_gate = z[..., MLA_IN + RWKV_IN:].reshape(B, S, N_BRANCH, D)
        o_mla = mla_branch(z_mla, q_norm_g[l], kv_norm_g[l], w_uq[l], w_ukv[l])
        o_rwkv = rwkv_branch(z_rwkv, mu_prev[l], mu_next[l], w0[l], w_up[l], a0[l], a_up[l],
                             g_up[l], k_k[l], k_a[l], r_k[l], lnx_g[l], lnx_b[l])
        gates = jax.nn.sigmoid(z_gate + gate_b[l])
        mixed = gates[:, :, 0] * (o_mla @ w_br_mla[l]) + gates[:, :, 1] * (o_rwkv @ w_br_rwkv[l])
        x = x + mixed @ w_out[l]
        h2 = rms_norm(x, norm_ffn_g[l])
        x = x + hier_moe(h2, router_group_w[l], router_group_b[l], router_expert_w[l],
                         router_expert_b[l], w1[l], w3[l], w2[l])
    return rms_norm(x, norm_final_g)


DEPTH_2 = 2

N_MIXERS = 2
HEAD_DIM = 64
N_Q_HEADS = D_MODEL // HEAD_DIM
N_KV_HEADS = N_Q_HEADS // 4
GQA_GROUP = N_Q_HEADS // N_KV_HEADS
WINDOW = 128
BLOCK = 128
ROT_DIM = HEAD_DIM // 4
ROPE_THETA = 500000.0
LRU_WIDTH = D_MODEL
LRU_BLOCKS = 4
LRU_BLOCK_W = LRU_WIDTH // LRU_BLOCKS
CONV_WIDTH = 4
CONV_LEFT = 2
LRU_C = 8.0
N_EXPERTS_2 = 16
EXPERT_FF = D_MODEL
CAPACITY_FACTOR = 2
LN_EPS = 1e-5
ALPHA = (2 * DEPTH_2) ** 0.25
BETA = (8 * DEPTH_2) ** -0.25
N_ATTN_LAYERS = (DEPTH_2 + 1) // 2
N_LRU_LAYERS = DEPTH_2 // 2


def layer_norm(x, g, b):
    xf = x.astype(jnp.float32)
    mu = jnp.mean(xf, axis=-1, keepdims=True)
    var = jnp.mean(jnp.square(xf - mu), axis=-1, keepdims=True)
    y = (xf - mu) * lax.rsqrt(var + LN_EPS) * g.astype(jnp.float32) + b.astype(jnp.float32)
    return y.astype(x.dtype)

def partial_rotary(t, cos, sin):
    tr, tp = t[..., :ROT_DIM], t[..., ROT_DIM:]
    t1, t2 = tr[..., :ROT_DIM // 2], tr[..., ROT_DIM // 2:]
    rot = jnp.concatenate([-t2, t1], axis=-1)
    return jnp.concatenate([tr * cos + rot * sin, tp], axis=-1)

def windowed_gqa_sink(x, w_qkv, w_o, sink):
    B, S, _ = x.shape
    nb = S // BLOCK
    qkv = x @ w_qkv
    q, k, v = jnp.split(qkv, [N_Q_HEADS * HEAD_DIM, (N_Q_HEADS + N_KV_HEADS) * HEAD_DIM], axis=-1)
    q = q.reshape(B, S, N_KV_HEADS, GQA_GROUP, HEAD_DIM)
    k = k.reshape(B, S, N_KV_HEADS, HEAD_DIM)
    v = v.reshape(B, S, N_KV_HEADS, HEAD_DIM)
    pos = jnp.arange(S, dtype=jnp.float32)
    inv_freq = ROPE_THETA ** (-jnp.arange(0, ROT_DIM, 2, dtype=jnp.float32) / ROT_DIM)
    ang = pos[:, None] * inv_freq[None, :]
    ang = jnp.concatenate([ang, ang], axis=-1)
    cos, sin = jnp.cos(ang).astype(x.dtype), jnp.sin(ang).astype(x.dtype)
    q = partial_rotary(q, cos[None, :, None, None, :], sin[None, :, None, None, :])
    k = partial_rotary(k, cos[None, :, None, :], sin[None, :, None, :])

    pad = ((0, 0), (BLOCK, BLOCK), (0, 0), (0, 0))
    kb = jnp.pad(k, pad).reshape(B, nb + 2, BLOCK, N_KV_HEADS, HEAD_DIM)
    vb = jnp.pad(v, pad).reshape(B, nb + 2, BLOCK, N_KV_HEADS, HEAD_DIM)
    k_band = jnp.concatenate([kb[:, :-2], kb[:, 1:-1], kb[:, 2:]], axis=2)
    v_band = jnp.concatenate([vb[:, :-2], vb[:, 1:-1], vb[:, 2:]], axis=2)
    qb = q.reshape(B, nb, BLOCK, N_KV_HEADS, GQA_GROUP, HEAD_DIM)

    s = jnp.einsum('bnqhgd,bnkhd->bnhgqk', qb, k_band).astype(jnp.float32) * (HEAD_DIM ** -0.5)
    blk = jnp.arange(nb)
    qpos = blk[:, None] * BLOCK + jnp.arange(BLOCK)[None, :]
    kpos = (blk[:, None] - 1) * BLOCK + jnp.arange(3 * BLOCK)[None, :]
    valid = ((jnp.abs(qpos[:, :, None] - kpos[:, None, :]) <= WINDOW)
             & (kpos[:, None, :] >= 0) & (kpos[:, None, :] < S))
    s = jnp.where(valid[None, :, None, None], s, -jnp.inf)
    sink_l = sink.astype(jnp.float32).reshape(N_KV_HEADS, GQA_GROUP)[None, None, :, :, None, None]
    m = jnp.maximum(jnp.max(s, axis=-1, keepdims=True), sink_l)
    p = jnp.exp(s - m)
    denom = jnp.sum(p, axis=-1, keepdims=True) + jnp.exp(sink_l - m)
    probs = (p / denom).astype(x.dtype)
    o = jnp.einsum('bnhgqk,bnkhd->bnqhgd', probs, v_band).reshape(B, S, D_MODEL)
    return o @ w_o

def _linear_combine(left, right):
    a1, b1 = left
    a2, b2 = right
    return a1 * a2, a2 * b1 + b2

def bidir_rglru_block(x, w_in, conv_w, conv_b, w_rgate, b_rgate, w_igate, b_igate, lam, w_out):
    B, S, _ = x.shape
    gate_br, xb = jnp.split(x @ w_in, 2, axis=-1)
    xp = jnp.pad(xb, ((0, 0), (CONV_LEFT, CONV_WIDTH - 1 - CONV_LEFT), (0, 0)))
    xc = conv_b
    for j in range(CONV_WIDTH):
        xc = xc + conv_w[j] * xp[:, j:j + S]
    xr = xc.reshape(B, S, LRU_BLOCKS, LRU_BLOCK_W)
    r = jax.nn.sigmoid(jnp.einsum('bsnc,zncf->zbsnf', xr, w_rgate).reshape(2, B, S, LRU_WIDTH).astype(jnp.float32)
                       + b_rgate.astype(jnp.float32)[:, None, None, :])
    i = jax.nn.sigmoid(jnp.einsum('bsnc,zncf->zbsnf', xr, w_igate).reshape(2, B, S, LRU_WIDTH).astype(jnp.float32)
                       + b_igate.astype(jnp.float32)[:, None, None, :])
    log_a = -LRU_C * r * jax.nn.softplus(-lam.astype(jnp.float32))[:, None, None, :]
    a = jnp.exp(log_a)
    mult = jnp.sqrt(-jnp.expm1(2.0 * log_a))
    t = jnp.arange(S)
    is_start = jnp.stack([t == 0, t == S - 1])
    mult = jnp.where(is_start[:, None, :, None], 1.0, mult)
    u = mult * i * xc.astype(jnp.float32)[None]
    _, h_f = lax.associative_scan(_linear_combine, (a[0], u[0]), axis=1)
    _, h_b = lax.associative_scan(_linear_combine, (a[1], u[1]), reverse=True, axis=1)
    h = (h_f + h_b).astype(x.dtype)
    return (h * jax.nn.gelu(gate_br)) @ w_out

def expert_choice_moe(x, w_router, w_gate_up, w_down):
    B, S, _ = x.shape
    cap = CAPACITY_FACTOR * S // N_EXPERTS_2
    aff = jax.nn.softmax((x @ w_router).astype(jnp.float32), axis=-1)
    gates, idx = lax.top_k(jnp.swapaxes(aff, 1, 2), cap)
    bi = jnp.arange(B)[:, None, None]
    xs = x[bi, idx]
    g, u = jnp.split(jnp.einsum('becd,edf->becf', xs, w_gate_up), 2, axis=-1)
    out = jnp.einsum('becf,efd->becd', jax.nn.silu(g) * u, w_down) * gates[..., None].astype(x.dtype)
    return jnp.zeros_like(x).at[bi, idx].add(out)

def second_inputs(seed: int = 0) -> dict:
    key = jax.random.key(seed)
    ks = jax.random.split(key, 24)
    f32 = jnp.float32
    nrm = lambda k, shape, scale: jax.random.normal(k, shape, f32) * scale
    qkv_out = (N_Q_HEADS + 2 * N_KV_HEADS) * HEAD_DIM
    a8 = jax.random.uniform(ks[11], (N_LRU_LAYERS, 2, LRU_WIDTH), f32, 0.9, 0.999)
    a_base = a8 ** (1.0 / LRU_C)
    lam = jnp.log(a_base) - jnp.log1p(-a_base)
    return {
        'x': jax.random.normal(ks[0], (BATCH, SEQ, D_MODEL), f32),
        'attn_w_qkv': nrm(ks[1], (N_ATTN_LAYERS, D_MODEL, qkv_out), D_MODEL ** -0.5),
        'attn_w_o': nrm(ks[2], (N_ATTN_LAYERS, D_MODEL, D_MODEL), BETA * D_MODEL ** -0.5),
        'attn_sink': nrm(ks[3], (N_ATTN_LAYERS, N_Q_HEADS), 0.5),
        'lru_w_in': nrm(ks[4], (N_LRU_LAYERS, D_MODEL, 2 * LRU_WIDTH), D_MODEL ** -0.5),
        'lru_conv_w': nrm(ks[5], (N_LRU_LAYERS, CONV_WIDTH, LRU_WIDTH), CONV_WIDTH ** -0.5),
        'lru_conv_b': nrm(ks[6], (N_LRU_LAYERS, LRU_WIDTH), 0.02),
        'lru_w_rgate': nrm(ks[7], (N_LRU_LAYERS, 2, LRU_BLOCKS, LRU_BLOCK_W, LRU_BLOCK_W), LRU_BLOCK_W ** -0.5),
        'lru_b_rgate': nrm(ks[8], (N_LRU_LAYERS, 2, LRU_WIDTH), 0.02),
        'lru_w_igate': nrm(ks[9], (N_LRU_LAYERS, 2, LRU_BLOCKS, LRU_BLOCK_W, LRU_BLOCK_W), LRU_BLOCK_W ** -0.5),
        'lru_b_igate': nrm(ks[10], (N_LRU_LAYERS, 2, LRU_WIDTH), 0.02),
        'lru_lambda': lam,
        'lru_w_out': nrm(ks[12], (N_LRU_LAYERS, LRU_WIDTH, D_MODEL), BETA * LRU_WIDTH ** -0.5),
        'moe_w_router': nrm(ks[13], (DEPTH_2, D_MODEL, N_EXPERTS_2), D_MODEL ** -0.5),
        'moe_w_gate_up': nrm(ks[14], (DEPTH_2, N_EXPERTS_2, D_MODEL, 2 * EXPERT_FF), D_MODEL ** -0.5),
        'moe_w_down': nrm(ks[15], (DEPTH_2, N_EXPERTS_2, EXPERT_FF, D_MODEL), BETA * EXPERT_FF ** -0.5),
        'ln_mix_g': 1.0 + nrm(ks[16], (DEPTH_2, D_MODEL), 0.02),
        'ln_mix_b': nrm(ks[17], (DEPTH_2, D_MODEL), 0.02),
        'ln_ffn_g': 1.0 + nrm(ks[18], (DEPTH_2, D_MODEL), 0.02),
        'ln_ffn_b': nrm(ks[19], (DEPTH_2, D_MODEL), 0.02),
    }

def second_block(x, attn_w_qkv, attn_w_o, attn_sink, lru_w_in, lru_conv_w, lru_conv_b,
              lru_w_rgate, lru_b_rgate, lru_w_igate, lru_b_igate, lru_lambda, lru_w_out,
              moe_w_router, moe_w_gate_up, moe_w_down, ln_mix_g, ln_mix_b, ln_ffn_g, ln_ffn_b):
    for layer in range(DEPTH_2):
        j = layer // N_MIXERS
        if layer % N_MIXERS == 0:
            mix = windowed_gqa_sink(x, attn_w_qkv[j], attn_w_o[j], attn_sink[j])
        else:
            mix = bidir_rglru_block(x, lru_w_in[j], lru_conv_w[j], lru_conv_b[j],
                                    lru_w_rgate[j], lru_b_rgate[j], lru_w_igate[j], lru_b_igate[j],
                                    lru_lambda[j], lru_w_out[j])
        x = layer_norm(ALPHA * x + mix, ln_mix_g[layer], ln_mix_b[layer])
        ffn = expert_choice_moe(x, moe_w_router[layer], moe_w_gate_up[layer], moe_w_down[layer])
        x = layer_norm(ALPHA * x + ffn, ln_ffn_g[layer], ln_ffn_b[layer])
    return x


def setup_inputs(seed=0):
    out = dict(first_inputs(seed))
    for name, value in second_inputs(seed + 1).items():
        if name != "x":
            out[name + "_2"] = value
    return out


def reference(
    x, norm_mix_g, w_in, q_norm_g, kv_norm_g, w_uq, w_ukv, w_br_mla, mu_prev, mu_next, w0, w_up,
    a0, a_up, g_up, k_k, k_a, r_k, lnx_g, lnx_b, w_br_rwkv, gate_b, w_out, norm_ffn_g,
    router_group_w, router_group_b, router_expert_w, router_expert_b, w1, w3, w2, norm_final_g,
    attn_w_qkv_2, attn_w_o_2, attn_sink_2, lru_w_in_2, lru_conv_w_2, lru_conv_b_2,
    lru_w_rgate_2, lru_b_rgate_2, lru_w_igate_2, lru_b_igate_2, lru_lambda_2, lru_w_out_2,
    moe_w_router_2, moe_w_gate_up_2, moe_w_down_2, ln_mix_g_2, ln_mix_b_2, ln_ffn_g_2,
    ln_ffn_b_2,
):
    x = first_block(
        x, norm_mix_g, w_in, q_norm_g, kv_norm_g, w_uq, w_ukv, w_br_mla, mu_prev, mu_next, w0,
        w_up, a0, a_up, g_up, k_k, k_a, r_k, lnx_g, lnx_b, w_br_rwkv, gate_b, w_out, norm_ffn_g,
        router_group_w, router_group_b, router_expert_w, router_expert_b, w1, w3, w2,
        norm_final_g,
    )
    return second_block(
        x, attn_w_qkv_2, attn_w_o_2, attn_sink_2, lru_w_in_2, lru_conv_w_2, lru_conv_b_2,
        lru_w_rgate_2, lru_b_rgate_2, lru_w_igate_2, lru_b_igate_2, lru_lambda_2, lru_w_out_2,
        moe_w_router_2, moe_w_gate_up_2, moe_w_down_2, ln_mix_g_2, ln_mix_b_2, ln_ffn_g_2,
        ln_ffn_b_2,
    )


_drawn_inputs = setup_inputs


def setup_inputs(seed=0):
    import zlib

    import numpy as np

    out = dict(_drawn_inputs(seed))
    spreads = {}
    factors = {'q_norm_g': 8.0,
     'kv_norm_g': 8.0,
     'k_k': 62.824,
     'lnx_g': 29.592,
     'lnx_b': 29.685,
     'gate_b': 8.0,
     'router_group_b': 23.763,
     'router_expert_b': 27.484,
     'attn_sink_2': 64.0,
     'lru_b_rgate_2': 56.771,
     'lru_b_igate_2': 33.373,
     'w_up': 3.797,
     'a0': 4.512,
     'k_a': 6.872,
     'r_k': 3.189,
     'norm_ffn_g': 6.366}
    for name, (base, spread) in spreads.items():
        noise = np.random.default_rng([zlib.crc32(name.encode()), seed]).standard_normal(out[name].shape)
        drawn = base * np.exp(spread * noise) if base else spread * noise
        out[name] = __import__('jax').numpy.asarray(drawn.astype(out[name].dtype))
    for name, factor in factors.items():
        out[name] = (out[name] * factor).astype(out[name].dtype)
    return out
```

```python
from contextlib import ExitStack

import concourse.bass as bass
import numpy as np
from concourse import mybir

ALU = mybir.AluOpType
ACT = mybir.ActivationFunctionType
F32 = mybir.dt.float32
U32 = mybir.dt.uint32
AX_X = mybir.AxisListType.X
ds = bass.ds

P = 128
T = 1024
NT = T // P
D = 1024
KD = D // P
HALF = 512


def now(i, n=1, k=None):
    return (i + 1) * n + (n if k is None else k)


def last(i, n=1, k=None):
    return i * n + (n if k is None else k)


class Engine:

    def __init__(self, eng, chain, pace):
        self.eng, self.chain, self.pace = eng, chain, pace
        self.turn, self.per, self.steps, self.base = 0, 0, 0, 0

    def hold(self, sem, value):
        self.eng.wait_ge(sem, value)
        if not isinstance(value, int):
            self.eng.sem_inc(self.pace, 1)

    def link(self, instruction):
        self.steps += 1
        instruction.then_inc(self.chain, 1)
        self.hold(self.chain, self.turn * self.per + self.base + self.steps)

    def loop(self, turn, per):
        self.base += self.steps
        self.turn, self.per, self.steps = turn, per, 0

    def open(self, *sems, n=1):
        for s in sems:
            self.eng.sem_inc(s, n)

    def done(self, turns):
        assert self.steps == self.per, (self.chain.name, self.steps)
        self.base += turns * self.per
        self.turn, self.per, self.steps = 0, 0, 0


class Phase:

    def __init__(self, nc, name):
        self.nc, self.name, self.ctx, self.sems = nc, name, ExitStack(), []

    def __enter__(self):
        return self

    def __exit__(self, *a):
        self.ctx.close()
        if self.sems:
            self.nc.clear_and_free_semaphores(self.sems)
            self.nc.all_engine_barrier()

    def sb(self, name, shape, dt=F32):
        return self.ctx.enter_context(self.nc.sbuf_tensor(f"{self.name}_{name}", shape, dt))

    def ps(self, name, shape):
        return self.ctx.enter_context(self.nc.psum_tensor(f"{self.name}_{name}", shape, F32))

    def sem(self, name):
        self.sems.append(self.nc.alloc_semaphore(name=f"{self.name}_{name}"))
        return self.sems[-1]

    def engine(self, eng, name):
        return Engine(eng, self.sem(f"{name}_chain"), self.sem(f"{name}_pace"))


MLA_H, QK_NOPE, QK_ROPE, V_DIM, Q_LORA, KV_LORA = 8, 64, 32, 64, 384, 256
QK = QK_NOPE + QK_ROPE
MLA_IN = Q_LORA + KV_LORA + QK_ROPE
NORM_EPS = 1e-6


VECS = dict(norm_mix_g=8, q_norm_g=3, kv_norm_g=2, mu_prev=15, mu_next=15, w0=8, a0=8, k_k=4, k_a=4, r_k=4, lnx_g=4,
            lnx_b=4, gate_b=16, norm_ffn_g=8, lru_conv_w_2=32, lru_conv_b_2=8, lru_b_rgate_2=16, lru_b_igate_2=16,
            lru_lambda_2=16)
VEC_N = sum(VECS.values())


def vec_at(name):
    names = list(VECS)
    at = sum(VECS[n] for n in names[:names.index(name)])
    return at, at + VECS[name]


def mla_tables():
    pos = np.arange(T, dtype=np.float32)
    inv = np.float32(10000.0) ** (-np.arange(0, QK_ROPE, 2, dtype=np.float32) / QK_ROPE)
    ang = (pos[:, None] * inv[None, :]).astype(np.float32)
    t = np.concatenate([np.cos(ang), np.sin(ang)], axis=1).astype(np.float32)
    return np.ascontiguousarray(t.reshape(NT, P, QK_ROPE).transpose(1, 0, 2))


def mla_phase(nc, x, vecs, w_in, w_uq, w_ukv, eye, rope, hT_dram, oT_dram):
    with Phase(nc, "mla") as ph:
        ident = ph.sb("ident", [P, P])
        q_all = ph.sb("qT", [QK, MLA_H, T])
        k_all = ph.sb("kT", [QK, MLA_H, T])
        v_all = ph.sb("v", [P, NT, MLA_H * V_DIM])
        with ExitStack() as one:
            proj = Phase(nc, "mlap")
            one.enter_context(proj)
            mla_project(nc, proj, x, vecs, w_in, w_uq, w_ukv, eye, rope, hT_dram,
                        ident, q_all, k_all, v_all)
        with ExitStack() as two:
            att = Phase(nc, "mlaa")
            two.enter_context(att)
            mla_attend(nc, att, ident, q_all, k_all, v_all, oT_dram)



def mla_project(nc, ph, x, vecs, w_in, w_uq, w_ukv, eye, rope, hT_dram,
                ident, q_all, k_all, v_all):
    NC = (Q_LORA + KV_LORA) // P
    w_z = ph.sb("w_z", [P, KD, MLA_IN])
    w_q = ph.sb("w_q", [P, Q_LORA // P, MLA_H * QK])
    w_kv = ph.sb("w_kv", [P, KV_LORA // P, MLA_H * P])
    tab = ph.sb("tab", [P, NT, QK_ROPE])
    vec = ph.sb("vec", [P, VEC_N])
    g_h = vec[:, slice(*vec_at("norm_mix_g"))]
    g_c = vec[:, vec_at("q_norm_g")[0]:vec_at("kv_norm_g")[1]]
    xt = ph.sb("xt", [P, D])
    junk = ph.sb("junk", [P, D])
    h = ph.sb("h", [P, D])
    hT = ph.sb("hT", [P, KD, P])
    ssq = ph.sb("ssq", [P, 4])
    ms = ph.sb("ms", [P, 4])
    root = ph.sb("root", [P, 4])
    rstd = ph.sb("rstd", [P, 4])
    c = ph.sb("c", [P, NC * P])
    cT = ph.sb("cT", [P, NC, P])
    krope = ph.sb("krope", [P, QK_ROPE])
    krot = ph.sb("krot", [P, QK_ROPE])
    qcat = ph.sb("qcat", [P, MLA_H, QK])
    kcat = ph.sb("kcat", [P, MLA_H, QK])
    qr = ph.sb("qr", [P, 4, MLA_H, 16])
    kr = ph.sb("kr", [P, 4, 16])

    pT = ph.ps("pT", [P, 2, HALF])
    pZ = ph.ps("pZ", [P, 2, HALF])
    pQ = ph.ps("pQ", [P, 2, HALF])
    pK = ph.ps("pK", [P, 2, HALF])

    names = ("x_in x_sq ms_h rt_h h_ready hT_psum hT_ready hT_out z_psum sq_c ms_c rt_c c_ready cT_psum cT_ready q_psum "
             "kv_psum qcat_ready kcat_ready qT_psum kT_psum qT_kept kT_kept v_kept").split()
    (x_in, x_sq, ms_h, rt_h, h_ready, hT_psum, hT_ready, hT_out, z_psum, sq_c, ms_c, rt_c, c_ready, cT_psum, cT_ready, q_psum,
     kv_psum, qcat_ready, kcat_ready, qT_psum, kT_psum, qT_kept, kT_kept, v_kept) = [ph.sem(n) for n in names]
    consts = ph.sem("consts")
    V, G, A, E, S = (ph.engine(e, n) for e, n in ((nc.vector, "dve"), (nc.gpsimd, "pool"), (nc.scalar, "act"),
                                                  (nc.tensor, "pe"), (nc.sync, "sp")))
    hT_view = hT_dram.rearrange("(k p) t -> p k t", p=P)

    with nc.Block() as block:

        @block.sync
        def _(sp):
            S.open(x_in, hT_out, n=16)
            for out, src in (
                (ident[:, :], eye), (vec[:, :], vecs),
                (w_z[:, :, :], w_in[0, :, 0:MLA_IN].rearrange("(k p) n -> p k n", p=P)),
                (w_q[:, :, :], w_uq[0].rearrange("(k p) n -> p k n", p=P)),
                (w_kv[:, :, :], w_ukv[0].rearrange("(k p) n -> p k n", p=P)),
                (tab[:, :, :], rope),
            ):
                sp.dma_start(out, src).then_inc(consts, 16)
            with sp.Fori(0, NT) as i:
                S.hold(x_sq, last(i))
                S.hold(h_ready, last(i))
                sp.dma_start(xt[:, :], x[ds(i * P, P), :]).then_inc(x_in, 16)
                S.hold(hT_ready, now(i))
                sp.dma_start(hT_view[:, :, ds(i * P, P)], hT[:, :, :]).then_inc(hT_out, 16)
            sp.wait_ge(hT_out, (NT + 1) * 16)

        @block.scalar
        def _(act):
            A.open(x_sq, rt_h, sq_c, rt_c, v_kept)
            act.wait_ge(consts, 6 * 16)
            with act.Fori(0, NT) as i:
                A.hold(x_in, now(i, 16))
                nc.scalar.activation(junk[:, :], xt[:, :], ACT.Square, accum_out=ssq[:, 0:1]).then_inc(x_sq, 1)
                A.hold(ms_h, now(i))
                nc.scalar.activation(root[:, 0:1], ms[:, 0:1], ACT.Sqrt).then_inc(rt_h, 1)
                A.hold(z_psum, now(i))
                A.hold(x_sq, now(i))
                nc.scalar.activation(junk[:, 0:Q_LORA], pZ[:, 0, 0:Q_LORA], ACT.Square, accum_out=ssq[:, 1:2])
                nc.scalar.activation(junk[:, Q_LORA:Q_LORA + KV_LORA], pZ[:, 1, 0:KV_LORA], ACT.Square,
                                     accum_out=ssq[:, 2:3]).then_inc(sq_c, 1)
                A.hold(ms_c, now(i))
                nc.scalar.activation(root[:, 1:3], ms[:, 1:3], ACT.Sqrt).then_inc(rt_c, 1)
                A.hold(kcat_ready, now(i))
                for b in range(2):
                    vb = nc.scalar.copy(v_all[:, ds(i, 1), b * 256:b * 256 + 256].rearrange("p o (h d) -> p (o h) d", h=4),
                                        pK[:, b, :].rearrange("p (h d) -> p h d", h=4)[:, :, QK_NOPE:P])
                vb.then_inc(v_kept, 1)

        @block.vector
        def _(dve):
            V.open(ms_h, ms_c, h_ready, hT_ready, c_ready, cT_ready, qcat_ready, kcat_ready, qT_kept, kT_kept)
            dve.wait_ge(consts, 6 * 16)

            def rotate(out1, out2, x1, x2, co, si, r):
                nc.vector.tensor_tensor(r[0], x1, co, ALU.mult)
                nc.vector.tensor_tensor(r[1], x2, si, ALU.mult)
                nc.vector.tensor_tensor(r[2], x1, si, ALU.mult)
                V.link(nc.vector.tensor_tensor(r[3], x2, co, ALU.mult))
                nc.vector.tensor_tensor(out1, r[0], r[1], ALU.subtract)
                return nc.vector.tensor_tensor(out2, r[2], r[3], ALU.add)

            with dve.Fori(0, NT) as i:
                V.loop(i, 7)
                V.hold(x_sq, now(i))
                nc.vector.tensor_scalar(ms[:, 0:1], ssq[:, 0:1], 1.0 / D, NORM_EPS, ALU.mult, ALU.add).then_inc(ms_h, 1)
                V.hold(rt_h, now(i))
                V.link(nc.vector.reciprocal(rstd[:, 0:1], root[:, 0:1]))
                V.hold(hT_psum, last(i))
                nc.vector.tensor_scalar(h[:, :], xt[:, :], rstd[:, 0:1], None, ALU.mult).then_inc(h_ready, 1)
                V.hold(z_psum, last(i))
                V.hold(hT_out, last(i, 16))
                V.hold(hT_psum, now(i))
                nc.vector.tensor_tensor(hT[:, :, :].rearrange("p (b k) t -> p b k t", b=2),
                                        pT[:, :, :].rearrange("p b (k t) -> p b k t", k=4),
                                        g_h[:, :].rearrange("p (b k) -> p b k", b=2).unsqueeze(3).to_broadcast([P, 2, 4, P]),
                                        ALU.mult).then_inc(hT_ready, 1)
                V.hold(sq_c, now(i))
                nc.vector.tensor_scalar(ms[:, 1:2], ssq[:, 1:2], 1.0 / Q_LORA, NORM_EPS, ALU.mult, ALU.add)
                nc.vector.tensor_scalar(ms[:, 2:3], ssq[:, 2:3], 1.0 / KV_LORA, NORM_EPS, ALU.mult, ALU.add).then_inc(ms_c, 1)
                V.hold(rt_c, now(i))
                V.link(nc.vector.reciprocal(rstd[:, 1:3], root[:, 1:3]))
                nc.vector.tensor_scalar(c[:, 0:Q_LORA], pZ[:, 0, 0:Q_LORA], rstd[:, 1:2], None, ALU.mult)
                V.link(nc.vector.tensor_copy(krope[:, :], pZ[:, 1, KV_LORA:KV_LORA + QK_ROPE]))
                nc.vector.tensor_scalar(c[:, Q_LORA:NC * P], pZ[:, 1, 0:KV_LORA], rstd[:, 2:3], None, ALU.mult).then_inc(c_ready, 1)
                co, si = tab[:, ds(i, 1), 0:16], tab[:, ds(i, 1), 16:32]
                V.link(rotate(krot[:, 0:16], krot[:, 16:32], krope[:, 0:16], krope[:, 16:32],
                              co.rearrange("p o d -> p (o d)"), si.rearrange("p o d -> p (o d)"),
                              [kr[:, n, :] for n in range(4)]))
                V.hold(cT_psum, now(i))
                nc.vector.tensor_tensor(cT[:, 0:4, :], pT[:, 0, :].rearrange("p (k t) -> p k t", k=4),
                                        g_c[:, 0:4].unsqueeze(2).to_broadcast([P, 4, P]), ALU.mult)
                nc.vector.tensor_scalar(cT[:, 4, :], pT[:, 1, 0:P], g_c[:, 4:5], None, ALU.mult).then_inc(cT_ready, 1)
                V.hold(q_psum, now(i))
                for b in range(2):
                    src = pQ[:, b, 0:4 * QK].rearrange("p (h d) -> p h d", h=4)
                    hs = slice(4 * b, 4 * b + 4)
                    nc.vector.tensor_copy(qcat[:, hs, 0:QK_NOPE], src[:, :, 0:QK_NOPE])
                    done = rotate(qcat[:, hs, 64:80], qcat[:, hs, 80:96], src[:, :, 64:80], src[:, :, 80:96],
                                  co.to_broadcast([P, 4, 16]), si.to_broadcast([P, 4, 16]),
                                  [qr[:, n, hs, :] for n in range(4)])
                done.then_inc(qcat_ready, 1)
                V.hold(kv_psum, now(i))
                for b in range(2):
                    nc.vector.tensor_copy(kcat[:, 4 * b:4 * b + 4, 0:QK_NOPE],
                                          pK[:, b, :].rearrange("p (h d) -> p h d", h=4)[:, :, 0:QK_NOPE])
                nc.vector.tensor_copy(kcat[:, :, QK_NOPE:QK], krot[:, :].unsqueeze(1).to_broadcast([P, MLA_H, QK_ROPE])).then_inc(kcat_ready, 1)
                V.hold(qT_psum, now(i))
                for b in range(2):
                    kept = nc.vector.tensor_copy(q_all[:, 4 * b:4 * b + 4, ds(i * P, P)],
                                                 pT[0:QK, b, :].rearrange("p (h t) -> p h t", h=4))
                kept.then_inc(qT_kept, 1)
                V.hold(kT_psum, now(i))
                for b in range(2):
                    kept = nc.vector.tensor_copy(k_all[:, 4 * b:4 * b + 4, ds(i * P, P)],
                                                 pZ[0:QK, b, :].rearrange("p (h t) -> p h t", h=4))
                kept.then_inc(kT_kept, 1)
            V.done(NT)

        @block.tensor
        def _(pe):
            E.open(hT_psum, z_psum, cT_psum, q_psum, kv_psum, qT_psum, kT_psum)
            pe.wait_ge(consts, 6 * 16)
            with pe.Fori(0, NT) as i:
                E.hold(h_ready, now(i))
                E.hold(qT_kept, last(i))
                for k in range(KD):
                    t = nc.tensor.transpose(pT[:, k // 4, k % 4 * P:k % 4 * P + P], h[:, k * P:k * P + P], ident[:, :])
                t.then_inc(hT_psum, 1)
                E.hold(hT_ready, now(i))
                E.hold(kT_kept, last(i))
                for o, lo, n in ((0, 0, Q_LORA), (1, Q_LORA, MLA_IN - Q_LORA)):
                    for k in range(KD):
                        m = nc.tensor.matmul(pZ[:, o, 0:n], hT[:, k, :], w_z[:, k, lo:lo + n], start=k == 0, stop=k == KD - 1)
                m.then_inc(z_psum, 1)
                E.hold(c_ready, now(i))
                for k in range(NC):
                    t = nc.tensor.transpose(pT[:, k // 4, k % 4 * P:k % 4 * P + P], c[:, k * P:k * P + P], ident[:, :])
                t.then_inc(cT_psum, 1)
                E.hold(cT_ready, now(i))
                E.hold(qcat_ready, last(i))
                for o in range(2):
                    for k in range(3):
                        m = nc.tensor.matmul(pQ[:, o, 0:4 * QK], cT[:, k, :], w_q[:, k, o * 4 * QK:(o + 1) * 4 * QK], start=k == 0, stop=k == 2)
                m.then_inc(q_psum, 1)
                E.hold(kcat_ready, last(i))
                E.hold(v_kept, last(i))
                for o in range(2):
                    for k in range(2):
                        m = nc.tensor.matmul(pK[:, o, :], cT[:, 3 + k, :], w_kv[:, k, o * HALF:(o + 1) * HALF], start=k == 0, stop=k == 1)
                m.then_inc(kv_psum, 1)
                E.hold(qcat_ready, now(i))
                for n in range(MLA_H):
                    t = nc.tensor.transpose(pT[0:QK, n // 4, n % 4 * P:n % 4 * P + P], qcat[:, n, :], ident[:, :])
                t.then_inc(qT_psum, 1)
                E.hold(kcat_ready, now(i))
                for n in range(MLA_H):
                    t = nc.tensor.transpose(pZ[0:QK, n // 4, n % 4 * P:n % 4 * P + P], kcat[:, n, :], ident[:, :])
                t.then_inc(kT_psum, 1)


def mla_attend(nc, ph, ident, q_all, k_all, v_all, oT_dram):
    H = MLA_H
    SCALE = float(QK) ** -0.5
    q_t = ph.sb("q_t", [QK, H, P])
    probs = ph.sb("probs", [P, 2, T])
    pT_sb = ph.sb("probsT", [P, 2, NT, P])
    mx = ph.sb("mx", [P, H])
    nmx = ph.sb("nmx", [P, H])
    den = ph.sb("den", [P, H])
    rden = ph.sb("rden", [P, H])
    o = ph.sb("o", [P, H * V_DIM])
    oT = ph.sb("oT", [P, 4, P])
    pS = ph.ps("pS", [P, 4, HALF])
    pP = ph.ps("pP", [P, 2, HALF])
    pO = ph.ps("pO", [P, HALF])
    pOT = ph.ps("pOT", [P, HALF])
    names = "q_in s_psum max_ready exp_done pT_psum pT_v pT_a o_psum o_ready oT_psum oT_ready oT_out".split()
    q_in, s_psum, max_ready, exp_done, pT_psum, pT_v, pT_a, o_psum, o_ready, oT_psum, oT_ready, oT_out = [ph.sem(n) for n in names]
    V, G, A, E, S = (ph.engine(e, n) for e, n in ((nc.vector, "dve"), (nc.gpsimd, "pool"), (nc.scalar, "act"),
                                                  (nc.tensor, "pe"), (nc.sync, "sp")))
    oT_view = oT_dram.rearrange("(k p) t -> p k t", p=P)

    with nc.Block() as block:

        @block.gpsimd
        def _(pool):
            G.open(q_in, n=H)
            with pool.Fori(0, NT) as i:
                for h in range(H):
                    G.hold(s_psum, last(i, H, h + 1))
                    nc.gpsimd.tensor_copy(q_t[:, h, :], q_all[:, h, ds(i * P, P)]).then_inc(q_in, 1)

        @block.tensor
        def _(pe):
            E.open(s_psum, pT_psum, o_psum, n=H)
            E.open(oT_psum)

            def scores(h, i):
                E.hold(q_in, now(i, H, h + 1))
                E.hold(exp_done, now(i, H, h - 1) if h >= 2 else last(i, H, H + h - 1))
                for j in range(2):
                    m = nc.tensor.matmul(pS[:, h % 2 * 2 + j, :], q_t[:, h, :], k_all[:, h, j * HALF:(j + 1) * HALF], start=True, stop=True)
                m.then_inc(s_psum, 1)

            with pe.Fori(0, NT) as i:
                scores(0, i)
                for h in range(H):
                    if h + 1 < H:
                        scores(h + 1, i)
                    E.hold(exp_done, now(i, H, h + 1))
                    E.hold(pT_v, now(i, H, h) if h else last(i, H))
                    E.hold(pT_a, now(i, H, h) if h else last(i, H))
                    for k in range(NT):
                        t = nc.tensor.transpose(pP[:, k // 4, k % 4 * P:k % 4 * P + P], probs[:, h % 2, k * P:k * P + P], ident[:, :])
                    t.then_inc(pT_psum, 1)
                    if h == 0:
                        E.hold(o_ready, last(i))
                    E.hold(pT_v, now(i, H, h + 1))
                    E.hold(pT_a, now(i, H, h + 1))
                    for k in range(NT):
                        m = nc.tensor.matmul(pO[:, h * V_DIM:(h + 1) * V_DIM], pT_sb[:, h % 2, k, :],
                                             v_all[:, k, h * V_DIM:(h + 1) * V_DIM], start=k == 0, stop=k == NT - 1)
                    m.then_inc(o_psum, 1)
                E.hold(o_ready, now(i))
                E.hold(oT_ready, last(i))
                for k in range(4):
                    t = nc.tensor.transpose(pOT[:, k * P:k * P + P], o[:, k * P:k * P + P], ident[:, :])
                t.then_inc(oT_psum, 1)

        @block.vector
        def _(dve):
            V.open(max_ready, pT_v, n=H)
            V.open(o_ready, oT_ready)
            with dve.Fori(0, NT) as i:
                V.loop(i, H + 1)
                for h in range(H + 1):
                    if h < H:
                        V.hold(s_psum, now(i, H, h + 1))
                        if h == 0:
                            V.hold(exp_done, last(i, H))
                        V.link(nc.vector.reduce_max(mx[:, h:h + 1], pS[:, h % 2 * 2:h % 2 * 2 + 2, :], mybir.AxisListType.XY))
                        nc.vector.tensor_scalar(nmx[:, h:h + 1], mx[:, h:h + 1], -SCALE, None, ALU.mult).then_inc(max_ready, 1)
                    if h:
                        V.hold(pT_psum, now(i, H, h))
                        V.hold(o_psum, now(i, H, h - 2) if h > 2 else last(i, H, H + h - 2))
                        nc.vector.tensor_copy(pT_sb[:, (h - 1) % 2, 0:4, :], pP[:, 0, :].rearrange("p (k t) -> p k t", k=4)).then_inc(pT_v, 1)
                V.link(nc.vector.reciprocal(rden[:, :], den[:, :]))
                V.hold(o_psum, now(i, H))
                V.hold(oT_psum, last(i))
                nc.vector.tensor_tensor(o[:, :].rearrange("p (h d) -> p h d", h=H), pO[:, :].rearrange("p (h d) -> p h d", h=H),
                                        rden[:, :].unsqueeze(2).to_broadcast([P, H, V_DIM]), ALU.mult).then_inc(o_ready, 1)
                V.hold(oT_psum, now(i))
                V.hold(oT_out, last(i, 16))
                nc.vector.tensor_copy(oT[:, :, :], pOT[:, :].rearrange("p (k t) -> p k t", k=4)).then_inc(oT_ready, 1)
            V.done(NT)

        @block.scalar
        def _(act):
            A.open(exp_done, pT_a, n=H)
            with act.Fori(0, NT) as i:
                for h in range(H + 1):
                    if h < H:
                        A.hold(max_ready, now(i, H, h + 1))
                        A.hold(pT_psum, now(i, H, h - 1) if h >= 2 else last(i, H, H + h - 1))
                        if h == 0:
                            A.hold(o_ready, last(i))
                        nc.scalar.activation(probs[:, h % 2, :], pS[:, h % 2 * 2:h % 2 * 2 + 2, :], ACT.Exp,
                                             bias=nmx[:, h:h + 1], scale=SCALE, accum_out=den[:, h:h + 1]).then_inc(exp_done, 1)
                    if h:
                        A.hold(pT_psum, now(i, H, h))
                        A.hold(o_psum, now(i, H, h - 2) if h > 2 else last(i, H, H + h - 2))
                        nc.scalar.copy(pT_sb[:, (h - 1) % 2, 4:8, :], pP[:, 1, :].rearrange("p (k t) -> p k t", k=4)).then_inc(pT_a, 1)

        @block.sync
        def _(sp):
            S.open(oT_out, n=16)
            with sp.Fori(0, NT) as i:
                S.hold(oT_ready, now(i))
                sp.dma_start(oT_view[:, :, ds(i * P, P)], oT[:, :, :]).then_inc(oT_out, 16)
            sp.wait_ge(oT_out, (NT + 1) * 16)



RC = 512
RJ = RC // P
C = 64
NCH = T // C
W_SCALE = float(np.exp(np.float32(-0.5)))
ARR = dict(r=0, v=1, nkk=2, b0=3, b1=4, kd0=5, kd1=6, L0=7, L1=8, g=9, bonus=10)
RWKV_TILES = 15


def shift_phase(nc, vecs, w_in, hT_dram, zf_dram):
    with Phase(nc, "shift") as ph:
        hT = ph.sb("hT", [P, KD, T])
        U = 3
        w = ph.sb("w", [P, U, KD, P])
        zf = ph.sb("zf", [P, U, T])
        vec = ph.sb("vec", [P, VEC_N])
        keep = ph.sb("keep", [P, RWKV_TILES])
        pz = ph.ps("pz", [P, U, T])
        names = "z_psum kept shifted zf_out".split()
        z_psum, kept, shifted, zf_out = [ph.sem(n) for n in names]
        w_in_u = [ph.sem(f"w_in{u}") for u in range(U)]
        consts = ph.sem("consts")
        keep_v = ph.sem("keep_v")
        V, A, E, S = (ph.engine(e, n) for e, n in ((nc.vector, "dve"), (nc.scalar, "act"), (nc.tensor, "pe"), (nc.sync, "sp")))
        mp, mn = vec_at("mu_prev")[0], vec_at("mu_next")[0]
        w_view = w_in[0].rearrange("(k p) n -> p k n", p=P)
        zf_view = zf_dram.rearrange("(k p) t -> p k t", p=P)

        with nc.Block() as block:

            @block.sync
            def _(sp):
                for u in range(U):
                    S.open(w_in_u[u], n=16)
                sp.dma_start(vec[:, :], vecs).then_inc(consts, 16)
                for k in range(KD):
                    sp.dma_start(hT[:, k, :], hT_dram[k * P:(k + 1) * P, :]).then_inc(consts, 16)
                with sp.Fori(0, RWKV_TILES // U) as i:
                    for u in range(U):
                        S.hold(z_psum, last(i, U, u + 1))
                        sp.dma_start(w[:, u, :, :], w_view[:, :, ds(i * (U * P) + (MLA_IN + u * P), P)]).then_inc(w_in_u[u], 16)

            @block.tensor
            def _(pe):
                E.open(z_psum, n=U)
                pe.wait_ge(consts, (1 + KD) * 16)
                with pe.Fori(0, RWKV_TILES // U) as i:
                    for u in range(U):
                        E.hold(w_in_u[u], now(i, 16))
                        E.hold(shifted, last(i, U, u + 1))
                        for half in range(2):
                            for k in range(KD):
                                m = nc.tensor.matmul(pz[:, u, half * HALF:(half + 1) * HALF], w[:, u, k, :],
                                                     hT[:, k, half * HALF:(half + 1) * HALF], start=k == 0, stop=k == KD - 1)
                        m.then_inc(z_psum, 1)

            @block.scalar
            def _(act):
                A.open(kept, n=U)
                A.open(zf_out, n=16 * U)
                act.wait_ge(keep_v, 1)
                with act.Fori(0, RWKV_TILES // U) as i:
                    for u in range(U):
                        A.hold(z_psum, now(i, U, u + 1))
                        A.hold(zf_out, last(i, 16 * U))
                        nc.scalar.activation(zf[:, u, :], pz[:, u, :], ACT.Copy, scale=keep[:, ds(i * U + u, 1)]).then_inc(kept, 1)
                    for u in range(U):
                        A.hold(shifted, now(i, U, u + 1))
                        act.dma_start(zf_view[:, ds(i * U + u, 1), :], zf[:, u:u + 1, :]).then_inc(zf_out, 16)
                act.wait_ge(zf_out, 16 * (RWKV_TILES + U))

            @block.vector
            def _(dve):
                V.open(shifted, n=U)
                dve.wait_ge(consts, (1 + KD) * 16)
                V.link(nc.vector.tensor_tensor(keep[:, :], vec[:, mp:mp + RWKV_TILES], vec[:, mn:mn + RWKV_TILES], ALU.add))
                V.link(nc.vector.tensor_scalar(keep[:, :], keep[:, :], -1.0, 1.0, ALU.mult, ALU.add))
                dve.sem_inc(keep_v, 1)
                with dve.Fori(0, RWKV_TILES // U) as i:
                    V.loop(i, U)
                    for u in range(U):
                        V.hold(kept, now(i, U, u + 1))
                        V.link(nc.vector.scalar_tensor_tensor(zf[:, u, 1:T], pz[:, u, 0:T - 1], vec[:, ds(i * U + (mp + u), 1)],
                                                              zf[:, u, 1:T], ALU.mult, ALU.add))
                        nc.vector.scalar_tensor_tensor(zf[:, u, 0:T - 1], pz[:, u, 1:T], vec[:, ds(i * U + (mn + u), 1)],
                                                       zf[:, u, 0:T - 1], ALU.mult, ALU.add).then_inc(shifted, 1)
                V.done(RWKV_TILES // U)


def prep_tables():
    t = np.arange(T)
    starts = np.stack([(t % C != 0), (t % C != C - 1)]).astype(np.float32)
    q = np.arange(P) // 64
    return np.ascontiguousarray(np.broadcast_to(starts, (P, 2, T))), (q[:, None] == q[None, :]).astype(np.float32)


def prep_phase(nc, vecs, w_up, a_up, g_up, zf_dram, starts, head_ones, arr_dram):
    with Phase(nc, "prep") as ph:
        vec = ph.sb("vec", [P, VEC_N])
        ups = ph.sb("ups", [P, 3, RC])
        up = ph.sb("up", [P, 3, P])
        go = ph.sb("go", [P, 2, T])
        ones = ph.sb("ones", [P, P])
        low = ph.sb("low", [P, 3, T])
        rkv = ph.sb("rkv", [P, 3, T])
        a = ph.sb("a", [P, 2, T])
        s = ph.sb("s", [P, 2, T])
        t1 = ph.sb("t1", [P, T])
        t2 = ph.sb("t2", [P, T])
        nrm = ph.sb("nrm", [P, T])
        kmix = ph.sb("kmix", [P, 2, T])
        onek = ph.sb("onek", [P, RJ])
        out = ph.sb("out", [P, 9, T])
        pw = [ph.ps(f"pw{n}", [P, T]) for n in range(4)]
        names = "up_ready z_in z_free sq_ready ss_psum nrm_a g_psum g_a w_psum w_a a_psum a_a nkk_v d_done bt_ready bonus_psum bonus_v arr_out".split()
        (up_ready, z_in, z_free, sq_ready, ss_psum, nrm_a, g_psum, g_a, w_psum, w_a, a_psum, a_a, nkk_v, d_done, bt_ready,
         bonus_psum, bonus_v, arr_out) = [ph.sem(n) for n in names]
        consts = ph.sem("consts")
        low_a = ph.sem("low_a")
        V, G, A, E, S = (ph.engine(e, n) for e, n in ((nc.vector, "dve"), (nc.gpsimd, "pool"), (nc.scalar, "act"),
                                                      (nc.tensor, "pe"), (nc.sync, "sp")))
        at = lambda n: vec_at(n)[0]
        zf_view = zf_dram.rearrange("(k p) t -> p k t", p=P)
        arr_view = arr_dram.rearrange("a (k p) t -> p a k t", p=P)
        OUT = ["nkk", "b0", "b1", "kd0", "kd1", "L0", "L1", "g", "bonus"]

        with nc.Block() as block:

            @block.sync
            def _(sp):
                S.open(z_in, n=16)
                S.open(arr_out, n=16 * 11)
                for dst, src in ((vec[:, :], vecs), (go[:, :, :], starts), (ones[:, :], head_ones),
                                 (ups[:, 0, :], w_up[0].rearrange("d r c -> (d r) c")),
                                 (ups[:, 1, :], a_up[0].rearrange("d r c -> (d r) c")), (ups[:, 2, :], g_up[0]),
                                 (low[:, :, :], zf_view[:, 12:15, :])):
                    sp.dma_start(dst, src).then_inc(consts, 16)
                with sp.Fori(0, RJ) as j:
                    S.hold(bonus_v, last(j))
                    S.hold(arr_out, last(j, 16 * 11))
                    sp.dma_start(rkv[:, :, :], zf_view[:, 0:3 * RJ, :].rearrange("p (a j) t -> p a j t", j=RJ)[:, :, ds(j, 1), :].rearrange("p a o t -> p (a o) t")).then_inc(z_in, 16)
                    S.hold(z_in, now(j, 16))
                    sp.dma_start(arr_view[:, 0, ds(j, 1), :], rkv[:, 0:1, :]).then_inc(arr_out, 16)
                    sp.dma_start(arr_view[:, 1, ds(j, 1), :], rkv[:, 2:3, :]).then_inc(arr_out, 16)
                    S.hold(bonus_v, now(j))
                    S.hold(g_a, now(j))
                    for n, name in enumerate(OUT):
                        sp.dma_start(arr_view[:, ARR[name], ds(j, 1), :], out[:, n:n + 1, :]).then_inc(arr_out, 16)
                sp.wait_ge(arr_out, 16 * 11 * (RJ + 1))

            @block.gpsimd
            def _(pool):
                G.open(up_ready)
                pool.wait_ge(consts, 7 * 16)
                with pool.Fori(0, RJ) as j:
                    G.hold(a_psum, last(j, 2))
                    nc.gpsimd.tensor_copy(up[:, :, :], ups[:, :, ds(j * P, P)]).then_inc(up_ready, 1)

            @block.scalar
            def _(act):
                A.open(nrm_a, g_a)
                A.open(w_a, a_a, n=2)
                act.wait_ge(consts, 7 * 16)
                nc.scalar.activation(low[:, 0, :], low[:, 0, :], ACT.Tanh).then_inc(low_a, 1)
                nc.scalar.activation(low[:, 2, :], low[:, 2, :], ACT.Sigmoid).then_inc(low_a, 1)
                with act.Fori(0, RJ) as j:
                    A.hold(ss_psum, now(j))
                    nc.scalar.activation(nrm[:, :], pw[0][:, :], ACT.Sqrt).then_inc(nrm_a, 1)
                    A.hold(g_psum, now(j))
                    A.hold(arr_out, last(j, 16 * 11))
                    nc.scalar.copy(out[:, 7, :], pw[1][:, :]).then_inc(g_a, 1)
                    for d in range(2):
                        A.hold(w_psum, now(j, 2, d + 1))
                        A.hold(d_done, last(j, 2, d + 1))
                        nc.scalar.activation(s[:, d, :], pw[2 - 2 * d][:, :], ACT.Sigmoid, bias=vec[:, ds(j + (at("w0") + 4 * d), 1)]).then_inc(w_a, 1)
                        A.hold(a_psum, now(j, 2, d + 1))
                        nc.scalar.activation(a[:, d, :], pw[3 - 2 * d][:, :], ACT.Sigmoid, bias=vec[:, ds(j + (at("a0") + 4 * d), 1)]).then_inc(a_a, 1)

            @block.tensor
            def _(pe):
                E.open(ss_psum, g_psum, bonus_psum)
                E.open(w_psum, a_psum, n=2)
                pe.wait_ge(consts, 7 * 16)
                pe.wait_ge(low_a, 2)

                def two(ps, lhsT, rhs, sem):
                    for half in range(2):
                        m = nc.tensor.matmul(ps[:, half * HALF:(half + 1) * HALF], lhsT, rhs[:, half * HALF:(half + 1) * HALF], start=True, stop=True)
                    m.then_inc(sem, 1)

                with pe.Fori(0, RJ) as j:
                    E.hold(sq_ready, now(j))
                    E.hold(w_a, last(j, 2))
                    two(pw[0], ones[:, :], t2, ss_psum)
                    E.hold(up_ready, now(j))
                    E.hold(a_a, last(j, 2))
                    two(pw[1], up[:, 2, :], low[:, 2, :], g_psum)
                    for d in range(2):
                        lo = slice(64 * d, 64 * d + 64)
                        if d == 0:
                            E.hold(bonus_v, last(j))
                        else:
                            E.hold(nrm_a, now(j))
                        two(pw[2 - 2 * d], up[lo, 0, :], low[lo, 0, :], w_psum)
                        if d:
                            E.hold(g_a, now(j))
                        else:
                            E.hold(a_a, last(j, 2))
                        two(pw[3 - 2 * d], up[lo, 1, :], low[lo, 1, :], a_psum)
                    E.hold(bt_ready, now(j))
                    E.hold(w_a, now(j, 2))
                    two(pw[2], ones[:, :], t1, bonus_psum)

            @block.vector
            def _(dve):
                V.open(sq_ready, bt_ready, bonus_v)
                V.open(d_done, n=2)
                dve.wait_ge(consts, 7 * 16)
                ka, rk, kkv = at("k_a"), at("r_k"), at("k_k")
                V.link(nc.vector.tensor_scalar(onek[:, :], vec[:, ka:ka + RJ], -1.0, 1.0, ALU.mult, ALU.add))
                with dve.Fori(0, RJ) as j:
                    V.loop(j, 11)
                    V.hold(z_in, now(j, 16))
                    V.hold(arr_out, last(j, 16 * 11))
                    V.hold(bonus_psum, last(j))
                    r_, k_, v_ = (rkv[:, n, :] for n in range(3))
                    V.link(nc.vector.tensor_scalar(t1[:, :], k_, vec[:, ds(j + kkv, 1)], None, ALU.mult))
                    nc.vector.tensor_tensor(t2[:, :], t1[:, :], t1[:, :], ALU.mult).then_inc(sq_ready, 1)
                    V.hold(nrm_a, now(j))
                    V.link(nc.vector.tensor_scalar(nrm[:, :], nrm[:, :], 1e-12, -1.0, ALU.max, ALU.mult))
                    V.link(nc.vector.reciprocal(nrm[:, :], nrm[:, :]))
                    V.link(nc.vector.tensor_tensor(out[:, 0, :], t1[:, :], nrm[:, :], ALU.mult))
                    for d in range(2):
                        V.hold(w_a, now(j, 2, d + 1))
                        step = slice(None) if d == 0 else slice(None, None, -1)
                        nc.vector.tensor_tensor_scan(out[:, 5 + d, step], go[:, d, step], s[:, d, step], 0.0, ALU.mult, ALU.add)
                        V.hold(a_a, now(j, 2, d + 1))
                        V.link(nc.vector.tensor_scalar(kmix[:, d, :], a[:, d, :], vec[:, ds(j + ka, 1)], onek[:, ds(j, 1)], ALU.mult, ALU.add))
                        nc.vector.scalar_tensor_tensor(out[:, 1 + d, :], out[:, 0, :], -1.0, a[:, d, :], ALU.mult, ALU.mult)
                        V.link(nc.vector.tensor_tensor(out[:, 3 + d, :], kmix[:, d, :], k_, ALU.mult))
                        dve.sem_inc(d_done, 1)
                    V.link(nc.vector.tensor_tensor(t1[:, :], out[:, 3, :], out[:, 4, :], ALU.add))
                    V.link(nc.vector.scalar_tensor_tensor(t2[:, :], t1[:, :], vec[:, ds(j + rk, 1)], r_, ALU.mult, ALU.mult))
                    nc.vector.tensor_copy(t1[:, :], t2[:, :]).then_inc(bt_ready, 1)
                    V.hold(bonus_psum, now(j))
                    V.link(nc.vector.tensor_tensor(out[:, 8, :], pw[2][:, :], v_, ALU.mult))
                    dve.sem_inc(bonus_v, 1)
                V.done(RJ)



LEVELS = (1, 2, 4, 8, 16, 32)


def wkv_tables():
    t = np.arange(C)
    r, c = t[:, None], t[None, :]
    masks = []
    for b in LEVELS:
        later, earlier = (r // b) % 2 == 1, (c // b) % 2 == 0
        masks.append((r // (2 * b) == c // (2 * b)) & later & earlier)
    masks.append(masks[0].T)
    masks.append(r < c)
    masks.append(r <= c)
    both = np.stack([np.stack([m, m.T]) for m in masks])
    both = both.transpose(2, 0, 1, 3).astype(np.float32)
    eye = np.broadcast_to(np.eye(C, dtype=np.float32)[:, None], (C, 2, C))
    one = np.concatenate([both.reshape(C, -1), eye.reshape(C, -1)], axis=1)
    return np.ascontiguousarray(np.concatenate([one, one]))


N_MASKS = len(LEVELS) + 3


def wkv_phase(nc, tables, arr_dram, y_dram):
    W = 2 * RJ * C
    with Phase(nc, "wkv") as ph:
        tab = ph.sb("tab", [P, (N_MASKS + 1) * 2 * C])
        NA = 6
        inp = ph.sb("inp", [P, NA, W])
        ex = ph.sb("ex", [P, W])
        inv = ph.sb("inv", [P, W])
        at = ph.sb("at", [P, W])
        rt = ph.sb("rt", [P, W])
        bh = ph.sb("bh", [P, W])
        kh = ph.sb("kh", [P, W])
        v_ = ph.sb("v_", [P, W])
        a_raw = ph.sb("a_raw", [P, W])
        a_l = ph.sb("a_l", [P, 5, W])
        x1 = ph.sb("x1", [P, 2, W])
        ak = ph.sb("ak", [P, W])
        rb = ph.sb("rb", [P, W])
        rk = ph.sb("rk", [P, W])
        bt = ph.sb("bt", [P, W])
        kt = ph.sb("kt", [P, W])
        vt = ph.sb("vt", [P, W])
        X = ph.sb("X", [P, W])
        Z = ph.sb("Z", [P, W])
        Q = ph.sb("Q", [P, W])
        pp = ph.sb("pp", [P, W])
        uu = ph.sb("uu", [P, W])
        st = ph.sb("st", [P, W])
        st1 = ph.sb("st1", [P, W])
        dec = ph.sb("dec", [P, 2 * RJ])
        yy = ph.sb("yy", [P, W])
        bank = [ph.ps(f"b{n}", [P, W]) for n in range(8)]

        names = ("in_done exps operands inp_free g_v g_a a_masked q_psum q_kept xz_psum xz_kept p_psum p_kept u_psum u_kept "
                 "y_psum y_kept y_out s_psum s_kept grams tabs st0").split()
        (in_done, exps, operands, inp_free, g_v, g_a, a_masked, q_psum, q_kept, xz_psum, xz_kept, p_psum, p_kept, u_psum, u_kept,
         y_psum, y_kept, y_out, s_psum, s_kept, grams, tabs, st0) = [ph.sem(n) for n in names]
        V, G, A, E, S = (ph.engine(e, n) for e, n in ((nc.vector, "dve"), (nc.gpsimd, "pool"), (nc.scalar, "act"),
                                                      (nc.tensor, "pe"), (nc.sync, "sp")))
        NL = len(LEVELS) - 1

        def mask(n):
            return tab[:, n * 2 * C:(n + 1) * 2 * C].rearrange("p (d c) -> p d c", d=2).unsqueeze(2).to_broadcast([P, 2, RJ, C])

        def grid(a):
            return a.rearrange("p (d j c) -> p d j c", d=2, j=RJ)

        def unit(t, p, n):
            return t[64 * p:64 * p + 64, n * C:(n + 1) * C]

        arr_view = arr_dram.rearrange("a (j p) t -> p a j t", p=P)
        y_view = y_dram.rearrange("d (j p) t -> p d j t", p=P)

        with nc.Block() as block:

            @block.sync
            def _(sp):
                S.open(in_done, n=16 * 2 * NA)
                S.open(y_out, n=32)
                sp.dma_start(tab[:, :], tables).then_inc(tabs, 16)
                with sp.Fori(0, NCH) as i:
                    S.hold(operands, last(i))
                    S.hold(exps, last(i))
                    for d in range(2):
                        cols = ds(i * C, C) if d == 0 else ds(i * (-C) + (T - C), C)
                        for n, name in enumerate(("r", "v", "nkk", f"b{d}", f"kd{d}", f"L{d}")):
                            sp.dma_start(grid(inp[:, n, :])[:, d, :, :], arr_view[:, ARR[name], :, cols]).then_inc(in_done, 16)
                    S.hold(y_kept, now(i))
                    for d in range(2):
                        cols = ds(i * C, C) if d == 0 else ds(i * (-C) + (T - C), C)
                        sp.dma_start(y_view[:, d, :, cols], grid(yy[:, :])[:, d, :, :]).then_inc(y_out, 16)
                sp.wait_ge(y_out, 32 * (NCH + 1))

            @block.gpsimd
            def _(pool):
                G.open(a_masked, n=NL)
                pool.wait_ge(tabs, 16)
                with pool.Fori(0, NCH) as i:
                    G.hold(g_a, now(i, 4, 1))
                    for n in range(NL):
                        G.hold(q_psum, last(i, NL, n + 1))
                        nc.gpsimd.tensor_tensor(grid(a_l[:, n, :]), grid(a_raw[:, :]), mask(n + 1), ALU.mult).then_inc(a_masked, 1)

            @block.scalar
            def _(act):
                A.open(exps, p_kept, u_kept)
                A.open(y_kept)
                A.open(g_a, n=4)
                A.open(q_kept, n=NL)
                with act.Fori(0, NCH) as i:
                    A.loop(i, 1)
                    A.hold(in_done, now(i, 32 * NA))
                    A.hold(operands, last(i))
                    A.hold(s_kept, last(i))
                    nc.scalar.activation(ex[:, :], inp[:, 5, :], ACT.Exp, scale=-W_SCALE)
                    A.link(nc.scalar.activation(inv[:, :], inp[:, 5, :], ACT.Exp, scale=W_SCALE))
                    act.sem_inc(exps, 1)
                    A.hold(grams, now(i, 8, 1))
                    A.hold(a_masked, last(i, NL))
                    nc.scalar.copy(a_raw[:, :], bank[0][:, :]).then_inc(g_a, 1)
                    for n, dst in enumerate((bt, kt, vt)):
                        A.hold(grams, now(i, 8, 6 + n))
                        if n == 0:
                            A.hold(s_psum, last(i))
                        nc.scalar.copy(dst[:, :], bank[5 + n][:, :]).then_inc(g_a, 1)
                    for n in range(NL):
                        A.hold(q_psum, now(i, NL, n + 1))
                        A.hold(xz_psum, now(i, NL, n) if n else last(i, NL))
                        nc.scalar.copy(Q[:, :], bank[3][:, :]).then_inc(q_kept, 1)
                    A.hold(p_psum, now(i))
                    A.hold(u_psum, last(i))
                    nc.scalar.copy(pp[:, :], bank[4][:, :]).then_inc(p_kept, 1)
                    A.hold(u_psum, now(i))
                    A.hold(s_psum, last(i))
                    nc.scalar.copy(uu[:, :], bank[5][:, :]).then_inc(u_kept, 1)
                    A.hold(y_psum, now(i))
                    A.hold(y_out, last(i, 32))
                    nc.scalar.copy(yy[:, :], bank[6][:, :]).then_inc(y_kept, 1)
                A.done(NCH)

            @block.vector
            def _(dve):
                V.open(operands, s_kept)
                V.open(g_v, n=4)
                V.open(xz_kept, n=NL)
                dve.wait_ge(tabs, 16)
                V.link(nc.vector.memset(st[:, :], 0.0))
                dve.sem_inc(st0, 1)
                with dve.Fori(0, NCH) as i:
                    V.loop(i, 4)
                    V.hold(exps, now(i))
                    V.hold(grams, last(i, 8))
                    V.hold(y_psum, last(i))
                    gi = [grid(inp[:, n, :]) for n in range(NA)]
                    ge, ga, = grid(ex[:, :]), grid(at[:, :])
                    nc.vector.tensor_tensor(rt[:, :], inp[:, 0, :], ex[:, :], ALU.mult)
                    nc.vector.tensor_tensor(bh[:, :], inp[:, 3, :], inv[:, :], ALU.mult)
                    nc.vector.tensor_tensor(kh[:, :], inp[:, 4, :], inv[:, :], ALU.mult)
                    nc.vector.tensor_copy(v_[:, :], inp[:, 1, :])
                    nc.vector.tensor_tensor(ga[:, 0, :, 1:C], gi[2][:, 0, :, 1:C], ge[:, 0, :, 0:C - 1], ALU.mult)
                    nc.vector.tensor_tensor(ga[:, 1, :, 0:C - 1], gi[2][:, 1, :, 0:C - 1], ge[:, 1, :, 1:C], ALU.mult)
                    nc.vector.tensor_copy(ga[:, 0, :, 0:1], gi[2][:, 0, :, 0:1])
                    nc.vector.tensor_copy(ga[:, 1, :, C - 1:C], gi[2][:, 1, :, C - 1:C])
                    nc.vector.tensor_copy(dec[:, 0:RJ], ge[:, 0, :, C - 1])
                    V.link(nc.vector.tensor_copy(dec[:, RJ:2 * RJ], ge[:, 1, :, 0]))
                    dve.sem_inc(operands, 1)
                    V.hold(g_a, now(i, 4, 1))
                    V.hold(xz_psum, last(i, NL))
                    V.hold(u_psum, last(i))
                    nc.vector.tensor_tensor(grid(x1[:, 0, :]), grid(bank[0][:, :]), mask(0), ALU.mult).then_inc(g_v, 1)
                    V.hold(grams, now(i, 8, 2))
                    V.link(nc.vector.tensor_tensor(grid(x1[:, 1, :]), grid(bank[1][:, :]), mask(NL + 1), ALU.mult))
                    eye = mask(N_MASKS)
                    nc.vector.tensor_tensor(grid(X[:, :]), grid(x1[:, 0, :]), eye, ALU.add)
                    nc.vector.tensor_tensor(grid(Z[:, :]), grid(x1[:, 1, :]), eye, ALU.add).then_inc(g_v, 1)
                    V.hold(grams, now(i, 8, 3))
                    nc.vector.tensor_tensor(grid(ak[:, :]), grid(bank[2][:, :]), mask(NL + 2), ALU.mult)
                    V.hold(grams, now(i, 8, 4))
                    nc.vector.tensor_tensor(grid(rb[:, :]), grid(bank[3][:, :]), mask(NL + 3), ALU.mult).then_inc(g_v, 1)
                    V.hold(grams, now(i, 8, 5))
                    nc.vector.tensor_tensor(grid(rk[:, :]), grid(bank[4][:, :]), mask(NL + 3), ALU.mult).then_inc(g_v, 1)
                    V.hold(g_v, now(i, 4, 2))
                    for n in range(NL):
                        V.hold(xz_psum, now(i, NL, n + 1))
                        if n < NL - 1:
                            nc.vector.tensor_tensor(X[:, :], X[:, :], bank[0][:, :], ALU.add)
                        nc.vector.tensor_tensor(Z[:, :], Z[:, :], bank[1][:, :], ALU.add).then_inc(xz_kept, 1)
                        V.hold(xz_kept, now(i, NL, n + 1))
                    V.hold(s_psum, now(i))
                    V.link(nc.vector.tensor_tensor(st1[:, :], st[:, :], bank[7][:, :], ALU.add))
                    V.link(nc.vector.tensor_tensor(st[:, :].rearrange("p (n c) -> p n c", c=C), st1[:, :].rearrange("p (n c) -> p n c", c=C),
                                                   dec[:, :].unsqueeze(2).to_broadcast([P, 2 * RJ, C]), ALU.mult))
                    dve.sem_inc(s_kept, 1)
                V.done(NCH)

            @block.tensor
            def _(pe):
                E.open(p_psum, u_psum, y_psum, s_psum)
                E.open(grams, n=8)
                E.open(q_psum, xz_psum, n=NL)
                pe.wait_ge(tabs, 16)
                pe.wait_ge(st0, 1)
                units = [(p, n) for n in range(2 * RJ) for p in range(2)]
                eye = tab[:, N_MASKS * 2 * C:N_MASKS * 2 * C + C]

                def product(dst, pairs):
                    for p, n in units:
                        for k, (lhsT, rhs) in enumerate(pairs):
                            right = rhs[64 * p:64 * p + 64, :] if rhs is eye else unit(rhs, p, n)
                            m = nc.tensor.matmul(unit(dst, p, n), unit(lhsT, p, n), right, start=k == 0, stop=k == len(pairs) - 1)
                    return m

                with pe.Fori(0, NCH) as i:
                    E.hold(operands, now(i))
                    E.hold(s_kept, last(i))
                    E.hold(y_kept, last(i))
                    for n, pair in enumerate(((at, bh), (bh, at), (kh, at), (bh, rt), (kh, rt), (bh, eye), (kh, eye), (v_, eye))):
                        product(bank[n], [pair]).then_inc(grams, 1)
                    for n in range(NL):
                        if n == 0:
                            E.hold(g_v, now(i, 4, 4))
                        else:
                            E.hold(xz_kept, now(i, NL, n))
                        E.hold(a_masked, now(i, NL, n + 1))
                        product(bank[3], [(a_l[:, n, :], Z)]).then_inc(q_psum, 1)
                        E.hold(q_kept, now(i, NL, n + 1))
                        if n < NL - 1:
                            product(bank[0], [(Q, X)])
                        product(bank[1], [(X, Q)]).then_inc(xz_psum, 1)
                    E.hold(g_a, now(i, 4, 4))
                    product(bank[4], [(at, st), (ak, vt)]).then_inc(p_psum, 1)
                    E.hold(xz_kept, now(i, NL))
                    E.hold(p_kept, now(i))
                    product(bank[5], [(Z, pp)]).then_inc(u_psum, 1)
                    E.hold(u_kept, now(i))
                    product(bank[6], [(st, rt), (uu, rb), (vt, rk)]).then_inc(y_psum, 1)
                    product(bank[7], [(bt, uu), (kt, vt)]).then_inc(s_psum, 1)



LNX_EPS = 64e-5
GATE_AT = MLA_IN + RWKV_TILES * P


def mix_phase(nc, vecs, w_in, w_br_mla, w_br_rwkv, head_ones, hT_dram, oT_dram, arr_dram, y_dram, mixT_dram):
    with Phase(nc, "mix") as ph:
        vec = ph.sb("vec", [P, VEC_N])
        ones = ph.sb("ones", [P, P])
        hT = ph.sb("hT", [P, KD, T])
        oT = ph.sb("oT", [P, 2 * RJ, T])
        inp = ph.sb("inp", [P, 4, T])
        y = ph.sb("y", [P, T])
        sq = ph.sb("sq", [P, T])
        rt = ph.sb("rt", [P, T])
        w = ph.sb("w", [P, 2, 24, P])
        sg = ph.sb("sg", [P, 2, T])
        mixed = ph.sb("mixed", [P, T])
        m1 = ph.sb("m1", [P, T])
        pb = [ph.ps(f"pb{n}", [P, T]) for n in range(4)]
        names = "in_done y_sum mean_psum cent sq_ready var_psum root o_ready consts late rt_ready z_psum gates br_psum mixed_ready mixed_out".split()
        (in_done, y_sum, mean_psum, cent, sq_ready, var_psum, root, o_ready, consts, late, rt_ready, z_psum, gates, br_psum, mixed_ready,
         mixed_out) = [ph.sem(n) for n in names]
        w_done = [ph.sem(f"w_done{u}") for u in range(2)]
        V, A, E, S = (ph.engine(e, n) for e, n in ((nc.vector, "dve"), (nc.scalar, "act"), (nc.tensor, "pe"), (nc.sync, "sp")))
        at = lambda n: vec_at(n)[0]
        arr_view = arr_dram.rearrange("a (k p) t -> p a k t", p=P)
        y_view = y_dram.rearrange("d (k p) t -> p d k t", p=P)
        hT_view = hT_dram.rearrange("(k p) t -> p k t", p=P)
        mix_view = mixT_dram.rearrange("(k p) t -> p k t", p=P)
        wi = w_in[0].rearrange("(k p) n -> p k n", p=P)
        wa = w_br_mla[0].rearrange("(k p) n -> p k n", p=P)
        wr = w_br_rwkv[0].rearrange("(k p) n -> p k n", p=P)

        with nc.Block() as block:

            @block.sync
            def _(sp):
                S.open(in_done, n=64)
                S.open(mixed_out, n=32)
                for u in range(2):
                    S.open(w_done[u], n=64)
                sp.dma_start(vec[:, :], vecs).then_inc(consts, 16)
                sp.dma_start(ones[:, :], head_ones).then_inc(consts, 16)

                def weights(u, cols, gate_cols):
                    for n, (src, k, c) in enumerate(((wi, KD, gate_cols(0)), (wi, KD, gate_cols(1)), (wa, RJ, cols), (wr, RJ, cols))):
                        lo = (0, 8, 16, 20)[n]
                        sp.dma_start(w[:, u, lo:lo + k, :], src[:, :, c]).then_inc(w_done[u], 16)

                with sp.Fori(0, RJ) as j:
                    S.hold(o_ready, last(j))
                    for n in range(2):
                        sp.dma_start(inp[:, n:n + 1, :], y_view[:, n, ds(j, 1), :]).then_inc(in_done, 16)
                    sp.dma_start(inp[:, 2:3, :], arr_view[:, ARR["bonus"], ds(j, 1), :]).then_inc(in_done, 16)
                    sp.dma_start(inp[:, 3:4, :], arr_view[:, ARR["g"], ds(j, 1), :]).then_inc(in_done, 16)
                for k in range(KD):
                    sp.dma_start(hT[:, k, :], hT_view[:, k, :]).then_inc(late, 16)
                sp.dma_start(oT[:, 0:RJ, :], oT_dram.rearrange("(k p) t -> p k t", p=P)).then_inc(late, 16)
                with sp.Fori(0, KD // 2) as i:
                    for u in range(2):
                        S.hold(br_psum, last(i, 2, u + 1))
                        weights(u, ds(i * 2 * P + u * P, P), lambda b, i=i, u=u: ds(i * 2 * P + (GATE_AT + b * D + u * P), P))
                        if u:
                            S.hold(mixed_ready, now(i, 2, u))
                            sp.dma_start(mix_view[:, ds(i * 2, 1), :], mixed[:, :].unsqueeze(1)).then_inc(mixed_out, 16)
                    S.hold(mixed_ready, now(i, 2, 2))
                    sp.dma_start(mix_view[:, ds(i * 2 + 1, 1), :], mixed[:, :].unsqueeze(1)).then_inc(mixed_out, 16)
                sp.wait_ge(mixed_out, 16 * (KD + 2))

            @block.tensor
            def _(pe):
                E.open(mean_psum, var_psum)
                E.open(br_psum, n=2)
                E.open(z_psum, n=4)
                pe.wait_ge(consts, 32)

                def two(ps, lhsT, rhs):
                    for half in range(2):
                        m = nc.tensor.matmul(ps[:, half * HALF:(half + 1) * HALF], lhsT, rhs[:, half * HALF:(half + 1) * HALF], start=True, stop=True)
                    return m

                with pe.Fori(0, RJ) as j:
                    E.hold(y_sum, now(j))
                    two(pb[0], ones[:, :], y).then_inc(mean_psum, 1)
                    E.hold(sq_ready, now(j))
                    two(pb[1], ones[:, :], sq).then_inc(var_psum, 1)
                E.hold(o_ready, RJ + 1)
                pe.wait_ge(late, (KD + 1) * 16)

                def many(ps, u, lo, n, rhs):
                    for half in range(2):
                        for k in range(n):
                            m = nc.tensor.matmul(ps[:, half * HALF:(half + 1) * HALF], w[:, u, lo + k, :],
                                                 rhs[:, k, half * HALF:(half + 1) * HALF], start=k == 0, stop=k == n - 1)
                    return m

                with pe.Fori(0, KD // 2) as i:
                    for u in range(2):
                        E.hold(w_done[u], now(i, 64))
                        E.hold(gates, now(i, 4, 2) if u else last(i, 4))
                        many(pb[0], u, 0, KD, hT).then_inc(z_psum, 1)
                        many(pb[1], u, 8, KD, hT).then_inc(z_psum, 1)
                        E.hold(mixed_ready, now(i, 2, 1) if u else last(i, 2))
                        many(pb[2], u, 16, RJ, oT)
                        many(pb[3], u, 20, RJ, oT[:, RJ:2 * RJ, :]).then_inc(br_psum, 1)

            @block.scalar
            def _(act):
                A.open(root, sq_ready)
                A.open(gates, n=4)
                act.wait_ge(consts, 32)
                with act.Fori(0, RJ) as j:
                    A.hold(cent, now(j))
                    A.hold(var_psum, last(j))
                    nc.scalar.activation(sq[:, :], y[:, :], ACT.Square).then_inc(sq_ready, 1)
                    A.hold(rt_ready, now(j))
                    nc.scalar.activation(rt[:, :], rt[:, :], ACT.Sqrt).then_inc(root, 1)
                with act.Fori(0, KD // 2) as i:
                    for u in range(2):
                        for b in range(2):
                            A.hold(z_psum, now(i, 4, 2 * u + b + 1))
                            A.hold(mixed_ready, now(i, 2, 1) if u else last(i, 2))
                            nc.scalar.activation(sg[:, b, :], pb[b][:, :], ACT.Sigmoid,
                                                 bias=vec[:, ds(i * 2 + (at("gate_b") + b * KD + u), 1)]).then_inc(gates, 1)

            @block.vector
            def _(dve):
                V.open(y_sum, cent, o_ready, rt_ready)
                V.open(mixed_ready, n=2)
                dve.wait_ge(consts, 32)
                with dve.Fori(0, RJ) as j:
                    V.loop(j, 5)
                    V.hold(in_done, now(j, 64))
                    nc.vector.tensor_tensor(y[:, :], inp[:, 0, :], inp[:, 1, :], ALU.add).then_inc(y_sum, 1)
                    V.hold(mean_psum, now(j))
                    nc.vector.scalar_tensor_tensor(y[:, :], pb[0][:, :], -1.0 / 64, y[:, :], ALU.mult, ALU.add).then_inc(cent, 1)
                    V.hold(var_psum, now(j))
                    nc.vector.tensor_scalar(rt[:, :], pb[1][:, :], 1.0 / 64, LNX_EPS, ALU.mult, ALU.add).then_inc(rt_ready, 1)
                    V.hold(root, now(j))
                    V.link(nc.vector.reciprocal(rt[:, :], rt[:, :]))
                    V.link(nc.vector.tensor_tensor(y[:, :], y[:, :], rt[:, :], ALU.mult))
                    V.link(nc.vector.tensor_scalar(y[:, :], y[:, :], vec[:, ds(j + at("lnx_g"), 1)], vec[:, ds(j + at("lnx_b"), 1)], ALU.mult, ALU.add))
                    V.link(nc.vector.tensor_tensor(y[:, :], y[:, :], inp[:, 2, :], ALU.add))
                    V.link(nc.vector.tensor_tensor(oT[:, ds(j + RJ, 1), :].rearrange("p o t -> p (o t)"), y[:, :], inp[:, 3, :], ALU.mult))
                    dve.sem_inc(o_ready, 1)
                V.done(RJ)
                with dve.Fori(0, KD // 2) as i:
                    V.loop(i, 4)
                    for u in range(2):
                        V.hold(gates, now(i, 4, 2 * u + 2))
                        V.hold(br_psum, now(i, 2, u + 1))
                        V.hold(mixed_out, now(i, 32, 16) if u else last(i, 32))
                        nc.vector.tensor_tensor(mixed[:, :], pb[2][:, :], sg[:, 0, :], ALU.mult)
                        V.link(nc.vector.tensor_tensor(m1[:, :], pb[3][:, :], sg[:, 1, :], ALU.mult))
                        V.link(nc.vector.tensor_tensor(mixed[:, :], mixed[:, :], m1[:, :], ALU.add))
                        dve.sem_inc(mixed_ready, 1)
                V.done(KD // 2)


N_GROUPS, PER_GROUP = 4, 8
N_EXP = N_GROUPS * PER_GROUP
MOE_BLOCKS = 2 * T // P + N_EXP
SLOTS = MOE_BLOCKS * P
LOGITS = N_GROUPS + N_EXP


def route_tables():
    t = np.arange(P)
    before = (t[:, None] < t[None, :]).astype(np.float32)
    row = np.concatenate([8.0 - np.arange(8), 128.0 * np.arange(8), 128.0 * np.arange(MOE_BLOCKS)])
    tok = (np.arange(NT)[None, :] * P + t[:, None])
    return np.ascontiguousarray(np.concatenate([before, np.ones((P, P)), np.broadcast_to(row, (P, row.size))], axis=1).astype(np.float32)), \
        np.ascontiguousarray(tok.astype(np.uint32))


def route_phase(nc, x, vecs, w_out, rg_w, rg_b, re_w, re_b, eye, tables, tok_ids, mixT_dram, x1_dram, h2_dram, slot_tok, keep):
    slot_u, wts, block_e = keep
    with Phase(nc, "route") as ph:
        ident = ph.sb("ident", [P, P])
        vec = ph.sb("vec", [P, VEC_N])
        wo = ph.sb("wo", [P, KD, D])
        rw = ph.sb("rw", [P, KD, LOGITS])
        rb = ph.sb("rb", [P, LOGITS])
        mT = ph.sb("mT", [P, KD, T])
        m_t = ph.sb("m_t", [P, KD, P])
        xt = ph.sb("xt", [P, D])
        x1 = ph.sb("x1", [P, D])
        junk = ph.sb("junk", [P, D])
        h2 = ph.sb("h2", [P, D])
        h2T = ph.sb("h2T", [P, KD, P])
        small = ph.sb("small", [P, 4])
        lg = ph.sb("lg", [P, NT, LOGITS])
        tab = ph.sb("tab", [P, 2 * P + 16 + MOE_BLOCKS])
        tok = ph.sb("tok", [P, NT], U32)
        zero = ph.sb("zero", [P, MOE_BLOCKS + 1], U32)
        gdiff = ph.sb("gdiff", [P, NT, N_GROUPS])
        e21 = ph.sb("e21", [P, NT])
        mem = ph.sb("mem", [P, NT, N_EXP])
        cum = ph.sb("cum", [P, NT + 1, N_EXP])
        gmax = ph.sb("gmax", [P, NT])
        goh = ph.sb("goh", [P, NT, N_GROUPS])
        el = ph.sb("el", [P, NT, N_GROUPS, PER_GROUP])
        sel = ph.sb("sel", [P, NT, PER_GROUP])
        sel2 = ph.sb("sel2", [P, NT, PER_GROUP])
        top = ph.sb("top", [P, 2, NT])
        oh = ph.sb("oh", [P, 2, NT, PER_GROUP])
        ohe = ph.sb("ohe", [P, 2, NT, N_GROUPS, PER_GROUP])
        pref = ph.sb("pref", [P, NT, PER_GROUP])
        pmax = ph.sb("pmax", [P, NT])
        gs = ph.sb("gs", [P, NT])
        rank = ph.sb("rank", [P, NT, N_EXP])
        pick = ph.sb("pick", [P, NT, N_EXP])
        slot_f = ph.sb("slot_f", [P, 2 * NT])
        over = ph.sb("over", [P, N_EXP, PER_GROUP])
        padded = ph.sb("padded", [P, N_EXP])
        pend = ph.sb("pend", [P, N_EXP])
        pstart = ph.sb("pstart", [P, N_EXP])
        cmp = ph.sb("cmp", [P, MOE_BLOCKS, N_EXP])
        be_f = ph.sb("be_f", [P, MOE_BLOCKS])
        po = ph.ps("po", [P, D])
        pt = ph.ps("pt", [P, D])
        pl = ph.ps("pl", [P, HALF])
        pr = ph.ps("pr", [P, HALF])
        names = ("consts x_in m_in xo_psum x1_ready x1_out sq ms root h2_ready h2_out hT_psum hT_ready l_psum l_kept "
                 "members rank_psum exp_in exp_out slots scattered zeroed").split()
        (consts, x_in, m_in, xo_psum, x1_ready, x1_out, sq, ms, root, h2_ready, h2_out, hT_psum, hT_ready, l_psum, l_kept,
         members, rank_psum, exp_in, exp_out, slots, scattered, zeroed) = [ph.sem(n) for n in names]
        V, G, A, E, S = (ph.engine(e, n) for e, n in ((nc.vector, "dve"), (nc.gpsimd, "pool"), (nc.scalar, "act"),
                                                      (nc.tensor, "pe"), (nc.sync, "sp")))
        g0 = vec_at("norm_ffn_g")[0]
        NCONST = 9 + KD

        with nc.Block() as block:

            @block.sync
            def _(sp):
                S.open(x_in, x1_out, h2_out, n=16)
                for dst, src in ((ident[:, :], eye), (vec[:, :], vecs), (wo[:, :, :], w_out[0].rearrange("(k p) n -> p k n", p=P)),
                                 (rw[:, :, 0:N_GROUPS], rg_w[0].rearrange("(k p) n -> p k n", p=P)),
                                 (rw[:, :, N_GROUPS:LOGITS], re_w[0].rearrange("(k p) n -> p k n", p=P)),
                                 (rb[:, 0:N_GROUPS], rg_b[0].partition_broadcast(P)), (rb[:, N_GROUPS:LOGITS], re_b[0].partition_broadcast(P)),
                                 (tab[:, :], tables), (tok[:, :], tok_ids)):
                    sp.dma_start(dst, src).then_inc(consts, 16)
                for k in range(KD):
                    sp.dma_start(mT[:, k, :], mixT_dram[k * P:(k + 1) * P, :]).then_inc(consts, 16)
                with sp.Fori(0, NT) as i:
                    S.hold(x1_ready, last(i))
                    sp.dma_start(xt[:, :], x[ds(i * P, P), :]).then_inc(x_in, 16)
                    S.hold(x1_ready, now(i))
                    sp.dma_start(x1_dram[ds(i * P, P), :], x1[:, :]).then_inc(x1_out, 16)
                    S.hold(h2_ready, now(i))
                    sp.dma_start(h2_dram[ds(i * P, P), :], h2[:, :]).then_inc(h2_out, 16)
                sp.wait_ge(x1_out, 16 * (NT + 1))
                sp.wait_ge(h2_out, 16 * (NT + 1))
                sp.wait_ge(zeroed, 1)
                sp.dma_start(slot_tok.rearrange("(p b) o -> p (b o)", p=P), zero[:, :]).then_inc(zeroed, 16)

            @block.gpsimd
            def _(pool):
                G.open(m_in)
                pool.wait_ge(consts, NCONST * 16)
                nc.gpsimd.memset(zero[:, :], 0).then_inc(zeroed, 1)
                with pool.Fori(0, NT) as i:
                    G.hold(xo_psum, last(i))
                    nc.gpsimd.tensor_copy(m_t[:, :, :], mT[:, :, ds(i * P, P)]).then_inc(m_in, 1)
                pool.wait_ge(slots, 1)
                pool.wait_ge(zeroed, 17)
                for n in range(2 * NT):
                    pool.indirect_dma_start(slot_tok, bass.IndirectOffsetOnAxis(ap=slot_u[:, n:n + 1], axis=0),
                                            tok[:, n % NT:n % NT + 1], None).then_inc(scattered, 16)
                pool.wait_ge(scattered, 16 * 2 * NT)

            @block.tensor
            def _(pe):
                E.open(xo_psum, hT_psum, l_psum)
                pe.wait_ge(consts, NCONST * 16)
                with pe.Fori(0, NT) as i:
                    E.hold(m_in, now(i))
                    E.hold(x1_ready, last(i))
                    for half in range(2):
                        for k in range(KD):
                            m = nc.tensor.matmul(po[:, half * HALF:(half + 1) * HALF], m_t[:, k, :], wo[:, k, half * HALF:(half + 1) * HALF],
                                                 start=k == 0, stop=k == KD - 1)
                    m.then_inc(xo_psum, 1)
                    E.hold(h2_ready, now(i))
                    for k in range(KD):
                        t = nc.tensor.transpose(pt[:, k * P:(k + 1) * P], h2[:, k * P:(k + 1) * P], ident[:, :])
                    t.then_inc(hT_psum, 1)
                    E.hold(hT_ready, now(i))
                    E.hold(l_kept, last(i))
                    for k in range(KD):
                        m = nc.tensor.matmul(pl[:, 0:LOGITS], h2T[:, k, :], rw[:, k, :], start=k == 0, stop=k == KD - 1)
                    m.then_inc(l_psum, 1)
                pe.wait_ge(members, 1)
                nc.tensor.matmul(pr[:, 0:NT * N_EXP], tab[:, 0:P], mem[:, :, :], start=True, stop=False)
                nc.tensor.matmul(pr[:, 0:NT * N_EXP], tab[:, P:2 * P], cum[:, 0:NT, :], start=False, stop=True)
                nc.tensor.matmul(pl[:, 0:N_EXP], tab[:, P:2 * P], cum[:, NT, :], start=True, stop=True).then_inc(rank_psum, 1)

            @block.scalar
            def _(act):
                A.open(sq, root)
                with act.Fori(0, NT) as i:
                    A.hold(x1_ready, now(i))
                    nc.scalar.activation(junk[:, :], x1[:, :], ACT.Square, accum_out=small[:, 0:1]).then_inc(sq, 1)
                    A.hold(ms, now(i))
                    nc.scalar.activation(small[:, 2:3], small[:, 1:2], ACT.Sqrt).then_inc(root, 1)
                act.wait_ge(exp_in, 1)
                nc.scalar.activation(gdiff[:, :, :], gdiff[:, :, :], ACT.Exp)
                nc.scalar.activation(e21[:, :], e21[:, :], ACT.Exp).then_inc(exp_out, 1)

            @block.vector
            def _(dve):
                V.open(x1_ready, ms, h2_ready, hT_ready, l_kept)
                dve.wait_ge(consts, NCONST * 16)
                with dve.Fori(0, NT) as i:
                    V.loop(i, 1)
                    V.hold(x_in, now(i, 16))
                    V.hold(xo_psum, now(i))
                    V.hold(x1_out, last(i, 16))
                    V.hold(sq, last(i))
                    nc.vector.tensor_tensor(x1[:, :], po[:, :], xt[:, :], ALU.add).then_inc(x1_ready, 1)
                    V.hold(sq, now(i))
                    nc.vector.tensor_scalar(small[:, 1:2], small[:, 0:1], 1.0 / D, NORM_EPS, ALU.mult, ALU.add).then_inc(ms, 1)
                    V.hold(root, now(i))
                    V.link(nc.vector.reciprocal(small[:, 3:4], small[:, 2:3]))
                    V.hold(h2_out, last(i, 16))
                    V.hold(hT_psum, last(i))
                    nc.vector.tensor_scalar(h2[:, :], x1[:, :], small[:, 3:4], None, ALU.mult).then_inc(h2_ready, 1)
                    V.hold(hT_psum, now(i))
                    V.hold(l_psum, last(i))
                    nc.vector.tensor_tensor(h2T[:, :, :], pt[:, :].rearrange("p (k t) -> p k t", k=KD),
                                            vec[:, g0:g0 + KD].unsqueeze(2).to_broadcast([P, KD, P]), ALU.mult).then_inc(hT_ready, 1)
                    V.hold(l_psum, now(i))
                    nc.vector.tensor_tensor(lg[:, ds(i, 1), :].rearrange("p o n -> p (o n)"), pl[:, 0:LOGITS], rb[:, :], ALU.add).then_inc(l_kept, 1)
                V.done(NT)
                dve.wait_ge(l_kept, NT + 1)

                def first_of(out, vals, best, n):
                    V.link(nc.vector.tensor_tensor(out, vals, best.unsqueeze(2).to_broadcast([P, NT, n]), ALU.is_equal))
                    V.link(nc.vector.tensor_tensor(pref[:, :, 0:n], out, tab[:, 2 * P:2 * P + n].unsqueeze(1).to_broadcast([P, NT, n]), ALU.mult))
                    V.link(nc.vector.reduce_max(pmax[:, :], pref[:, :, 0:n], AX_X))
                    V.link(nc.vector.tensor_tensor(out, pref[:, :, 0:n], pmax[:, :].unsqueeze(2).to_broadcast([P, NT, n]), ALU.is_equal))

                gl = lg[:, :, 0:N_GROUPS]
                V.link(nc.vector.reduce_max(gmax[:, :], gl, AX_X))
                first_of(goh[:, :, :], gl, gmax[:, :], N_GROUPS)
                V.link(nc.vector.tensor_tensor(gdiff[:, :, :], gl, gmax[:, :].unsqueeze(2).to_broadcast([P, NT, N_GROUPS]), ALU.subtract))
                for g in range(N_GROUPS):
                    V.link(nc.vector.tensor_tensor(el[:, :, g, :], lg[:, :, N_GROUPS + g * PER_GROUP:N_GROUPS + (g + 1) * PER_GROUP],
                                                   goh[:, :, g:g + 1].to_broadcast([P, NT, PER_GROUP]), ALU.mult))
                V.link(nc.vector.tensor_reduce(sel[:, :, :], el[:, :, :, :].rearrange("p t g e -> p t e g"), AX_X, ALU.add))
                V.link(nc.vector.reduce_max(top[:, 0, :], sel[:, :, :], AX_X))
                first_of(oh[:, 0, :, :], sel[:, :, :], top[:, 0, :], PER_GROUP)
                V.link(nc.vector.scalar_tensor_tensor(sel2[:, :, :], oh[:, 0, :, :], -3e38, sel[:, :, :], ALU.mult, ALU.add))
                V.link(nc.vector.reduce_max(top[:, 1, :], sel2[:, :, :], AX_X))
                first_of(oh[:, 1, :, :], sel2[:, :, :], top[:, 1, :], PER_GROUP)
                V.link(nc.vector.tensor_tensor(e21[:, :], top[:, 1, :], top[:, 0, :], ALU.subtract))
                dve.sem_inc(exp_in, 1)
                for n in range(2):
                    for g in range(N_GROUPS):
                        V.link(nc.vector.tensor_tensor(ohe[:, n, :, g, :], oh[:, n, :, :], goh[:, :, g:g + 1].to_broadcast([P, NT, PER_GROUP]), ALU.mult))
                V.link(nc.vector.tensor_tensor(mem[:, :, :], ohe[:, 0, :, :, :].rearrange("p t g e -> p t (g e)"),
                                               ohe[:, 1, :, :, :].rearrange("p t g e -> p t (g e)"), ALU.add))
                V.link(nc.vector.memset(cum[:, 0, :], 0.0))
                for n in range(NT):
                    V.link(nc.vector.tensor_tensor(cum[:, n + 1, :], cum[:, n, :], mem[:, n, :], ALU.add))
                dve.sem_inc(members, 1)
                dve.wait_ge(exp_out, 1)
                V.link(nc.vector.tensor_reduce(gs[:, :], gdiff[:, :, :], AX_X, ALU.add))
                V.link(nc.vector.tensor_scalar(pmax[:, :], e21[:, :], 1.0, None, ALU.add))
                V.link(nc.vector.tensor_tensor(gs[:, :], gs[:, :], pmax[:, :], ALU.mult))
                V.link(nc.vector.reciprocal(wts[:, 0:NT], gs[:, :]))
                V.link(nc.vector.tensor_tensor(wts[:, NT:2 * NT], wts[:, 0:NT], e21[:, :], ALU.mult))
                dve.wait_ge(rank_psum, 1)
                V.link(nc.vector.tensor_tensor(over[:, :, :], pl[:, 0:N_EXP].unsqueeze(2).to_broadcast([P, N_EXP, 8]),
                                               tab[:, 2 * P + 8:2 * P + 16].unsqueeze(1).to_broadcast([P, N_EXP, 8]), ALU.is_gt))
                V.link(nc.vector.tensor_reduce(padded[:, :], over[:, :, :], AX_X, ALU.add))
                V.link(nc.vector.tensor_scalar(padded[:, :], padded[:, :], float(P), None, ALU.mult))
                V.link(nc.vector.tensor_tensor_scan(pend[:, :], tab[:, P:P + N_EXP], padded[:, :], 0.0, ALU.mult, ALU.add))
                V.link(nc.vector.tensor_tensor(pstart[:, :], pend[:, :], padded[:, :], ALU.subtract))
                V.link(nc.vector.tensor_tensor(rank[:, :, :], pr[:, 0:NT * N_EXP].rearrange("p (t e) -> p t e", e=N_EXP),
                                               pstart[:, :].unsqueeze(1).to_broadcast([P, NT, N_EXP]), ALU.add))
                for n in range(2):
                    V.link(nc.vector.tensor_tensor(pick[:, :, :], rank[:, :, :], ohe[:, n, :, :, :].rearrange("p t g e -> p t (g e)"), ALU.mult))
                    V.link(nc.vector.tensor_reduce(slot_f[:, n * NT:(n + 1) * NT], pick[:, :, :], AX_X, ALU.add))
                V.link(nc.vector.tensor_copy(slot_u[:, :], slot_f[:, :]))
                dve.sem_inc(slots, 1)
                V.link(nc.vector.tensor_tensor(cmp[:, :, :], pend[:, :].unsqueeze(1).to_broadcast([P, MOE_BLOCKS, N_EXP]),
                                               tab[:, 2 * P + 16:2 * P + 16 + MOE_BLOCKS].unsqueeze(2).to_broadcast([P, MOE_BLOCKS, N_EXP]), ALU.is_le))
                V.link(nc.vector.tensor_reduce(be_f[:, :], cmp[:, :, :], AX_X, ALU.add))
                V.link(nc.vector.tensor_scalar(block_e[:, :], be_f[:, :], float(N_EXP - 1), None, ALU.min))



D_EXP = 256


def experts_phase(nc, vecs, w1, w3, w2, eye, block_e, slot_tok, h2_dram, yb_dram):
    with Phase(nc, "exp") as ph:
        U = 2
        ident = ph.sb("ident", [P, P])
        vec = ph.sb("vec", [P, VEC_N])
        wb = ph.sb("wb", [P, U, 2, KD, D_EXP])
        w2b = ph.sb("w2b", [P, U, 2, D])
        idx = ph.sb("idx", [P, U], U32)
        xg = ph.sb("xg", [P, U, D])
        xT = ph.sb("xT", [P, U, KD, P])
        sg = ph.sb("sg", [P, D_EXP])
        hid = ph.sb("hid", [P, D_EXP])
        hidT = ph.sb("hidT", [P, 2, P])
        y = ph.sb("y", [P, U, D])
        pt = ph.ps("pt", [P, D])
        pg = ph.ps("pg", [P, HALF])
        phT = ph.ps("phT", [P, HALF])
        py = ph.ps("py", [P, D])
        names = "consts idx_u x_psum x_ready gu_psum act_done hid_ready hT_psum hT_ready y_psum y_a y_v y_out".split()
        (consts, idx_u, x_psum, x_ready, gu_psum, act_done, hid_ready, hT_psum, hT_ready, y_psum, y_a, y_v, y_out) = [ph.sem(n) for n in names]
        w_done = [ph.sem(f"w_done{u}") for u in range(U)]
        idx_done = [ph.sem(f"idx_done{u}") for u in range(U)]
        x_in = [ph.sem(f"x_in{u}") for u in range(U)]
        V, G, A, E, S = (ph.engine(e, n) for e, n in ((nc.vector, "dve"), (nc.gpsimd, "pool"), (nc.scalar, "act"),
                                                      (nc.tensor, "pe"), (nc.sync, "sp")))
        g0 = vec_at("norm_ffn_g")[0]
        NB = MOE_BLOCKS

        with nc.Block() as block:

            @block.sync
            def _(sp):
                for u in range(U):
                    S.open(w_done[u], n=48)
                    S.open(idx_done[u], n=16)
                sp.dma_start(ident[:, :], eye).then_inc(consts, 16)
                sp.dma_start(vec[:, :], vecs).then_inc(consts, 16)
                sp.dma_start(idx[:, 0:1], slot_tok[0:P, :]).then_inc(idx_done[0], 16)
                with sp.Fori(0, NB // U) as i:
                    for u in range(U):
                        S.hold(y_psum, last(i, U, u + 1))
                        e = sp.value_load(block_e[0:1, ds(i * U + u, 1)], min_val=0, max_val=N_EXP - 1)
                        for n, w in enumerate((w1, w3)):
                            sp.dma_start(wb[:, u, n, :, :], w[0][ds(e, 1), :, :].rearrange("o (k p) f -> p (o k) f", p=P)).then_inc(w_done[u], 16)
                        sp.dma_start(w2b[:, u, :, :], w2[0][ds(e, 1), :, :].rearrange("o (k p) f -> p (o k) f", p=P)).then_inc(w_done[u], 16)
                        S.hold(x_psum, i * U + (U + u))
                        sp.dma_start(idx[:, 1 - u:2 - u], slot_tok[ds((i * U + (u + 1)) * P, P), :]).then_inc(idx_done[1 - u], 16)

            @block.gpsimd
            def _(pool):
                def gather(u):
                    pool.indirect_dma_start(xg[:, u, :], None, h2_dram, bass.IndirectOffsetOnAxis(ap=idx[:, u:u + 1], axis=0)).then_inc(x_in[u], 16)

                pool.wait_ge(idx_done[0], 32)
                gather(0)
                with pool.Fori(0, NB // U) as i:
                    for u in range(U):
                        v = 1 - u
                        G.hold(idx_done[v], now(i, 16) if u == 0 else now(i + 1, 16))
                        G.hold(x_psum, last(i, U, u + 1))
                        gather(v)
                pool.wait_ge(x_in[0], (NB // U + 1) * 16)

            @block.tensor
            def _(pe):
                E.open(gu_psum, hT_psum, y_psum, x_psum, n=U)
                pe.wait_ge(consts, 32)

                def turn_x(v):
                    for k in range(KD):
                        t = nc.tensor.transpose(pt[:, k * P:(k + 1) * P], xg[:, v, k * P:(k + 1) * P], ident[:, :])
                    t.then_inc(x_psum, 1)

                pe.wait_ge(x_in[0], 16)
                turn_x(0)
                with pe.Fori(0, NB // U) as i:
                    for u in range(U):
                        v = 1 - u
                        E.hold(x_ready, now(i, U, u + 1))
                        E.hold(w_done[u], now(i, 48))
                        E.hold(hid_ready, last(i, U, u + U) if u == 0 else now(i, U, u))
                        for k in range(KD):
                            m = nc.tensor.matmul(pg[:, :], xT[:, u, k, :], wb[:, u, :, k, :], start=k == 0, stop=k == KD - 1)
                        m.then_inc(gu_psum, 1)
                        E.hold(x_in[v], i * 16 + (16 if u == 0 else 32))
                        turn_x(v)
                        E.hold(hid_ready, now(i, U, u + 1))
                        for k in range(2):
                            t = nc.tensor.transpose(phT[:, k * P:(k + 1) * P], hid[:, k * P:(k + 1) * P], ident[:, :])
                        t.then_inc(hT_psum, 1)
                        E.hold(hT_ready, now(i, U, u + 1))
                        E.hold(y_a, now(i, U, u) if u else last(i, U))
                        E.hold(y_v, now(i, U, u) if u else last(i, U))
                        for half in range(2):
                            for k in range(2):
                                m = nc.tensor.matmul(py[:, half * HALF:(half + 1) * HALF], hidT[:, k, :], w2b[:, u, k, half * HALF:(half + 1) * HALF],
                                                     start=k == 0, stop=k == 1)
                        m.then_inc(y_psum, 1)

            @block.scalar
            def _(act):
                A.open(act_done, y_a, n=U)
                A.open(y_out, n=32)
                with act.Fori(0, NB // U) as i:
                    for u in range(U):
                        A.hold(gu_psum, now(i, U, u + 1))
                        nc.scalar.activation(sg[:, :], pg[:, 0:D_EXP], ACT.Silu).then_inc(act_done, 1)
                        A.hold(y_psum, now(i, U, u + 1))
                        A.hold(y_out, last(i, 32))
                        nc.scalar.copy(y[:, u, 0:HALF], py[:, 0:HALF]).then_inc(y_a, 1)
                        A.hold(y_a, now(i, U, u + 1))
                        A.hold(y_v, now(i, U, u + 1))
                        act.dma_start(yb_dram[ds((i * U + u) * P, P), :], y[:, u, :]).then_inc(y_out, 16)
                act.wait_ge(y_out, 16 * (NB + U))

            @block.vector
            def _(dve):
                V.open(hid_ready, hT_ready, y_v, n=U)
                V.open(x_ready, n=U)
                dve.wait_ge(consts, 32)
                gx = vec[:, g0:g0 + KD].unsqueeze(2).to_broadcast([P, KD, P])

                def keep_x(v):
                    nc.vector.tensor_tensor(xT[:, v, :, :], pt[:, :].rearrange("p (k t) -> p k t", k=KD), gx, ALU.mult).then_inc(x_ready, 1)

                dve.wait_ge(x_psum, U + 1)
                keep_x(0)
                with dve.Fori(0, NB // U) as i:
                    for u in range(U):
                        V.hold(act_done, now(i, U, u + 1))
                        V.hold(hT_psum, last(i, U, u + U) if u == 0 else now(i, U, u))
                        nc.vector.tensor_tensor(hid[:, :], sg[:, :], pg[:, D_EXP:HALF], ALU.mult).then_inc(hid_ready, 1)
                        V.hold(x_psum, now(i, U, u + 2))
                        keep_x(1 - u)
                        V.hold(hT_psum, now(i, U, u + 1))
                        V.hold(y_psum, last(i, U, u + U) if u == 0 else now(i, U, u))
                        nc.vector.tensor_copy(hidT[:, :, :], phT[:, 0:D_EXP].rearrange("p (k t) -> p k t", k=2)).then_inc(hT_ready, 1)
                        V.hold(y_psum, now(i, U, u + 1))
                        V.hold(y_out, last(i, 32))
                        nc.vector.tensor_copy(y[:, u, HALF:D], py[:, HALF:D]).then_inc(y_v, 1)


def combine_phase(nc, norm_final_g, slot_u, wts, x1_dram, yb_dram, x2_dram):
    with Phase(nc, "comb") as ph:
        g = ph.sb("g", [P, D])
        x1 = ph.sb("x1", [P, 2, D])
        ya = ph.sb("ya", [P, 2, 2, D])
        junk = ph.sb("junk", [P, D])
        small = ph.sb("small", [P, 2, 4])
        out = ph.sb("out", [P, 2, D])
        names = "consts summed sq ms root out_ready".split()
        consts, summed, sq, ms, root, out_ready = [ph.sem(n) for n in names]
        rows_in = [ph.sem(f"rows_in{u}") for u in range(2)]
        x_in = [ph.sem(f"x_in{u}") for u in range(2)]
        x_out = [ph.sem(f"x_out{u}") for u in range(2)]
        V = ph.engine(nc.vector, "dve")

        with nc.Block() as block:

            @block.sync
            def _(sp):
                sp.dma_start(g[:, :], norm_final_g.partition_broadcast(P)).then_inc(consts, 16)
                for i in range(NT):
                    u = i % 2
                    if i >= 2:
                        sp.wait_ge(out_ready, i - 1)
                    sp.dma_start(x1[:, u, :], x1_dram[i * P:(i + 1) * P, :]).then_inc(x_in[u], 16)
                    if i:
                        sp.wait_ge(out_ready, i)
                        sp.dma_start(x2_dram[(i - 1) * P:i * P, :], out[:, 1 - u, :]).then_inc(x_out[1 - u], 16)
                sp.wait_ge(out_ready, NT)
                sp.dma_start(x2_dram[(NT - 1) * P:T, :], out[:, 1, :]).then_inc(x_out[1], 16)
                for u in range(2):
                    sp.wait_ge(x_out[u], 16 * NT // 2)

            @block.gpsimd
            def _(pool):
                for i in range(NT):
                    u = i % 2
                    if i >= 2:
                        pool.wait_ge(summed, i - 1)
                    for n in range(2):
                        pool.indirect_dma_start(ya[:, u, n, :], None, yb_dram, bass.IndirectOffsetOnAxis(ap=slot_u[:, n * NT + i:n * NT + i + 1], axis=0)).then_inc(rows_in[u], 16)
                for u in range(2):
                    pool.wait_ge(rows_in[u], 16 * NT)

            @block.scalar
            def _(act):
                for i in range(NT):
                    u = i % 2
                    act.wait_ge(summed, i + 1)
                    nc.scalar.activation(junk[:, :], x1[:, u, :], ACT.Square, accum_out=small[:, u, 0:1]).then_inc(sq, 1)
                    act.wait_ge(ms, i + 1)
                    nc.scalar.activation(small[:, u, 2:3], small[:, u, 1:2], ACT.Sqrt).then_inc(root, 1)

            @block.vector
            def _(dve):
                dve.wait_ge(consts, 16)
                for i in range(NT):
                    u = i % 2
                    dve.wait_ge(x_in[u], 16 * (i // 2 + 1))
                    dve.wait_ge(rows_in[u], 32 * (i // 2 + 1))
                    V.link(nc.vector.scalar_tensor_tensor(x1[:, u, :], ya[:, u, 0, :], wts[:, i:i + 1], x1[:, u, :], ALU.mult, ALU.add))
                    nc.vector.scalar_tensor_tensor(x1[:, u, :], ya[:, u, 1, :], wts[:, NT + i:NT + i + 1], x1[:, u, :], ALU.mult, ALU.add).then_inc(summed, 1)
                    dve.wait_ge(sq, i + 1)
                    nc.vector.tensor_scalar(small[:, u, 1:2], small[:, u, 0:1], 1.0 / D, NORM_EPS, ALU.mult, ALU.add).then_inc(ms, 1)
                    dve.wait_ge(root, i + 1)
                    V.link(nc.vector.reciprocal(small[:, u, 3:4], small[:, u, 2:3]))
                    if i >= 2:
                        dve.wait_ge(x_out[u], 16 * (i // 2))
                    nc.vector.scalar_tensor_tensor(out[:, u, :], x1[:, u, :], small[:, u, 3:4], g[:, :], ALU.mult, ALU.mult).then_inc(out_ready, 1)



HD, NQ, NKV, GRP = 64, 16, 4, 4
QKV = (NQ + 2 * NKV) * HD
BAND = 3 * P
ROT = HD // 4
ALPHA = 4.0 ** 0.25
LN_EPS = 1e-5
NEG = -1e30


def gqa_tables():
    pos = np.arange(T, dtype=np.float32)
    inv = np.float32(500000.0) ** (-np.arange(0, ROT, 2, dtype=np.float32) / ROT)
    ang = (pos[:, None] * inv[None, :]).astype(np.float32)
    rope = np.concatenate([np.cos(ang), np.sin(ang)], axis=1).astype(np.float32).reshape(NT, P, ROT).transpose(1, 0, 2)
    q = np.arange(P)[:, None, None] + P * np.arange(NT)[None, :, None]
    k = P * (np.arange(NT)[None, :, None] - 1) + np.arange(BAND)[None, None, :]
    ok = (np.abs(q - k) <= P) & (k >= 0) & (k < T)
    return np.ascontiguousarray(rope), np.where(ok, 0.0, NEG).astype(np.float32)


def gqa_phase(nc, w_qkv, w_o, sink, eye, rope, masks, x_dram, mix_dram):
    with Phase(nc, "gqa") as ph:
        ident = ph.sb("ident", [P, P])
        qT = ph.sb("qT", [P, NQ // 2, T])
        kT = ph.sb("kT", [P, NKV, T + 2 * P])
        v = ph.sb("v", [P, NT + 2, NKV * HD])
        with Phase(nc, "gqap") as one:
            gqa_project(nc, one, w_qkv, eye, rope, x_dram, ident, qT, kT, v)
        with Phase(nc, "gqaa") as two:
            gqa_attend(nc, two, w_o, sink, masks, ident, qT, kT, v, mix_dram)


def gqa_project(nc, ph, w_qkv, eye, rope, x_dram, ident, qT, kT, v):
    w = ph.sb("w", [P, KD, QKV])
    tab = ph.sb("tab", [P, NT, ROT])
    xt = ph.sb("xt", [P, D])
    xT = ph.sb("xT", [P, KD, P])
    qs = ph.sb("qs", [P, NQ, HD])
    ks = ph.sb("ks", [P, NKV, 2, HD])
    rr = ph.sb("rr", [P, 4, NQ + NKV, 8])
    pt = ph.ps("pt", [P, D])
    pq = ph.ps("pq", [P, 3, HALF])
    pk = ph.ps("pk", [P, HALF])
    names = "consts x_in x_psum xT_ready qkv_psum v_kept qk_ready qT_psum qT_kept kT_psum kT_kept zeros".split()
    consts, x_in, x_psum, xT_ready, qkv_psum, v_kept, qk_ready, qT_psum, qT_kept, kT_psum, kT_kept, zeros = [ph.sem(n) for n in names]
    V, A, E, S = (ph.engine(e, n) for e, n in ((nc.vector, "dve"), (nc.scalar, "act"), (nc.tensor, "pe"), (nc.sync, "sp")))

    with nc.Block() as block:

        @block.sync
        def _(sp):
            S.open(x_in, n=16)
            sp.dma_start(ident[:, :], eye).then_inc(consts, 16)
            sp.dma_start(tab[:, :, :], rope).then_inc(consts, 16)
            for k in range(KD):
                sp.dma_start(w[:, k, :], w_qkv[0, k * P:(k + 1) * P, :]).then_inc(consts, 16)
            with sp.Fori(0, NT) as i:
                S.hold(x_psum, last(i))
                sp.dma_start(xt[:, :], x_dram[ds(i * P, P), :]).then_inc(x_in, 16)

        @block.gpsimd
        def _(pool):
            for b in (0, T + P):
                nc.gpsimd.memset(kT[:, :, b:b + P], 0.0)
            for b in (0, NT + 1):
                z = nc.gpsimd.memset(v[:, b, :], 0.0)
            z.then_inc(zeros, 1)

        @block.tensor
        def _(pe):
            E.open(x_psum, qkv_psum, qT_psum, kT_psum)
            pe.wait_ge(consts, (2 + KD) * 16)
            with pe.Fori(0, NT) as i:
                E.hold(x_in, now(i, 16))
                E.hold(qT_kept, last(i))
                for k in range(KD):
                    t = nc.tensor.transpose(pt[:, k * P:(k + 1) * P], xt[:, k * P:(k + 1) * P], ident[:, :])
                t.then_inc(x_psum, 1)
                E.hold(xT_ready, now(i))
                E.hold(qk_ready, last(i))
                E.hold(v_kept, last(i))
                for b in range(3):
                    for k in range(KD):
                        m = nc.tensor.matmul(pq[:, b, :], xT[:, k, :], w[:, k, b * HALF:(b + 1) * HALF], start=k == 0, stop=k == KD - 1)
                m.then_inc(qkv_psum, 1)
                E.hold(qk_ready, now(i))
                for n in range(NQ // 2):
                    t = nc.tensor.transpose(pt[:, n * P:(n + 1) * P], qs[:, 2 * n:2 * n + 2, :].rearrange("p h d -> p (h d)"), ident[:, :])
                t.then_inc(qT_psum, 1)
                E.hold(kT_kept, last(i))
                for n in range(NKV):
                    t = nc.tensor.transpose(pk[:, n * P:(n + 1) * P], ks[:, n, :, :].rearrange("p h d -> p (h d)"), ident[:, :])
                t.then_inc(kT_psum, 1)

        @block.scalar
        def _(act):
            A.open(xT_ready, v_kept, qT_kept)
            with act.Fori(0, NT) as i:
                A.hold(x_psum, now(i))
                A.hold(qkv_psum, last(i))
                nc.scalar.copy(xT[:, :, :], pt[:, :].rearrange("p (k t) -> p k t", k=KD)).then_inc(xT_ready, 1)
                A.hold(qk_ready, now(i))
                nc.scalar.copy(v[:, ds(i + 1, 1), :].rearrange("p o n -> p (o n)"), pq[:, 2, NKV * HD:HALF]).then_inc(v_kept, 1)
                A.hold(qT_psum, now(i))
                nc.scalar.copy(qT[:, :, ds(i * P, P)], pt[:, :].rearrange("p (k t) -> p k t", k=NQ // 2)).then_inc(qT_kept, 1)

        @block.vector
        def _(dve):
            V.open(qk_ready, kT_kept)
            dve.wait_ge(zeros, 1)
            dve.wait_ge(consts, (2 + KD) * 16)
            with dve.Fori(0, NT) as i:
                V.loop(i, 1)
                V.hold(qkv_psum, now(i))
                V.hold(kT_psum, last(i))
                q_src = pq[:, 0:2, :].rearrange("p b (h d) -> p (b h) d", d=HD)
                k_src = pq[:, 2, 0:NKV * HD].rearrange("p (h d) -> p h d", d=HD)
                co, si = tab[:, ds(i, 1), 0:8], tab[:, ds(i, 1), 8:16]
                nc.vector.tensor_copy(qs[:, :, ROT:HD], q_src[:, :, ROT:HD])
                for b in range(2):
                    nc.vector.tensor_copy(ks[:, :, b, ROT:HD], k_src[:, :, ROT:HD])
                for src, lo, n in ((q_src, 0, NQ), (k_src, NQ, NKV)):
                    for m, (c, half) in enumerate(((co, 0), (si, 8), (si, 0), (co, 8))):
                        r = nc.vector.tensor_tensor(rr[:, m, lo:lo + n, :], src[:, :, half:half + 8], c.to_broadcast([P, n, 8]), ALU.mult)
                V.link(r)
                nc.vector.tensor_tensor(qs[:, :, 0:8], rr[:, 0, 0:NQ, :], rr[:, 1, 0:NQ, :], ALU.subtract)
                nc.vector.tensor_tensor(qs[:, :, 8:16], rr[:, 2, 0:NQ, :], rr[:, 3, 0:NQ, :], ALU.add)
                for b in range(2):
                    nc.vector.tensor_tensor(ks[:, :, b, 0:8], rr[:, 0, NQ:NQ + NKV, :], rr[:, 1, NQ:NQ + NKV, :], ALU.subtract)
                    r = nc.vector.tensor_tensor(ks[:, :, b, 8:16], rr[:, 2, NQ:NQ + NKV, :], rr[:, 3, NQ:NQ + NKV, :], ALU.add)
                r.then_inc(qk_ready, 1)
                V.hold(kT_psum, now(i))
                nc.vector.tensor_copy(kT[:, :, ds(i * P + P, P)], pk[:, :].rearrange("p (k t) -> p k t", k=NKV)).then_inc(kT_kept, 1)
            V.done(NT)


def gqa_attend(nc, ph, w_o, sink, masks, ident, qT, kT, v, mix_dram):
    SCALE = float(HD) ** -0.5
    wo = ph.sb("wo", [P, KD, D])
    mask = ph.sb("mask", [P, NT, BAND])
    mk = ph.sb("mk", [P, BAND])
    sk = ph.sb("sk", [P, NQ])
    q_t = ph.sb("q_t", [P, NQ // 2, P])
    k_t = ph.sb("k_t", [P, NKV, BAND])
    s = ph.sb("s", [P, GRP, BAND])
    pr = ph.sb("pr", [P, GRP, BAND])
    pT = ph.sb("pT", [P, 3, GRP, P])
    mx = ph.sb("mx", [P, GRP])
    nmx = ph.sb("nmx", [P, GRP])
    ex = ph.sb("ex", [P, GRP])
    den = ph.sb("den", [P, GRP])
    rden = ph.sb("rden", [P, GRP])
    o = ph.sb("o", [P, D])
    oT = ph.sb("oT", [P, KD, P])
    out = ph.sb("out", [P, D])
    pS = ph.ps("pS", [P, GRP, HALF])
    pP = ph.ps("pP", [P, 3, HALF])
    pO = ph.ps("pO", [P, HALF])
    names = "consts q_in s_psum s_ready sh_ready exp_done p_psum p_kept o_psum o_ready oT_psum oT_kept out_psum out_ready out_done mk_in rd".split()
    (consts, q_in, s_psum, s_ready, sh_ready, exp_done, p_psum, p_kept, o_psum, o_ready, oT_psum, oT_kept, out_psum, out_ready, out_done,
     mk_in, rd) = [ph.sem(n) for n in names]
    V, G, A, E, S = (ph.engine(e, n) for e, n in ((nc.vector, "dve"), (nc.gpsimd, "pool"), (nc.scalar, "act"),
                                                  (nc.tensor, "pe"), (nc.sync, "sp")))
    NCONST = 2 + KD

    with nc.Block() as block:

        @block.sync
        def _(sp):
            S.open(out_done, n=16)
            sp.dma_start(mask[:, :, :], masks).then_inc(consts, 16)
            sp.dma_start(sk[:, :], sink[0].partition_broadcast(P)).then_inc(consts, 16)
            for k in range(KD):
                sp.dma_start(wo[:, k, :], w_o[0, k * P:(k + 1) * P, :]).then_inc(consts, 16)
            with sp.Fori(0, NT) as i:
                S.hold(out_ready, now(i))
                sp.dma_start(mix_dram[ds(i * P, P), :], out[:, :]).then_inc(out_done, 16)
            sp.wait_ge(out_done, 16 * (NT + 1))

        @block.gpsimd
        def _(pool):
            G.open(q_in, mk_in)
            pool.wait_ge(consts, NCONST * 16)
            with pool.Fori(0, NT) as i:
                G.hold(s_psum, last(i, NKV))
                nc.gpsimd.tensor_copy(k_t[:, :, :], kT[:, :, ds(i * P, BAND)])
                nc.gpsimd.tensor_copy(q_t[:, :, :], qT[:, :, ds(i * P, P)]).then_inc(q_in, 1)
                G.hold(s_ready, last(i, NKV))
                nc.gpsimd.tensor_copy(mk[:, :], mask[:, ds(i, 1), :].rearrange("p o n -> p (o n)")).then_inc(mk_in, 1)

        @block.tensor
        def _(pe):
            E.open(s_psum, p_psum, o_psum, n=NKV)
            E.open(oT_psum, out_psum)
            pe.wait_ge(consts, NCONST * 16)

            def scores(i, g):
                for h in range(GRP):
                    hh = GRP * g + h
                    half = slice(64 * (hh % 2), 64 * (hh % 2) + 64)
                    m = nc.tensor.matmul(pS[:, h, 0:BAND], q_t[half, hh // 2, :], k_t[half, g, :], start=True, stop=True)
                m.then_inc(s_psum, 1)

            with pe.Fori(0, NT) as i:
                for g in range(NKV):
                    if g == 0:
                        E.hold(q_in, now(i))
                        E.hold(out_ready, last(i))
                        scores(i, 0)
                    E.hold(exp_done, now(i, NKV, g + 1))
                    if g == 0:
                        E.hold(oT_kept, last(i))
                    E.hold(p_kept, now(i, NKV, g) if g else last(i, NKV))
                    for kb in range(3):
                        for h in range(GRP):
                            t = nc.tensor.transpose(pP[:, kb, h * P:(h + 1) * P], pr[:, h, kb * P:(kb + 1) * P], ident[:, :])
                    t.then_inc(p_psum, 1)
                    if g + 1 < NKV:
                        E.hold(s_ready, now(i, NKV, g + 1))
                        scores(i, g + 1)
                    E.hold(p_kept, now(i, NKV, g + 1))
                    E.hold(o_ready, now(i, NKV, g) if g else last(i, NKV))
                    for h in range(GRP):
                        for kb in range(3):
                            m = nc.tensor.matmul(pO[:, h * HD:(h + 1) * HD], pT[:, kb, h, :], v[:, ds(i + kb, 1), g * HD:(g + 1) * HD].rearrange("p o n -> p (o n)"),
                                                 start=kb == 0, stop=kb == 2)
                    m.then_inc(o_psum, 1)
                E.hold(o_ready, now(i, NKV))
                for k in range(KD):
                    t = nc.tensor.transpose(pP[:, k // 4, k % 4 * P:(k % 4 + 1) * P], o[:, k * P:(k + 1) * P], ident[:, :])
                t.then_inc(oT_psum, 1)
                E.hold(oT_kept, now(i))
                E.hold(s_ready, now(i, NKV))
                for half in range(2):
                    for k in range(KD):
                        m = nc.tensor.matmul(pS[:, half, :], oT[:, k, :], wo[:, k, half * HALF:(half + 1) * HALF], start=k == 0, stop=k == KD - 1)
                m.then_inc(out_psum, 1)

        @block.scalar
        def _(act):
            A.open(exp_done, p_kept, n=NKV)
            A.open(oT_kept)
            with act.Fori(0, NT) as i:
                for g in range(NKV):
                    A.hold(sh_ready, now(i, NKV, g + 1))
                    A.hold(p_psum, now(i, NKV, g) if g else last(i, NKV))
                    for h in range(GRP):
                        nc.scalar.activation(pr[:, h, :], s[:, h, :], ACT.Exp, bias=nmx[:, h:h + 1], accum_out=den[:, h:h + 1])
                    nc.scalar.activation(ex[:, :], ex[:, :], ACT.Exp).then_inc(exp_done, 1)
                    A.hold(p_psum, now(i, NKV, g + 1))
                    A.hold(o_psum, now(i, NKV, g) if g else last(i, NKV))
                    nc.scalar.copy(pT[:, :, :, :].rearrange("p k h t -> p k (h t)"), pP[:, :, :]).then_inc(p_kept, 1)
                A.hold(oT_psum, now(i))
                A.hold(out_psum, last(i))
                nc.scalar.copy(oT[:, :, :].rearrange("p (b k) t -> p b (k t)", b=2), pP[:, 0:2, :]).then_inc(oT_kept, 1)

        @block.vector
        def _(dve):
            V.open(s_ready, sh_ready, o_ready, n=NKV)
            V.open(out_ready)
            dve.wait_ge(consts, NCONST * 16)
            with dve.Fori(0, NT) as i:
                V.loop(i, 4 * NKV)
                for g in range(NKV):
                    if g == 0:
                        V.hold(mk_in, now(i))
                    V.hold(s_psum, now(i, NKV, g + 1))
                    V.hold(exp_done, now(i, NKV, g) if g else last(i, NKV))
                    V.link(nc.vector.scalar_tensor_tensor(s[:, :, :], pS[:, :, 0:BAND], SCALE, mk[:, :].unsqueeze(1).to_broadcast([P, GRP, BAND]), ALU.mult, ALU.add))
                    dve.sem_inc(s_ready, 1)
                    V.link(nc.vector.reduce_max(mx[:, :], s[:, :, :], AX_X))
                    V.link(nc.vector.tensor_tensor(mx[:, :], mx[:, :], sk[:, GRP * g:GRP * (g + 1)], ALU.max))
                    nc.vector.tensor_scalar(nmx[:, :], mx[:, :], -1.0, None, ALU.mult)
                    nc.vector.tensor_tensor(ex[:, :], sk[:, GRP * g:GRP * (g + 1)], mx[:, :], ALU.subtract).then_inc(sh_ready, 1)
                    V.hold(exp_done, now(i, NKV, g + 1))
                    V.link(nc.vector.tensor_tensor(den[:, :], den[:, :], ex[:, :], ALU.add))
                    nc.vector.reciprocal(rden[:, :], den[:, :]).then_inc(rd, 1)
                    V.hold(rd, i * NKV + (g + 1))
                    V.hold(o_psum, now(i, NKV, g + 1))
                    V.hold(oT_psum, last(i))
                    nc.vector.tensor_tensor(o[:, g * 256:(g + 1) * 256].rearrange("p (h d) -> p h d", h=GRP), pO[:, 0:256].rearrange("p (h d) -> p h d", h=GRP),
                                            rden[:, :].unsqueeze(2).to_broadcast([P, GRP, HD]), ALU.mult).then_inc(o_ready, 1)
                V.hold(out_psum, now(i))
                V.hold(out_done, last(i, 16))
                nc.vector.tensor_copy(out[:, :].rearrange("p (b n) -> p b n", b=2), pS[:, 0:2, :]).then_inc(out_ready, 1)
            V.done(NT)


def norm_phase(nc, name, ln_g, ln_b, x_dram, add_dram, out_dram, final=False):
    with Phase(nc, name) as ph:
        gb = ph.sb("gb", [P, 2, D])
        U = 2
        xt = ph.sb("xt", [P, U, D])
        at = ph.sb("at", [P, U, D])
        r = ph.sb("r", [P, D])
        junk = ph.sb("junk", [P, D])
        small = ph.sb("small", [P, 8])
        out = ph.sb("out", [P, U, D])
        names = "consts summed mean cent sq ms root ready".split()
        consts, summed, mean, cent, sq, ms, root, ready = [ph.sem(n) for n in names]
        x_in = [ph.sem(f"x_in{u}") for u in range(U)]
        done = [ph.sem(f"done{u}") for u in range(U)]
        V, A, S = (ph.engine(e, n) for e, n in ((nc.vector, "dve"), (nc.scalar, "act"), (nc.sync, "sp")))

        with nc.Block() as block:

            @block.sync
            def _(sp):
                for u in range(U):
                    S.open(x_in[u], n=32)
                sp.dma_start(gb[:, 0, :], ln_g.partition_broadcast(P)).then_inc(consts, 16)
                sp.dma_start(gb[:, 1, :], ln_b.partition_broadcast(P)).then_inc(consts, 16)
                with sp.Fori(0, NT // U) as i:
                    for u in range(U):
                        S.hold(summed, last(i, U, u + 1))
                        sp.dma_start(xt[:, u, :], x_dram[ds((i * U + u) * P, P), :]).then_inc(x_in[u], 16)
                        sp.dma_start(at[:, u, :], add_dram[ds((i * U + u) * P, P), :]).then_inc(x_in[u], 16)

            @block.scalar
            def _(act):
                A.open(sq, root, mean, n=U)
                for u in range(U):
                    A.open(done[u], n=16)
                with act.Fori(0, NT // U) as i:
                    for u in range(U):
                        A.hold(summed, now(i, U, u + 1))
                        nc.scalar.activation(junk[:, :], r[:, :], ACT.Copy, accum_out=small[:, 0:1]).then_inc(mean, 1)
                        A.hold(cent, now(i, U, u + 1))
                        nc.scalar.activation(junk[:, :], r[:, :], ACT.Square, accum_out=small[:, 2:3]).then_inc(sq, 1)
                        A.hold(ms, now(i, U, u + 1))
                        nc.scalar.activation(small[:, 4:5], small[:, 3:4], ACT.Sqrt).then_inc(root, 1)
                        A.hold(ready, now(i, U, u + 1))
                        act.dma_start(out_dram[ds((i * U + u) * P, P), :], out[:, u, :]).then_inc(done[u], 16)
                for u in range(U):
                    act.wait_ge(done[u], 16 * (NT // U + 1))

            @block.vector
            def _(dve):
                V.open(summed, cent, ms, ready, n=U)
                dve.wait_ge(consts, 32)
                with dve.Fori(0, NT // U) as i:
                    V.loop(i, 4 * U)
                    for u in range(U):
                        V.hold(x_in[u], now(i, 32))
                        nc.vector.scalar_tensor_tensor(r[:, :], xt[:, u, :], ALPHA, at[:, u, :], ALU.mult, ALU.add).then_inc(summed, 1)
                        V.hold(mean, now(i, U, u + 1))
                        V.link(nc.vector.tensor_scalar(small[:, 1:2], small[:, 0:1], 1.0 / D, None, ALU.mult))
                        nc.vector.tensor_scalar(r[:, :], r[:, :], small[:, 1:2], None, ALU.subtract).then_inc(cent, 1)
                        V.hold(sq, now(i, U, u + 1))
                        nc.vector.tensor_scalar(small[:, 3:4], small[:, 2:3], 1.0 / D, LN_EPS, ALU.mult, ALU.add).then_inc(ms, 1)
                        V.hold(root, now(i, U, u + 1))
                        V.link(nc.vector.reciprocal(small[:, 5:6], small[:, 4:5]))
                        V.hold(done[u], last(i, 16))
                        V.link(nc.vector.scalar_tensor_tensor(out[:, u, :], r[:, :], small[:, 5:6], gb[:, 0, :], ALU.mult, ALU.mult))
                        V.link(nc.vector.tensor_tensor(out[:, u, :], out[:, u, :], gb[:, 1, :], ALU.add))
                        dve.sem_inc(ready, 1)
                V.done(NT // U)



E2 = 16
CAP = 2 * T // E2
FF = D


def choose_phase(nc, name, w_router, eye, x_dram, acc_dram, gate, idx):
    with Phase(nc, name) as ph:
        ident = ph.sb("ident", [P, P])
        w = ph.sb("w", [P, KD, E2])
        xt = ph.sb("xt", [P, 2, D])
        xT = ph.sb("xT", [P, KD, P])
        lg = ph.sb("lg", [P, E2])
        small = ph.sb("small", [P, 4])
        ex = ph.sb("ex", [P, E2])
        aff = ph.sb("aff", [P, E2])
        affT = ph.sb("affT", [E2, 2, T])
        top = ph.sb("top", [E2, CAP])
        top_i = ph.sb("top_i", [E2, CAP], U32)
        top_f = ph.sb("top_f", [E2, CAP])
        zero = ph.sb("zero", [P, D])
        pt = ph.ps("pt", [P, D])
        pl = ph.ps("pl", [P, HALF])
        pa = ph.ps("pa", [P, HALF])
        names = "consts zeroed acc_out x_psum xT_ready l_psum sh_ready exp_done aff_ready a_psum a_kept tops f_psum".split()
        consts, zeroed, acc_out, x_psum, xT_ready, l_psum, sh_ready, exp_done, aff_ready, a_psum, a_kept, tops, f_psum = [ph.sem(n) for n in names]
        x_in = [ph.sem(f"x_in{u}") for u in range(2)]
        V, A, E, S = (ph.engine(e, n) for e, n in ((nc.vector, "dve"), (nc.scalar, "act"), (nc.tensor, "pe"), (nc.sync, "sp")))
        U = 2

        with nc.Block() as block:

            @block.sync
            def _(sp):
                for u in range(U):
                    S.open(x_in[u], n=16)
                sp.dma_start(ident[:, :], eye).then_inc(consts, 16)
                sp.dma_start(w[:, :, :], w_router.rearrange("(k p) e -> p k e", p=P)).then_inc(consts, 16)
                with sp.Fori(0, NT // U) as i:
                    for u in range(U):
                        S.hold(x_psum, last(i, U, u + 1))
                        sp.dma_start(xt[:, u, :], x_dram[ds((i * U + u) * P, P), :]).then_inc(x_in[u], 16)
                sp.wait_ge(zeroed, 1)
                for n in range(NT):
                    sp.dma_start(acc_dram[n * P:(n + 1) * P, :], zero[:, :]).then_inc(acc_out, 16)
                sp.wait_ge(acc_out, 16 * NT)

            @block.gpsimd
            def _(pool):
                nc.gpsimd.memset(zero[:, :], 0.0).then_inc(zeroed, 1)

            @block.tensor
            def _(pe):
                E.open(x_psum, l_psum, a_psum, n=U)
                pe.wait_ge(consts, 32)
                with pe.Fori(0, NT // U) as i:
                    for u in range(U):
                        E.hold(x_in[u], now(i, 16))
                        E.hold(xT_ready, last(i, U, u + U) if u == 0 else now(i, U, u))
                        for k in range(KD):
                            t = nc.tensor.transpose(pt[:, k * P:(k + 1) * P], xt[:, u, k * P:(k + 1) * P], ident[:, :])
                        t.then_inc(x_psum, 1)
                        E.hold(xT_ready, now(i, U, u + 1))
                        E.hold(exp_done, last(i, U, u + U) if u == 0 else now(i, U, u))
                        for k in range(KD):
                            m = nc.tensor.matmul(pl[:, 0:E2], xT[:, k, :], w[:, k, :], start=k == 0, stop=k == KD - 1)
                        m.then_inc(l_psum, 1)
                        E.hold(aff_ready, now(i, U, u + 1))
                        E.hold(a_kept, last(i, U, u + U) if u == 0 else now(i, U, u))
                        nc.tensor.transpose(pa[0:E2, 0:P], aff[:, :], ident[:, :]).then_inc(a_psum, 1)
                pe.wait_ge(tops, 1)
                nc.tensor.transpose(pl[:, 0:E2], top[:, :], ident[0:E2, 0:E2])
                nc.tensor.transpose(pl[:, E2:2 * E2], top_f[:, :], ident[0:E2, 0:E2]).then_inc(f_psum, 1)

            @block.scalar
            def _(act):
                A.open(xT_ready, exp_done, n=U)
                with act.Fori(0, NT // U) as i:
                    for u in range(U):
                        A.hold(x_psum, now(i, U, u + 1))
                        A.hold(l_psum, last(i, U, u + U) if u == 0 else now(i, U, u))
                        nc.scalar.copy(xT[:, :, :], pt[:, :].rearrange("p (k t) -> p k t", k=KD)).then_inc(xT_ready, 1)
                        A.hold(sh_ready, now(i, U, u + 1))
                        A.hold(aff_ready, last(i, U, u + U) if u == 0 else now(i, U, u))
                        nc.scalar.activation(ex[:, :], pl[:, 0:E2], ACT.Exp, bias=small[:, 1:2], accum_out=small[:, 2:3]).then_inc(exp_done, 1)

            @block.vector
            def _(dve):
                V.open(sh_ready, aff_ready, a_kept, n=U)
                with dve.Fori(0, NT // U) as i:
                    V.loop(i, 2 * U)
                    for u in range(U):
                        V.hold(l_psum, now(i, U, u + 1))
                        V.link(nc.vector.reduce_max(small[:, 0:1], pl[:, 0:E2], AX_X))
                        nc.vector.tensor_scalar(small[:, 1:2], small[:, 0:1], -1.0, None, ALU.mult).then_inc(sh_ready, 1)
                        V.hold(exp_done, now(i, U, u + 1))
                        V.link(nc.vector.reciprocal(small[:, 3:4], small[:, 2:3]))
                        V.hold(a_psum, last(i, U, u + U) if u == 0 else now(i, U, u))
                        nc.vector.tensor_scalar(aff[:, :], ex[:, :], small[:, 3:4], None, ALU.mult).then_inc(aff_ready, 1)
                        V.hold(a_psum, now(i, U, u + 1))
                        nc.vector.tensor_copy(affT[:, 0, ds((i * U + u) * P, P)], pa[0:E2, 0:P]).then_inc(a_kept, 1)
                V.done(NT // U)
                dve.wait_ge(a_kept, NT + U)
                for n in range(CAP // 8):
                    eight = slice(8 * n, 8 * n + 8)
                    V.link(nc.vector.max(top[:, eight], affT[:, n % 2, :]))
                    nc.vector.max_index(top_i[:, eight], top[:, eight], affT[:, n % 2, :])
                    V.link(nc.vector.match_replace(affT[:, (n + 1) % 2, :], top[:, eight], affT[:, n % 2, :], -1.0))
                V.link(nc.vector.tensor_copy(top_f[:, :], top_i[:, :]))
                dve.sem_inc(tops, 1)
                dve.wait_ge(f_psum, 1)
                nc.vector.tensor_copy(gate[:, :], pl[:, 0:E2])
                nc.vector.tensor_copy(idx[:, E2:E2 + 1], pl[:, E2:E2 + 1])
                V.link(nc.vector.tensor_copy(idx[:, 0:E2], pl[:, E2:2 * E2]))


def choice_phase(nc, name, w_gu, w_dn, eye, x_dram, acc_dram, gate, idx):
    with Phase(nc, name) as ph:
        ident = ph.sb("ident", [P, P])
        wg = ph.sb("wg", [P, KD, 2 * FF])
        wd = ph.sb("wd", [P, KD, D])
        ic = [ph.sb(f"ic{v}", [P, 1], U32) for v in range(2)]
        xg = ph.sb("xg", [P, D])
        xT = ph.sb("xT", [P, KD, P])
        sg = ph.sb("sg", [P, FF])
        hid = ph.sb("hid", [P, FF])
        hidT = ph.sb("hidT", [P, KD, P])
        y = ph.sb("y", [P, D])
        pg = ph.ps("pg", [P, 4, HALF])
        pt = ph.ps("pt", [P, D])
        py = ph.ps("py", [P, D])
        names = "consts ic_ready x_in x_psum x_ready g_used silu hid_ready h_psum hT_ready d_used y_ready sent added".split()
        (consts, ic_ready, x_in, x_psum, x_ready, g_used, silu, hid_ready, h_psum, hT_ready, d_used, y_ready, sent,
         added) = [ph.sem(n) for n in names]
        wg_in = [ph.sem(f"wg_in{k}") for k in range(KD)]
        wd_in = [ph.sem(f"wd_in{k}") for k in range(KD)]
        V, G, A, E, S = (ph.engine(e, n) for e, n in ((nc.vector, "dve"), (nc.gpsimd, "pool"), (nc.scalar, "act"),
                                                      (nc.tensor, "pe"), (nc.sync, "sp")))

        with nc.Block() as block:

            @block.sync
            def _(sp):
                for k in range(KD):
                    S.open(wg_in[k], wd_in[k], n=16)
                sp.dma_start(ident[:, :], eye).then_inc(consts, 16)
                with sp.Fori(0, E2) as e:
                    for k in range(KD):
                        S.hold(g_used, last(e, KD, k + 1))
                        sp.dma_start(wg[:, k, :].unsqueeze(1), w_gu[ds(e, 1), k * P:(k + 1) * P, :].rearrange("o p n -> p o n")).then_inc(wg_in[k], 16)
                    for k in range(KD):
                        S.hold(d_used, last(e, KD, k + 1))
                        sp.dma_start(wd[:, k, :].unsqueeze(1), w_dn[ds(e, 1), k * P:(k + 1) * P, :].rearrange("o p n -> p o n")).then_inc(wd_in[k], 16)

            @block.gpsimd
            def _(pool):
                G.open(ic_ready, sent)

                def gather(v):
                    pool.indirect_dma_start(xg[:, :], None, x_dram, bass.IndirectOffsetOnAxis(ap=ic[v][:, :], axis=0)).then_inc(x_in, 16)

                nc.gpsimd.tensor_copy(ic[0][:, :], idx[:, 0:1]).then_inc(ic_ready, 1)
                pool.wait_ge(ic_ready, 2)
                gather(0)
                with pool.Fori(0, E2 // 2) as i:
                    for u in range(2):
                        v = 1 - u
                        nc.gpsimd.tensor_copy(ic[v][:, :], idx[:, ds(i * 2 + (u + 1), 1)]).then_inc(ic_ready, 1)
                        G.hold(ic_ready, i * 2 + (u + 3))
                        G.hold(x_psum, i * 2 + (u + 2))
                        gather(v)
                        G.hold(y_ready, i * 2 + (u + 2))
                        pool.indirect_dma_start(acc_dram, bass.IndirectOffsetOnAxis(ap=ic[u][:, :], axis=0), y[:, :], None, compute_op=ALU.add).then_inc(added, 16)
                        G.hold(added, i * 32 + (16 * u + 16))
                        pool.sem_inc(sent, 1)
                pool.wait_ge(x_in, 16 * (E2 + 1))

            @block.tensor
            def _(pe):
                E.open(h_psum, x_psum)
                E.open(g_used, d_used, n=KD)
                pe.wait_ge(consts, 16)

                def turn_x():
                    for k in range(KD):
                        t = nc.tensor.transpose(pt[:, k * P:(k + 1) * P], xg[:, k * P:(k + 1) * P], ident[:, :])
                    t.then_inc(x_psum, 1)

                pe.wait_ge(x_in, 16)
                turn_x()
                with pe.Fori(0, E2) as e:
                    E.hold(x_ready, now(e))
                    for k in range(KD):
                        E.hold(wg_in[k], now(e, 16))
                        for b in range(4):
                            m = nc.tensor.matmul(pg[:, b, :], xT[:, k, :], wg[:, k, b * HALF:(b + 1) * HALF], start=k == 0, stop=k == KD - 1)
                        m.then_inc(g_used, 1)
                    E.hold(x_in, e * 16 + 32)
                    turn_x()
                    E.hold(hid_ready, now(e))
                    E.hold(x_ready, now(e + 1))
                    for k in range(KD):
                        t = nc.tensor.transpose(pt[:, k * P:(k + 1) * P], hid[:, k * P:(k + 1) * P], ident[:, :])
                    t.then_inc(h_psum, 1)
                    E.hold(hT_ready, now(e))
                    E.hold(y_ready, last(e))
                    for k in range(KD):
                        E.hold(wd_in[k], now(e, 16))
                        for b in range(2):
                            m = nc.tensor.matmul(py[:, b * HALF:(b + 1) * HALF], hidT[:, k, :], wd[:, k, b * HALF:(b + 1) * HALF], start=k == 0, stop=k == KD - 1)
                        m.then_inc(d_used, 1)

            @block.scalar
            def _(act):
                A.open(silu, hT_ready)
                with act.Fori(0, E2) as e:
                    A.hold(g_used, now(e, KD))
                    A.hold(hid_ready, last(e))
                    nc.scalar.activation(sg[:, :].rearrange("p (b n) -> p b n", b=2), pg[:, 0:2, :], ACT.Silu).then_inc(silu, 1)
                    A.hold(h_psum, now(e))
                    A.hold(d_used, last(e, KD))
                    nc.scalar.copy(hidT[:, :, :], pt[:, :].rearrange("p (k t) -> p k t", k=KD)).then_inc(hT_ready, 1)

            @block.vector
            def _(dve):
                V.open(hid_ready, x_ready, y_ready)
                dve.wait_ge(x_psum, 2)

                def keep_x():
                    nc.vector.tensor_copy(xT[:, :, :], pt[:, :].rearrange("p (k t) -> p k t", k=KD)).then_inc(x_ready, 1)

                keep_x()
                with dve.Fori(0, E2) as e:
                    V.hold(silu, now(e))
                    V.hold(h_psum, last(e))
                    nc.vector.tensor_tensor(hid[:, :].rearrange("p (b n) -> p b n", b=2), sg[:, :].rearrange("p (b n) -> p b n", b=2),
                                            pg[:, 2:4, :], ALU.mult).then_inc(hid_ready, 1)
                    V.hold(x_psum, now(e + 1))
                    keep_x()
                    V.hold(d_used, now(e, KD))
                    V.hold(sent, e + 1)
                    nc.vector.tensor_scalar(y[:, :], py[:, :], gate[:, ds(e, 1)], None, ALU.mult).then_inc(y_ready, 1)



NBLK, BW = 4, 256
GELU_C = float(np.sqrt(2.0 / np.pi))
CONV = 4


def lru_phase(nc, vecs, w_in, w_r, w_i, w_out, eye, x_dram, ggT_dram, mix_dram):
    with Phase(nc, "lru") as ph:
        vec = ph.sb("vec", [P, VEC_N])
        xc = ph.sb("xc", [P, KD, T])
        with Phase(nc, "lrui") as one:
            lru_in(nc, one, vec, xc, vecs, w_in, eye, x_dram, ggT_dram)
        with Phase(nc, "lrus") as two:
            lru_scan(nc, two, vec, xc, w_r, w_i, ggT_dram)
    with Phase(nc, "lruo") as three:
        lru_out(nc, three, w_out, ggT_dram, mix_dram)


def lru_in(nc, ph, vec, xc, vecs, w_in, eye, x_dram, ggT_dram):
    ident = ph.sb("ident", [P, P])
    xt = ph.sb("xt", [P, 2, D])
    xT = ph.sb("xT", [P, KD, T])
    w = ph.sb("w", [P, 2, 2, KD, P])
    gx = ph.sb("gx", [P, T])
    g2 = ph.sb("g2", [P, T])
    g3 = ph.sb("g3", [P, T])
    gg = ph.sb("gg", [P, T])
    cv = ph.sb("cv", [P, T])
    cw = ph.sb("cw", [P, CONV + 1])
    pt = ph.ps("pt", [P, D])
    pg = ph.ps("pg", [P, T])
    px = ph.ps("px", [P, T])
    U = 2
    names = "consts x_psum xT_ready g_psum b_psum g_copied cube sig gg_ready gg_out cw_ready conv_v conv_done".split()
    consts, x_psum, xT_ready, g_psum, b_psum, g_copied, cube, sig, gg_ready, gg_out, cw_ready, conv_v, conv_done = [ph.sem(n) for n in names]
    x_in = [ph.sem(f"x_in{u}") for u in range(U)]
    w_done = [ph.sem(f"w_done{u}") for u in range(U)]
    V, G, A, E, S = (ph.engine(e, n) for e, n in ((nc.vector, "dve"), (nc.gpsimd, "pool"), (nc.scalar, "act"),
                                                  (nc.tensor, "pe"), (nc.sync, "sp")))
    wv = w_in[0].rearrange("(k p) n -> p k n", p=P)
    gg_view = ggT_dram.rearrange("(k p) t -> p k t", p=P)
    c0 = vec_at("lru_conv_w_2")[0]
    cb = vec_at("lru_conv_b_2")[0]

    with nc.Block() as block:

        @block.sync
        def _(sp):
            for u in range(U):
                S.open(x_in[u], n=16)
                S.open(w_done[u], n=32)
            sp.dma_start(ident[:, :], eye).then_inc(consts, 16)
            sp.dma_start(vec[:, :], vecs).then_inc(consts, 16)
            with sp.Fori(0, NT // U) as i:
                for u in range(U):
                    S.hold(x_psum, last(i, U, u + 1))
                    sp.dma_start(xt[:, u, :], x_dram[ds((i * U + u) * P, P), :]).then_inc(x_in[u], 16)
            with sp.Fori(0, KD // U) as i:
                for u in range(U):
                    S.hold(b_psum, last(i, U, u + 1))
                    for n in range(2):
                        sp.dma_start(w[:, u, n, :, :], wv[:, :, ds(i * (U * P) + (n * D + u * P), P)]).then_inc(w_done[u], 16)

        @block.gpsimd
        def _(pool):
            G.open(cw_ready)
            pool.wait_ge(consts, 32)
            with pool.Fori(0, KD) as i:
                G.hold(conv_done, last(i))
                for j in range(CONV):
                    nc.gpsimd.tensor_copy(cw[:, j:j + 1], vec[:, ds(i + (c0 + j * KD), 1)])
                nc.gpsimd.tensor_copy(cw[:, CONV:CONV + 1], vec[:, ds(i + cb, 1)]).then_inc(cw_ready, 1)

        @block.tensor
        def _(pe):
            E.open(x_psum, g_psum, b_psum, n=U)
            pe.wait_ge(consts, 32)
            with pe.Fori(0, NT // U) as i:
                for u in range(U):
                    E.hold(x_in[u], now(i, 16))
                    E.hold(xT_ready, last(i, U, u + U) if u == 0 else now(i, U, u))
                    for k in range(KD):
                        t = nc.tensor.transpose(pt[:, k * P:(k + 1) * P], xt[:, u, k * P:(k + 1) * P], ident[:, :])
                    t.then_inc(x_psum, 1)
            pe.wait_ge(xT_ready, NT + U)
            with pe.Fori(0, KD // U) as i:
                for u in range(U):
                    E.hold(w_done[u], now(i, 32))
                    for n, ps in enumerate((pg, px)):
                        if n == 0:
                            E.hold(g_copied, i * U + (u + 1))
                        else:
                            E.hold(conv_done, i * U + (u + 1))
                        for half in range(2):
                            for k in range(KD):
                                m = nc.tensor.matmul(ps[:, half * HALF:(half + 1) * HALF], w[:, u, n, k, :], xT[:, k, half * HALF:(half + 1) * HALF],
                                                     start=k == 0, stop=k == KD - 1)
                        m.then_inc(b_psum if n else g_psum, 1)

        @block.scalar
        def _(act):
            A.open(xT_ready, n=U)
            A.open(g_copied, sig)
            A.open(gg_out, n=16)
            with act.Fori(0, NT // U) as i:
                for u in range(U):
                    A.hold(x_psum, now(i, U, u + 1))
                    nc.scalar.copy(xT[:, :, ds((i * U + u) * P, P)], pt[:, :].rearrange("p (k t) -> p k t", k=KD)).then_inc(xT_ready, 1)
            with act.Fori(0, KD) as i:
                A.hold(g_psum, i + (U + 1))
                A.hold(gg_ready, last(i))
                nc.scalar.copy(gx[:, :], pg[:, :]).then_inc(g_copied, 1)
                A.hold(cube, now(i))
                nc.scalar.activation(g3[:, :], g3[:, :], ACT.Sigmoid, scale=2.0 * GELU_C).then_inc(sig, 1)
                A.hold(gg_ready, now(i))
                act.dma_start(gg_view[:, ds(i, 1), :], gg[:, :].unsqueeze(1)).then_inc(gg_out, 16)
            act.wait_ge(gg_out, 16 * (KD + 1))

        @block.vector
        def _(dve):
            V.open(cube, gg_ready, conv_done)
            with dve.Fori(0, KD) as i:
                V.loop(i, 6)
                V.hold(g_copied, now(i))
                V.link(nc.vector.tensor_tensor(g2[:, :], gx[:, :], gx[:, :], ALU.mult))
                V.link(nc.vector.tensor_scalar(g2[:, :], g2[:, :], 0.044715, 1.0, ALU.mult, ALU.add))
                nc.vector.tensor_tensor(g3[:, :], g2[:, :], gx[:, :], ALU.mult).then_inc(cube, 1)
                V.hold(b_psum, i + (U + 1))
                V.hold(cw_ready, now(i))
                V.link(nc.vector.tensor_scalar(cv[:, :], px[:, :], cw[:, 2:3], cw[:, CONV:CONV + 1], ALU.mult, ALU.add))
                V.link(nc.vector.scalar_tensor_tensor(cv[:, 2:T], px[:, 0:T - 2], cw[:, 0:1], cv[:, 2:T], ALU.mult, ALU.add))
                V.link(nc.vector.scalar_tensor_tensor(cv[:, 1:T], px[:, 0:T - 1], cw[:, 1:2], cv[:, 1:T], ALU.mult, ALU.add))
                V.link(nc.vector.scalar_tensor_tensor(cv[:, 0:T - 1], px[:, 1:T], cw[:, 3:4], cv[:, 0:T - 1], ALU.mult, ALU.add))
                nc.vector.tensor_copy(xc[:, ds(i, 1), :].rearrange("p o t -> p (o t)"), cv[:, :]).then_inc(conv_done, 1)
                V.hold(sig, now(i))
                V.hold(gg_out, last(i, 16))
                nc.vector.tensor_tensor(gg[:, :], gx[:, :], g3[:, :], ALU.mult).then_inc(gg_ready, 1)
            V.done(KD)
            dve.wait_ge(conv_done, KD + 1)


def lru_scan(nc, ph, vec, xc, w_r, w_i, ggT_dram):
    w = ph.sb("w", [P, 2, 2, 2, 2, P])
    gg = ph.sb("gg", [P, T])
    r = ph.sb("r", [P, 2, T])
    ig = ph.sb("ig", [P, 2, T])
    th = ph.sb("th", [P, 2, T])
    a = ph.sb("a", [P, 2, T])
    m = ph.sb("m", [P, 2, T])
    q = ph.sb("q", [P, 2, T])
    h = ph.sb("h", [P, 2, T])
    out = ph.sb("out", [P, T])
    dec = ph.sb("dec", [P, 2 * KD])
    sm = ph.sb("sm", [P, 6, 2 * KD])
    pw = ph.ps("pw", [P, 4, T])
    names = "sp_a dec_ready w_psum gates th_ready m2_ready mult ready gg_in out_done".split()
    sp_a, dec_ready, w_psum, gates, th_ready, m2_ready, mult, ready, gg_in, out_done = [ph.sem(n) for n in names]
    w_done = [ph.sem(f"w_done{u}") for u in range(2)]
    V, G, A, E, S = (ph.engine(e, n) for e, n in ((nc.vector, "dve"), (nc.gpsimd, "pool"), (nc.scalar, "act"),
                                                  (nc.tensor, "pe"), (nc.sync, "sp")))
    gg_view = ggT_dram.rearrange("(k p) t -> p k t", p=P)
    lam = vec_at("lru_lambda_2")[0]
    br, bi = vec_at("lru_b_rgate_2")[0], vec_at("lru_b_igate_2")[0]

    with nc.Block() as block:

        @block.sync
        def _(sp):
            S.open(gg_in, out_done, n=16)
            for u in range(2):
                S.open(w_done[u], n=64)
            with sp.Fori(0, NBLK) as n:
                for u in range(2):
                    S.hold(w_psum, last(n, 8, 4 * u + 4))
                    for z in range(2):
                        for k, wt in enumerate((w_r, w_i)):
                            sp.dma_start(w[:, u, z, k, :, :], wt[0, z][ds(n, 1), :, u * P:(u + 1) * P].rearrange("o (c p) f -> p (o c) f", p=P)).then_inc(w_done[u], 16)
                    S.hold(ready, last(n, 2, 2) if u == 0 else now(n, 2, 1))
                    sp.dma_start(gg[:, :].unsqueeze(1), gg_view[:, ds(n * 2 + u, 1), :]).then_inc(gg_in, 16)
                    S.hold(ready, now(n, 2, u + 1))
                    sp.dma_start(gg_view[:, ds(n * 2 + u, 1), :], out[:, :].unsqueeze(1)).then_inc(out_done, 16)
            sp.wait_ge(out_done, 16 * (KD + 1))

        @block.tensor
        def _(pe):
            E.open(w_psum, n=8)
            with pe.Fori(0, NBLK) as n:
                for u in range(2):
                    E.hold(w_done[u], now(n, 64))
                    for z in range(2):
                        for k in range(2):
                            at = 2 * z + k
                            E.hold(gates, now(n, 8, at + 1) if u else last(n, 8, 4 + at + 1))
                            for half in range(2):
                                for c in range(2):
                                    mm = nc.tensor.matmul(pw[:, at, half * HALF:(half + 1) * HALF], w[:, u, z, k, c, :],
                                                          xc[:, ds(n * 2 + c, 1), half * HALF:(half + 1) * HALF].rearrange("p o t -> p (o t)"), start=c == 0, stop=c == 1)
                            mm.then_inc(w_psum, 1)

        @block.scalar
        def _(act):
            A.open(gates, n=8)
            A.open(th_ready, mult, n=4)
            nc.scalar.activation(sm[:, 0, :], vec[:, lam:lam + 2 * KD], ACT.Abs).then_inc(sp_a, 1)
            act.wait_ge(sp_a, 1)
            nc.scalar.activation(sm[:, 1, :], sm[:, 0, :], ACT.Exp, scale=-1.0).then_inc(sp_a, 1)
            with act.Fori(0, NBLK) as n:
                for u in range(2):
                    A.hold(ready, last(n, 2, 2) if u == 0 else now(n, 2, 1))
                    for z in range(2):
                        for k, (dst, b0) in enumerate(((r, br), (ig, bi))):
                            A.hold(w_psum, now(n, 8, 4 * u + 2 * z + k + 1))
                            nc.scalar.activation(dst[:, z, :], pw[:, 2 * z + k, :], ACT.Sigmoid, bias=vec[:, ds(n * 2 + (b0 + z * KD + u), 1)]).then_inc(gates, 1)
                    A.hold(gates, now(n, 8, 4 * u + 4))
                    A.hold(dec_ready, 1)
                    for z in range(2):
                        nc.scalar.activation(th[:, z, :], r[:, z, :], ACT.Tanh, scale=dec[:, ds(n * 2 + (z * KD + u), 1)])
                        tt = nc.scalar.activation(a[:, z, :], r[:, z, :], ACT.Exp, scale=dec[:, ds(n * 2 + (z * KD + u), 1)])
                    tt.then_inc(th_ready, 2)
                    A.hold(m2_ready, now(n, 2, u + 1))
                    nc.scalar.activation(m[:, :, :], m[:, :, :], ACT.Sqrt).then_inc(mult, 2)

        @block.vector
        def _(dve):
            V.open(m2_ready, ready, n=2)
            dve.wait_ge(sp_a, 2)
            y, s_, s2, acc = sm[:, 1, :], sm[:, 2, :], sm[:, 3, :], sm[:, 4, :]
            V.link(nc.vector.tensor_scalar(acc, y, 2.0, None, ALU.add))
            V.link(nc.vector.reciprocal(acc, acc))
            V.link(nc.vector.tensor_tensor(s_, y, acc, ALU.mult))
            V.link(nc.vector.tensor_tensor(s2, s_, s_, ALU.mult))
            V.link(nc.vector.memset(acc, 1.0 / 19))
            for odd in range(17, 0, -2):
                V.link(nc.vector.tensor_tensor(acc, acc, s2, ALU.mult))
                V.link(nc.vector.tensor_scalar(acc, acc, 1.0 / odd, None, ALU.add))
            V.link(nc.vector.tensor_tensor(acc, acc, s_, ALU.mult))
            V.link(nc.vector.tensor_scalar(sm[:, 5, :], vec[:, lam:lam + 2 * KD], -1.0, 0.0, ALU.mult, ALU.max))
            V.link(nc.vector.tensor_scalar(acc, acc, 2.0, None, ALU.mult))
            V.link(nc.vector.tensor_tensor(acc, acc, sm[:, 5, :], ALU.add))
            V.link(nc.vector.tensor_scalar(dec[:, :], acc, -8.0, None, ALU.mult))
            dve.sem_inc(dec_ready, 1)
            with dve.Fori(0, NBLK) as n:
                V.loop(n, 18)
                for u in range(2):
                    V.hold(th_ready, now(n, 4, 2 * u + 2))
                    V.link(nc.vector.tensor_scalar(q[:, :, :], th[:, :, :], -1.0, 1.0, ALU.mult, ALU.add))
                    V.link(nc.vector.reciprocal(q[:, :, :], q[:, :, :]))
                    V.link(nc.vector.scalar_tensor_tensor(m[:, :, :], th[:, :, :], -2.0, q[:, :, :], ALU.mult, ALU.mult))
                    dve.sem_inc(m2_ready, 1)
                    xcu = xc[:, ds(n * 2 + u, 1), :]
                    V.link(nc.vector.tensor_tensor(ig[:, :, :], ig[:, :, :], xcu.to_broadcast([P, 2, T]), ALU.mult))
                    V.hold(mult, now(n, 4, 2 * u + 2))
                    nc.vector.memset(m[:, 0, 0:1], 1.0)
                    V.link(nc.vector.memset(m[:, 1, T - 1:T], 1.0))
                    V.link(nc.vector.tensor_tensor(m[:, :, :], m[:, :, :], ig[:, :, :], ALU.mult))
                    nc.vector.tensor_tensor_scan(h[:, 0, :], a[:, 0, :], m[:, 0, :], 0.0, ALU.mult, ALU.add)
                    V.link(nc.vector.tensor_tensor_scan(h[:, 1, ::-1], a[:, 1, ::-1], m[:, 1, ::-1], 0.0, ALU.mult, ALU.add))
                    V.link(nc.vector.tensor_tensor(h[:, 0, :], h[:, 0, :], h[:, 1, :], ALU.add))
                    V.hold(gg_in, n * 32 + (16 * u + 32))
                    V.hold(out_done, n * 32 + (16 * u + 16))
                    V.link(nc.vector.tensor_tensor(out[:, :], h[:, 0, :], gg[:, :], ALU.mult))
                    dve.sem_inc(ready, 1)
            V.done(NBLK)


def lru_out(nc, ph, w_out, hT_dram, mix_dram):
    hT = ph.sb("hT", [P, KD, T])
    wo = ph.sb("wo", [P, KD, D])
    h_t = ph.sb("h_t", [P, KD, P])
    out = ph.sb("out", [P, D])
    po = ph.ps("po", [P, 2, D])
    consts, h_in, o_psum, ready, out_done = [ph.sem(n) for n in "consts h_in o_psum ready out_done".split()]
    V, G, E, S = (ph.engine(e, n) for e, n in ((nc.vector, "dve"), (nc.gpsimd, "pool"), (nc.tensor, "pe"), (nc.sync, "sp")))
    U = 2

    with nc.Block() as block:

        @block.sync
        def _(sp):
            S.open(out_done, n=16)
            for k in range(KD):
                sp.dma_start(hT[:, k, :], hT_dram[k * P:(k + 1) * P, :]).then_inc(consts, 16)
                sp.dma_start(wo[:, k, :], w_out[0, k * P:(k + 1) * P, :]).then_inc(consts, 16)
            with sp.Fori(0, NT) as i:
                S.hold(ready, i + 2)
                sp.dma_start(mix_dram[ds(i * P, P), :], out[:, :]).then_inc(out_done, 16)
            sp.wait_ge(out_done, 16 * (NT + 1))

        @block.gpsimd
        def _(pool):
            pool.wait_ge(consts, 32 * KD)
            with pool.Fori(0, NT) as i:
                G.hold(o_psum, i + 1)
                nc.gpsimd.tensor_copy(h_t[:, :, :], hT[:, :, ds(i * P, P)]).then_inc(h_in, 1)

        @block.tensor
        def _(pe):
            E.open(o_psum)
            pe.wait_ge(consts, 32 * KD)
            with pe.Fori(0, NT // U) as i:
                for u in range(U):
                    E.hold(h_in, i * U + (u + 1))
                    E.hold(ready, i * U + (u + 1))
                    for half in range(2):
                        for k in range(KD):
                            m = nc.tensor.matmul(po[:, u, half * HALF:(half + 1) * HALF], h_t[:, k, :], wo[:, k, half * HALF:(half + 1) * HALF],
                                                 start=k == 0, stop=k == KD - 1)
                    m.then_inc(o_psum, 1)

        @block.vector
        def _(dve):
            V.open(ready)
            with dve.Fori(0, NT // U) as i:
                for u in range(U):
                    V.hold(o_psum, i * U + (u + 2))
                    V.hold(out_done, i * 32 + (16 * u + 16))
                    nc.vector.tensor_copy(out[:, :], po[:, u, :]).then_inc(ready, 1)


def moe_and_transformer_kernel(nc, I, out):
    def scratch(name, shape, dt=F32):
        return nc.dram_tensor(name, shape, dt, kind="Internal").ap()

    hT, oT = scratch("hT", [D, T]), scratch("oT", [MLA_H * V_DIM, T])
    mla_phase(nc, I["x"], I["vecs"], I["w_in"], I["w_uq"], I["w_ukv"], I["eye"], I["mla_rope"], hT, oT)

    zfT = scratch("zfT", [RWKV_TILES * P, T])
    arrays = scratch("arrays", [len(ARR), RC, T])
    shift_phase(nc, I["vecs"], I["w_in"], hT, zfT)
    prep_phase(nc, I["vecs"], I["w_up"], I["a_up"], I["g_up"], zfT, I["starts"], I["head_ones"], arrays)
    yT = scratch("yT", [2, RC, T])
    wkv_phase(nc, I["wkv_tables"], arrays, yT)

    mixT = scratch("mixT", [D, T])
    mix_phase(nc, I["vecs"], I["w_in"], I["w_br_mla"], I["w_br_rwkv"], I["head_ones"], hT, oT, arrays, yT, mixT)
    x1, h2, x2 = scratch("x1", [T, D]), scratch("h2", [T, D]), scratch("x2", [T, D])
    slot_tok = scratch("slot_tok", [SLOTS + P, 1], U32)
    yb = scratch("yb", [SLOTS, D])
    with ExitStack() as routes:
        slots = routes.enter_context(nc.sbuf_tensor("slots", [P, 2 * NT], U32))
        weights = routes.enter_context(nc.sbuf_tensor("weights", [P, 2 * NT], F32))
        block_e = routes.enter_context(nc.sbuf_tensor("block_e", [P, MOE_BLOCKS], U32))
        route_phase(nc, I["x"], I["vecs"], I["w_out"], I["router_group_w"], I["router_group_b"], I["router_expert_w"],
                    I["router_expert_b"], I["eye"], I["route_tables"], I["tok_ids"], mixT, x1, h2, slot_tok,
                    (slots, weights, block_e))
        experts_phase(nc, I["vecs"], I["w1"], I["w3"], I["w2"], I["eye"], block_e, slot_tok, h2, yb)
        combine_phase(nc, I["norm_final_g"], slots, weights, x1, yb, x2)

    mix, acc, x3, x4, x5 = (scratch(n, [T, D]) for n in ("mix", "acc", "x3", "x4", "x5"))
    ggT = scratch("ggT", [D, T])
    gate = nc.alloc_sbuf_tensor("gate", [P, E2], F32)
    idx = nc.alloc_sbuf_tensor("idx", [P, E2 + 1], U32)
    gqa_phase(nc, I["attn_w_qkv_2"], I["attn_w_o_2"], I["attn_sink_2"], I["eye"], I["gqa_rope"], I["gqa_masks"], x2, mix)
    norm_phase(nc, "norm0", I["ln_mix_g_2"][0], I["ln_mix_b_2"][0], x2, mix, x3)
    choose_phase(nc, "choose0", I["moe_w_router_2"][0], I["eye"], x3, acc, gate, idx)
    choice_phase(nc, "choice0", I["moe_w_gate_up_2"][0], I["moe_w_down_2"][0], I["eye"], x3, acc, gate, idx)
    norm_phase(nc, "norm1", I["ln_ffn_g_2"][0], I["ln_ffn_b_2"][0], x3, acc, x4)

    lru_phase(nc, I["vecs"], I["lru_w_in_2"], I["lru_w_rgate_2"], I["lru_w_igate_2"], I["lru_w_out_2"], I["eye"],
              x4, ggT, mix)
    norm_phase(nc, "norm2", I["ln_mix_g_2"][1], I["ln_mix_b_2"][1], x4, mix, x5)
    choose_phase(nc, "choose1", I["moe_w_router_2"][1], I["eye"], x5, acc, gate, idx)
    choice_phase(nc, "choice1", I["moe_w_gate_up_2"][1], I["moe_w_down_2"][1], I["eye"], x5, acc, gate, idx)
    norm_phase(nc, "norm3", I["ln_ffn_g_2"][1], I["ln_ffn_b_2"][1], x5, acc, out)


_WHOLE = ["w_in", "w_uq", "w_ukv", "w_br_mla", "w_up", "a_up", "g_up", "w_br_rwkv", "w_out", "router_group_w",
          "router_group_b", "router_expert_w", "router_expert_b", "w1", "w3", "w2", "norm_final_g", "attn_w_qkv_2",
          "attn_w_o_2", "attn_sink_2", "lru_w_in_2", "lru_w_rgate_2", "lru_w_igate_2", "lru_w_out_2",
          "moe_w_router_2", "moe_w_gate_up_2", "moe_w_down_2", "ln_mix_g_2", "ln_mix_b_2", "ln_ffn_g_2",
          "ln_ffn_b_2"]


def kernel(**inputs):
    import concourse.bacc as _bacc
    from concourse.bass_utils import run_bass_kernel_spmd as _run

    a = {n: np.ascontiguousarray(inputs[n]) for n in _WHOLE}
    a["x"] = np.ascontiguousarray(inputs["x"]).reshape(T, D)
    a["vecs"] = np.ascontiguousarray(
        np.concatenate([np.asarray(inputs[n]).reshape(-1, P).T for n in VECS], axis=1))
    a["eye"] = np.eye(P, dtype=np.float32)
    a["mla_rope"] = mla_tables()
    a["starts"], a["head_ones"] = prep_tables()
    a["wkv_tables"] = wkv_tables()
    a["route_tables"], a["tok_ids"] = route_tables()
    a["gqa_rope"], a["gqa_masks"] = gqa_tables()
    nc = _bacc.Bacc("TRN2", target_bir_lowering=False, num_devices=1)
    arrays = {f"in_{n}_dram": v for n, v in a.items()}
    aps = {n: nc.dram_tensor(f"in_{n}_dram", v.shape, mybir.dt.from_np(v.dtype), kind="ExternalInput").ap()
           for n, v in a.items()}
    out = nc.dram_tensor("out_0_dram", (T, D), F32, kind="ExternalOutput").ap()
    moe_and_transformer_kernel(nc, aps, out)
    r = _run(nc, [arrays], core_ids=[0])
    return r.results[0]["out_0_dram"].reshape(1, T, D)
```

```python
from contextlib import ExitStack

import concourse.bass as bass
import numpy as np
from concourse import mybir

ALU = mybir.AluOpType
ACT = mybir.ActivationFunctionType
F32 = mybir.dt.float32
U32 = mybir.dt.uint32
AX_X = mybir.AxisListType.X
ds = bass.ds

P = 128
T = 1024
NT = T // P
D = 1024
KD = D // P
HALF = 512


def now(i, n=1, k=None):
    return (i + 1) * n + (n if k is None else k)


def last(i, n=1, k=None):
    return i * n + (n if k is None else k)


class Engine:

    def __init__(self, eng, chain, pace):
        self.eng, self.chain, self.pace = eng, chain, pace
        self.turn, self.per, self.steps, self.base = 0, 0, 0, 0

    def hold(self, sem, value):
        self.eng.wait_ge(sem, value)
        if not isinstance(value, int):
            self.eng.sem_inc(self.pace, 1)

    def link(self, instruction):
        self.steps += 1
        instruction.then_inc(self.chain, 1)
        self.hold(self.chain, self.turn * self.per + self.base + self.steps)

    def loop(self, turn, per):
        self.base += self.steps
        self.turn, self.per, self.steps = turn, per, 0

    def open(self, *sems, n=1):
        for s in sems:
            self.eng.sem_inc(s, n)

    def done(self, turns):
        assert self.steps == self.per, (self.chain.name, self.steps)
        self.base += turns * self.per
        self.turn, self.per, self.steps = 0, 0, 0


class Phase:

    def __init__(self, nc, name):
        self.nc, self.name, self.ctx, self.sems = nc, name, ExitStack(), []

    def __enter__(self):
        return self

    def __exit__(self, *a):
        self.ctx.close()
        if self.sems:
            self.nc.clear_and_free_semaphores(self.sems)
            self.nc.all_engine_barrier()

    def sb(self, name, shape, dt=F32):
        return self.ctx.enter_context(self.nc.sbuf_tensor(f"{self.name}_{name}", shape, dt))

    def ps(self, name, shape):
        return self.ctx.enter_context(self.nc.psum_tensor(f"{self.name}_{name}", shape, F32))

    def sem(self, name):
        self.sems.append(self.nc.alloc_semaphore(name=f"{self.name}_{name}"))
        return self.sems[-1]

    def engine(self, eng, name):
        return Engine(eng, self.sem(f"{name}_chain"), self.sem(f"{name}_pace"))


MLA_H, QK_NOPE, QK_ROPE, V_DIM, Q_LORA, KV_LORA = 8, 64, 32, 64, 384, 256
QK = QK_NOPE + QK_ROPE
MLA_IN = Q_LORA + KV_LORA + QK_ROPE
NORM_EPS = 1e-6


VECS = dict(norm_mix_g=8, q_norm_g=3, kv_norm_g=2, mu_prev=15, mu_next=15, w0=8, a0=8, k_k=4, k_a=4, r_k=4, lnx_g=4,
            lnx_b=4, gate_b=16, norm_ffn_g=8, lru_conv_w_2=32, lru_conv_b_2=8, lru_b_rgate_2=16, lru_b_igate_2=16,
            lru_lambda_2=16)
VEC_N = sum(VECS.values())


def vec_at(name):
    names = list(VECS)
    at = sum(VECS[n] for n in names[:names.index(name)])
    return at, at + VECS[name]


def mla_tables():
    pos = np.arange(T, dtype=np.float32)
    inv = np.float32(10000.0) ** (-np.arange(0, QK_ROPE, 2, dtype=np.float32) / QK_ROPE)
    ang = (pos[:, None] * inv[None, :]).astype(np.float32)
    t = np.concatenate([np.cos(ang), np.sin(ang)], axis=1).astype(np.float32)
    return np.ascontiguousarray(t.reshape(NT, P, QK_ROPE).transpose(1, 0, 2))


def mla_phase(nc, x, vecs, w_in, w_uq, w_ukv, eye, rope, hT_dram, oT_dram):
    with Phase(nc, "mla") as ph:
        ident = ph.sb("ident", [P, P])
        q_all = ph.sb("qT", [QK, MLA_H, T])
        k_all = ph.sb("kT", [QK, MLA_H, T])
        v_all = ph.sb("v", [P, NT, MLA_H * V_DIM])
        with ExitStack() as one:
            proj = Phase(nc, "mlap")
            one.enter_context(proj)
            mla_project(nc, proj, x, vecs, w_in, w_uq, w_ukv, eye, rope, hT_dram,
                        ident, q_all, k_all, v_all)
        with ExitStack() as two:
            att = Phase(nc, "mlaa")
            two.enter_context(att)
            mla_attend(nc, att, ident, q_all, k_all, v_all, oT_dram)



def mla_project(nc, ph, x, vecs, w_in, w_uq, w_ukv, eye, rope, hT_dram,
                ident, q_all, k_all, v_all):
    NC = (Q_LORA + KV_LORA) // P
    w_z = ph.sb("w_z", [P, KD, MLA_IN])
    w_q = ph.sb("w_q", [P, Q_LORA // P, MLA_H * QK])
    w_kv = ph.sb("w_kv", [P, KV_LORA // P, MLA_H * P])
    tab = ph.sb("tab", [P, NT, QK_ROPE])
    vec = ph.sb("vec", [P, VEC_N])
    g_h = vec[:, slice(*vec_at("norm_mix_g"))]
    g_c = vec[:, vec_at("q_norm_g")[0]:vec_at("kv_norm_g")[1]]
    xt = ph.sb("xt", [P, D])
    junk = ph.sb("junk", [P, D])
    h = ph.sb("h", [P, D])
    hT = ph.sb("hT", [P, KD, P])
    ssq = ph.sb("ssq", [P, 4])
    ms = ph.sb("ms", [P, 4])
    root = ph.sb("root", [P, 4])
    rstd = ph.sb("rstd", [P, 4])
    c = ph.sb("c", [P, NC * P])
    cT = ph.sb("cT", [P, NC, P])
    krope = ph.sb("krope", [P, QK_ROPE])
    krot = ph.sb("krot", [P, QK_ROPE])
    qcat = ph.sb("qcat", [P, MLA_H, QK])
    kcat = ph.sb("kcat", [P, MLA_H, QK])
    qr = ph.sb("qr", [P, 4, MLA_H, 16])
    kr = ph.sb("kr", [P, 4, 16])

    pT = ph.ps("pT", [P, 2, HALF])
    pZ = ph.ps("pZ", [P, 2, HALF])
    pQ = ph.ps("pQ", [P, 2, HALF])
    pK = ph.ps("pK", [P, 2, HALF])

    names = ("x_in x_sq ms_h rt_h h_ready hT_psum hT_ready hT_out z_psum sq_c ms_c rt_c c_ready cT_psum cT_ready q_psum "
             "kv_psum qcat_ready kcat_ready qT_psum kT_psum qT_kept kT_kept v_kept").split()
    (x_in, x_sq, ms_h, rt_h, h_ready, hT_psum, hT_ready, hT_out, z_psum, sq_c, ms_c, rt_c, c_ready, cT_psum, cT_ready, q_psum,
     kv_psum, qcat_ready, kcat_ready, qT_psum, kT_psum, qT_kept, kT_kept, v_kept) = [ph.sem(n) for n in names]
    consts = ph.sem("consts")
    V, G, A, E, S = (ph.engine(e, n) for e, n in ((nc.vector, "dve"), (nc.gpsimd, "pool"), (nc.scalar, "act"),
                                                  (nc.tensor, "pe"), (nc.sync, "sp")))
    hT_view = hT_dram.rearrange("(k p) t -> p k t", p=P)

    with nc.Block() as block:

        @block.sync
        def _(sp):
            S.open(x_in, hT_out, n=16)
            for out, src in (
                (ident[:, :], eye), (vec[:, :], vecs),
                (w_z[:, :, :], w_in[0, :, 0:MLA_IN].rearrange("(k p) n -> p k n", p=P)),
                (w_q[:, :, :], w_uq[0].rearrange("(k p) n -> p k n", p=P)),
                (w_kv[:, :, :], w_ukv[0].rearrange("(k p) n -> p k n", p=P)),
                (tab[:, :, :], rope),
            ):
                sp.dma_start(out, src).then_inc(consts, 16)
            with sp.Fori(0, NT) as i:
                S.hold(x_sq, last(i))
                S.hold(h_ready, last(i))
                sp.dma_start(xt[:, :], x[ds(i * P, P), :]).then_inc(x_in, 16)
                S.hold(hT_ready, now(i))
                sp.dma_start(hT_view[:, :, ds(i * P, P)], hT[:, :, :]).then_inc(hT_out, 16)
            sp.wait_ge(hT_out, (NT + 1) * 16)

        @block.scalar
        def _(act):
            A.open(x_sq, rt_h, sq_c, rt_c, v_kept)
            act.wait_ge(consts, 6 * 16)
            with act.Fori(0, NT) as i:
                A.hold(x_in, now(i, 16))
                nc.scalar.activation(junk[:, :], xt[:, :], ACT.Square, accum_out=ssq[:, 0:1]).then_inc(x_sq, 1)
                A.hold(ms_h, now(i))
                nc.scalar.activation(root[:, 0:1], ms[:, 0:1], ACT.Sqrt).then_inc(rt_h, 1)
                A.hold(z_psum, now(i))
                A.hold(x_sq, now(i))
                nc.scalar.activation(junk[:, 0:Q_LORA], pZ[:, 0, 0:Q_LORA], ACT.Square, accum_out=ssq[:, 1:2])
                nc.scalar.activation(junk[:, Q_LORA:Q_LORA + KV_LORA], pZ[:, 1, 0:KV_LORA], ACT.Square,
                                     accum_out=ssq[:, 2:3]).then_inc(sq_c, 1)
                A.hold(ms_c, now(i))
                nc.scalar.activation(root[:, 1:3], ms[:, 1:3], ACT.Sqrt).then_inc(rt_c, 1)
                A.hold(kcat_ready, now(i))
                for b in range(2):
                    vb = nc.scalar.copy(v_all[:, ds(i, 1), b * 256:b * 256 + 256].rearrange("p o (h d) -> p (o h) d", h=4),
                                        pK[:, b, :].rearrange("p (h d) -> p h d", h=4)[:, :, QK_NOPE:P])
                vb.then_inc(v_kept, 1)

        @block.vector
        def _(dve):
            V.open(ms_h, ms_c, h_ready, hT_ready, c_ready, cT_ready, qcat_ready, kcat_ready, qT_kept, kT_kept)
            dve.wait_ge(consts, 6 * 16)

            def rotate(out1, out2, x1, x2, co, si, r):
                nc.vector.tensor_tensor(r[0], x1, co, ALU.mult)
                nc.vector.tensor_tensor(r[1], x2, si, ALU.mult)
                nc.vector.tensor_tensor(r[2], x1, si, ALU.mult)
                V.link(nc.vector.tensor_tensor(r[3], x2, co, ALU.mult))
                nc.vector.tensor_tensor(out1, r[0], r[1], ALU.subtract)
                return nc.vector.tensor_tensor(out2, r[2], r[3], ALU.add)

            with dve.Fori(0, NT) as i:
                V.loop(i, 7)
                V.hold(x_sq, now(i))
                nc.vector.tensor_scalar(ms[:, 0:1], ssq[:, 0:1], 1.0 / D, NORM_EPS, ALU.mult, ALU.add).then_inc(ms_h, 1)
                V.hold(rt_h, now(i))
                V.link(nc.vector.reciprocal(rstd[:, 0:1], root[:, 0:1]))
                V.hold(hT_psum, last(i))
                nc.vector.tensor_scalar(h[:, :], xt[:, :], rstd[:, 0:1], None, ALU.mult).then_inc(h_ready, 1)
                V.hold(z_psum, last(i))
                V.hold(hT_out, last(i, 16))
                V.hold(hT_psum, now(i))
                nc.vector.tensor_tensor(hT[:, :, :].rearrange("p (b k) t -> p b k t", b=2),
                                        pT[:, :, :].rearrange("p b (k t) -> p b k t", k=4),
                                        g_h[:, :].rearrange("p (b k) -> p b k", b=2).unsqueeze(3).to_broadcast([P, 2, 4, P]),
                                        ALU.mult).then_inc(hT_ready, 1)
                V.hold(sq_c, now(i))
                nc.vector.tensor_scalar(ms[:, 1:2], ssq[:, 1:2], 1.0 / Q_LORA, NORM_EPS, ALU.mult, ALU.add)
                nc.vector.tensor_scalar(ms[:, 2:3], ssq[:, 2:3], 1.0 / KV_LORA, NORM_EPS, ALU.mult, ALU.add).then_inc(ms_c, 1)
                V.hold(rt_c, now(i))
                V.link(nc.vector.reciprocal(rstd[:, 1:3], root[:, 1:3]))
                nc.vector.tensor_scalar(c[:, 0:Q_LORA], pZ[:, 0, 0:Q_LORA], rstd[:, 1:2], None, ALU.mult)
                V.link(nc.vector.tensor_copy(krope[:, :], pZ[:, 1, KV_LORA:KV_LORA + QK_ROPE]))
                nc.vector.tensor_scalar(c[:, Q_LORA:NC * P], pZ[:, 1, 0:KV_LORA], rstd[:, 2:3], None, ALU.mult).then_inc(c_ready, 1)
                co, si = tab[:, ds(i, 1), 0:16], tab[:, ds(i, 1), 16:32]
                V.link(rotate(krot[:, 0:16], krot[:, 16:32], krope[:, 0:16], krope[:, 16:32],
                              co.rearrange("p o d -> p (o d)"), si.rearrange("p o d -> p (o d)"),
                              [kr[:, n, :] for n in range(4)]))
                V.hold(cT_psum, now(i))
                nc.vector.tensor_tensor(cT[:, 0:4, :], pT[:, 0, :].rearrange("p (k t) -> p k t", k=4),
                                        g_c[:, 0:4].unsqueeze(2).to_broadcast([P, 4, P]), ALU.mult)
                nc.vector.tensor_scalar(cT[:, 4, :], pT[:, 1, 0:P], g_c[:, 4:5], None, ALU.mult).then_inc(cT_ready, 1)
                V.hold(q_psum, now(i))
                for b in range(2):
                    src = pQ[:, b, 0:4 * QK].rearrange("p (h d) -> p h d", h=4)
                    hs = slice(4 * b, 4 * b + 4)
                    nc.vector.tensor_copy(qcat[:, hs, 0:QK_NOPE], src[:, :, 0:QK_NOPE])
                    done = rotate(qcat[:, hs, 64:80], qcat[:, hs, 80:96], src[:, :, 64:80], src[:, :, 80:96],
                                  co.to_broadcast([P, 4, 16]), si.to_broadcast([P, 4, 16]),
                                  [qr[:, n, hs, :] for n in range(4)])
                done.then_inc(qcat_ready, 1)
                V.hold(kv_psum, now(i))
                for b in range(2):
                    nc.vector.tensor_copy(kcat[:, 4 * b:4 * b + 4, 0:QK_NOPE],
                                          pK[:, b, :].rearrange("p (h d) -> p h d", h=4)[:, :, 0:QK_NOPE])
                nc.vector.tensor_copy(kcat[:, :, QK_NOPE:QK], krot[:, :].unsqueeze(1).to_broadcast([P, MLA_H, QK_ROPE])).then_inc(kcat_ready, 1)
                V.hold(qT_psum, now(i))
                for b in range(2):
                    kept = nc.vector.tensor_copy(q_all[:, 4 * b:4 * b + 4, ds(i * P, P)],
                                                 pT[0:QK, b, :].rearrange("p (h t) -> p h t", h=4))
                kept.then_inc(qT_kept, 1)
                V.hold(kT_psum, now(i))
                for b in range(2):
                    kept = nc.vector.tensor_copy(k_all[:, 4 * b:4 * b + 4, ds(i * P, P)],
                                                 pZ[0:QK, b, :].rearrange("p (h t) -> p h t", h=4))
                kept.then_inc(kT_kept, 1)
            V.done(NT)

        @block.tensor
        def _(pe):
            E.open(hT_psum, z_psum, cT_psum, q_psum, kv_psum, qT_psum, kT_psum)
            pe.wait_ge(consts, 6 * 16)
            with pe.Fori(0, NT) as i:
                E.hold(h_ready, now(i))
                E.hold(qT_kept, last(i))
                for k in range(KD):
                    t = nc.tensor.transpose(pT[:, k // 4, k % 4 * P:k % 4 * P + P], h[:, k * P:k * P + P], ident[:, :])
                t.then_inc(hT_psum, 1)
                E.hold(hT_ready, now(i))
                E.hold(kT_kept, last(i))
                for o, lo, n in ((0, 0, Q_LORA), (1, Q_LORA, MLA_IN - Q_LORA)):
                    for k in range(KD):
                        m = nc.tensor.matmul(pZ[:, o, 0:n], hT[:, k, :], w_z[:, k, lo:lo + n], start=k == 0, stop=k == KD - 1)
                m.then_inc(z_psum, 1)
                E.hold(c_ready, now(i))
                for k in range(NC):
                    t = nc.tensor.transpose(pT[:, k // 4, k % 4 * P:k % 4 * P + P], c[:, k * P:k * P + P], ident[:, :])
                t.then_inc(cT_psum, 1)
                E.hold(cT_ready, now(i))
                E.hold(qcat_ready, last(i))
                for o in range(2):
                    for k in range(3):
                        m = nc.tensor.matmul(pQ[:, o, 0:4 * QK], cT[:, k, :], w_q[:, k, o * 4 * QK:(o + 1) * 4 * QK], start=k == 0, stop=k == 2)
                m.then_inc(q_psum, 1)
                E.hold(kcat_ready, last(i))
                E.hold(v_kept, last(i))
                for o in range(2):
                    for k in range(2):
                        m = nc.tensor.matmul(pK[:, o, :], cT[:, 3 + k, :], w_kv[:, k, o * HALF:(o + 1) * HALF], start=k == 0, stop=k == 1)
                m.then_inc(kv_psum, 1)
                E.hold(qcat_ready, now(i))
                for n in range(MLA_H):
                    t = nc.tensor.transpose(pT[0:QK, n // 4, n % 4 * P:n % 4 * P + P], qcat[:, n, :], ident[:, :])
                t.then_inc(qT_psum, 1)
                E.hold(kcat_ready, now(i))
                for n in range(MLA_H):
                    t = nc.tensor.transpose(pZ[0:QK, n // 4, n % 4 * P:n % 4 * P + P], kcat[:, n, :], ident[:, :])
                t.then_inc(kT_psum, 1)


def mla_attend(nc, ph, ident, q_all, k_all, v_all, oT_dram):
    PAIRS, QB = MLA_H // 2, HALF // P
    U, NG = 2 * NT, 2 * NT // QB
    SCALE = float(QK) ** -0.5
    q_s = ph.sb("q_s", [QK, 2, T])
    v_s = ph.sb("v_s", [P, 2, NT, V_DIM])
    probs = ph.sb("probs", [P, 2, T])
    pT_sb = ph.sb("probsT", [P, 2, NT, HALF])
    mx = ph.sb("mx", [P, 2])
    nmx = ph.sb("nmx", [P, 2])
    den = ph.sb("den", [P, 2])
    rden = ph.sb("rden", [P, 2])
    oT = ph.sb("oT", [P, 2, HALF])
    pS = ph.ps("pS", [P, 4, HALF])
    pP = ph.ps("pP", [P, 2, HALF])
    pO = ph.ps("pO", [P, 2, HALF])
    names = "q_in v_in s_psum max_ready exp_done normed pT_psum pT_v pT_a o_psum oT_ready oT_out".split()
    q_in, v_in, s_psum, max_ready, exp_done, normed, pT_psum, pT_v, pT_a, o_psum, oT_ready, oT_out = [ph.sem(n) for n in names]
    V, G, A, E, S = (ph.engine(e, n) for e, n in ((nc.vector, "dve"), (nc.gpsimd, "pool"), (nc.scalar, "act"),
                                                  (nc.tensor, "pe"), (nc.sync, "sp")))

    def per_unit(i, u):
        return now(i, U, u + 1) if u >= 0 else last(i, U, U + u + 1)

    def per_group(i, g):
        return now(i, NG, g + 1) if g >= 0 else last(i, NG, NG + g + 1)

    with nc.Block() as block:

        @block.gpsimd
        def _(pool):
            G.open(q_in, v_in, n=2)
            with pool.Fori(0, PAIRS) as i:
                for e in range(2):
                    G.hold(s_psum, last(i, U, (e + 1) * NT))
                    nc.gpsimd.tensor_copy(q_s[:, e, :], q_all[:, ds(i * 2 + e, 1), :].rearrange("p o t -> p (o t)")).then_inc(q_in, 1)
                    G.hold(o_psum, last(i, NG, (e + 1) * NG // 2))
                    nc.gpsimd.tensor_copy(v_s[:, e, :, :], v_all[:, :, ds(i * 2 * V_DIM + e * V_DIM, V_DIM)]).then_inc(v_in, 1)

        @block.tensor
        def _(pe):
            E.open(s_psum, pT_psum, n=U)
            E.open(o_psum, n=NG)

            def scores(i, u):
                e, tile = u // NT, u % NT
                if tile == 0:
                    E.hold(q_in, now(i, 2, e + 1))
                E.hold(exp_done, per_unit(i, u - 2))
                for j in range(2):
                    m = nc.tensor.matmul(pS[:, u % 2 * 2 + j, :], q_s[:, e, tile * P:(tile + 1) * P],
                                         k_all[:, ds(i * 2 + e, 1), j * HALF:(j + 1) * HALF].rearrange("p o t -> p (o t)"), start=True, stop=True)
                m.then_inc(s_psum, 1)

            def outputs(i, g):
                e, half = g // 2, g % 2
                if g < 2:
                    E.hold(oT_ready, last(i, 2, half + 1))
                E.hold(v_in, now(i, 2, e + 1))
                E.hold(pT_v, per_unit(i, (g + 1) * QB - 1))
                E.hold(pT_a, per_unit(i, (g + 1) * QB - 1))
                for k in range(NT):
                    m = nc.tensor.matmul(pO[e * V_DIM:(e + 1) * V_DIM, half, :], v_s[:, e, k, :], pT_sb[:, g % 2, k, :], start=k == 0, stop=k == NT - 1)
                m.then_inc(o_psum, 1)

            with pe.Fori(0, PAIRS) as i:
                scores(i, 0)
                for u in range(U):
                    if u + 1 < U:
                        scores(i, u + 1)
                    if u and u % QB == 0:
                        outputs(i, u // QB - 1)
                    E.hold(normed, per_unit(i, u))
                    E.hold(pT_v, per_unit(i, u - 1))
                    E.hold(pT_a, per_unit(i, u - 1))
                    for k in range(NT):
                        t = nc.tensor.transpose(pP[:, k // 4, k % 4 * P:k % 4 * P + P], probs[:, u % 2, k * P:k * P + P], ident[:, :])
                    t.then_inc(pT_psum, 1)
                outputs(i, NG - 1)

        def place(u, lo):
            return pT_sb[:, u // QB % 2, lo:lo + 4, u % QB * P:(u % QB + 1) * P]

        @block.vector
        def _(dve):
            V.open(max_ready, normed, pT_v, n=U)
            with dve.Fori(0, PAIRS) as i:
                V.loop(i, 2 * U)

                def maximum(u):
                    c = u % 2
                    V.hold(s_psum, per_unit(i, u))
                    V.hold(exp_done, per_unit(i, u - 2))
                    V.link(nc.vector.reduce_max(mx[:, c:c + 1], pS[:, c * 2:c * 2 + 2, :], mybir.AxisListType.XY))
                    nc.vector.tensor_scalar(nmx[:, c:c + 1], mx[:, c:c + 1], -SCALE, None, ALU.mult).then_inc(max_ready, 1)

                def copy(u):
                    V.hold(pT_psum, per_unit(i, u))
                    if u % QB == 0:
                        V.hold(o_psum, per_group(i, u // QB - 2))
                    nc.vector.tensor_copy(place(u, 0), pP[:, 0, :].rearrange("p (k t) -> p k t", k=4)).then_inc(pT_v, 1)

                maximum(0)
                for u in range(U):
                    if u:
                        copy(u - 1)
                    V.hold(exp_done, per_unit(i, u))
                    V.link(nc.vector.reciprocal(rden[:, u % 2:u % 2 + 1], den[:, u % 2:u % 2 + 1]))
                    nc.vector.tensor_scalar(probs[:, u % 2, :], probs[:, u % 2, :], rden[:, u % 2:u % 2 + 1], None, ALU.mult).then_inc(normed, 1)
                    if u + 1 < U:
                        maximum(u + 1)
                copy(U - 1)
            V.done(PAIRS)

        @block.scalar
        def _(act):
            A.open(exp_done, pT_a, n=U)
            A.open(oT_ready, n=2)
            with act.Fori(0, PAIRS) as i:

                def copy(u):
                    A.hold(pT_psum, per_unit(i, u))
                    if u % QB == 0:
                        A.hold(o_psum, per_group(i, u // QB - 2))
                    nc.scalar.copy(place(u, 4), pP[:, 1, :].rearrange("p (k t) -> p k t", k=4)).then_inc(pT_a, 1)

                def keep(half):
                    A.hold(o_psum, per_group(i, 2 + half))
                    A.hold(oT_out, last(i, 16))
                    nc.scalar.copy(oT[:, half, :], pO[:, half, :]).then_inc(oT_ready, 1)

                for u in range(U):
                    A.hold(max_ready, per_unit(i, u))
                    A.hold(pT_psum, per_unit(i, u - 2))
                    nc.scalar.activation(probs[:, u % 2, :], pS[:, u % 2 * 2:u % 2 * 2 + 2, :], ACT.Exp,
                                         bias=nmx[:, u % 2:u % 2 + 1], scale=SCALE, accum_out=den[:, u % 2:u % 2 + 1]).then_inc(exp_done, 1)
                    if u:
                        copy(u - 1)
                    if u == U - 3:
                        keep(0)
                copy(U - 1)
                keep(1)

        @block.sync
        def _(sp):
            S.open(oT_out, n=16)
            with sp.Fori(0, PAIRS) as i:
                S.hold(oT_ready, now(i, 2))
                sp.dma_start(oT_dram[ds(i * P, P), :], oT[:, :, :].rearrange("p b t -> p (b t)")).then_inc(oT_out, 16)
            sp.wait_ge(oT_out, (PAIRS + 1) * 16)



RC = 512
RJ = RC // P
C = 64
NCH = T // C
W_SCALE = float(np.exp(np.float32(-0.5)))
ARR = dict(r=0, v=1, nkk=2, b0=3, b1=4, kd0=5, kd1=6, L0=7, L1=8, g=9, bonus=10)
RWKV_TILES = 15


def shift_phase(nc, vecs, w_in, hT_dram, zf_dram):
    with Phase(nc, "shift") as ph:
        hT = ph.sb("hT", [P, KD, T])
        U = 3
        w = ph.sb("w", [P, U, KD, P])
        zf = ph.sb("zf", [P, U, T])
        vec = ph.sb("vec", [P, VEC_N])
        keep = ph.sb("keep", [P, RWKV_TILES])
        pz = ph.ps("pz", [P, U, T])
        names = "z_psum kept shifted zf_out".split()
        z_psum, kept, shifted, zf_out = [ph.sem(n) for n in names]
        w_in_u = [ph.sem(f"w_in{u}") for u in range(U)]
        consts = ph.sem("consts")
        keep_v = ph.sem("keep_v")
        V, A, E, S = (ph.engine(e, n) for e, n in ((nc.vector, "dve"), (nc.scalar, "act"), (nc.tensor, "pe"), (nc.sync, "sp")))
        mp, mn = vec_at("mu_prev")[0], vec_at("mu_next")[0]
        w_view = w_in[0].rearrange("(k p) n -> p k n", p=P)
        zf_view = zf_dram.rearrange("(k p) t -> p k t", p=P)

        with nc.Block() as block:

            @block.sync
            def _(sp):
                for u in range(U):
                    S.open(w_in_u[u], n=16)
                sp.dma_start(vec[:, :], vecs).then_inc(consts, 16)
                for k in range(KD):
                    sp.dma_start(hT[:, k, :], hT_dram[k * P:(k + 1) * P, :]).then_inc(consts, 16)
                with sp.Fori(0, RWKV_TILES // U) as i:
                    for u in range(U):
                        S.hold(z_psum, last(i, U, u + 1))
                        sp.dma_start(w[:, u, :, :], w_view[:, :, ds(i * (U * P) + (MLA_IN + u * P), P)]).then_inc(w_in_u[u], 16)

            @block.tensor
            def _(pe):
                E.open(z_psum, n=U)
                pe.wait_ge(consts, (1 + KD) * 16)
                with pe.Fori(0, RWKV_TILES // U) as i:
                    for u in range(U):
                        E.hold(w_in_u[u], now(i, 16))
                        E.hold(shifted, last(i, U, u + 1))
                        for half in range(2):
                            for k in range(KD):
                                m = nc.tensor.matmul(pz[:, u, half * HALF:(half + 1) * HALF], w[:, u, k, :],
                                                     hT[:, k, half * HALF:(half + 1) * HALF], start=k == 0, stop=k == KD - 1)
                        m.then_inc(z_psum, 1)

            @block.scalar
            def _(act):
                A.open(kept, n=U)
                A.open(zf_out, n=16 * U)
                act.wait_ge(keep_v, 1)
                with act.Fori(0, RWKV_TILES // U) as i:
                    for u in range(U):
                        A.hold(z_psum, now(i, U, u + 1))
                        A.hold(zf_out, last(i, 16 * U))
                        nc.scalar.activation(zf[:, u, :], pz[:, u, :], ACT.Copy, scale=keep[:, ds(i * U + u, 1)]).then_inc(kept, 1)
                    for u in range(U):
                        A.hold(shifted, now(i, U, u + 1))
                        act.dma_start(zf_view[:, ds(i * U + u, 1), :], zf[:, u:u + 1, :]).then_inc(zf_out, 16)
                act.wait_ge(zf_out, 16 * (RWKV_TILES + U))

            @block.vector
            def _(dve):
                V.open(shifted, n=U)
                dve.wait_ge(consts, (1 + KD) * 16)
                V.link(nc.vector.tensor_tensor(keep[:, :], vec[:, mp:mp + RWKV_TILES], vec[:, mn:mn + RWKV_TILES], ALU.add))
                V.link(nc.vector.tensor_scalar(keep[:, :], keep[:, :], -1.0, 1.0, ALU.mult, ALU.add))
                dve.sem_inc(keep_v, 1)
                with dve.Fori(0, RWKV_TILES // U) as i:
                    V.loop(i, U)
                    for u in range(U):
                        V.hold(kept, now(i, U, u + 1))
                        V.link(nc.vector.scalar_tensor_tensor(zf[:, u, 1:T], pz[:, u, 0:T - 1], vec[:, ds(i * U + (mp + u), 1)],
                                                              zf[:, u, 1:T], ALU.mult, ALU.add))
                        nc.vector.scalar_tensor_tensor(zf[:, u, 0:T - 1], pz[:, u, 1:T], vec[:, ds(i * U + (mn + u), 1)],
                                                       zf[:, u, 0:T - 1], ALU.mult, ALU.add).then_inc(shifted, 1)
                V.done(RWKV_TILES // U)


def prep_tables():
    t = np.arange(T)
    starts = np.stack([(t % C != 0), (t % C != C - 1)]).astype(np.float32)
    q = np.arange(P) // 64
    return np.ascontiguousarray(np.broadcast_to(starts, (P, 2, T))), (q[:, None] == q[None, :]).astype(np.float32)


def prep_phase(nc, vecs, w_up, a_up, g_up, zf_dram, starts, head_ones, arr_dram):
    with Phase(nc, "prep") as ph:
        vec = ph.sb("vec", [P, VEC_N])
        ups = ph.sb("ups", [P, 3, RC])
        up = ph.sb("up", [P, 3, P])
        go = ph.sb("go", [P, 2, T])
        ones = ph.sb("ones", [P, P])
        low = ph.sb("low", [P, 3, T])
        rkv = ph.sb("rkv", [P, 3, T])
        a = ph.sb("a", [P, 2, T])
        s = ph.sb("s", [P, 2, T])
        t1 = ph.sb("t1", [P, T])
        t2 = ph.sb("t2", [P, T])
        nrm = ph.sb("nrm", [P, T])
        kmix = ph.sb("kmix", [P, 2, T])
        onek = ph.sb("onek", [P, RJ])
        out = ph.sb("out", [P, 9, T])
        pw = [ph.ps(f"pw{n}", [P, T]) for n in range(4)]
        names = "up_ready z_in z_free sq_ready ss_psum nrm_a g_psum g_a w_psum w_a a_psum a_a nkk_v d_done bt_ready bonus_psum bonus_v arr_out".split()
        (up_ready, z_in, z_free, sq_ready, ss_psum, nrm_a, g_psum, g_a, w_psum, w_a, a_psum, a_a, nkk_v, d_done, bt_ready,
         bonus_psum, bonus_v, arr_out) = [ph.sem(n) for n in names]
        consts = ph.sem("consts")
        low_a = ph.sem("low_a")
        V, G, A, E, S = (ph.engine(e, n) for e, n in ((nc.vector, "dve"), (nc.gpsimd, "pool"), (nc.scalar, "act"),
                                                      (nc.tensor, "pe"), (nc.sync, "sp")))
        at = lambda n: vec_at(n)[0]
        zf_view = zf_dram.rearrange("(k p) t -> p k t", p=P)
        arr_view = arr_dram.rearrange("a (k p) t -> p a k t", p=P)
        OUT = ["nkk", "b0", "b1", "kd0", "kd1", "L0", "L1", "g", "bonus"]

        with nc.Block() as block:

            @block.sync
            def _(sp):
                S.open(z_in, n=16)
                S.open(arr_out, n=16 * 11)
                for dst, src in ((vec[:, :], vecs), (go[:, :, :], starts), (ones[:, :], head_ones),
                                 (ups[:, 0, :], w_up[0].rearrange("d r c -> (d r) c")),
                                 (ups[:, 1, :], a_up[0].rearrange("d r c -> (d r) c")), (ups[:, 2, :], g_up[0]),
                                 (low[:, :, :], zf_view[:, 12:15, :])):
                    sp.dma_start(dst, src).then_inc(consts, 16)
                with sp.Fori(0, RJ) as j:
                    S.hold(bonus_v, last(j))
                    S.hold(arr_out, last(j, 16 * 11))
                    sp.dma_start(rkv[:, :, :], zf_view[:, 0:3 * RJ, :].rearrange("p (a j) t -> p a j t", j=RJ)[:, :, ds(j, 1), :].rearrange("p a o t -> p (a o) t")).then_inc(z_in, 16)
                    S.hold(z_in, now(j, 16))
                    sp.dma_start(arr_view[:, 0, ds(j, 1), :], rkv[:, 0:1, :]).then_inc(arr_out, 16)
                    sp.dma_start(arr_view[:, 1, ds(j, 1), :], rkv[:, 2:3, :]).then_inc(arr_out, 16)
                    S.hold(bonus_v, now(j))
                    S.hold(g_a, now(j))
                    for n, name in enumerate(OUT):
                        sp.dma_start(arr_view[:, ARR[name], ds(j, 1), :], out[:, n:n + 1, :]).then_inc(arr_out, 16)
                sp.wait_ge(arr_out, 16 * 11 * (RJ + 1))

            @block.gpsimd
            def _(pool):
                G.open(up_ready)
                pool.wait_ge(consts, 7 * 16)
                with pool.Fori(0, RJ) as j:
                    G.hold(a_psum, last(j, 2))
                    nc.gpsimd.tensor_copy(up[:, :, :], ups[:, :, ds(j * P, P)]).then_inc(up_ready, 1)

            @block.scalar
            def _(act):
                A.open(nrm_a, g_a)
                A.open(w_a, a_a, n=2)
                act.wait_ge(consts, 7 * 16)
                nc.scalar.activation(low[:, 0, :], low[:, 0, :], ACT.Tanh).then_inc(low_a, 1)
                nc.scalar.activation(low[:, 2, :], low[:, 2, :], ACT.Sigmoid).then_inc(low_a, 1)
                with act.Fori(0, RJ) as j:
                    A.hold(ss_psum, now(j))
                    nc.scalar.activation(nrm[:, :], pw[0][:, :], ACT.Sqrt).then_inc(nrm_a, 1)
                    A.hold(g_psum, now(j))
                    A.hold(arr_out, last(j, 16 * 11))
                    nc.scalar.copy(out[:, 7, :], pw[1][:, :]).then_inc(g_a, 1)
                    for d in range(2):
                        A.hold(w_psum, now(j, 2, d + 1))
                        A.hold(d_done, last(j, 2, d + 1))
                        nc.scalar.activation(s[:, d, :], pw[2 - 2 * d][:, :], ACT.Sigmoid, bias=vec[:, ds(j + (at("w0") + 4 * d), 1)]).then_inc(w_a, 1)
                        A.hold(a_psum, now(j, 2, d + 1))
                        nc.scalar.activation(a[:, d, :], pw[3 - 2 * d][:, :], ACT.Sigmoid, bias=vec[:, ds(j + (at("a0") + 4 * d), 1)]).then_inc(a_a, 1)

            @block.tensor
            def _(pe):
                E.open(ss_psum, g_psum, bonus_psum)
                E.open(w_psum, a_psum, n=2)
                pe.wait_ge(consts, 7 * 16)
                pe.wait_ge(low_a, 2)

                def two(ps, lhsT, rhs, sem):
                    for half in range(2):
                        m = nc.tensor.matmul(ps[:, half * HALF:(half + 1) * HALF], lhsT, rhs[:, half * HALF:(half + 1) * HALF], start=True, stop=True)
                    m.then_inc(sem, 1)

                with pe.Fori(0, RJ) as j:
                    E.hold(sq_ready, now(j))
                    E.hold(w_a, last(j, 2))
                    two(pw[0], ones[:, :], t2, ss_psum)
                    E.hold(up_ready, now(j))
                    E.hold(a_a, last(j, 2))
                    two(pw[1], up[:, 2, :], low[:, 2, :], g_psum)
                    for d in range(2):
                        lo = slice(64 * d, 64 * d + 64)
                        if d == 0:
                            E.hold(bonus_v, last(j))
                        else:
                            E.hold(nrm_a, now(j))
                        two(pw[2 - 2 * d], up[lo, 0, :], low[lo, 0, :], w_psum)
                        if d:
                            E.hold(g_a, now(j))
                        else:
                            E.hold(a_a, last(j, 2))
                        two(pw[3 - 2 * d], up[lo, 1, :], low[lo, 1, :], a_psum)
                    E.hold(bt_ready, now(j))
                    E.hold(w_a, now(j, 2))
                    two(pw[2], ones[:, :], t1, bonus_psum)

            @block.vector
            def _(dve):
                V.open(sq_ready, bt_ready, bonus_v)
                V.open(d_done, n=2)
                dve.wait_ge(consts, 7 * 16)
                ka, rk, kkv = at("k_a"), at("r_k"), at("k_k")
                V.link(nc.vector.tensor_scalar(onek[:, :], vec[:, ka:ka + RJ], -1.0, 1.0, ALU.mult, ALU.add))
                with dve.Fori(0, RJ) as j:
                    V.loop(j, 11)
                    V.hold(z_in, now(j, 16))
                    V.hold(arr_out, last(j, 16 * 11))
                    V.hold(bonus_psum, last(j))
                    r_, k_, v_ = (rkv[:, n, :] for n in range(3))
                    V.link(nc.vector.tensor_scalar(t1[:, :], k_, vec[:, ds(j + kkv, 1)], None, ALU.mult))
                    nc.vector.tensor_tensor(t2[:, :], t1[:, :], t1[:, :], ALU.mult).then_inc(sq_ready, 1)
                    V.hold(nrm_a, now(j))
                    V.link(nc.vector.tensor_scalar(nrm[:, :], nrm[:, :], 1e-12, -1.0, ALU.max, ALU.mult))
                    V.link(nc.vector.reciprocal(nrm[:, :], nrm[:, :]))
                    V.link(nc.vector.tensor_tensor(out[:, 0, :], t1[:, :], nrm[:, :], ALU.mult))
                    for d in range(2):
                        V.hold(w_a, now(j, 2, d + 1))
                        step = slice(None) if d == 0 else slice(None, None, -1)
                        nc.vector.tensor_tensor_scan(out[:, 5 + d, step], go[:, d, step], s[:, d, step], 0.0, ALU.mult, ALU.add)
                        V.hold(a_a, now(j, 2, d + 1))
                        V.link(nc.vector.tensor_scalar(kmix[:, d, :], a[:, d, :], vec[:, ds(j + ka, 1)], onek[:, ds(j, 1)], ALU.mult, ALU.add))
                        nc.vector.scalar_tensor_tensor(out[:, 1 + d, :], out[:, 0, :], -1.0, a[:, d, :], ALU.mult, ALU.mult)
                        V.link(nc.vector.tensor_tensor(out[:, 3 + d, :], kmix[:, d, :], k_, ALU.mult))
                        dve.sem_inc(d_done, 1)
                    V.link(nc.vector.tensor_tensor(t1[:, :], out[:, 3, :], out[:, 4, :], ALU.add))
                    V.link(nc.vector.scalar_tensor_tensor(t2[:, :], t1[:, :], vec[:, ds(j + rk, 1)], r_, ALU.mult, ALU.mult))
                    nc.vector.tensor_copy(t1[:, :], t2[:, :]).then_inc(bt_ready, 1)
                    V.hold(bonus_psum, now(j))
                    V.link(nc.vector.tensor_tensor(out[:, 8, :], pw[2][:, :], v_, ALU.mult))
                    dve.sem_inc(bonus_v, 1)
                V.done(RJ)



LEVELS = (1, 2, 4, 8, 16, 32)


def wkv_tables():
    t = np.arange(C)
    r, c = t[:, None], t[None, :]
    masks = []
    for b in LEVELS:
        later, earlier = (r // b) % 2 == 1, (c // b) % 2 == 0
        masks.append((r // (2 * b) == c // (2 * b)) & later & earlier)
    masks.append(masks[0].T)
    masks.append(r < c)
    masks.append(r <= c)
    both = np.stack([np.stack([m, m.T]) for m in masks])
    both = both.transpose(2, 0, 1, 3).astype(np.float32)
    eye = np.broadcast_to(np.eye(C, dtype=np.float32)[:, None], (C, 2, C))
    one = np.concatenate([both.reshape(C, -1), eye.reshape(C, -1)], axis=1)
    return np.ascontiguousarray(np.concatenate([one, one]))


N_MASKS = len(LEVELS) + 3


def wkv_phase(nc, tables, arr_dram, y_dram):
    W = 2 * RJ * C
    NA = 6
    NL = len(LEVELS) - 1
    NG, NV, NK = 8, 5, 4
    IN = 16 * 2 * NA
    with Phase(nc, "wkv") as ph:
        def two(name):
            return [ph.sb(f"{name}{v}", [P, W]) for v in range(2)]

        tab = ph.sb("tab", [P, (N_MASKS + 1) * 2 * C])
        inp = [ph.sb(f"inp{v}", [P, NA, W]) for v in range(2)]
        ex = ph.sb("ex", [P, W])
        inv = ph.sb("inv", [P, W])
        at, rt, bh, kh, ak, rb, rk, bt, kt, vt, Z = (two(n) for n in "at rt bh kh ak rb rk bt kt vt Z".split())
        a_raw = ph.sb("a_raw", [P, W])
        a_l = ph.sb("a_l", [P, NL, W])
        x1 = ph.sb("x1", [P, 2, W])
        X = ph.sb("X", [P, W])
        Q = ph.sb("Q", [P, W])
        pp = ph.sb("pp", [P, W])
        uu = ph.sb("uu", [P, W])
        st = ph.sb("st", [P, W])
        st1 = ph.sb("st1", [P, W])
        dec = ph.sb("dec", [P, 2, 2 * RJ])
        yy = ph.sb("yy", [P, W])
        bX, bZ, bQ, b3, b4, b5, b6, b7 = [ph.ps(f"b{n}", [P, W]) for n in range(8)]

        names = ("exps operands g_v g_a a_masked q_psum q_kept xz_psum xz_kept p_psum p_kept u_psum u_kept "
                 "y_psum y_kept y_out s_psum s_kept grams tabs st0").split()
        (exps, operands, g_v, g_a, a_masked, q_psum, q_kept, xz_psum, xz_kept, p_psum, p_kept, u_psum, u_kept,
         y_psum, y_kept, y_out, s_psum, s_kept, grams, tabs, st0) = [ph.sem(n) for n in names]
        in_done = [ph.sem(f"in_done{v}") for v in range(2)]
        V, G, A, E, S = (ph.engine(e, n) for e, n in ((nc.vector, "dve"), (nc.gpsimd, "pool"), (nc.scalar, "act"),
                                                      (nc.tensor, "pe"), (nc.sync, "sp")))

        def mask(n):
            return tab[:, n * 2 * C:(n + 1) * 2 * C].rearrange("p (d c) -> p d c", d=2).unsqueeze(2).to_broadcast([P, 2, RJ, C])

        def grid(a):
            return a.rearrange("p (d j c) -> p d j c", d=2, j=RJ)

        def unit(t, p, n):
            return t[64 * p:64 * p + 64, n * C:(n + 1) * C]

        arr_view = arr_dram.rearrange("a (j p) t -> p a j t", p=P)
        y_view = y_dram.rearrange("d (j p) t -> p d j t", p=P)

        def turns(eng, E_, turn, links):
            turn(0, 0, 0, True, False, True)
            with eng.Fori(0, (NCH - 2) // 2) as n:
                E_.loop(n, 2 * links)
                turn(n * 2 + 1, 1, n, True, True, True)
                turn(n * 2 + 2, 0, n + 1, True, True, True)
            E_.done((NCH - 2) // 2)
            turn(NCH - 1, 1, NCH // 2 - 1, True, True, False)
            turn(NCH, 0, NCH // 2, False, True, False)

        with nc.Block() as block:

            @block.sync
            def _(sp):
                S.open(y_out, n=32)
                sp.dma_start(tab[:, :], tables).then_inc(tabs, 16)

                def load(i, v):
                    for d in range(2):
                        cols = ds(i * C, C) if d == 0 else ds(i * (-C) + (T - C), C)
                        for n, name in enumerate(("r", "v", "nkk", f"b{d}", f"kd{d}", f"L{d}")):
                            sp.dma_start(grid(inp[v][:, n, :])[:, d, :, :], arr_view[:, ARR[name], :, cols]).then_inc(in_done[v], 16)

                def turn(i, v, q, a, b, more):
                    if more:
                        if b:
                            S.hold(operands, last(i))
                            S.hold(exps, last(i))
                            S.hold(grams, last(i, NG))
                        load(i + 1, 1 - v)
                    if b:
                        S.hold(y_kept, i + 1)
                        for d in range(2):
                            cols = ds(i * C - C, C) if d == 0 else ds(i * (-C) + T, C)
                            sp.dma_start(y_view[:, d, :, cols], grid(yy[:, :])[:, d, :, :]).then_inc(y_out, 16)

                load(0, 0)
                turns(sp, S, turn, 0)
                sp.wait_ge(y_out, 32 * (NCH + 1))

            @block.gpsimd
            def _(pool):
                G.open(a_masked, n=NL)
                pool.wait_ge(tabs, 16)
                with pool.Fori(0, NCH) as i:
                    G.hold(g_a, now(i, NK, 1))
                    for n in range(NL):
                        G.hold(q_psum, last(i, NL, n + 1))
                        nc.gpsimd.tensor_tensor(grid(a_l[:, n, :]), grid(a_raw[:, :]), mask(n + 1), ALU.mult).then_inc(a_masked, 1)

            @block.scalar
            def _(act):
                A.open(exps, p_kept, u_kept, y_kept)
                A.open(g_a, n=NK)
                A.open(q_kept, n=NL)

                def turn(i, v, q, a, b, more):
                    o = 1 - v

                    def keep_q(n):
                        A.hold(q_psum, now(i, NL, n + 1))
                        A.hold(xz_psum, now(i, NL, n) if n else last(i, NL))
                        nc.scalar.copy(Q[:, :], bQ[:, :]).then_inc(q_kept, 1)

                    def keep(dst, src, gram):
                        A.hold(grams, now(i, NG, gram))
                        if b:
                            A.hold(s_psum, i)
                        nc.scalar.copy(dst[:, :], src[:, :]).then_inc(g_a, 1)

                    if a:
                        A.hold(grams, now(i, NG, 1))
                        A.hold(a_masked, last(i, NL))
                        nc.scalar.copy(a_raw[:, :], bX[:, :]).then_inc(g_a, 1)
                    if b:
                        A.hold(p_psum, i + 1)
                        A.hold(u_psum, i)
                        nc.scalar.copy(pp[:, :], b4[:, :]).then_inc(p_kept, 1)
                    if a:
                        keep_q(0)
                    if b:
                        A.hold(u_psum, i + 1)
                        A.hold(s_psum, i)
                        nc.scalar.copy(uu[:, :], b5[:, :]).then_inc(u_kept, 1)
                    if a:
                        keep_q(1)
                        keep(bt[v], b3, 6)
                    if more:
                        A.hold(in_done[o], (q + v + 1) * IN)
                        A.hold(operands, now(i))
                        nc.scalar.activation(ex[:, :], inp[o][:, 5, :], ACT.Exp, scale=-W_SCALE)
                    if a:
                        keep(kt[v], b4, 7)
                        keep_q(2)
                    if more:
                        nc.scalar.activation(inv[:, :], inp[o][:, 5, :], ACT.Exp, scale=W_SCALE).then_inc(exps, 1)
                    if b:
                        A.hold(y_psum, i + 1)
                        A.hold(y_out, i * 32)
                        nc.scalar.copy(yy[:, :], b6[:, :]).then_inc(y_kept, 1)
                    if a:
                        keep_q(3)
                        keep(vt[v], b5, 8)
                        keep_q(4)

                act.wait_ge(in_done[0], IN)
                nc.scalar.activation(ex[:, :], inp[0][:, 5, :], ACT.Exp, scale=-W_SCALE)
                nc.scalar.activation(inv[:, :], inp[0][:, 5, :], ACT.Exp, scale=W_SCALE).then_inc(exps, 1)
                turns(act, A, turn, 0)

            @block.vector
            def _(dve):
                V.open(operands, s_kept)
                V.open(g_v, n=NV)
                V.open(xz_kept, n=NL)

                def inverse_decayed(v):
                    nc.vector.tensor_tensor(bh[v][:, :], inp[v][:, 3, :], inv[:, :], ALU.mult)
                    nc.vector.tensor_tensor(kh[v][:, :], inp[v][:, 4, :], inv[:, :], ALU.mult)

                def decayed_a(v):
                    ge, ga, gi = grid(ex[:, :]), grid(at[v][:, :]), grid(inp[v][:, 2, :])
                    nc.vector.tensor_tensor(ga[:, 0, :, 1:C], gi[:, 0, :, 1:C], ge[:, 0, :, 0:C - 1], ALU.mult)
                    nc.vector.tensor_tensor(ga[:, 1, :, 0:C - 1], gi[:, 1, :, 0:C - 1], ge[:, 1, :, 1:C], ALU.mult)
                    nc.vector.tensor_copy(ga[:, 0, :, 0:1], gi[:, 0, :, 0:1])
                    nc.vector.tensor_copy(ga[:, 1, :, C - 1:C], gi[:, 1, :, C - 1:C])

                def decayed_r(v):
                    ge = grid(ex[:, :])
                    nc.vector.tensor_copy(dec[:, v, 0:RJ], ge[:, 0, :, C - 1])
                    nc.vector.tensor_copy(dec[:, v, RJ:2 * RJ], ge[:, 1, :, 0])
                    nc.vector.tensor_tensor(rt[v][:, :], inp[v][:, 0, :], ex[:, :], ALU.mult).then_inc(operands, 1)

                def turn(i, v, q, a, b, more):
                    o = 1 - v

                    def level(n):
                        V.hold(xz_psum, now(i, NL, n + 1))
                        if n < NL - 1:
                            nc.vector.tensor_tensor(X[:, :], X[:, :], bX[:, :], ALU.add)
                        nc.vector.tensor_tensor(Z[v][:, :], Z[v][:, :], bZ[:, :], ALU.add).then_inc(xz_kept, 1)
                        V.hold(xz_kept, now(i, NL, n + 1))

                    def masked(dst, src, gram, m):
                        V.hold(grams, now(i, NG, gram))
                        nc.vector.tensor_tensor(grid(dst[:, :]), grid(src[:, :]), mask(m), ALU.mult).then_inc(g_v, 1)

                    if a:
                        V.hold(g_a, now(i, NK, 1))
                        V.hold(xz_psum, last(i, NL))
                        masked(x1[:, 0, :], bX, 1, 0)
                        V.hold(grams, now(i, NG, 2))
                        V.link(nc.vector.tensor_tensor(grid(x1[:, 1, :]), grid(bZ[:, :]), mask(NL + 1), ALU.mult))
                        eye = mask(N_MASKS)
                        nc.vector.tensor_tensor(grid(X[:, :]), grid(x1[:, 0, :]), eye, ALU.add)
                        if b:
                            V.hold(u_psum, i)
                        nc.vector.tensor_tensor(grid(Z[v][:, :]), grid(x1[:, 1, :]), eye, ALU.add).then_inc(g_v, 1)
                        if b:
                            V.hold(y_psum, i)
                        masked(ak[v], b3, 3, NL + 2)
                        masked(rb[v], b6, 4, NL + 3)
                        masked(rk[v], b7, 5, NL + 3)
                        V.hold(g_v, now(i, NV, 2))
                        level(0)
                        level(1)
                        level(2)
                    if more:
                        V.hold(exps, now(i + 1))
                        if b:
                            V.hold(grams, last(i, NG))
                            V.hold(p_psum, i + 1)
                        inverse_decayed(o)
                        decayed_a(o)
                    if a:
                        level(3)
                    if b:
                        V.hold(s_psum, i + 1)
                        V.link(nc.vector.tensor_tensor(st1[:, :], st[:, :], b7[:, :], ALU.add))
                        V.link(nc.vector.tensor_tensor(st[:, :].rearrange("p (n c) -> p n c", c=C), st1[:, :].rearrange("p (n c) -> p n c", c=C),
                                                       dec[:, o, :].unsqueeze(2).to_broadcast([P, 2 * RJ, C]), ALU.mult))
                        dve.sem_inc(s_kept, 1)
                    if more:
                        if b:
                            V.hold(y_psum, i + 1)
                        decayed_r(o)
                    if a:
                        level(4)

                dve.wait_ge(tabs, 16)
                V.link(nc.vector.memset(st[:, :], 0.0))
                dve.sem_inc(st0, 1)
                dve.wait_ge(exps, 2)
                inverse_decayed(0)
                decayed_a(0)
                decayed_r(0)
                turns(dve, V, turn, 3)

            @block.tensor
            def _(pe):
                E.open(p_psum, u_psum, y_psum, s_psum)
                E.open(grams, n=NG)
                E.open(q_psum, xz_psum, n=NL)
                pe.wait_ge(tabs, 16)
                pe.wait_ge(st0, 1)
                units = [(p, n) for n in range(2 * RJ) for p in range(2)]
                eye = tab[:, N_MASKS * 2 * C:N_MASKS * 2 * C + C]

                def product(dst, pairs, some=slice(None)):
                    for p, n in units[some]:
                        for k, (lhsT, rhs) in enumerate(pairs):
                            right = rhs[64 * p:64 * p + 64, :] if rhs is eye else unit(rhs, p, n)
                            m = nc.tensor.matmul(unit(dst, p, n), unit(lhsT, p, n), right, start=k == 0, stop=k == len(pairs) - 1)
                    return m

                first, second = slice(0, 8), slice(8, 16)

                def turn(i, v, q, a, b, more):
                    o = 1 - v

                    def gram(dst, lhsT, rhs):
                        product(dst, [(lhsT, rhs)]).then_inc(grams, 1)

                    def blocks(n):
                        if a:
                            if n == 0:
                                E.hold(g_v, now(i, NV, 2))
                            else:
                                E.hold(xz_kept, now(i, NL, n))
                            E.hold(a_masked, now(i, NL, n + 1))
                            product(bQ, [(a_l[:, n, :], Z[v])]).then_inc(q_psum, 1)

                    def extend(n):
                        if a:
                            E.hold(q_kept, now(i, NL, n + 1))
                            if n < NL - 1:
                                product(bX, [(Q, X)])
                            product(bZ, [(X, Q)]).then_inc(xz_psum, 1)

                    outputs = [(st, rt[o]), (uu, rb[o]), (vt[o], rk[o])]
                    update = [(bt[o], uu), (kt[o], vt[o])]
                    if a:
                        E.hold(operands, now(i))
                        E.hold(xz_kept, last(i, NL))
                        gram(bX, at[v], bh[v])
                        gram(bZ, bh[v], at[v])
                        E.hold(g_a, last(i, NK))
                        gram(b3, kh[v], at[v])
                        if b:
                            E.hold(y_kept, i)
                        gram(b6, bh[v], rt[v])
                    if b:
                        E.hold(s_kept, i)
                        E.hold(g_v, last(i, NV))
                        E.hold(g_a, last(i, NK))
                        product(b4, [(at[o], st), (ak[o], vt[o])]).then_inc(p_psum, 1)
                    blocks(0)
                    if a:
                        gram(b7, kh[v], rt[v])
                    extend(0)
                    if b:
                        E.hold(p_kept, i + 1)
                        E.hold(xz_kept, last(i, NL))
                        product(b5, [(Z[o], pp)]).then_inc(u_psum, 1)
                    blocks(1)
                    if a:
                        E.hold(g_v, now(i, NV, 3))
                        gram(b3, bh[v], eye)
                    extend(1)
                    if a:
                        gram(b4, kh[v], eye)
                    blocks(2)
                    if b:
                        E.hold(u_kept, i + 1)
                        if a:
                            E.hold(g_v, now(i, NV, NV))
                        else:
                            E.hold(y_kept, i)
                        product(b6, outputs, first)
                    extend(2)
                    if b:
                        product(b6, outputs, second).then_inc(y_psum, 1)
                    blocks(3)
                    if b:
                        product(b7, update, first)
                    extend(3)
                    if a:
                        if b:
                            E.hold(u_kept, i + 1)
                        gram(b5, inp[v][:, 1, :], eye)
                    blocks(4)
                    if b:
                        product(b7, update, second).then_inc(s_psum, 1)
                    extend(4)

                turns(pe, E, turn, 0)



LNX_EPS = 64e-5
GATE_AT = MLA_IN + RWKV_TILES * P


def mix_phase(nc, vecs, w_in, w_br_mla, w_br_rwkv, head_ones, hT_dram, oT_dram, arr_dram, y_dram, mixT_dram):
    with Phase(nc, "mix") as ph:
        vec = ph.sb("vec", [P, VEC_N])
        ones = ph.sb("ones", [P, P])
        hT = ph.sb("hT", [P, KD, T])
        oT = ph.sb("oT", [P, 2 * RJ, T])
        inp = ph.sb("inp", [P, 4, T])
        y = ph.sb("y", [P, T])
        sq = ph.sb("sq", [P, T])
        rt = ph.sb("rt", [P, T])
        w = ph.sb("w", [P, 2, 24, P])
        sg = ph.sb("sg", [P, 2, T])
        mixed = ph.sb("mixed", [P, T])
        m1 = ph.sb("m1", [P, T])
        pb = [ph.ps(f"pb{n}", [P, T]) for n in range(4)]
        names = "in_done y_sum mean_psum cent sq_ready var_psum root o_ready consts late rt_ready z_psum gates br_psum mixed_ready mixed_out".split()
        (in_done, y_sum, mean_psum, cent, sq_ready, var_psum, root, o_ready, consts, late, rt_ready, z_psum, gates, br_psum, mixed_ready,
         mixed_out) = [ph.sem(n) for n in names]
        w_done = [ph.sem(f"w_done{u}") for u in range(2)]
        V, A, E, S = (ph.engine(e, n) for e, n in ((nc.vector, "dve"), (nc.scalar, "act"), (nc.tensor, "pe"), (nc.sync, "sp")))
        at = lambda n: vec_at(n)[0]
        arr_view = arr_dram.rearrange("a (k p) t -> p a k t", p=P)
        y_view = y_dram.rearrange("d (k p) t -> p d k t", p=P)
        hT_view = hT_dram.rearrange("(k p) t -> p k t", p=P)
        mix_view = mixT_dram.rearrange("(k p) t -> p k t", p=P)
        wi = w_in[0].rearrange("(k p) n -> p k n", p=P)
        wa = w_br_mla[0].rearrange("(k p) n -> p k n", p=P)
        wr = w_br_rwkv[0].rearrange("(k p) n -> p k n", p=P)

        with nc.Block() as block:

            @block.sync
            def _(sp):
                S.open(in_done, n=64)
                S.open(mixed_out, n=32)
                for u in range(2):
                    S.open(w_done[u], n=64)
                sp.dma_start(vec[:, :], vecs).then_inc(consts, 16)
                sp.dma_start(ones[:, :], head_ones).then_inc(consts, 16)

                def weights(u, cols, gate_cols):
                    for n, (src, k, c) in enumerate(((wi, KD, gate_cols(0)), (wi, KD, gate_cols(1)), (wa, RJ, cols), (wr, RJ, cols))):
                        lo = (0, 8, 16, 20)[n]
                        sp.dma_start(w[:, u, lo:lo + k, :], src[:, :, c]).then_inc(w_done[u], 16)

                with sp.Fori(0, RJ) as j:
                    S.hold(o_ready, last(j))
                    for n in range(2):
                        sp.dma_start(inp[:, n:n + 1, :], y_view[:, n, ds(j, 1), :]).then_inc(in_done, 16)
                    sp.dma_start(inp[:, 2:3, :], arr_view[:, ARR["bonus"], ds(j, 1), :]).then_inc(in_done, 16)
                    sp.dma_start(inp[:, 3:4, :], arr_view[:, ARR["g"], ds(j, 1), :]).then_inc(in_done, 16)
                for k in range(KD):
                    sp.dma_start(hT[:, k, :], hT_view[:, k, :]).then_inc(late, 16)
                sp.dma_start(oT[:, 0:RJ, :], oT_dram.rearrange("(k p) t -> p k t", p=P)).then_inc(late, 16)
                with sp.Fori(0, KD // 2) as i:
                    for u in range(2):
                        S.hold(br_psum, last(i, 2, u + 1))
                        weights(u, ds(i * 2 * P + u * P, P), lambda b, i=i, u=u: ds(i * 2 * P + (GATE_AT + b * D + u * P), P))
                        if u:
                            S.hold(mixed_ready, now(i, 2, u))
                            sp.dma_start(mix_view[:, ds(i * 2, 1), :], mixed[:, :].unsqueeze(1)).then_inc(mixed_out, 16)
                    S.hold(mixed_ready, now(i, 2, 2))
                    sp.dma_start(mix_view[:, ds(i * 2 + 1, 1), :], mixed[:, :].unsqueeze(1)).then_inc(mixed_out, 16)
                sp.wait_ge(mixed_out, 16 * (KD + 2))

            @block.tensor
            def _(pe):
                E.open(mean_psum, var_psum)
                E.open(br_psum, n=2)
                E.open(z_psum, n=4)
                pe.wait_ge(consts, 32)

                def two(ps, lhsT, rhs):
                    for half in range(2):
                        m = nc.tensor.matmul(ps[:, half * HALF:(half + 1) * HALF], lhsT, rhs[:, half * HALF:(half + 1) * HALF], start=True, stop=True)
                    return m

                with pe.Fori(0, RJ) as j:
                    E.hold(y_sum, now(j))
                    two(pb[0], ones[:, :], y).then_inc(mean_psum, 1)
                    E.hold(sq_ready, now(j))
                    two(pb[1], ones[:, :], sq).then_inc(var_psum, 1)
                E.hold(o_ready, RJ + 1)
                pe.wait_ge(late, (KD + 1) * 16)

                def many(ps, u, lo, n, rhs):
                    for half in range(2):
                        for k in range(n):
                            m = nc.tensor.matmul(ps[:, half * HALF:(half + 1) * HALF], w[:, u, lo + k, :],
                                                 rhs[:, k, half * HALF:(half + 1) * HALF], start=k == 0, stop=k == n - 1)
                    return m

                with pe.Fori(0, KD // 2) as i:
                    for u in range(2):
                        E.hold(w_done[u], now(i, 64))
                        E.hold(gates, now(i, 4, 2) if u else last(i, 4))
                        many(pb[0], u, 0, KD, hT).then_inc(z_psum, 1)
                        many(pb[1], u, 8, KD, hT).then_inc(z_psum, 1)
                        E.hold(mixed_ready, now(i, 2, 1) if u else last(i, 2))
                        many(pb[2], u, 16, RJ, oT)
                        many(pb[3], u, 20, RJ, oT[:, RJ:2 * RJ, :]).then_inc(br_psum, 1)

            @block.scalar
            def _(act):
                A.open(root, sq_ready)
                A.open(gates, n=4)
                act.wait_ge(consts, 32)
                with act.Fori(0, RJ) as j:
                    A.hold(cent, now(j))
                    A.hold(var_psum, last(j))
                    nc.scalar.activation(sq[:, :], y[:, :], ACT.Square).then_inc(sq_ready, 1)
                    A.hold(rt_ready, now(j))
                    nc.scalar.activation(rt[:, :], rt[:, :], ACT.Sqrt).then_inc(root, 1)
                with act.Fori(0, KD // 2) as i:
                    for u in range(2):
                        for b in range(2):
                            A.hold(z_psum, now(i, 4, 2 * u + b + 1))
                            A.hold(mixed_ready, now(i, 2, 1) if u else last(i, 2))
                            nc.scalar.activation(sg[:, b, :], pb[b][:, :], ACT.Sigmoid,
                                                 bias=vec[:, ds(i * 2 + (at("gate_b") + b * KD + u), 1)]).then_inc(gates, 1)

            @block.vector
            def _(dve):
                V.open(y_sum, cent, o_ready, rt_ready)
                V.open(mixed_ready, n=2)
                dve.wait_ge(consts, 32)
                with dve.Fori(0, RJ) as j:
                    V.loop(j, 5)
                    V.hold(in_done, now(j, 64))
                    nc.vector.tensor_tensor(y[:, :], inp[:, 0, :], inp[:, 1, :], ALU.add).then_inc(y_sum, 1)
                    V.hold(mean_psum, now(j))
                    nc.vector.scalar_tensor_tensor(y[:, :], pb[0][:, :], -1.0 / 64, y[:, :], ALU.mult, ALU.add).then_inc(cent, 1)
                    V.hold(var_psum, now(j))
                    nc.vector.tensor_scalar(rt[:, :], pb[1][:, :], 1.0 / 64, LNX_EPS, ALU.mult, ALU.add).then_inc(rt_ready, 1)
                    V.hold(root, now(j))
                    V.link(nc.vector.reciprocal(rt[:, :], rt[:, :]))
                    V.link(nc.vector.tensor_tensor(y[:, :], y[:, :], rt[:, :], ALU.mult))
                    V.link(nc.vector.tensor_scalar(y[:, :], y[:, :], vec[:, ds(j + at("lnx_g"), 1)], vec[:, ds(j + at("lnx_b"), 1)], ALU.mult, ALU.add))
                    V.link(nc.vector.tensor_tensor(y[:, :], y[:, :], inp[:, 2, :], ALU.add))
                    V.link(nc.vector.tensor_tensor(oT[:, ds(j + RJ, 1), :].rearrange("p o t -> p (o t)"), y[:, :], inp[:, 3, :], ALU.mult))
                    dve.sem_inc(o_ready, 1)
                V.done(RJ)
                with dve.Fori(0, KD // 2) as i:
                    V.loop(i, 4)
                    for u in range(2):
                        V.hold(gates, now(i, 4, 2 * u + 2))
                        V.hold(br_psum, now(i, 2, u + 1))
                        V.hold(mixed_out, now(i, 32, 16) if u else last(i, 32))
                        nc.vector.tensor_tensor(mixed[:, :], pb[2][:, :], sg[:, 0, :], ALU.mult)
                        V.link(nc.vector.tensor_tensor(m1[:, :], pb[3][:, :], sg[:, 1, :], ALU.mult))
                        V.link(nc.vector.tensor_tensor(mixed[:, :], mixed[:, :], m1[:, :], ALU.add))
                        dve.sem_inc(mixed_ready, 1)
                V.done(KD // 2)


N_GROUPS, PER_GROUP = 4, 8
N_EXP = N_GROUPS * PER_GROUP
MOE_BLOCKS = 2 * T // P + N_EXP
SLOTS = MOE_BLOCKS * P
LOGITS = N_GROUPS + N_EXP


def route_tables():
    t = np.arange(P)
    before = (t[:, None] < t[None, :]).astype(np.float32)
    row = np.concatenate([8.0 - np.arange(8), 128.0 * np.arange(8), 128.0 * np.arange(MOE_BLOCKS)])
    tok = (np.arange(NT)[None, :] * P + t[:, None])
    return np.ascontiguousarray(np.concatenate([before, np.ones((P, P)), np.broadcast_to(row, (P, row.size))], axis=1).astype(np.float32)), \
        np.ascontiguousarray(tok.astype(np.uint32))


def route_phase(nc, x, vecs, w_out, rg_w, rg_b, re_w, re_b, eye, tables, tok_ids, mixT_dram, x1_dram, h2_dram, slot_tok, keep):
    slot_u, wts, block_e = keep
    with Phase(nc, "route") as ph:
        ident = ph.sb("ident", [P, P])
        vec = ph.sb("vec", [P, VEC_N])
        wo = ph.sb("wo", [P, KD, D])
        rw = ph.sb("rw", [P, KD, LOGITS])
        rb = ph.sb("rb", [P, LOGITS])
        mT = ph.sb("mT", [P, KD, T])
        m_t = ph.sb("m_t", [P, KD, P])
        xt = ph.sb("xt", [P, D])
        x1 = ph.sb("x1", [P, D])
        junk = ph.sb("junk", [P, D])
        h2 = ph.sb("h2", [P, D])
        h2T = ph.sb("h2T", [P, KD, P])
        small = ph.sb("small", [P, 4])
        lg = ph.sb("lg", [P, NT, LOGITS])
        tab = ph.sb("tab", [P, 2 * P + 16 + MOE_BLOCKS])
        tok = ph.sb("tok", [P, NT], U32)
        zero = ph.sb("zero", [P, MOE_BLOCKS + 1], U32)
        gdiff = ph.sb("gdiff", [P, NT, N_GROUPS])
        e21 = ph.sb("e21", [P, NT])
        mem = ph.sb("mem", [P, NT, N_EXP])
        cum = ph.sb("cum", [P, NT + 1, N_EXP])
        gmax = ph.sb("gmax", [P, NT])
        goh = ph.sb("goh", [P, NT, N_GROUPS])
        el = ph.sb("el", [P, NT, N_GROUPS, PER_GROUP])
        sel = ph.sb("sel", [P, NT, PER_GROUP])
        sel2 = ph.sb("sel2", [P, NT, PER_GROUP])
        top = ph.sb("top", [P, 2, NT])
        oh = ph.sb("oh", [P, 2, NT, PER_GROUP])
        ohe = ph.sb("ohe", [P, 2, NT, N_GROUPS, PER_GROUP])
        pref = ph.sb("pref", [P, NT, PER_GROUP])
        pmax = ph.sb("pmax", [P, NT])
        gs = ph.sb("gs", [P, NT])
        rank = ph.sb("rank", [P, NT, N_EXP])
        pick = ph.sb("pick", [P, NT, N_EXP])
        slot_f = ph.sb("slot_f", [P, 2 * NT])
        over = ph.sb("over", [P, N_EXP, PER_GROUP])
        padded = ph.sb("padded", [P, N_EXP])
        pend = ph.sb("pend", [P, N_EXP])
        pstart = ph.sb("pstart", [P, N_EXP])
        cmp = ph.sb("cmp", [P, MOE_BLOCKS, N_EXP])
        be_f = ph.sb("be_f", [P, MOE_BLOCKS])
        po = ph.ps("po", [P, D])
        pt = ph.ps("pt", [P, D])
        pl = ph.ps("pl", [P, HALF])
        pr = ph.ps("pr", [P, HALF])
        names = ("consts x_in m_in xo_psum x1_ready x1_out sq ms root h2_ready h2_out hT_psum hT_ready l_psum l_kept "
                 "members rank_psum exp_in exp_out slots scattered zeroed").split()
        (consts, x_in, m_in, xo_psum, x1_ready, x1_out, sq, ms, root, h2_ready, h2_out, hT_psum, hT_ready, l_psum, l_kept,
         members, rank_psum, exp_in, exp_out, slots, scattered, zeroed) = [ph.sem(n) for n in names]
        V, G, A, E, S = (ph.engine(e, n) for e, n in ((nc.vector, "dve"), (nc.gpsimd, "pool"), (nc.scalar, "act"),
                                                      (nc.tensor, "pe"), (nc.sync, "sp")))
        g0 = vec_at("norm_ffn_g")[0]
        NCONST = 9 + KD

        with nc.Block() as block:

            @block.sync
            def _(sp):
                S.open(x_in, x1_out, h2_out, n=16)
                for dst, src in ((ident[:, :], eye), (vec[:, :], vecs), (wo[:, :, :], w_out[0].rearrange("(k p) n -> p k n", p=P)),
                                 (rw[:, :, 0:N_GROUPS], rg_w[0].rearrange("(k p) n -> p k n", p=P)),
                                 (rw[:, :, N_GROUPS:LOGITS], re_w[0].rearrange("(k p) n -> p k n", p=P)),
                                 (rb[:, 0:N_GROUPS], rg_b[0].partition_broadcast(P)), (rb[:, N_GROUPS:LOGITS], re_b[0].partition_broadcast(P)),
                                 (tab[:, :], tables), (tok[:, :], tok_ids)):
                    sp.dma_start(dst, src).then_inc(consts, 16)
                for k in range(KD):
                    sp.dma_start(mT[:, k, :], mixT_dram[k * P:(k + 1) * P, :]).then_inc(consts, 16)
                with sp.Fori(0, NT) as i:
                    S.hold(x1_ready, last(i))
                    sp.dma_start(xt[:, :], x[ds(i * P, P), :]).then_inc(x_in, 16)
                    S.hold(x1_ready, now(i))
                    sp.dma_start(x1_dram[ds(i * P, P), :], x1[:, :]).then_inc(x1_out, 16)
                    S.hold(h2_ready, now(i))
                    sp.dma_start(h2_dram[ds(i * P, P), :], h2[:, :]).then_inc(h2_out, 16)
                sp.wait_ge(x1_out, 16 * (NT + 1))
                sp.wait_ge(h2_out, 16 * (NT + 1))
                sp.wait_ge(zeroed, 1)
                sp.dma_start(slot_tok.rearrange("(p b) o -> p (b o)", p=P), zero[:, :]).then_inc(zeroed, 16)

            @block.gpsimd
            def _(pool):
                G.open(m_in)
                pool.wait_ge(consts, NCONST * 16)
                nc.gpsimd.memset(zero[:, :], 0).then_inc(zeroed, 1)
                with pool.Fori(0, NT) as i:
                    G.hold(xo_psum, last(i))
                    nc.gpsimd.tensor_copy(m_t[:, :, :], mT[:, :, ds(i * P, P)]).then_inc(m_in, 1)
                pool.wait_ge(slots, 1)
                pool.wait_ge(zeroed, 17)
                for n in range(2 * NT):
                    pool.indirect_dma_start(slot_tok, bass.IndirectOffsetOnAxis(ap=slot_u[:, n:n + 1], axis=0),
                                            tok[:, n % NT:n % NT + 1], None).then_inc(scattered, 16)
                pool.wait_ge(scattered, 16 * 2 * NT)

            @block.tensor
            def _(pe):
                E.open(xo_psum, hT_psum, l_psum)
                pe.wait_ge(consts, NCONST * 16)
                with pe.Fori(0, NT) as i:
                    E.hold(m_in, now(i))
                    E.hold(x1_ready, last(i))
                    for half in range(2):
                        for k in range(KD):
                            m = nc.tensor.matmul(po[:, half * HALF:(half + 1) * HALF], m_t[:, k, :], wo[:, k, half * HALF:(half + 1) * HALF],
                                                 start=k == 0, stop=k == KD - 1)
                    m.then_inc(xo_psum, 1)
                    E.hold(h2_ready, now(i))
                    for k in range(KD):
                        t = nc.tensor.transpose(pt[:, k * P:(k + 1) * P], h2[:, k * P:(k + 1) * P], ident[:, :])
                    t.then_inc(hT_psum, 1)
                    E.hold(hT_ready, now(i))
                    E.hold(l_kept, last(i))
                    for k in range(KD):
                        m = nc.tensor.matmul(pl[:, 0:LOGITS], h2T[:, k, :], rw[:, k, :], start=k == 0, stop=k == KD - 1)
                    m.then_inc(l_psum, 1)
                pe.wait_ge(members, 1)
                nc.tensor.matmul(pr[:, 0:NT * N_EXP], tab[:, 0:P], mem[:, :, :], start=True, stop=False)
                nc.tensor.matmul(pr[:, 0:NT * N_EXP], tab[:, P:2 * P], cum[:, 0:NT, :], start=False, stop=True)
                nc.tensor.matmul(pl[:, 0:N_EXP], tab[:, P:2 * P], cum[:, NT, :], start=True, stop=True).then_inc(rank_psum, 1)

            @block.scalar
            def _(act):
                A.open(sq, root)
                with act.Fori(0, NT) as i:
                    A.hold(x1_ready, now(i))
                    nc.scalar.activation(junk[:, :], x1[:, :], ACT.Square, accum_out=small[:, 0:1]).then_inc(sq, 1)
                    A.hold(ms, now(i))
                    nc.scalar.activation(small[:, 2:3], small[:, 1:2], ACT.Sqrt).then_inc(root, 1)
                act.wait_ge(exp_in, 1)
                nc.scalar.activation(gdiff[:, :, :], gdiff[:, :, :], ACT.Exp)
                nc.scalar.activation(e21[:, :], e21[:, :], ACT.Exp).then_inc(exp_out, 1)

            @block.vector
            def _(dve):
                V.open(x1_ready, ms, h2_ready, hT_ready, l_kept)
                dve.wait_ge(consts, NCONST * 16)
                with dve.Fori(0, NT) as i:
                    V.loop(i, 1)
                    V.hold(x_in, now(i, 16))
                    V.hold(xo_psum, now(i))
                    V.hold(x1_out, last(i, 16))
                    V.hold(sq, last(i))
                    nc.vector.tensor_tensor(x1[:, :], po[:, :], xt[:, :], ALU.add).then_inc(x1_ready, 1)
                    V.hold(sq, now(i))
                    nc.vector.tensor_scalar(small[:, 1:2], small[:, 0:1], 1.0 / D, NORM_EPS, ALU.mult, ALU.add).then_inc(ms, 1)
                    V.hold(root, now(i))
                    V.link(nc.vector.reciprocal(small[:, 3:4], small[:, 2:3]))
                    V.hold(h2_out, last(i, 16))
                    V.hold(hT_psum, last(i))
                    nc.vector.tensor_scalar(h2[:, :], x1[:, :], small[:, 3:4], None, ALU.mult).then_inc(h2_ready, 1)
                    V.hold(hT_psum, now(i))
                    V.hold(l_psum, last(i))
                    nc.vector.tensor_tensor(h2T[:, :, :], pt[:, :].rearrange("p (k t) -> p k t", k=KD),
                                            vec[:, g0:g0 + KD].unsqueeze(2).to_broadcast([P, KD, P]), ALU.mult).then_inc(hT_ready, 1)
                    V.hold(l_psum, now(i))
                    nc.vector.tensor_tensor(lg[:, ds(i, 1), :].rearrange("p o n -> p (o n)"), pl[:, 0:LOGITS], rb[:, :], ALU.add).then_inc(l_kept, 1)
                V.done(NT)
                dve.wait_ge(l_kept, NT + 1)

                def first_of(out, vals, best, n):
                    V.link(nc.vector.tensor_tensor(out, vals, best.unsqueeze(2).to_broadcast([P, NT, n]), ALU.is_equal))
                    V.link(nc.vector.tensor_tensor(pref[:, :, 0:n], out, tab[:, 2 * P:2 * P + n].unsqueeze(1).to_broadcast([P, NT, n]), ALU.mult))
                    V.link(nc.vector.reduce_max(pmax[:, :], pref[:, :, 0:n], AX_X))
                    V.link(nc.vector.tensor_tensor(out, pref[:, :, 0:n], pmax[:, :].unsqueeze(2).to_broadcast([P, NT, n]), ALU.is_equal))

                gl = lg[:, :, 0:N_GROUPS]
                V.link(nc.vector.reduce_max(gmax[:, :], gl, AX_X))
                first_of(goh[:, :, :], gl, gmax[:, :], N_GROUPS)
                V.link(nc.vector.tensor_tensor(gdiff[:, :, :], gl, gmax[:, :].unsqueeze(2).to_broadcast([P, NT, N_GROUPS]), ALU.subtract))
                for g in range(N_GROUPS):
                    V.link(nc.vector.tensor_tensor(el[:, :, g, :], lg[:, :, N_GROUPS + g * PER_GROUP:N_GROUPS + (g + 1) * PER_GROUP],
                                                   goh[:, :, g:g + 1].to_broadcast([P, NT, PER_GROUP]), ALU.mult))
                V.link(nc.vector.tensor_reduce(sel[:, :, :], el[:, :, :, :].rearrange("p t g e -> p t e g"), AX_X, ALU.add))
                V.link(nc.vector.reduce_max(top[:, 0, :], sel[:, :, :], AX_X))
                first_of(oh[:, 0, :, :], sel[:, :, :], top[:, 0, :], PER_GROUP)
                V.link(nc.vector.scalar_tensor_tensor(sel2[:, :, :], oh[:, 0, :, :], -3e38, sel[:, :, :], ALU.mult, ALU.add))
                V.link(nc.vector.reduce_max(top[:, 1, :], sel2[:, :, :], AX_X))
                first_of(oh[:, 1, :, :], sel2[:, :, :], top[:, 1, :], PER_GROUP)
                V.link(nc.vector.tensor_tensor(e21[:, :], top[:, 1, :], top[:, 0, :], ALU.subtract))
                dve.sem_inc(exp_in, 1)
                for n in range(2):
                    for g in range(N_GROUPS):
                        V.link(nc.vector.tensor_tensor(ohe[:, n, :, g, :], oh[:, n, :, :], goh[:, :, g:g + 1].to_broadcast([P, NT, PER_GROUP]), ALU.mult))
                V.link(nc.vector.tensor_tensor(mem[:, :, :], ohe[:, 0, :, :, :].rearrange("p t g e -> p t (g e)"),
                                               ohe[:, 1, :, :, :].rearrange("p t g e -> p t (g e)"), ALU.add))
                V.link(nc.vector.memset(cum[:, 0, :], 0.0))
                for n in range(NT):
                    V.link(nc.vector.tensor_tensor(cum[:, n + 1, :], cum[:, n, :], mem[:, n, :], ALU.add))
                dve.sem_inc(members, 1)
                dve.wait_ge(exp_out, 1)
                V.link(nc.vector.tensor_reduce(gs[:, :], gdiff[:, :, :], AX_X, ALU.add))
                V.link(nc.vector.tensor_scalar(pmax[:, :], e21[:, :], 1.0, None, ALU.add))
                V.link(nc.vector.tensor_tensor(gs[:, :], gs[:, :], pmax[:, :], ALU.mult))
                V.link(nc.vector.reciprocal(wts[:, 0:NT], gs[:, :]))
                V.link(nc.vector.tensor_tensor(wts[:, NT:2 * NT], wts[:, 0:NT], e21[:, :], ALU.mult))
                dve.wait_ge(rank_psum, 1)
                V.link(nc.vector.tensor_tensor(over[:, :, :], pl[:, 0:N_EXP].unsqueeze(2).to_broadcast([P, N_EXP, 8]),
                                               tab[:, 2 * P + 8:2 * P + 16].unsqueeze(1).to_broadcast([P, N_EXP, 8]), ALU.is_gt))
                V.link(nc.vector.tensor_reduce(padded[:, :], over[:, :, :], AX_X, ALU.add))
                V.link(nc.vector.tensor_scalar(padded[:, :], padded[:, :], float(P), None, ALU.mult))
                V.link(nc.vector.tensor_tensor_scan(pend[:, :], tab[:, P:P + N_EXP], padded[:, :], 0.0, ALU.mult, ALU.add))
                V.link(nc.vector.tensor_tensor(pstart[:, :], pend[:, :], padded[:, :], ALU.subtract))
                V.link(nc.vector.tensor_tensor(rank[:, :, :], pr[:, 0:NT * N_EXP].rearrange("p (t e) -> p t e", e=N_EXP),
                                               pstart[:, :].unsqueeze(1).to_broadcast([P, NT, N_EXP]), ALU.add))
                for n in range(2):
                    V.link(nc.vector.tensor_tensor(pick[:, :, :], rank[:, :, :], ohe[:, n, :, :, :].rearrange("p t g e -> p t (g e)"), ALU.mult))
                    V.link(nc.vector.tensor_reduce(slot_f[:, n * NT:(n + 1) * NT], pick[:, :, :], AX_X, ALU.add))
                V.link(nc.vector.tensor_copy(slot_u[:, :], slot_f[:, :]))
                dve.sem_inc(slots, 1)
                V.link(nc.vector.tensor_tensor(cmp[:, :, :], pend[:, :].unsqueeze(1).to_broadcast([P, MOE_BLOCKS, N_EXP]),
                                               tab[:, 2 * P + 16:2 * P + 16 + MOE_BLOCKS].unsqueeze(2).to_broadcast([P, MOE_BLOCKS, N_EXP]), ALU.is_le))
                V.link(nc.vector.tensor_reduce(be_f[:, :], cmp[:, :, :], AX_X, ALU.add))
                V.link(nc.vector.tensor_scalar(block_e[:, :], be_f[:, :], float(N_EXP - 1), None, ALU.min))



D_EXP = 256


def experts_phase(nc, vecs, w1, w3, w2, eye, block_e, slot_tok, h2_dram, yb_dram):
    with Phase(nc, "exp") as ph:
        U = 2
        ident = ph.sb("ident", [P, P])
        vec = ph.sb("vec", [P, VEC_N])
        wb = ph.sb("wb", [P, U, 2, KD, D_EXP])
        w2b = ph.sb("w2b", [P, U, 2, D])
        idx = ph.sb("idx", [P, U], U32)
        xg = ph.sb("xg", [P, U, D])
        xT = ph.sb("xT", [P, U, KD, P])
        sg = ph.sb("sg", [P, D_EXP])
        hid = ph.sb("hid", [P, D_EXP])
        hidT = ph.sb("hidT", [P, 2, P])
        y = ph.sb("y", [P, U, D])
        pt = ph.ps("pt", [P, D])
        pg = ph.ps("pg", [P, HALF])
        phT = ph.ps("phT", [P, HALF])
        py = ph.ps("py", [P, D])
        names = "consts idx_u x_psum x_ready gu_psum act_done hid_ready hT_psum hT_ready y_psum y_a y_v y_out".split()
        (consts, idx_u, x_psum, x_ready, gu_psum, act_done, hid_ready, hT_psum, hT_ready, y_psum, y_a, y_v, y_out) = [ph.sem(n) for n in names]
        w_done = [ph.sem(f"w_done{u}") for u in range(U)]
        idx_done = [ph.sem(f"idx_done{u}") for u in range(U)]
        x_in = [ph.sem(f"x_in{u}") for u in range(U)]
        V, G, A, E, S = (ph.engine(e, n) for e, n in ((nc.vector, "dve"), (nc.gpsimd, "pool"), (nc.scalar, "act"),
                                                      (nc.tensor, "pe"), (nc.sync, "sp")))
        g0 = vec_at("norm_ffn_g")[0]
        NB = MOE_BLOCKS

        with nc.Block() as block:

            @block.sync
            def _(sp):
                for u in range(U):
                    S.open(w_done[u], n=48)
                    S.open(idx_done[u], n=16)
                sp.dma_start(ident[:, :], eye).then_inc(consts, 16)
                sp.dma_start(vec[:, :], vecs).then_inc(consts, 16)
                sp.dma_start(idx[:, 0:1], slot_tok[0:P, :]).then_inc(idx_done[0], 16)
                with sp.Fori(0, NB // U) as i:
                    for u in range(U):
                        S.hold(y_psum, last(i, U, u + 1))
                        e = sp.value_load(block_e[0:1, ds(i * U + u, 1)], min_val=0, max_val=N_EXP - 1)
                        for n, w in enumerate((w1, w3)):
                            sp.dma_start(wb[:, u, n, :, :], w[0][ds(e, 1), :, :].rearrange("o (k p) f -> p (o k) f", p=P)).then_inc(w_done[u], 16)
                        sp.dma_start(w2b[:, u, :, :], w2[0][ds(e, 1), :, :].rearrange("o (k p) f -> p (o k) f", p=P)).then_inc(w_done[u], 16)
                        S.hold(x_psum, i * U + (U + u))
                        sp.dma_start(idx[:, 1 - u:2 - u], slot_tok[ds((i * U + (u + 1)) * P, P), :]).then_inc(idx_done[1 - u], 16)

            @block.gpsimd
            def _(pool):
                def gather(u):
                    pool.indirect_dma_start(xg[:, u, :], None, h2_dram, bass.IndirectOffsetOnAxis(ap=idx[:, u:u + 1], axis=0)).then_inc(x_in[u], 16)

                pool.wait_ge(idx_done[0], 32)
                gather(0)
                with pool.Fori(0, NB // U) as i:
                    for u in range(U):
                        v = 1 - u
                        G.hold(idx_done[v], now(i, 16) if u == 0 else now(i + 1, 16))
                        G.hold(x_psum, last(i, U, u + 1))
                        gather(v)
                pool.wait_ge(x_in[0], (NB // U + 1) * 16)

            @block.tensor
            def _(pe):
                E.open(gu_psum, hT_psum, y_psum, x_psum, n=U)
                pe.wait_ge(consts, 32)

                def turn_x(v):
                    for k in range(KD):
                        t = nc.tensor.transpose(pt[:, k * P:(k + 1) * P], xg[:, v, k * P:(k + 1) * P], ident[:, :])
                    t.then_inc(x_psum, 1)

                pe.wait_ge(x_in[0], 16)
                turn_x(0)
                with pe.Fori(0, NB // U) as i:
                    for u in range(U):
                        v = 1 - u
                        E.hold(x_ready, now(i, U, u + 1))
                        E.hold(w_done[u], now(i, 48))
                        E.hold(hid_ready, last(i, U, u + U) if u == 0 else now(i, U, u))
                        for k in range(KD):
                            m = nc.tensor.matmul(pg[:, :], xT[:, u, k, :], wb[:, u, :, k, :], start=k == 0, stop=k == KD - 1)
                        m.then_inc(gu_psum, 1)
                        E.hold(x_in[v], i * 16 + (16 if u == 0 else 32))
                        turn_x(v)
                        E.hold(hid_ready, now(i, U, u + 1))
                        for k in range(2):
                            t = nc.tensor.transpose(phT[:, k * P:(k + 1) * P], hid[:, k * P:(k + 1) * P], ident[:, :])
                        t.then_inc(hT_psum, 1)
                        E.hold(hT_ready, now(i, U, u + 1))
                        E.hold(y_a, now(i, U, u) if u else last(i, U))
                        E.hold(y_v, now(i, U, u) if u else last(i, U))
                        for half in range(2):
                            for k in range(2):
                                m = nc.tensor.matmul(py[:, half * HALF:(half + 1) * HALF], hidT[:, k, :], w2b[:, u, k, half * HALF:(half + 1) * HALF],
                                                     start=k == 0, stop=k == 1)
                        m.then_inc(y_psum, 1)

            @block.scalar
            def _(act):
                A.open(act_done, y_a, n=U)
                A.open(y_out, n=32)
                with act.Fori(0, NB // U) as i:
                    for u in range(U):
                        A.hold(gu_psum, now(i, U, u + 1))
                        nc.scalar.activation(sg[:, :], pg[:, 0:D_EXP], ACT.Silu).then_inc(act_done, 1)
                        A.hold(y_psum, now(i, U, u + 1))
                        A.hold(y_out, last(i, 32))
                        nc.scalar.copy(y[:, u, 0:HALF], py[:, 0:HALF]).then_inc(y_a, 1)
                        A.hold(y_a, now(i, U, u + 1))
                        A.hold(y_v, now(i, U, u + 1))
                        act.dma_start(yb_dram[ds((i * U + u) * P, P), :], y[:, u, :]).then_inc(y_out, 16)
                act.wait_ge(y_out, 16 * (NB + U))

            @block.vector
            def _(dve):
                V.open(hid_ready, hT_ready, y_v, n=U)
                V.open(x_ready, n=U)
                dve.wait_ge(consts, 32)
                gx = vec[:, g0:g0 + KD].unsqueeze(2).to_broadcast([P, KD, P])

                def keep_x(v):
                    nc.vector.tensor_tensor(xT[:, v, :, :], pt[:, :].rearrange("p (k t) -> p k t", k=KD), gx, ALU.mult).then_inc(x_ready, 1)

                dve.wait_ge(x_psum, U + 1)
                keep_x(0)
                with dve.Fori(0, NB // U) as i:
                    for u in range(U):
                        V.hold(act_done, now(i, U, u + 1))
                        V.hold(hT_psum, last(i, U, u + U) if u == 0 else now(i, U, u))
                        nc.vector.tensor_tensor(hid[:, :], sg[:, :], pg[:, D_EXP:HALF], ALU.mult).then_inc(hid_ready, 1)
                        V.hold(x_psum, now(i, U, u + 2))
                        keep_x(1 - u)
                        V.hold(hT_psum, now(i, U, u + 1))
                        V.hold(y_psum, last(i, U, u + U) if u == 0 else now(i, U, u))
                        nc.vector.tensor_copy(hidT[:, :, :], phT[:, 0:D_EXP].rearrange("p (k t) -> p k t", k=2)).then_inc(hT_ready, 1)
                        V.hold(y_psum, now(i, U, u + 1))
                        V.hold(y_out, last(i, 32))
                        nc.vector.tensor_copy(y[:, u, HALF:D], py[:, HALF:D]).then_inc(y_v, 1)


def combine_phase(nc, norm_final_g, slot_u, wts, x1_dram, yb_dram, x2_dram):
    with Phase(nc, "comb") as ph:
        g = ph.sb("g", [P, D])
        x1 = ph.sb("x1", [P, 2, D])
        ya = ph.sb("ya", [P, 2, 2, D])
        junk = ph.sb("junk", [P, D])
        small = ph.sb("small", [P, 2, 4])
        out = ph.sb("out", [P, 2, D])
        names = "consts summed sq ms root out_ready".split()
        consts, summed, sq, ms, root, out_ready = [ph.sem(n) for n in names]
        rows_in = [ph.sem(f"rows_in{u}") for u in range(2)]
        x_in = [ph.sem(f"x_in{u}") for u in range(2)]
        x_out = [ph.sem(f"x_out{u}") for u in range(2)]
        V = ph.engine(nc.vector, "dve")

        with nc.Block() as block:

            @block.sync
            def _(sp):
                sp.dma_start(g[:, :], norm_final_g.partition_broadcast(P)).then_inc(consts, 16)
                for i in range(NT):
                    u = i % 2
                    if i >= 2:
                        sp.wait_ge(out_ready, i - 1)
                    sp.dma_start(x1[:, u, :], x1_dram[i * P:(i + 1) * P, :]).then_inc(x_in[u], 16)
                    if i:
                        sp.wait_ge(out_ready, i)
                        sp.dma_start(x2_dram[(i - 1) * P:i * P, :], out[:, 1 - u, :]).then_inc(x_out[1 - u], 16)
                sp.wait_ge(out_ready, NT)
                sp.dma_start(x2_dram[(NT - 1) * P:T, :], out[:, 1, :]).then_inc(x_out[1], 16)
                for u in range(2):
                    sp.wait_ge(x_out[u], 16 * NT // 2)

            @block.gpsimd
            def _(pool):
                for i in range(NT):
                    u = i % 2
                    if i >= 2:
                        pool.wait_ge(summed, i - 1)
                    for n in range(2):
                        pool.indirect_dma_start(ya[:, u, n, :], None, yb_dram, bass.IndirectOffsetOnAxis(ap=slot_u[:, n * NT + i:n * NT + i + 1], axis=0)).then_inc(rows_in[u], 16)
                for u in range(2):
                    pool.wait_ge(rows_in[u], 16 * NT)

            @block.scalar
            def _(act):
                for i in range(NT):
                    u = i % 2
                    act.wait_ge(summed, i + 1)
                    nc.scalar.activation(junk[:, :], x1[:, u, :], ACT.Square, accum_out=small[:, u, 0:1]).then_inc(sq, 1)
                    act.wait_ge(ms, i + 1)
                    nc.scalar.activation(small[:, u, 2:3], small[:, u, 1:2], ACT.Sqrt).then_inc(root, 1)

            @block.vector
            def _(dve):
                dve.wait_ge(consts, 16)
                for i in range(NT):
                    u = i % 2
                    dve.wait_ge(x_in[u], 16 * (i // 2 + 1))
                    dve.wait_ge(rows_in[u], 32 * (i // 2 + 1))
                    V.link(nc.vector.scalar_tensor_tensor(x1[:, u, :], ya[:, u, 0, :], wts[:, i:i + 1], x1[:, u, :], ALU.mult, ALU.add))
                    nc.vector.scalar_tensor_tensor(x1[:, u, :], ya[:, u, 1, :], wts[:, NT + i:NT + i + 1], x1[:, u, :], ALU.mult, ALU.add).then_inc(summed, 1)
                    dve.wait_ge(sq, i + 1)
                    nc.vector.tensor_scalar(small[:, u, 1:2], small[:, u, 0:1], 1.0 / D, NORM_EPS, ALU.mult, ALU.add).then_inc(ms, 1)
                    dve.wait_ge(root, i + 1)
                    V.link(nc.vector.reciprocal(small[:, u, 3:4], small[:, u, 2:3]))
                    if i >= 2:
                        dve.wait_ge(x_out[u], 16 * (i // 2))
                    nc.vector.scalar_tensor_tensor(out[:, u, :], x1[:, u, :], small[:, u, 3:4], g[:, :], ALU.mult, ALU.mult).then_inc(out_ready, 1)



HD, NQ, NKV, GRP = 64, 16, 4, 4
QKV = (NQ + 2 * NKV) * HD
BAND = 3 * P
ROT = HD // 4
ALPHA = 4.0 ** 0.25
LN_EPS = 1e-5
NEG = -1e30


def gqa_tables():
    pos = np.arange(T, dtype=np.float32)
    inv = np.float32(500000.0) ** (-np.arange(0, ROT, 2, dtype=np.float32) / ROT)
    ang = (pos[:, None] * inv[None, :]).astype(np.float32)
    rope = np.concatenate([np.cos(ang), np.sin(ang)], axis=1).astype(np.float32).reshape(NT, P, ROT).transpose(1, 0, 2)
    q = np.arange(P)[:, None, None] + P * np.arange(NT)[None, :, None]
    k = P * (np.arange(NT)[None, :, None] - 1) + np.arange(BAND)[None, None, :]
    ok = (np.abs(q - k) <= P) & (k >= 0) & (k < T)
    return np.ascontiguousarray(rope), np.where(ok, 0.0, NEG).astype(np.float32)


def gqa_phase(nc, w_qkv, w_o, sink, eye, rope, masks, ln_g, ln_b, x_dram, out_dram):
    with Phase(nc, "gqa") as ph:
        ident = ph.sb("ident", [P, P])
        oT = ph.sb("oT", [P, KD, T])
        with Phase(nc, "gqak") as kept:
            qT = kept.sb("qT", [P, NQ // 2, T])
            kT = kept.sb("kT", [P, NKV, T + 2 * P])
            v = kept.sb("v", [P, NT + 2, NKV * HD])
            with Phase(nc, "gqap") as one:
                gqa_project(nc, one, w_qkv, eye, rope, x_dram, ident, qT, kT, v)
            with Phase(nc, "gqaa") as two:
                gqa_attend(nc, two, sink, masks, ident, qT, kT, v, oT)
        with Phase(nc, "gqao") as three:
            product_and_norm(nc, three, oT, w_o, ln_g, ln_b, x_dram, out_dram)


def gqa_project(nc, ph, w_qkv, eye, rope, x_dram, ident, qT, kT, v):
    w = ph.sb("w", [P, KD, QKV])
    tab = ph.sb("tab", [P, NT, ROT])
    xt = ph.sb("xt", [P, D])
    xT = ph.sb("xT", [P, KD, P])
    qs = ph.sb("qs", [P, NQ, HD])
    ks = ph.sb("ks", [P, NKV, 2, HD])
    rr = ph.sb("rr", [P, 4, NQ + NKV, 8])
    pt = ph.ps("pt", [P, D])
    pq = ph.ps("pq", [P, 3, HALF])
    pk = ph.ps("pk", [P, HALF])
    names = "consts x_in x_psum xT_ready qkv_psum v_kept qk_ready qT_psum qT_kept kT_psum kT_kept zeros".split()
    consts, x_in, x_psum, xT_ready, qkv_psum, v_kept, qk_ready, qT_psum, qT_kept, kT_psum, kT_kept, zeros = [ph.sem(n) for n in names]
    V, A, E, S = (ph.engine(e, n) for e, n in ((nc.vector, "dve"), (nc.scalar, "act"), (nc.tensor, "pe"), (nc.sync, "sp")))

    with nc.Block() as block:

        @block.sync
        def _(sp):
            S.open(x_in, n=16)
            sp.dma_start(ident[:, :], eye).then_inc(consts, 16)
            sp.dma_start(tab[:, :, :], rope).then_inc(consts, 16)
            for k in range(KD):
                sp.dma_start(w[:, k, :], w_qkv[0, k * P:(k + 1) * P, :]).then_inc(consts, 16)
            with sp.Fori(0, NT) as i:
                S.hold(x_psum, last(i))
                sp.dma_start(xt[:, :], x_dram[ds(i * P, P), :]).then_inc(x_in, 16)

        @block.gpsimd
        def _(pool):
            for b in (0, T + P):
                nc.gpsimd.memset(kT[:, :, b:b + P], 0.0)
            for b in (0, NT + 1):
                z = nc.gpsimd.memset(v[:, b, :], 0.0)
            z.then_inc(zeros, 1)

        @block.tensor
        def _(pe):
            E.open(x_psum, qkv_psum, qT_psum, kT_psum)
            pe.wait_ge(consts, (2 + KD) * 16)
            with pe.Fori(0, NT) as i:
                E.hold(x_in, now(i, 16))
                E.hold(qT_kept, last(i))
                for k in range(KD):
                    t = nc.tensor.transpose(pt[:, k * P:(k + 1) * P], xt[:, k * P:(k + 1) * P], ident[:, :])
                t.then_inc(x_psum, 1)
                E.hold(xT_ready, now(i))
                E.hold(qk_ready, last(i))
                E.hold(v_kept, last(i))
                for b in range(3):
                    for k in range(KD):
                        m = nc.tensor.matmul(pq[:, b, :], xT[:, k, :], w[:, k, b * HALF:(b + 1) * HALF], start=k == 0, stop=k == KD - 1)
                m.then_inc(qkv_psum, 1)
                E.hold(qk_ready, now(i))
                for n in range(NQ // 2):
                    t = nc.tensor.transpose(pt[:, n * P:(n + 1) * P], qs[:, 2 * n:2 * n + 2, :].rearrange("p h d -> p (h d)"), ident[:, :])
                t.then_inc(qT_psum, 1)
                E.hold(kT_kept, last(i))
                for n in range(NKV):
                    t = nc.tensor.transpose(pk[:, n * P:(n + 1) * P], ks[:, n, :, :].rearrange("p h d -> p (h d)"), ident[:, :])
                t.then_inc(kT_psum, 1)

        @block.scalar
        def _(act):
            A.open(xT_ready, v_kept, qT_kept)
            with act.Fori(0, NT) as i:
                A.hold(x_psum, now(i))
                A.hold(qkv_psum, last(i))
                nc.scalar.copy(xT[:, :, :], pt[:, :].rearrange("p (k t) -> p k t", k=KD)).then_inc(xT_ready, 1)
                A.hold(qk_ready, now(i))
                nc.scalar.copy(v[:, ds(i + 1, 1), :].rearrange("p o n -> p (o n)"), pq[:, 2, NKV * HD:HALF]).then_inc(v_kept, 1)
                A.hold(qT_psum, now(i))
                nc.scalar.copy(qT[:, :, ds(i * P, P)], pt[:, :].rearrange("p (k t) -> p k t", k=NQ // 2)).then_inc(qT_kept, 1)

        @block.vector
        def _(dve):
            V.open(qk_ready, kT_kept)
            dve.wait_ge(zeros, 1)
            dve.wait_ge(consts, (2 + KD) * 16)
            with dve.Fori(0, NT) as i:
                V.loop(i, 1)
                V.hold(qkv_psum, now(i))
                V.hold(kT_psum, last(i))
                q_src = pq[:, 0:2, :].rearrange("p b (h d) -> p (b h) d", d=HD)
                k_src = pq[:, 2, 0:NKV * HD].rearrange("p (h d) -> p h d", d=HD)
                co, si = tab[:, ds(i, 1), 0:8], tab[:, ds(i, 1), 8:16]
                nc.vector.tensor_copy(qs[:, :, ROT:HD], q_src[:, :, ROT:HD])
                for b in range(2):
                    nc.vector.tensor_copy(ks[:, :, b, ROT:HD], k_src[:, :, ROT:HD])
                for src, lo, n in ((q_src, 0, NQ), (k_src, NQ, NKV)):
                    for m, (c, half) in enumerate(((co, 0), (si, 8), (si, 0), (co, 8))):
                        r = nc.vector.tensor_tensor(rr[:, m, lo:lo + n, :], src[:, :, half:half + 8], c.to_broadcast([P, n, 8]), ALU.mult)
                V.link(r)
                nc.vector.tensor_tensor(qs[:, :, 0:8], rr[:, 0, 0:NQ, :], rr[:, 1, 0:NQ, :], ALU.subtract)
                nc.vector.tensor_tensor(qs[:, :, 8:16], rr[:, 2, 0:NQ, :], rr[:, 3, 0:NQ, :], ALU.add)
                for b in range(2):
                    nc.vector.tensor_tensor(ks[:, :, b, 0:8], rr[:, 0, NQ:NQ + NKV, :], rr[:, 1, NQ:NQ + NKV, :], ALU.subtract)
                    r = nc.vector.tensor_tensor(ks[:, :, b, 8:16], rr[:, 2, NQ:NQ + NKV, :], rr[:, 3, NQ:NQ + NKV, :], ALU.add)
                r.then_inc(qk_ready, 1)
                V.hold(kT_psum, now(i))
                nc.vector.tensor_copy(kT[:, :, ds(i * P + P, P)], pk[:, :].rearrange("p (k t) -> p k t", k=NKV)).then_inc(kT_kept, 1)
            V.done(NT)


def gqa_attend(nc, ph, sink, masks, ident, qT, kT, v, oT):
    SCALE = float(HD) ** -0.5
    B, U = 2, 2 * NKV
    mask = ph.sb("mask", [P, NT, BAND])
    sk = ph.sb("sk", [P, NQ])
    q_t = [ph.sb(f"q_t{b}", [P, NQ // 2, P]) for b in range(B)]
    k_t = [ph.sb(f"k_t{b}", [P, NKV, BAND]) for b in range(B)]
    v_t = [ph.sb(f"v_t{b}", [P, 3, NKV * HD]) for b in range(B)]
    s = ph.sb("s", [P, 2, GRP, BAND])
    pr = ph.sb("pr", [P, 2, GRP, BAND])
    pT = ph.sb("pT", [P, 2, 3, GRP * P])
    mx = ph.sb("mx", [P, GRP])
    nmx = ph.sb("nmx", [P, 2, GRP])
    ex = ph.sb("ex", [P, 2, GRP])
    den = ph.sb("den", [P, 2, GRP])
    rden = ph.sb("rden", [P, GRP])
    pS = ph.ps("pS", [P, GRP, HALF])
    pP = ph.ps("pP", [P, 3, HALF])
    pO = ph.ps("pO", [P, HALF])
    names = "consts qkv_in s_psum s_ready sh_ready exp_done normed p_psum p_kept o_psum o_kept".split()
    consts, qkv_in, s_psum, s_ready, sh_ready, exp_done, normed, p_psum, p_kept, o_psum, o_kept = [ph.sem(n) for n in names]
    V, G, A, E = (ph.engine(e, n) for e, n in ((nc.vector, "dve"), (nc.gpsimd, "pool"), (nc.scalar, "act"), (nc.tensor, "pe")))

    def per_unit(i, u):
        return now(i, U, u + 1) if u >= 0 else last(i, U, U + u + 1)

    with nc.Block() as block:

        @block.sync
        def _(sp):
            sp.dma_start(mask[:, :, :], masks).then_inc(consts, 16)
            sp.dma_start(sk[:, :], sink[0].partition_broadcast(P)).then_inc(consts, 16)

        @block.gpsimd
        def _(pool):
            G.open(qkv_in, n=B)
            with pool.Fori(0, NT // B) as i:
                for b in range(B):
                    G.hold(o_psum, last(i, U, (b + 1) * NKV))
                    nc.gpsimd.tensor_copy(k_t[b][:, :, :], kT[:, :, ds(i * (B * P) + b * P, BAND)])
                    nc.gpsimd.tensor_copy(v_t[b][:, :, :], v[:, ds(i * B + b, 3), :])
                    nc.gpsimd.tensor_copy(q_t[b][:, :, :], qT[:, :, ds(i * (B * P) + b * P, P)]).then_inc(qkv_in, 1)

        @block.tensor
        def _(pe):
            E.open(s_psum, p_psum, o_psum, n=U)

            def scores(i, u):
                b, g = u // NKV, u % NKV
                if g == 0:
                    E.hold(qkv_in, now(i, B, b + 1))
                E.hold(s_ready, per_unit(i, u - 1))
                for h in range(GRP):
                    half = slice(64 * (h % 2), 64 * (h % 2) + 64)
                    m = nc.tensor.matmul(pS[:, h, 0:BAND], q_t[b][half, GRP // 2 * g + h // 2, :], k_t[b][half, g, :], start=True, stop=True)
                m.then_inc(s_psum, 1)

            def outputs(i, u):
                b, g = u // NKV, u % NKV
                E.hold(p_kept, per_unit(i, u))
                E.hold(o_kept, per_unit(i, u - 1))
                for odd in range(2):
                    for kb in range(3):
                        m = nc.tensor.matmul(pO[64 * odd:64 * odd + 64, 0:2 * P], v_t[b][:, kb, g * HD:(g + 1) * HD],
                                             pT[:, u % 2, kb, odd * 2 * P:(odd + 1) * 2 * P], start=kb == 0, stop=kb == 2)
                m.then_inc(o_psum, 1)

            with pe.Fori(0, NT // B) as i:
                scores(i, 0)
                for u in range(U):
                    if u + 1 < U:
                        scores(i, u + 1)
                    if u:
                        outputs(i, u - 1)
                    E.hold(normed, per_unit(i, u))
                    E.hold(p_kept, per_unit(i, u - 1))
                    for kb in range(3):
                        for h in range(GRP):
                            at = (h % 2 * 2 + h // 2) * P
                            t = nc.tensor.transpose(pP[:, kb, at:at + P], pr[:, u % 2, h, kb * P:(kb + 1) * P], ident[:, :])
                    t.then_inc(p_psum, 1)
                outputs(i, U - 1)

        @block.scalar
        def _(act):
            A.open(exp_done, p_kept, o_kept, n=U)
            with act.Fori(0, NT // B) as i:

                def keep_p(u):
                    A.hold(p_psum, per_unit(i, u))
                    A.hold(o_psum, per_unit(i, u - 2))
                    nc.scalar.copy(pT[:, u % 2, :, :], pP[:, :, :]).then_inc(p_kept, 1)

                def keep_o(u):
                    b, g = u // NKV, u % NKV
                    A.hold(o_psum, per_unit(i, u))
                    nc.scalar.copy(oT[:, 2 * g:2 * g + 2, ds(i * (B * P) + b * P, P)], pO[:, 0:2 * P].rearrange("p (k t) -> p k t", k=2)).then_inc(o_kept, 1)

                for u in range(U):
                    if u >= 2:
                        keep_o(u - 2)
                    A.hold(sh_ready, per_unit(i, u))
                    A.hold(p_psum, per_unit(i, u - 2))
                    A.hold(normed, per_unit(i, u - 2))
                    c = u % 2
                    for h in range(GRP):
                        nc.scalar.activation(pr[:, c, h, :], s[:, c, h, :], ACT.Exp, bias=nmx[:, c, h:h + 1], accum_out=den[:, c, h:h + 1])
                    nc.scalar.activation(ex[:, c, :], ex[:, c, :], ACT.Exp).then_inc(exp_done, 1)
                    if u:
                        keep_p(u - 1)
                keep_o(U - 2)
                keep_p(U - 1)
                keep_o(U - 1)

        @block.vector
        def _(dve):
            V.open(s_ready, sh_ready, normed, n=U)
            dve.wait_ge(consts, 32)
            with dve.Fori(0, NT // B) as i:
                V.loop(i, 5 * U)

                def shifted(u):
                    b, g, c = u // NKV, u % NKV, u % 2
                    heads = sk[:, GRP * g:GRP * (g + 1)]
                    V.hold(s_psum, per_unit(i, u))
                    V.hold(exp_done, per_unit(i, u - 2))
                    V.link(nc.vector.scalar_tensor_tensor(s[:, c, :, :], pS[:, :, 0:BAND], SCALE,
                                                          mask[:, ds(i * B + b, 1), :].to_broadcast([P, GRP, BAND]), ALU.mult, ALU.add))
                    dve.sem_inc(s_ready, 1)
                    V.link(nc.vector.reduce_max(mx[:, :], s[:, c, :, :], AX_X))
                    V.link(nc.vector.tensor_tensor(mx[:, :], mx[:, :], heads, ALU.max))
                    nc.vector.tensor_scalar(nmx[:, c, :], mx[:, :], -1.0, None, ALU.mult)
                    nc.vector.tensor_tensor(ex[:, c, :], heads, mx[:, :], ALU.subtract).then_inc(sh_ready, 1)

                shifted(0)
                for u in range(U):
                    c = u % 2
                    V.hold(exp_done, per_unit(i, u))
                    V.link(nc.vector.tensor_tensor(den[:, c, :], den[:, c, :], ex[:, c, :], ALU.add))
                    V.link(nc.vector.reciprocal(rden[:, :], den[:, c, :]))
                    nc.vector.tensor_tensor(pr[:, c, :, :], pr[:, c, :, :], rden[:, :].unsqueeze(2).to_broadcast([P, GRP, BAND]), ALU.mult).then_inc(normed, 1)
                    if u + 1 < U:
                        shifted(u + 1)
            V.done(NT // B)


def product_and_norm(nc, ph, aT, w_out, ln_g, ln_b, x_dram, out_dram):
    U = 2
    wo = ph.sb("wo", [P, KD, D])
    gb = ph.sb("gb", [P, 2, D])
    a_t = ph.sb("a_t", [P, U, KD, P])
    xt = ph.sb("xt", [P, U, D])
    r = ph.sb("r", [P, U, D])
    junk = ph.sb("junk", [P, D])
    small = ph.sb("small", [P, U, 8])
    out = ph.sb("out", [P, U, D])
    po = ph.ps("po", [P, U, D])
    names = "consts staged o_psum summed mean cent sq ms root ready".split()
    consts, staged, o_psum, summed, mean, cent, sq, ms, root, ready = [ph.sem(n) for n in names]
    w_in = [ph.sem(f"w_in{k}") for k in range(KD)]
    x_in = [ph.sem(f"x_in{u}") for u in range(U)]
    done = [ph.sem(f"done{u}") for u in range(U)]
    V, G, A, E, S = (ph.engine(e, n) for e, n in ((nc.vector, "dve"), (nc.gpsimd, "pool"), (nc.scalar, "act"),
                                                  (nc.tensor, "pe"), (nc.sync, "sp")))

    with nc.Block() as block:

        @block.sync
        def _(sp):
            for u in range(U):
                S.open(x_in[u], n=16)
            for k in range(KD):
                sp.dma_start(wo[:, k, :], w_out[0, k * P:(k + 1) * P, :]).then_inc(w_in[k], 16)
            sp.dma_start(gb[:, 0, :], ln_g.partition_broadcast(P)).then_inc(consts, 16)
            sp.dma_start(gb[:, 1, :], ln_b.partition_broadcast(P)).then_inc(consts, 16)
            with sp.Fori(0, NT // U) as i:
                for u in range(U):
                    S.hold(summed, last(i, U, u + 1))
                    sp.dma_start(xt[:, u, :], x_dram[ds((i * U + u) * P, P), :]).then_inc(x_in[u], 16)

        @block.gpsimd
        def _(pool):
            G.open(staged, n=U)
            with pool.Fori(0, NT // U) as i:
                for u in range(U):
                    G.hold(o_psum, last(i, U, u + 1))
                    nc.gpsimd.tensor_copy(a_t[:, u, :, :], aT[:, :, ds((i * U + u) * P, P)]).then_inc(staged, 1)

        @block.tensor
        def _(pe):
            E.open(o_psum, n=U)
            for k in range(KD):
                E.hold(w_in[k], 16)
            with pe.Fori(0, NT // U) as i:
                for u in range(U):
                    E.hold(staged, now(i, U, u + 1))
                    E.hold(summed, last(i, U, u + 1))
                    for half in range(2):
                        for k in range(KD):
                            m = nc.tensor.matmul(po[:, u, half * HALF:(half + 1) * HALF], a_t[:, u, k, :], wo[:, k, half * HALF:(half + 1) * HALF],
                                                 start=k == 0, stop=k == KD - 1)
                    m.then_inc(o_psum, 1)

        @block.scalar
        def _(act):
            A.open(sq, root, mean, n=U)
            for u in range(U):
                A.open(done[u], n=16)
            with act.Fori(0, NT // U) as i:
                for u in range(U):
                    A.hold(summed, now(i, U, u + 1))
                    nc.scalar.activation(junk[:, :], r[:, u, :], ACT.Copy, accum_out=small[:, u, 0:1]).then_inc(mean, 1)
                    A.hold(cent, now(i, U, u + 1))
                    nc.scalar.activation(junk[:, :], r[:, u, :], ACT.Square, accum_out=small[:, u, 2:3]).then_inc(sq, 1)
                    A.hold(ms, now(i, U, u + 1))
                    nc.scalar.activation(small[:, u, 4:5], small[:, u, 3:4], ACT.Sqrt).then_inc(root, 1)
                    A.hold(ready, now(i, U, u + 1))
                    act.dma_start(out_dram[ds((i * U + u) * P, P), :], out[:, u, :]).then_inc(done[u], 16)
            for u in range(U):
                act.wait_ge(done[u], 16 * (NT // U + 1))

        @block.vector
        def _(dve):
            V.open(summed, cent, ms, ready, n=U)
            dve.wait_ge(consts, 32)
            with dve.Fori(0, NT // U) as i:
                V.loop(i, 4 * U)
                for u in range(U):
                    V.hold(x_in[u], now(i, 16))
                    V.hold(o_psum, now(i, U, u + 1))
                    nc.vector.scalar_tensor_tensor(r[:, u, :], xt[:, u, :], ALPHA, po[:, u, :], ALU.mult, ALU.add).then_inc(summed, 1)
                    V.hold(mean, now(i, U, u + 1))
                    V.link(nc.vector.tensor_scalar(small[:, u, 1:2], small[:, u, 0:1], 1.0 / D, None, ALU.mult))
                    nc.vector.tensor_scalar(r[:, u, :], r[:, u, :], small[:, u, 1:2], None, ALU.subtract).then_inc(cent, 1)
                    V.hold(sq, now(i, U, u + 1))
                    nc.vector.tensor_scalar(small[:, u, 3:4], small[:, u, 2:3], 1.0 / D, LN_EPS, ALU.mult, ALU.add).then_inc(ms, 1)
                    V.hold(root, now(i, U, u + 1))
                    V.link(nc.vector.reciprocal(small[:, u, 5:6], small[:, u, 4:5]))
                    V.hold(done[u], last(i, 16))
                    V.link(nc.vector.scalar_tensor_tensor(out[:, u, :], r[:, u, :], small[:, u, 5:6], gb[:, 0, :], ALU.mult, ALU.mult))
                    V.link(nc.vector.tensor_tensor(out[:, u, :], out[:, u, :], gb[:, 1, :], ALU.add))
                    dve.sem_inc(ready, 1)
            V.done(NT // U)


def norm_phase(nc, name, ln_g, ln_b, x_dram, add_dram, out_dram):
    with Phase(nc, name) as ph:
        gb = ph.sb("gb", [P, 2, D])
        U = 2
        xt = ph.sb("xt", [P, U, D])
        at = ph.sb("at", [P, U, D])
        r = ph.sb("r", [P, D])
        junk = ph.sb("junk", [P, D])
        small = ph.sb("small", [P, 8])
        out = ph.sb("out", [P, U, D])
        names = "consts summed mean cent sq ms root ready".split()
        consts, summed, mean, cent, sq, ms, root, ready = [ph.sem(n) for n in names]
        x_in = [ph.sem(f"x_in{u}") for u in range(U)]
        done = [ph.sem(f"done{u}") for u in range(U)]
        V, A, S = (ph.engine(e, n) for e, n in ((nc.vector, "dve"), (nc.scalar, "act"), (nc.sync, "sp")))

        with nc.Block() as block:

            @block.sync
            def _(sp):
                for u in range(U):
                    S.open(x_in[u], n=32)
                sp.dma_start(gb[:, 0, :], ln_g.partition_broadcast(P)).then_inc(consts, 16)
                sp.dma_start(gb[:, 1, :], ln_b.partition_broadcast(P)).then_inc(consts, 16)
                with sp.Fori(0, NT // U) as i:
                    for u in range(U):
                        S.hold(summed, last(i, U, u + 1))
                        sp.dma_start(xt[:, u, :], x_dram[ds((i * U + u) * P, P), :]).then_inc(x_in[u], 16)
                        sp.dma_start(at[:, u, :], add_dram[ds((i * U + u) * P, P), :]).then_inc(x_in[u], 16)

            @block.scalar
            def _(act):
                A.open(sq, root, mean, n=U)
                for u in range(U):
                    A.open(done[u], n=16)
                with act.Fori(0, NT // U) as i:
                    for u in range(U):
                        A.hold(summed, now(i, U, u + 1))
                        nc.scalar.activation(junk[:, :], r[:, :], ACT.Copy, accum_out=small[:, 0:1]).then_inc(mean, 1)
                        A.hold(cent, now(i, U, u + 1))
                        nc.scalar.activation(junk[:, :], r[:, :], ACT.Square, accum_out=small[:, 2:3]).then_inc(sq, 1)
                        A.hold(ms, now(i, U, u + 1))
                        nc.scalar.activation(small[:, 4:5], small[:, 3:4], ACT.Sqrt).then_inc(root, 1)
                        A.hold(ready, now(i, U, u + 1))
                        act.dma_start(out_dram[ds((i * U + u) * P, P), :], out[:, u, :]).then_inc(done[u], 16)
                for u in range(U):
                    act.wait_ge(done[u], 16 * (NT // U + 1))

            @block.vector
            def _(dve):
                V.open(summed, cent, ms, ready, n=U)
                dve.wait_ge(consts, 32)
                with dve.Fori(0, NT // U) as i:
                    V.loop(i, 4 * U)
                    for u in range(U):
                        V.hold(x_in[u], now(i, 32))
                        nc.vector.scalar_tensor_tensor(r[:, :], xt[:, u, :], ALPHA, at[:, u, :], ALU.mult, ALU.add).then_inc(summed, 1)
                        V.hold(mean, now(i, U, u + 1))
                        V.link(nc.vector.tensor_scalar(small[:, 1:2], small[:, 0:1], 1.0 / D, None, ALU.mult))
                        nc.vector.tensor_scalar(r[:, :], r[:, :], small[:, 1:2], None, ALU.subtract).then_inc(cent, 1)
                        V.hold(sq, now(i, U, u + 1))
                        nc.vector.tensor_scalar(small[:, 3:4], small[:, 2:3], 1.0 / D, LN_EPS, ALU.mult, ALU.add).then_inc(ms, 1)
                        V.hold(root, now(i, U, u + 1))
                        V.link(nc.vector.reciprocal(small[:, 5:6], small[:, 4:5]))
                        V.hold(done[u], last(i, 16))
                        V.link(nc.vector.scalar_tensor_tensor(out[:, u, :], r[:, :], small[:, 5:6], gb[:, 0, :], ALU.mult, ALU.mult))
                        V.link(nc.vector.tensor_tensor(out[:, u, :], out[:, u, :], gb[:, 1, :], ALU.add))
                        dve.sem_inc(ready, 1)
                V.done(NT // U)



E2 = 16
CAP = 2 * T // E2
FF = D


def choose_phase(nc, name, w_router, eye, x_dram, acc_dram, gate, idx):
    with Phase(nc, name) as ph:
        ident = ph.sb("ident", [P, P])
        w = ph.sb("w", [P, KD, E2])
        xt = ph.sb("xt", [P, 2, D])
        xT = ph.sb("xT", [P, KD, P])
        lg = ph.sb("lg", [P, E2])
        small = ph.sb("small", [P, 4])
        ex = ph.sb("ex", [P, E2])
        aff = ph.sb("aff", [P, E2])
        affT = ph.sb("affT", [E2, 2, T])
        top = ph.sb("top", [E2, CAP])
        top_i = ph.sb("top_i", [E2, CAP], U32)
        top_f = ph.sb("top_f", [E2, CAP])
        zero = ph.sb("zero", [P, D])
        pt = ph.ps("pt", [P, D])
        pl = ph.ps("pl", [P, HALF])
        pa = ph.ps("pa", [P, HALF])
        names = "consts zeroed acc_out x_psum xT_ready l_psum sh_ready exp_done aff_ready a_psum a_kept tops f_psum".split()
        consts, zeroed, acc_out, x_psum, xT_ready, l_psum, sh_ready, exp_done, aff_ready, a_psum, a_kept, tops, f_psum = [ph.sem(n) for n in names]
        x_in = [ph.sem(f"x_in{u}") for u in range(2)]
        V, A, E, S = (ph.engine(e, n) for e, n in ((nc.vector, "dve"), (nc.scalar, "act"), (nc.tensor, "pe"), (nc.sync, "sp")))
        U = 2

        with nc.Block() as block:

            @block.sync
            def _(sp):
                for u in range(U):
                    S.open(x_in[u], n=16)
                sp.dma_start(ident[:, :], eye).then_inc(consts, 16)
                sp.dma_start(w[:, :, :], w_router.rearrange("(k p) e -> p k e", p=P)).then_inc(consts, 16)
                with sp.Fori(0, NT // U) as i:
                    for u in range(U):
                        S.hold(x_psum, last(i, U, u + 1))
                        sp.dma_start(xt[:, u, :], x_dram[ds((i * U + u) * P, P), :]).then_inc(x_in[u], 16)
                sp.wait_ge(zeroed, 1)
                for n in range(NT):
                    sp.dma_start(acc_dram[n * P:(n + 1) * P, :], zero[:, :]).then_inc(acc_out, 16)
                sp.wait_ge(acc_out, 16 * NT)

            @block.gpsimd
            def _(pool):
                nc.gpsimd.memset(zero[:, :], 0.0).then_inc(zeroed, 1)

            @block.tensor
            def _(pe):
                E.open(x_psum, l_psum, a_psum, n=U)
                pe.wait_ge(consts, 32)
                with pe.Fori(0, NT // U) as i:
                    for u in range(U):
                        E.hold(x_in[u], now(i, 16))
                        E.hold(xT_ready, last(i, U, u + U) if u == 0 else now(i, U, u))
                        for k in range(KD):
                            t = nc.tensor.transpose(pt[:, k * P:(k + 1) * P], xt[:, u, k * P:(k + 1) * P], ident[:, :])
                        t.then_inc(x_psum, 1)
                        E.hold(xT_ready, now(i, U, u + 1))
                        E.hold(exp_done, last(i, U, u + U) if u == 0 else now(i, U, u))
                        for k in range(KD):
                            m = nc.tensor.matmul(pl[:, 0:E2], xT[:, k, :], w[:, k, :], start=k == 0, stop=k == KD - 1)
                        m.then_inc(l_psum, 1)
                        E.hold(aff_ready, now(i, U, u + 1))
                        E.hold(a_kept, last(i, U, u + U) if u == 0 else now(i, U, u))
                        nc.tensor.transpose(pa[0:E2, 0:P], aff[:, :], ident[:, :]).then_inc(a_psum, 1)
                pe.wait_ge(tops, 1)
                nc.tensor.transpose(pl[:, 0:E2], top[:, :], ident[0:E2, 0:E2])
                nc.tensor.transpose(pl[:, E2:2 * E2], top_f[:, :], ident[0:E2, 0:E2]).then_inc(f_psum, 1)

            @block.scalar
            def _(act):
                A.open(xT_ready, exp_done, n=U)
                with act.Fori(0, NT // U) as i:
                    for u in range(U):
                        A.hold(x_psum, now(i, U, u + 1))
                        A.hold(l_psum, last(i, U, u + U) if u == 0 else now(i, U, u))
                        nc.scalar.copy(xT[:, :, :], pt[:, :].rearrange("p (k t) -> p k t", k=KD)).then_inc(xT_ready, 1)
                        A.hold(sh_ready, now(i, U, u + 1))
                        A.hold(aff_ready, last(i, U, u + U) if u == 0 else now(i, U, u))
                        nc.scalar.activation(ex[:, :], pl[:, 0:E2], ACT.Exp, bias=small[:, 1:2], accum_out=small[:, 2:3]).then_inc(exp_done, 1)

            @block.vector
            def _(dve):
                V.open(sh_ready, aff_ready, a_kept, n=U)
                with dve.Fori(0, NT // U) as i:
                    V.loop(i, 2 * U)
                    for u in range(U):
                        V.hold(l_psum, now(i, U, u + 1))
                        V.link(nc.vector.reduce_max(small[:, 0:1], pl[:, 0:E2], AX_X))
                        nc.vector.tensor_scalar(small[:, 1:2], small[:, 0:1], -1.0, None, ALU.mult).then_inc(sh_ready, 1)
                        V.hold(exp_done, now(i, U, u + 1))
                        V.link(nc.vector.reciprocal(small[:, 3:4], small[:, 2:3]))
                        V.hold(a_psum, last(i, U, u + U) if u == 0 else now(i, U, u))
                        nc.vector.tensor_scalar(aff[:, :], ex[:, :], small[:, 3:4], None, ALU.mult).then_inc(aff_ready, 1)
                        V.hold(a_psum, now(i, U, u + 1))
                        nc.vector.tensor_copy(affT[:, 0, ds((i * U + u) * P, P)], pa[0:E2, 0:P]).then_inc(a_kept, 1)
                V.done(NT // U)
                dve.wait_ge(a_kept, NT + U)
                for n in range(CAP // 8):
                    eight = slice(8 * n, 8 * n + 8)
                    V.link(nc.vector.max(top[:, eight], affT[:, n % 2, :]))
                    nc.vector.max_index(top_i[:, eight], top[:, eight], affT[:, n % 2, :])
                    V.link(nc.vector.match_replace(affT[:, (n + 1) % 2, :], top[:, eight], affT[:, n % 2, :], -1.0))
                V.link(nc.vector.tensor_copy(top_f[:, :], top_i[:, :]))
                dve.sem_inc(tops, 1)
                dve.wait_ge(f_psum, 1)
                nc.vector.tensor_copy(gate[:, :], pl[:, 0:E2])
                nc.vector.tensor_copy(idx[:, E2:E2 + 1], pl[:, E2:E2 + 1])
                V.link(nc.vector.tensor_copy(idx[:, 0:E2], pl[:, E2:2 * E2]))


def choice_phase(nc, name, w_gu, w_dn, eye, x_dram, acc_dram, gate, idx):
    with Phase(nc, name) as ph:
        ident = ph.sb("ident", [P, P])
        wg = ph.sb("wg", [P, KD, 2 * FF])
        wd = ph.sb("wd", [P, KD, D])
        ic = [ph.sb(f"ic{v}", [P, 1], U32) for v in range(2)]
        xg = ph.sb("xg", [P, D])
        xT = ph.sb("xT", [P, KD, P])
        sg = ph.sb("sg", [P, FF])
        hid = ph.sb("hid", [P, FF])
        hidT = ph.sb("hidT", [P, KD, P])
        y = ph.sb("y", [P, D])
        pg = ph.ps("pg", [P, 4, HALF])
        pt = ph.ps("pt", [P, D])
        py = ph.ps("py", [P, D])
        names = "consts ic_ready x_in x_psum x_ready g_used silu hid_ready h_psum hT_ready d_used y_ready sent added".split()
        (consts, ic_ready, x_in, x_psum, x_ready, g_used, silu, hid_ready, h_psum, hT_ready, d_used, y_ready, sent,
         added) = [ph.sem(n) for n in names]
        wg_in = [ph.sem(f"wg_in{k}") for k in range(KD)]
        wd_in = [ph.sem(f"wd_in{k}") for k in range(KD)]
        V, G, A, E, S = (ph.engine(e, n) for e, n in ((nc.vector, "dve"), (nc.gpsimd, "pool"), (nc.scalar, "act"),
                                                      (nc.tensor, "pe"), (nc.sync, "sp")))

        with nc.Block() as block:

            @block.sync
            def _(sp):
                for k in range(KD):
                    S.open(wg_in[k], wd_in[k], n=16)
                sp.dma_start(ident[:, :], eye).then_inc(consts, 16)
                with sp.Fori(0, E2) as e:
                    for k in range(KD):
                        S.hold(g_used, last(e, KD, k + 1))
                        sp.dma_start(wg[:, k, :].unsqueeze(1), w_gu[ds(e, 1), k * P:(k + 1) * P, :].rearrange("o p n -> p o n")).then_inc(wg_in[k], 16)
                    for k in range(KD):
                        S.hold(d_used, last(e, KD, k + 1))
                        sp.dma_start(wd[:, k, :].unsqueeze(1), w_dn[ds(e, 1), k * P:(k + 1) * P, :].rearrange("o p n -> p o n")).then_inc(wd_in[k], 16)

            @block.gpsimd
            def _(pool):
                G.open(ic_ready, sent)

                def gather(v):
                    pool.indirect_dma_start(xg[:, :], None, x_dram, bass.IndirectOffsetOnAxis(ap=ic[v][:, :], axis=0)).then_inc(x_in, 16)

                nc.gpsimd.tensor_copy(ic[0][:, :], idx[:, 0:1]).then_inc(ic_ready, 1)
                pool.wait_ge(ic_ready, 2)
                gather(0)
                with pool.Fori(0, E2 // 2) as i:
                    for u in range(2):
                        v = 1 - u
                        nc.gpsimd.tensor_copy(ic[v][:, :], idx[:, ds(i * 2 + (u + 1), 1)]).then_inc(ic_ready, 1)
                        G.hold(ic_ready, i * 2 + (u + 3))
                        G.hold(x_psum, i * 2 + (u + 2))
                        gather(v)
                        G.hold(y_ready, i * 2 + (u + 2))
                        pool.indirect_dma_start(acc_dram, bass.IndirectOffsetOnAxis(ap=ic[u][:, :], axis=0), y[:, :], None, compute_op=ALU.add).then_inc(added, 16)
                        G.hold(added, i * 32 + (16 * u + 16))
                        pool.sem_inc(sent, 1)
                pool.wait_ge(x_in, 16 * (E2 + 1))

            @block.tensor
            def _(pe):
                E.open(h_psum, x_psum)
                E.open(g_used, d_used, n=KD)
                pe.wait_ge(consts, 16)

                def turn_x():
                    for k in range(KD):
                        t = nc.tensor.transpose(pt[:, k * P:(k + 1) * P], xg[:, k * P:(k + 1) * P], ident[:, :])
                    t.then_inc(x_psum, 1)

                pe.wait_ge(x_in, 16)
                turn_x()
                with pe.Fori(0, E2) as e:
                    E.hold(x_ready, now(e))
                    for k in range(KD):
                        E.hold(wg_in[k], now(e, 16))
                        for b in range(4):
                            m = nc.tensor.matmul(pg[:, b, :], xT[:, k, :], wg[:, k, b * HALF:(b + 1) * HALF], start=k == 0, stop=k == KD - 1)
                        m.then_inc(g_used, 1)
                    E.hold(x_in, e * 16 + 32)
                    turn_x()
                    E.hold(hid_ready, now(e))
                    E.hold(x_ready, now(e + 1))
                    for k in range(KD):
                        t = nc.tensor.transpose(pt[:, k * P:(k + 1) * P], hid[:, k * P:(k + 1) * P], ident[:, :])
                    t.then_inc(h_psum, 1)
                    E.hold(hT_ready, now(e))
                    E.hold(y_ready, last(e))
                    for k in range(KD):
                        E.hold(wd_in[k], now(e, 16))
                        for b in range(2):
                            m = nc.tensor.matmul(py[:, b * HALF:(b + 1) * HALF], hidT[:, k, :], wd[:, k, b * HALF:(b + 1) * HALF], start=k == 0, stop=k == KD - 1)
                        m.then_inc(d_used, 1)

            @block.scalar
            def _(act):
                A.open(silu, hT_ready)
                with act.Fori(0, E2) as e:
                    A.hold(g_used, now(e, KD))
                    A.hold(hid_ready, last(e))
                    nc.scalar.activation(sg[:, :].rearrange("p (b n) -> p b n", b=2), pg[:, 0:2, :], ACT.Silu).then_inc(silu, 1)
                    A.hold(h_psum, now(e))
                    A.hold(d_used, last(e, KD))
                    nc.scalar.copy(hidT[:, :, :], pt[:, :].rearrange("p (k t) -> p k t", k=KD)).then_inc(hT_ready, 1)

            @block.vector
            def _(dve):
                V.open(hid_ready, x_ready, y_ready)
                dve.wait_ge(x_psum, 2)

                def keep_x():
                    nc.vector.tensor_copy(xT[:, :, :], pt[:, :].rearrange("p (k t) -> p k t", k=KD)).then_inc(x_ready, 1)

                keep_x()
                with dve.Fori(0, E2) as e:
                    V.hold(silu, now(e))
                    V.hold(h_psum, last(e))
                    nc.vector.tensor_tensor(hid[:, :].rearrange("p (b n) -> p b n", b=2), sg[:, :].rearrange("p (b n) -> p b n", b=2),
                                            pg[:, 2:4, :], ALU.mult).then_inc(hid_ready, 1)
                    V.hold(x_psum, now(e + 1))
                    keep_x()
                    V.hold(d_used, now(e, KD))
                    V.hold(sent, e + 1)
                    nc.vector.tensor_scalar(y[:, :], py[:, :], gate[:, ds(e, 1)], None, ALU.mult).then_inc(y_ready, 1)



NBLK, BW = 4, 256
GELU_C = float(np.sqrt(2.0 / np.pi))
CONV = 4


def lru_phase(nc, vecs, w_in, w_r, w_i, w_out, eye, ln_g, ln_b, x_dram, out_dram):
    with Phase(nc, "lru") as ph:
        ggT = ph.sb("ggT", [P, KD, T])
        with Phase(nc, "lruk") as kept:
            vec = kept.sb("vec", [P, VEC_N])
            xc = kept.sb("xc", [P, KD, T])
            with Phase(nc, "lrui") as one:
                lru_in(nc, one, vec, xc, vecs, w_in, eye, x_dram, ggT)
            with Phase(nc, "lrus") as two:
                lru_scan(nc, two, vec, xc, w_r, w_i, ggT)
        with Phase(nc, "lruo") as three:
            product_and_norm(nc, three, ggT, w_out, ln_g, ln_b, x_dram, out_dram)


def lru_in(nc, ph, vec, xc, vecs, w_in, eye, x_dram, ggT):
    ident = ph.sb("ident", [P, P])
    xt = ph.sb("xt", [P, 2, D])
    xT = ph.sb("xT", [P, KD, T])
    w = ph.sb("w", [P, 2, 2, KD, P])
    gx = ph.sb("gx", [P, T])
    g2 = ph.sb("g2", [P, T])
    g3 = ph.sb("g3", [P, T])
    cv = ph.sb("cv", [P, T])
    cw = ph.sb("cw", [P, CONV + 1])
    pt = ph.ps("pt", [P, D])
    pg = ph.ps("pg", [P, T])
    px = ph.ps("px", [P, T])
    U = 2
    names = "consts x_psum xT_ready g_psum b_psum g_copied cube sig gg_ready cw_ready conv_v conv_done".split()
    consts, x_psum, xT_ready, g_psum, b_psum, g_copied, cube, sig, gg_ready, cw_ready, conv_v, conv_done = [ph.sem(n) for n in names]
    x_in = [ph.sem(f"x_in{u}") for u in range(U)]
    w_done = [ph.sem(f"w_done{u}") for u in range(U)]
    V, G, A, E, S = (ph.engine(e, n) for e, n in ((nc.vector, "dve"), (nc.gpsimd, "pool"), (nc.scalar, "act"),
                                                  (nc.tensor, "pe"), (nc.sync, "sp")))
    wv = w_in[0].rearrange("(k p) n -> p k n", p=P)
    c0 = vec_at("lru_conv_w_2")[0]
    cb = vec_at("lru_conv_b_2")[0]

    with nc.Block() as block:

        @block.sync
        def _(sp):
            for u in range(U):
                S.open(x_in[u], n=16)
                S.open(w_done[u], n=32)
            sp.dma_start(ident[:, :], eye).then_inc(consts, 16)
            sp.dma_start(vec[:, :], vecs).then_inc(consts, 16)
            with sp.Fori(0, NT // U) as i:
                for u in range(U):
                    S.hold(x_psum, last(i, U, u + 1))
                    sp.dma_start(xt[:, u, :], x_dram[ds((i * U + u) * P, P), :]).then_inc(x_in[u], 16)
            with sp.Fori(0, KD // U) as i:
                for u in range(U):
                    S.hold(b_psum, last(i, U, u + 1))
                    for n in range(2):
                        sp.dma_start(w[:, u, n, :, :], wv[:, :, ds(i * (U * P) + (n * D + u * P), P)]).then_inc(w_done[u], 16)

        @block.gpsimd
        def _(pool):
            G.open(cw_ready)
            pool.wait_ge(consts, 32)
            with pool.Fori(0, KD) as i:
                G.hold(conv_done, last(i))
                for j in range(CONV):
                    nc.gpsimd.tensor_copy(cw[:, j:j + 1], vec[:, ds(i + (c0 + j * KD), 1)])
                nc.gpsimd.tensor_copy(cw[:, CONV:CONV + 1], vec[:, ds(i + cb, 1)]).then_inc(cw_ready, 1)

        @block.tensor
        def _(pe):
            E.open(x_psum, g_psum, b_psum, n=U)
            pe.wait_ge(consts, 32)
            with pe.Fori(0, NT // U) as i:
                for u in range(U):
                    E.hold(x_in[u], now(i, 16))
                    E.hold(xT_ready, last(i, U, u + U) if u == 0 else now(i, U, u))
                    for k in range(KD):
                        t = nc.tensor.transpose(pt[:, k * P:(k + 1) * P], xt[:, u, k * P:(k + 1) * P], ident[:, :])
                    t.then_inc(x_psum, 1)
            pe.wait_ge(xT_ready, NT + U)
            with pe.Fori(0, KD // U) as i:
                for u in range(U):
                    E.hold(w_done[u], now(i, 32))
                    for n, ps in enumerate((pg, px)):
                        if n == 0:
                            E.hold(g_copied, i * U + (u + 1))
                        else:
                            E.hold(conv_done, i * U + (u + 1))
                        for half in range(2):
                            for k in range(KD):
                                m = nc.tensor.matmul(ps[:, half * HALF:(half + 1) * HALF], w[:, u, n, k, :], xT[:, k, half * HALF:(half + 1) * HALF],
                                                     start=k == 0, stop=k == KD - 1)
                        m.then_inc(b_psum if n else g_psum, 1)

        @block.scalar
        def _(act):
            A.open(xT_ready, n=U)
            A.open(g_copied, sig)
            with act.Fori(0, NT // U) as i:
                for u in range(U):
                    A.hold(x_psum, now(i, U, u + 1))
                    nc.scalar.copy(xT[:, :, ds((i * U + u) * P, P)], pt[:, :].rearrange("p (k t) -> p k t", k=KD)).then_inc(xT_ready, 1)
            with act.Fori(0, KD) as i:
                A.hold(g_psum, i + (U + 1))
                A.hold(gg_ready, last(i))
                nc.scalar.copy(gx[:, :], pg[:, :]).then_inc(g_copied, 1)
                A.hold(cube, now(i))
                nc.scalar.activation(g3[:, :], g3[:, :], ACT.Sigmoid, scale=2.0 * GELU_C).then_inc(sig, 1)

        @block.vector
        def _(dve):
            V.open(cube, gg_ready, conv_done)
            with dve.Fori(0, KD) as i:
                V.loop(i, 6)
                V.hold(g_copied, now(i))
                V.link(nc.vector.tensor_tensor(g2[:, :], gx[:, :], gx[:, :], ALU.mult))
                V.link(nc.vector.tensor_scalar(g2[:, :], g2[:, :], 0.044715, 1.0, ALU.mult, ALU.add))
                nc.vector.tensor_tensor(g3[:, :], g2[:, :], gx[:, :], ALU.mult).then_inc(cube, 1)
                V.hold(b_psum, i + (U + 1))
                V.hold(cw_ready, now(i))
                V.link(nc.vector.tensor_scalar(cv[:, :], px[:, :], cw[:, 2:3], cw[:, CONV:CONV + 1], ALU.mult, ALU.add))
                V.link(nc.vector.scalar_tensor_tensor(cv[:, 2:T], px[:, 0:T - 2], cw[:, 0:1], cv[:, 2:T], ALU.mult, ALU.add))
                V.link(nc.vector.scalar_tensor_tensor(cv[:, 1:T], px[:, 0:T - 1], cw[:, 1:2], cv[:, 1:T], ALU.mult, ALU.add))
                V.link(nc.vector.scalar_tensor_tensor(cv[:, 0:T - 1], px[:, 1:T], cw[:, 3:4], cv[:, 0:T - 1], ALU.mult, ALU.add))
                nc.vector.tensor_copy(xc[:, ds(i, 1), :].rearrange("p o t -> p (o t)"), cv[:, :]).then_inc(conv_done, 1)
                V.hold(sig, now(i))
                nc.vector.tensor_tensor(ggT[:, ds(i, 1), :].rearrange("p o t -> p (o t)"), gx[:, :], g3[:, :], ALU.mult).then_inc(gg_ready, 1)
            V.done(KD)


def lru_scan(nc, ph, vec, xc, w_r, w_i, ggT):
    w = ph.sb("w", [P, 2, 2, 2, 2, P])
    r, ig, th, a, a2, m, h = ([ph.sb(f"{n}{u}", [P, 2, T]) for u in range(2)] for n in "r ig th a a2 m h".split())
    dec = ph.sb("dec", [P, 2 * KD])
    sm = ph.sb("sm", [P, 6, 2 * KD])
    pw = ph.ps("pw", [P, 4, T])
    names = "sp_a dec_ready w_psum gates th_ready squared input_ready m2_ready mult ready".split()
    sp_a, dec_ready, w_psum, gates, th_ready, squared, input_ready, m2_ready, mult, ready = [ph.sem(n) for n in names]
    w_done = [ph.sem(f"w_done{u}") for u in range(2)]
    V, G, A, E, S = (ph.engine(e, n) for e, n in ((nc.vector, "dve"), (nc.gpsimd, "pool"), (nc.scalar, "act"),
                                                  (nc.tensor, "pe"), (nc.sync, "sp")))
    lam = vec_at("lru_lambda_2")[0]
    br, bi = vec_at("lru_b_rgate_2")[0], vec_at("lru_b_igate_2")[0]

    with nc.Block() as block:

        @block.sync
        def _(sp):
            for u in range(2):
                S.open(w_done[u], n=64)
            with sp.Fori(0, NBLK) as n:
                for u in range(2):
                    S.hold(w_psum, last(n, 8, 4 * u + 4))
                    for z in range(2):
                        for k, wt in enumerate((w_r, w_i)):
                            sp.dma_start(w[:, u, z, k, :, :], wt[0, z][ds(n, 1), :, u * P:(u + 1) * P].rearrange("o (c p) f -> p (o c) f", p=P)).then_inc(w_done[u], 16)

        @block.tensor
        def _(pe):
            E.open(w_psum, n=8)
            with pe.Fori(0, NBLK) as n:
                for u in range(2):
                    E.hold(w_done[u], now(n, 64))
                    for z in range(2):
                        for k in range(2):
                            at = 2 * z + k
                            E.hold(gates, now(n, 8, at + 1) if u else last(n, 8, 4 + at + 1))
                            for half in range(2):
                                for c in range(2):
                                    mm = nc.tensor.matmul(pw[:, at, half * HALF:(half + 1) * HALF], w[:, u, z, k, c, :],
                                                          xc[:, ds(n * 2 + c, 1), half * HALF:(half + 1) * HALF].rearrange("p o t -> p (o t)"), start=c == 0, stop=c == 1)
                            mm.then_inc(w_psum, 1)

        @block.gpsimd
        def _(pool):
            G.open(squared, input_ready, n=2)
            with pool.Fori(0, NBLK) as n:
                for u in range(2):
                    G.hold(gates, now(n, 8, 4 * u + 4))
                    nc.gpsimd.tensor_tensor(ig[u][:, :, :], ig[u][:, :, :], xc[:, ds(n * 2 + u, 1), :].to_broadcast([P, 2, T]), ALU.mult).then_inc(input_ready, 1)
                    G.hold(th_ready, now(n, 2, u + 1))
                    G.hold(m2_ready, last(n, 2, u + 1))
                    nc.gpsimd.tensor_tensor(a2[u][:, :, :], a[u][:, :, :], a[u][:, :, :], ALU.mult).then_inc(squared, 1)

        @block.scalar
        def _(act):
            A.open(gates, n=8)
            A.open(th_ready, mult, n=2)
            nc.scalar.activation(sm[:, 0, :], vec[:, lam:lam + 2 * KD], ACT.Abs).then_inc(sp_a, 1)
            act.wait_ge(sp_a, 1)
            nc.scalar.activation(sm[:, 1, :], sm[:, 0, :], ACT.Exp, scale=-1.0).then_inc(sp_a, 1)
            act.wait_ge(dec_ready, 1)
            with act.Fori(0, NBLK) as n:

                def sigmoids(u):
                    A.hold(ready, last(n, 2, u + 1))
                    for z in range(2):
                        for k, (dst, b0) in enumerate(((r[u], br), (ig[u], bi))):
                            A.hold(w_psum, now(n, 8, 4 * u + 2 * z + k + 1))
                            nc.scalar.activation(dst[:, z, :], pw[:, 2 * z + k, :], ACT.Sigmoid, bias=vec[:, ds(n * 2 + (b0 + z * KD + u), 1)]).then_inc(gates, 1)

                def decays(u):
                    A.hold(gates, now(n, 8, 4 * u + 4))
                    A.hold(squared, last(n, 2, u + 1))
                    for z in range(2):
                        nc.scalar.activation(th[u][:, z, :], r[u][:, z, :], ACT.Tanh, scale=dec[:, ds(n * 2 + (z * KD + u), 1)])
                        tt = nc.scalar.activation(a[u][:, z, :], r[u][:, z, :], ACT.Exp, scale=dec[:, ds(n * 2 + (z * KD + u), 1)])
                    tt.then_inc(th_ready, 1)

                def root(u):
                    A.hold(m2_ready, now(n, 2, u + 1))
                    nc.scalar.activation(m[u][:, :, :], m[u][:, :, :], ACT.Sqrt, scale=-1.0).then_inc(mult, 1)

                sigmoids(0)
                decays(0)
                sigmoids(1)
                root(0)
                decays(1)
                root(1)

        @block.vector
        def _(dve):
            V.open(m2_ready, ready, n=2)
            dve.wait_ge(sp_a, 2)
            y, s_, s2, acc = sm[:, 1, :], sm[:, 2, :], sm[:, 3, :], sm[:, 4, :]
            V.link(nc.vector.tensor_scalar(acc, y, 2.0, None, ALU.add))
            V.link(nc.vector.reciprocal(acc, acc))
            V.link(nc.vector.tensor_tensor(s_, y, acc, ALU.mult))
            V.link(nc.vector.tensor_tensor(s2, s_, s_, ALU.mult))
            V.link(nc.vector.memset(acc, 1.0 / 19))
            for odd in range(17, 0, -2):
                V.link(nc.vector.tensor_tensor(acc, acc, s2, ALU.mult))
                V.link(nc.vector.tensor_scalar(acc, acc, 1.0 / odd, None, ALU.add))
            V.link(nc.vector.tensor_tensor(acc, acc, s_, ALU.mult))
            V.link(nc.vector.tensor_scalar(sm[:, 5, :], vec[:, lam:lam + 2 * KD], -1.0, 0.0, ALU.mult, ALU.max))
            V.link(nc.vector.tensor_scalar(acc, acc, 2.0, None, ALU.mult))
            V.link(nc.vector.tensor_tensor(acc, acc, sm[:, 5, :], ALU.add))
            V.link(nc.vector.tensor_scalar(dec[:, :], acc, -8.0, None, ALU.mult))
            dve.sem_inc(dec_ready, 1)
            with dve.Fori(0, NBLK) as n:
                V.loop(n, 8)

                def minus_mult2(u):
                    V.hold(th_ready, now(n, 2, u + 1))
                    V.hold(squared, now(n, 2, u + 1))
                    nc.vector.scalar_tensor_tensor(m[u][:, :, :], a2[u][:, :, :], 1.0, th[u][:, :, :], ALU.add, ALU.mult).then_inc(m2_ready, 1)

                def scans(u):
                    V.hold(mult, now(n, 2, u + 1))
                    V.hold(input_ready, now(n, 2, u + 1))
                    nc.vector.memset(m[u][:, 0, 0:1], 1.0)
                    V.link(nc.vector.memset(m[u][:, 1, T - 1:T], 1.0))
                    V.link(nc.vector.tensor_tensor(m[u][:, :, :], m[u][:, :, :], ig[u][:, :, :], ALU.mult))
                    nc.vector.tensor_tensor_scan(h[u][:, 0, :], a[u][:, 0, :], m[u][:, 0, :], 0.0, ALU.mult, ALU.add)
                    V.link(nc.vector.tensor_tensor_scan(h[u][:, 1, ::-1], a[u][:, 1, ::-1], m[u][:, 1, ::-1], 0.0, ALU.mult, ALU.add))

                def gated(u):
                    V.link(nc.vector.tensor_tensor(h[u][:, 0, :], h[u][:, 0, :], h[u][:, 1, :], ALU.add))
                    g = ggT[:, ds(n * 2 + u, 1), :].rearrange("p o t -> p (o t)")
                    nc.vector.tensor_tensor(g, h[u][:, 0, :], g, ALU.mult).then_inc(ready, 1)

                minus_mult2(0)
                scans(0)
                gated(0)
                minus_mult2(1)
                scans(1)
                gated(1)
            V.done(NBLK)


def moe_and_transformer_kernel(nc, I, out):
    def scratch(name, shape, dt=F32):
        return nc.dram_tensor(name, shape, dt, kind="Internal").ap()

    hT, oT = scratch("hT", [D, T]), scratch("oT", [MLA_H * V_DIM, T])
    mla_phase(nc, I["x"], I["vecs"], I["w_in"], I["w_uq"], I["w_ukv"], I["eye"], I["mla_rope"], hT, oT)

    zfT = scratch("zfT", [RWKV_TILES * P, T])
    arrays = scratch("arrays", [len(ARR), RC, T])
    shift_phase(nc, I["vecs"], I["w_in"], hT, zfT)
    prep_phase(nc, I["vecs"], I["w_up"], I["a_up"], I["g_up"], zfT, I["starts"], I["head_ones"], arrays)
    yT = scratch("yT", [2, RC, T])
    wkv_phase(nc, I["wkv_tables"], arrays, yT)

    mixT = scratch("mixT", [D, T])
    mix_phase(nc, I["vecs"], I["w_in"], I["w_br_mla"], I["w_br_rwkv"], I["head_ones"], hT, oT, arrays, yT, mixT)
    x1, h2, x2 = scratch("x1", [T, D]), scratch("h2", [T, D]), scratch("x2", [T, D])
    slot_tok = scratch("slot_tok", [SLOTS + P, 1], U32)
    yb = scratch("yb", [SLOTS, D])
    with ExitStack() as routes:
        slots = routes.enter_context(nc.sbuf_tensor("slots", [P, 2 * NT], U32))
        weights = routes.enter_context(nc.sbuf_tensor("weights", [P, 2 * NT], F32))
        block_e = routes.enter_context(nc.sbuf_tensor("block_e", [P, MOE_BLOCKS], U32))
        route_phase(nc, I["x"], I["vecs"], I["w_out"], I["router_group_w"], I["router_group_b"], I["router_expert_w"],
                    I["router_expert_b"], I["eye"], I["route_tables"], I["tok_ids"], mixT, x1, h2, slot_tok,
                    (slots, weights, block_e))
        experts_phase(nc, I["vecs"], I["w1"], I["w3"], I["w2"], I["eye"], block_e, slot_tok, h2, yb)
        combine_phase(nc, I["norm_final_g"], slots, weights, x1, yb, x2)

    acc, x3, x4, x5 = (scratch(n, [T, D]) for n in ("acc", "x3", "x4", "x5"))
    gate = nc.alloc_sbuf_tensor("gate", [P, E2], F32)
    idx = nc.alloc_sbuf_tensor("idx", [P, E2 + 1], U32)
    gqa_phase(nc, I["attn_w_qkv_2"], I["attn_w_o_2"], I["attn_sink_2"], I["eye"], I["gqa_rope"], I["gqa_masks"],
              I["ln_mix_g_2"][0], I["ln_mix_b_2"][0], x2, x3)
    choose_phase(nc, "choose0", I["moe_w_router_2"][0], I["eye"], x3, acc, gate, idx)
    choice_phase(nc, "choice0", I["moe_w_gate_up_2"][0], I["moe_w_down_2"][0], I["eye"], x3, acc, gate, idx)
    norm_phase(nc, "norm1", I["ln_ffn_g_2"][0], I["ln_ffn_b_2"][0], x3, acc, x4)

    lru_phase(nc, I["vecs"], I["lru_w_in_2"], I["lru_w_rgate_2"], I["lru_w_igate_2"], I["lru_w_out_2"], I["eye"],
              I["ln_mix_g_2"][1], I["ln_mix_b_2"][1], x4, x5)
    choose_phase(nc, "choose1", I["moe_w_router_2"][1], I["eye"], x5, acc, gate, idx)
    choice_phase(nc, "choice1", I["moe_w_gate_up_2"][1], I["moe_w_down_2"][1], I["eye"], x5, acc, gate, idx)
    norm_phase(nc, "norm3", I["ln_ffn_g_2"][1], I["ln_ffn_b_2"][1], x5, acc, out)


_WHOLE = ["w_in", "w_uq", "w_ukv", "w_br_mla", "w_up", "a_up", "g_up", "w_br_rwkv", "w_out", "router_group_w",
          "router_group_b", "router_expert_w", "router_expert_b", "w1", "w3", "w2", "norm_final_g", "attn_w_qkv_2",
          "attn_w_o_2", "attn_sink_2", "lru_w_in_2", "lru_w_rgate_2", "lru_w_igate_2", "lru_w_out_2",
          "moe_w_router_2", "moe_w_gate_up_2", "moe_w_down_2", "ln_mix_g_2", "ln_mix_b_2", "ln_ffn_g_2",
          "ln_ffn_b_2"]


def kernel(**inputs):
    import concourse.bacc as _bacc
    from concourse.bass_utils import run_bass_kernel_spmd as _run

    a = {n: np.ascontiguousarray(inputs[n]) for n in _WHOLE}
    a["x"] = np.ascontiguousarray(inputs["x"]).reshape(T, D)
    a["vecs"] = np.ascontiguousarray(
        np.concatenate([np.asarray(inputs[n]).reshape(-1, P).T for n in VECS], axis=1))
    a["eye"] = np.eye(P, dtype=np.float32)
    a["mla_rope"] = mla_tables()
    a["starts"], a["head_ones"] = prep_tables()
    a["wkv_tables"] = wkv_tables()
    a["route_tables"], a["tok_ids"] = route_tables()
    a["gqa_rope"], a["gqa_masks"] = gqa_tables()
    nc = _bacc.Bacc("TRN2", target_bir_lowering=False, num_devices=1)
    arrays = {f"in_{n}_dram": v for n, v in a.items()}
    aps = {n: nc.dram_tensor(f"in_{n}_dram", v.shape, mybir.dt.from_np(v.dtype), kind="ExternalInput").ap()
           for n, v in a.items()}
    out = nc.dram_tensor("out_0_dram", (T, D), F32, kind="ExternalOutput").ap()
    moe_and_transformer_kernel(nc, aps, out)
    r = _run(nc, [arrays], core_ids=[0])
    return r.results[0]["out_0_dram"].reshape(1, T, D)
```

```python
from contextlib import ExitStack

import concourse.bass as bass
import numpy as np
from concourse import mybir

ALU = mybir.AluOpType
ACT = mybir.ActivationFunctionType
F32 = mybir.dt.float32
U32 = mybir.dt.uint32
AX_X = mybir.AxisListType.X
ds = bass.ds

P = 128
T = 1024
NT = T // P
D = 1024
KD = D // P
HALF = 512


def now(i, n=1, k=None):
    return (i + 1) * n + (n if k is None else k)


def last(i, n=1, k=None):
    return i * n + (n if k is None else k)


class Engine:

    def __init__(self, eng, chain, pace):
        self.eng, self.chain, self.pace = eng, chain, pace
        self.turn, self.per, self.steps, self.base = 0, 0, 0, 0

    def hold(self, sem, value):
        self.eng.wait_ge(sem, value)
        if not isinstance(value, int):
            self.eng.sem_inc(self.pace, 1)

    def link(self, instruction):
        self.steps += 1
        instruction.then_inc(self.chain, 1)
        self.hold(self.chain, self.turn * self.per + self.base + self.steps)

    def loop(self, turn, per):
        self.base += self.steps
        self.turn, self.per, self.steps = turn, per, 0

    def open(self, *sems, n=1):
        for s in sems:
            self.eng.sem_inc(s, n)

    def done(self, turns):
        assert self.steps == self.per, (self.chain.name, self.steps)
        self.base += turns * self.per
        self.turn, self.per, self.steps = 0, 0, 0


class Phase:

    def __init__(self, nc, name):
        self.nc, self.name, self.ctx, self.sems = nc, name, ExitStack(), []

    def __enter__(self):
        return self

    def __exit__(self, *a):
        self.ctx.close()
        if self.sems:
            self.nc.clear_and_free_semaphores(self.sems)
            self.nc.all_engine_barrier()

    def sb(self, name, shape, dt=F32):
        return self.ctx.enter_context(self.nc.sbuf_tensor(f"{self.name}_{name}", shape, dt))

    def ps(self, name, shape):
        return self.ctx.enter_context(self.nc.psum_tensor(f"{self.name}_{name}", shape, F32))

    def sem(self, name):
        self.sems.append(self.nc.alloc_semaphore(name=f"{self.name}_{name}"))
        return self.sems[-1]

    def engine(self, eng, name):
        return Engine(eng, self.sem(f"{name}_chain"), self.sem(f"{name}_pace"))


MLA_H, QK_NOPE, QK_ROPE, V_DIM, Q_LORA, KV_LORA = 8, 64, 32, 64, 384, 256
QK = QK_NOPE + QK_ROPE
MLA_IN = Q_LORA + KV_LORA + QK_ROPE
NORM_EPS = 1e-6


VECS = dict(norm_mix_g=8, q_norm_g=3, kv_norm_g=2, mu_prev=15, mu_next=15, w0=8, a0=8, k_k=4, k_a=4, r_k=4, lnx_g=4,
            lnx_b=4, gate_b=16, norm_ffn_g=8, lru_conv_w_2=32, lru_conv_b_2=8, lru_b_rgate_2=16, lru_b_igate_2=16,
            lru_lambda_2=16)
VEC_N = sum(VECS.values())


def vec_at(name):
    names = list(VECS)
    at = sum(VECS[n] for n in names[:names.index(name)])
    return at, at + VECS[name]


def mla_tables():
    pos = np.arange(T, dtype=np.float32)
    inv = np.float32(10000.0) ** (-np.arange(0, QK_ROPE, 2, dtype=np.float32) / QK_ROPE)
    ang = (pos[:, None] * inv[None, :]).astype(np.float32)
    t = np.concatenate([np.cos(ang), np.sin(ang)], axis=1).astype(np.float32)
    return np.ascontiguousarray(t.reshape(NT, P, QK_ROPE).transpose(1, 0, 2))


def mla_phase(nc, x, vecs, w_in, w_uq, w_ukv, eye, rope, hT_dram, oT_dram, h_all, h_in):
    with Phase(nc, "mla") as ph:
        ident = ph.sb("ident", [P, P])
        q_all = ph.sb("qT", [QK, MLA_H, T])
        k_all = ph.sb("kT", [QK, MLA_H, T])
        v_all = ph.sb("v", [P, NT, MLA_H * V_DIM])
        with ExitStack() as one:
            proj = Phase(nc, "mlap")
            one.enter_context(proj)
            mla_project(nc, proj, x, vecs, w_in, w_uq, w_ukv, eye, rope, hT_dram,
                        ident, q_all, k_all, v_all)
        with ExitStack() as two:
            att = Phase(nc, "mlaa")
            two.enter_context(att)
            mla_attend(nc, att, ident, q_all, k_all, v_all, oT_dram, hT_dram, h_all, h_in)


def mla_project(nc, ph, x, vecs, w_in, w_uq, w_ukv, eye, rope, hT_dram,
                ident, q_all, k_all, v_all):
    NC = (Q_LORA + KV_LORA) // P
    w_z = ph.sb("w_z", [P, KD, MLA_IN])
    w_q = ph.sb("w_q", [P, Q_LORA // P, MLA_H * QK])
    w_kv = ph.sb("w_kv", [P, KV_LORA // P, MLA_H * P])
    tab = ph.sb("tab", [P, NT, QK_ROPE])
    vec = ph.sb("vec", [P, VEC_N])
    g_h = vec[:, slice(*vec_at("norm_mix_g"))]
    g_c = vec[:, vec_at("q_norm_g")[0]:vec_at("kv_norm_g")[1]]
    xt = ph.sb("xt", [P, D])
    junk = ph.sb("junk", [P, D])
    h = ph.sb("h", [P, D])
    hT = ph.sb("hT", [P, KD, P])
    ssq = ph.sb("ssq", [P, 4])
    ms = ph.sb("ms", [P, 4])
    root = ph.sb("root", [P, 4])
    rstd = ph.sb("rstd", [P, 4])
    c = ph.sb("c", [P, NC * P])
    cT = ph.sb("cT", [P, NC, P])
    krope = ph.sb("krope", [P, QK_ROPE])
    krot = ph.sb("krot", [P, QK_ROPE])
    qcat = ph.sb("qcat", [P, MLA_H, QK])
    kcat = ph.sb("kcat", [P, MLA_H, QK])
    qr = ph.sb("qr", [P, 4, MLA_H, 16])
    kr = ph.sb("kr", [P, 4, 16])

    pT = ph.ps("pT", [P, 2, HALF])
    pZ = ph.ps("pZ", [P, 2, HALF])
    pQ = ph.ps("pQ", [P, 2, HALF])
    pK = ph.ps("pK", [P, 2, HALF])

    names = ("x_in x_sq ms_h rt_h h_ready hT_psum hT_ready hT_out z_psum sq_c ms_c rt_c c_ready cT_psum cT_ready q_psum "
             "kv_psum qcat_ready kcat_ready qT_psum kT_psum qT_kept kT_kept v_kept").split()
    (x_in, x_sq, ms_h, rt_h, h_ready, hT_psum, hT_ready, hT_out, z_psum, sq_c, ms_c, rt_c, c_ready, cT_psum, cT_ready, q_psum,
     kv_psum, qcat_ready, kcat_ready, qT_psum, kT_psum, qT_kept, kT_kept, v_kept) = [ph.sem(n) for n in names]
    consts = ph.sem("consts")
    z_weights = ph.sem("z_weights")
    later = ph.sem("later")
    V, G, A, E, S = (ph.engine(e, n) for e, n in ((nc.vector, "dve"), (nc.gpsimd, "pool"), (nc.scalar, "act"),
                                                  (nc.tensor, "pe"), (nc.sync, "sp")))
    hT_view = hT_dram.rearrange("(k p) t -> p k t", p=P)

    with nc.Block() as block:

        def turns(eng, E_, turn, links):
            turn(0, False, True)
            with eng.Fori(0, NT - 2) as n:
                E_.loop(n, links)
                turn(n + 1, True, True)
            E_.done(NT - 2)
            turn(NT - 1, True, False)

        @block.sync
        def _(sp):
            S.open(x_in, hT_out, n=16)
            sp.dma_start(ident[:, :], eye).then_inc(consts, 16)
            sp.dma_start(vec[:, :], vecs).then_inc(consts, 16)
            with sp.Fori(0, NT) as i:
                S.hold(x_sq, last(i))
                S.hold(h_ready, last(i))
                sp.dma_start(xt[:, :], x[ds(i * P, P), :]).then_inc(x_in, 16)
                S.hold(hT_ready, now(i))
                sp.dma_start(hT_view[:, :, ds(i * P, P)], hT[:, :, :]).then_inc(hT_out, 16)
            sp.wait_ge(hT_out, (NT + 1) * 16)

        @block.scalar
        def _(act):
            A.open(x_sq, rt_h, sq_c, rt_c, v_kept, kT_kept)
            act.dma_start(w_z[:, :, :], w_in[0, :, 0:MLA_IN].rearrange("(k p) n -> p k n", p=P)).then_inc(z_weights, 16)
            act.dma_start(w_q[:, :, :], w_uq[0].rearrange("(k p) n -> p k n", p=P)).then_inc(later, 16)
            act.dma_start(w_kv[:, :, :], w_ukv[0].rearrange("(k p) n -> p k n", p=P)).then_inc(later, 16)
            act.dma_start(tab[:, :, :], rope).then_inc(later, 16)

            def norm_h(i):
                A.hold(x_in, now(i, 16))
                nc.scalar.activation(junk[:, :], xt[:, :], ACT.Square, accum_out=ssq[:, 0:1]).then_inc(x_sq, 1)
                A.hold(ms_h, now(i))
                nc.scalar.activation(root[:, 0:1], ms[:, 0:1], ACT.Sqrt).then_inc(rt_h, 1)

            def keep_v(i):
                A.hold(kcat_ready, now(i))
                for b in range(2):
                    vb = nc.scalar.copy(v_all[:, ds(i, 1), b * 256:b * 256 + 256].rearrange("p o (h d) -> p (o h) d", h=4),
                                        pK[:, b, :].rearrange("p (h d) -> p h d", h=4)[:, :, QK_NOPE:P])
                vb.then_inc(v_kept, 1)

            def keep_k(i):
                A.hold(kT_psum, now(i))
                for b in range(2):
                    kept = nc.scalar.copy(k_all[:, 4 * b:4 * b + 4, ds(i * P, P)], pK[0:QK, b, :].rearrange("p (h t) -> p h t", h=4))
                kept.then_inc(kT_kept, 1)

            def turn(i, prev, more):
                if prev:
                    keep_v(i - 1)
                if more:
                    norm_h(i + 1)
                A.hold(z_psum, now(i))
                A.hold(x_sq, now(i + 1) if more else now(i))
                nc.scalar.activation(junk[:, 0:Q_LORA], pZ[:, 0, 0:Q_LORA], ACT.Square, accum_out=ssq[:, 1:2])
                nc.scalar.activation(junk[:, Q_LORA:Q_LORA + KV_LORA], pZ[:, 1, 0:KV_LORA], ACT.Square,
                                     accum_out=ssq[:, 2:3]).then_inc(sq_c, 1)
                A.hold(ms_c, now(i))
                nc.scalar.activation(root[:, 1:3], ms[:, 1:3], ACT.Sqrt).then_inc(rt_c, 1)
                A.hold(sq_c, now(i))
                if prev:
                    keep_k(i - 1)

            norm_h(0)
            turns(act, A, turn, 0)
            keep_v(NT - 1)
            keep_k(NT - 1)

        @block.vector
        def _(dve):
            V.open(ms_h, ms_c, h_ready, hT_ready, c_ready, cT_ready, qcat_ready, kcat_ready, qT_kept)
            dve.wait_ge(consts, 2 * 16)

            def rotate(out1, out2, x1, x2, co, si, r):
                nc.vector.tensor_tensor(r[0], x1, co, ALU.mult)
                nc.vector.tensor_tensor(r[1], x2, si, ALU.mult)
                nc.vector.tensor_tensor(r[2], x1, si, ALU.mult)
                V.link(nc.vector.tensor_tensor(r[3], x2, co, ALU.mult))
                nc.vector.tensor_tensor(out1, r[0], r[1], ALU.subtract)
                return nc.vector.tensor_tensor(out2, r[2], r[3], ALU.add)

            def norm_h(i):
                V.hold(x_sq, now(i))
                nc.vector.tensor_scalar(ms[:, 0:1], ssq[:, 0:1], 1.0 / D, NORM_EPS, ALU.mult, ALU.add).then_inc(ms_h, 1)
                V.hold(rt_h, now(i))
                V.link(nc.vector.reciprocal(rstd[:, 0:1], root[:, 0:1]))
                V.hold(hT_psum, last(i))
                nc.vector.tensor_scalar(h[:, :], xt[:, :], rstd[:, 0:1], None, ALU.mult).then_inc(h_ready, 1)

            def keep_h(i):
                V.hold(z_psum, last(i))
                V.hold(hT_out, last(i, 16))
                V.hold(hT_psum, now(i))
                nc.vector.tensor_tensor(hT[:, :, :].rearrange("p (b k) t -> p b k t", b=2),
                                        pT[:, :, :].rearrange("p b (k t) -> p b k t", k=4),
                                        g_h[:, :].rearrange("p (b k) -> p b k", b=2).unsqueeze(3).to_broadcast([P, 2, 4, P]),
                                        ALU.mult).then_inc(hT_ready, 1)

            def heads(i):
                co, si = tab[:, ds(i, 1), 0:16], tab[:, ds(i, 1), 16:32]
                V.hold(q_psum, now(i))
                V.hold(qT_psum, last(i))
                for b in range(2):
                    src = pQ[:, b, 0:4 * QK].rearrange("p (h d) -> p h d", h=4)
                    hs = slice(4 * b, 4 * b + 4)
                    nc.vector.tensor_copy(qcat[:, hs, 0:QK_NOPE], src[:, :, 0:QK_NOPE])
                    done = rotate(qcat[:, hs, 64:80], qcat[:, hs, 80:96], src[:, :, 64:80], src[:, :, 80:96],
                                  co.to_broadcast([P, 4, 16]), si.to_broadcast([P, 4, 16]),
                                  [qr[:, n, hs, :] for n in range(4)])
                done.then_inc(qcat_ready, 1)
                V.hold(kv_psum, now(i))
                V.hold(kT_psum, last(i))
                for b in range(2):
                    nc.vector.tensor_copy(kcat[:, 4 * b:4 * b + 4, 0:QK_NOPE],
                                          pK[:, b, :].rearrange("p (h d) -> p h d", h=4)[:, :, 0:QK_NOPE])
                nc.vector.tensor_copy(kcat[:, :, QK_NOPE:QK], krot[:, :].unsqueeze(1).to_broadcast([P, MLA_H, QK_ROPE])).then_inc(kcat_ready, 1)

            def keep_q(i):
                V.hold(qT_psum, now(i))
                for b in range(2):
                    kept = nc.vector.tensor_copy(q_all[:, 4 * b:4 * b + 4, ds(i * P, P)],
                                                 pQ[0:QK, b, :].rearrange("p (h t) -> p h t", h=4))
                kept.then_inc(qT_kept, 1)

            def turn(i, prev, more):
                if prev:
                    heads(i - 1)
                if more:
                    norm_h(i + 1)
                V.hold(sq_c, now(i))
                nc.vector.tensor_scalar(ms[:, 1:2], ssq[:, 1:2], 1.0 / Q_LORA, NORM_EPS, ALU.mult, ALU.add)
                nc.vector.tensor_scalar(ms[:, 2:3], ssq[:, 2:3], 1.0 / KV_LORA, NORM_EPS, ALU.mult, ALU.add).then_inc(ms_c, 1)
                V.hold(rt_c, now(i))
                V.link(nc.vector.reciprocal(rstd[:, 1:3], root[:, 1:3]))
                V.hold(cT_psum, last(i))
                nc.vector.tensor_scalar(c[:, 0:Q_LORA], pZ[:, 0, 0:Q_LORA], rstd[:, 1:2], None, ALU.mult)
                V.link(nc.vector.tensor_copy(krope[:, :], pZ[:, 1, KV_LORA:KV_LORA + QK_ROPE]))
                nc.vector.tensor_scalar(c[:, Q_LORA:NC * P], pZ[:, 1, 0:KV_LORA], rstd[:, 2:3], None, ALU.mult).then_inc(c_ready, 1)
                if more:
                    keep_h(i + 1)
                co, si = tab[:, ds(i, 1), 0:16], tab[:, ds(i, 1), 16:32]
                if prev:
                    V.hold(kcat_ready, last(i))
                V.link(rotate(krot[:, 0:16], krot[:, 16:32], krope[:, 0:16], krope[:, 16:32],
                              co.rearrange("p o d -> p (o d)"), si.rearrange("p o d -> p (o d)"),
                              [kr[:, n, :] for n in range(4)]))
                if prev:
                    keep_q(i - 1)
                V.hold(kv_psum, last(i))
                V.hold(cT_psum, now(i))
                nc.vector.tensor_tensor(cT[:, 0:4, :], pT[:, 0, :].rearrange("p (k t) -> p k t", k=4),
                                        g_c[:, 0:4].unsqueeze(2).to_broadcast([P, 4, P]), ALU.mult)
                nc.vector.tensor_scalar(cT[:, 4, :], pT[:, 1, 0:P], g_c[:, 4:5], None, ALU.mult).then_inc(cT_ready, 1)

            norm_h(0)
            keep_h(0)
            dve.wait_ge(later, 3 * 16)
            turns(dve, V, turn, 7)
            heads(NT - 1)
            keep_q(NT - 1)

        @block.tensor
        def _(pe):
            E.open(hT_psum, z_psum, cT_psum, q_psum, kv_psum, qT_psum, kT_psum)
            pe.wait_ge(consts, 2 * 16)

            def turn_h(i):
                E.hold(h_ready, now(i))
                E.hold(cT_ready, last(i - 1) if not isinstance(i, int) or i else 1)
                for k in range(KD):
                    t = nc.tensor.transpose(pT[:, k // 4, k % 4 * P:k % 4 * P + P], h[:, k * P:k * P + P], ident[:, :])
                t.then_inc(hT_psum, 1)

            def turn_heads(i):
                E.hold(qcat_ready, now(i))
                for n in range(MLA_H):
                    t = nc.tensor.transpose(pQ[0:QK, n // 4, n % 4 * P:n % 4 * P + P], qcat[:, n, :], ident[:, :])
                t.then_inc(qT_psum, 1)
                E.hold(kcat_ready, now(i))
                E.hold(v_kept, now(i))
                for n in range(MLA_H):
                    t = nc.tensor.transpose(pK[0:QK, n // 4, n % 4 * P:n % 4 * P + P], kcat[:, n, :], ident[:, :])
                t.then_inc(kT_psum, 1)

            def turn(i, prev, more):
                E.hold(hT_ready, now(i))
                E.hold(c_ready, last(i))
                for o, lo, n in ((0, 0, Q_LORA), (1, Q_LORA, MLA_IN - Q_LORA)):
                    for k in range(KD):
                        m = nc.tensor.matmul(pZ[:, o, 0:n], hT[:, k, :], w_z[:, k, lo:lo + n], start=k == 0, stop=k == KD - 1)
                m.then_inc(z_psum, 1)
                if prev:
                    turn_heads(i - 1)
                if more:
                    turn_h(i + 1)
                    E.hold(hT_ready, now(i + 1))
                E.hold(c_ready, now(i))
                for k in range(NC):
                    t = nc.tensor.transpose(pT[:, k // 4, k % 4 * P:k % 4 * P + P], c[:, k * P:k * P + P], ident[:, :])
                t.then_inc(cT_psum, 1)
                E.hold(cT_ready, now(i))
                pe.wait_ge(later, 3 * 16)
                E.hold(qT_kept, last(i))
                for o in range(2):
                    for k in range(3):
                        m = nc.tensor.matmul(pQ[:, o, 0:4 * QK], cT[:, k, :], w_q[:, k, o * 4 * QK:(o + 1) * 4 * QK], start=k == 0, stop=k == 2)
                m.then_inc(q_psum, 1)
                E.hold(kT_kept, last(i))
                for o in range(2):
                    for k in range(2):
                        m = nc.tensor.matmul(pK[:, o, :], cT[:, 3 + k, :], w_kv[:, k, o * HALF:(o + 1) * HALF], start=k == 0, stop=k == 1)
                m.then_inc(kv_psum, 1)

            turn_h(0)
            pe.wait_ge(z_weights, 16)
            turns(pe, E, turn, 0)
            turn_heads(NT - 1)


def mla_attend(nc, ph, ident, q_all, k_all, v_all, oT_dram, hT_dram, h_all, h_in):
    PAIRS, QB = MLA_H // 2, HALF // P
    U, NG = 2 * NT, 2 * NT // QB
    SCALE = float(QK) ** -0.5
    q_s = ph.sb("q_s", [QK, 2, T])
    v_s = ph.sb("v_s", [P, 2, NT, V_DIM])
    probs = ph.sb("probs", [P, 2, T])
    pT_sb = ph.sb("probsT", [P, 2, NT, HALF])
    mx = ph.sb("mx", [P, 2])
    nmx = ph.sb("nmx", [P, 2])
    den = ph.sb("den", [P, 2])
    rden = ph.sb("rden", [P, 2])
    oT = ph.sb("oT", [P, 2, HALF])
    pS = ph.ps("pS", [P, 4, HALF])
    pP = ph.ps("pP", [P, 2, HALF])
    pO = ph.ps("pO", [P, 2, HALF])
    names = "q_in v_in s_psum max_ready exp_done normed pT_psum pT_v pT_a o_psum oT_ready oT_out".split()
    q_in, v_in, s_psum, max_ready, exp_done, normed, pT_psum, pT_v, pT_a, o_psum, oT_ready, oT_out = [ph.sem(n) for n in names]
    V, G, A, E, S = (ph.engine(e, n) for e, n in ((nc.vector, "dve"), (nc.gpsimd, "pool"), (nc.scalar, "act"),
                                                  (nc.tensor, "pe"), (nc.sync, "sp")))

    def per_unit(i, u):
        return now(i, U, u + 1) if u >= 0 else last(i, U, U + u + 1)

    def per_group(i, g):
        return now(i, NG, g + 1) if g >= 0 else last(i, NG, NG + g + 1)

    with nc.Block() as block:

        @block.gpsimd
        def _(pool):
            G.open(q_in, v_in, n=2)
            with pool.Fori(0, PAIRS) as i:
                for e in range(2):
                    G.hold(s_psum, last(i, U, (e + 1) * NT))
                    nc.gpsimd.tensor_copy(q_s[:, e, :], q_all[:, ds(i * 2 + e, 1), :].rearrange("p o t -> p (o t)")).then_inc(q_in, 1)
                    G.hold(o_psum, last(i, NG, (e + 1) * NG // 2))
                    nc.gpsimd.tensor_copy(v_s[:, e, :, :], v_all[:, :, ds(i * 2 * V_DIM + e * V_DIM, V_DIM)]).then_inc(v_in, 1)

        @block.tensor
        def _(pe):
            E.open(s_psum, pT_psum, n=U)
            E.open(o_psum, n=NG)

            def scores(i, u):
                e, tile = u // NT, u % NT
                if tile == 0:
                    E.hold(q_in, now(i, 2, e + 1))
                E.hold(exp_done, per_unit(i, u - 2))
                for j in range(2):
                    m = nc.tensor.matmul(pS[:, u % 2 * 2 + j, :], q_s[:, e, tile * P:(tile + 1) * P],
                                         k_all[:, ds(i * 2 + e, 1), j * HALF:(j + 1) * HALF].rearrange("p o t -> p (o t)"), start=True, stop=True)
                m.then_inc(s_psum, 1)

            def outputs(i, g):
                e, half = g // 2, g % 2
                if g < 2:
                    E.hold(oT_ready, last(i, 2, half + 1))
                E.hold(v_in, now(i, 2, e + 1))
                E.hold(pT_v, per_unit(i, (g + 1) * QB - 1))
                E.hold(pT_a, per_unit(i, (g + 1) * QB - 1))
                for k in range(NT):
                    m = nc.tensor.matmul(pO[e * V_DIM:(e + 1) * V_DIM, half, :], v_s[:, e, k, :], pT_sb[:, g % 2, k, :], start=k == 0, stop=k == NT - 1)
                m.then_inc(o_psum, 1)

            with pe.Fori(0, PAIRS) as i:
                scores(i, 0)
                for u in range(U):
                    if u + 1 < U:
                        scores(i, u + 1)
                    if u and u % QB == 0:
                        outputs(i, u // QB - 1)
                    E.hold(normed, per_unit(i, u))
                    E.hold(pT_v, per_unit(i, u - 1))
                    E.hold(pT_a, per_unit(i, u - 1))
                    for k in range(NT):
                        t = nc.tensor.transpose(pP[:, k // 4, k % 4 * P:k % 4 * P + P], probs[:, u % 2, k * P:k * P + P], ident[:, :])
                    t.then_inc(pT_psum, 1)
                outputs(i, NG - 1)

        def place(u, lo):
            return pT_sb[:, u // QB % 2, lo:lo + 4, u % QB * P:(u % QB + 1) * P]

        @block.vector
        def _(dve):
            V.open(max_ready, normed, pT_v, n=U)
            with dve.Fori(0, PAIRS) as i:
                V.loop(i, 2 * U)

                def maximum(u):
                    c = u % 2
                    V.hold(s_psum, per_unit(i, u))
                    V.hold(exp_done, per_unit(i, u - 2))
                    V.link(nc.vector.reduce_max(mx[:, c:c + 1], pS[:, c * 2:c * 2 + 2, :], mybir.AxisListType.XY))
                    nc.vector.tensor_scalar(nmx[:, c:c + 1], mx[:, c:c + 1], -SCALE, None, ALU.mult).then_inc(max_ready, 1)

                def copy(u):
                    V.hold(pT_psum, per_unit(i, u))
                    if u % QB == 0:
                        V.hold(o_psum, per_group(i, u // QB - 2))
                    nc.vector.tensor_copy(place(u, 0), pP[:, 0, :].rearrange("p (k t) -> p k t", k=4)).then_inc(pT_v, 1)

                maximum(0)
                for u in range(U):
                    if u:
                        copy(u - 1)
                    V.hold(exp_done, per_unit(i, u))
                    V.link(nc.vector.reciprocal(rden[:, u % 2:u % 2 + 1], den[:, u % 2:u % 2 + 1]))
                    nc.vector.tensor_scalar(probs[:, u % 2, :], probs[:, u % 2, :], rden[:, u % 2:u % 2 + 1], None, ALU.mult).then_inc(normed, 1)
                    if u + 1 < U:
                        maximum(u + 1)
                copy(U - 1)
            V.done(PAIRS)

        @block.scalar
        def _(act):
            A.open(exp_done, pT_a, n=U)
            A.open(oT_ready, n=2)
            with act.Fori(0, PAIRS) as i:

                def copy(u):
                    A.hold(pT_psum, per_unit(i, u))
                    if u % QB == 0:
                        A.hold(o_psum, per_group(i, u // QB - 2))
                    nc.scalar.copy(place(u, 4), pP[:, 1, :].rearrange("p (k t) -> p k t", k=4)).then_inc(pT_a, 1)

                def keep(half):
                    A.hold(o_psum, per_group(i, 2 + half))
                    A.hold(oT_out, last(i, 16))
                    nc.scalar.copy(oT[:, half, :], pO[:, half, :]).then_inc(oT_ready, 1)

                for u in range(U):
                    A.hold(max_ready, per_unit(i, u))
                    A.hold(pT_psum, per_unit(i, u - 2))
                    nc.scalar.activation(probs[:, u % 2, :], pS[:, u % 2 * 2:u % 2 * 2 + 2, :], ACT.Exp,
                                         bias=nmx[:, u % 2:u % 2 + 1], scale=SCALE, accum_out=den[:, u % 2:u % 2 + 1]).then_inc(exp_done, 1)
                    if u:
                        copy(u - 1)
                    if u == U - 3:
                        keep(0)
                copy(U - 1)
                keep(1)

        @block.sync
        def _(sp):
            S.open(oT_out, n=16)
            for k in range(KD):
                sp.dma_start(h_all[:, k, :], hT_dram[k * P:(k + 1) * P, :]).then_inc(h_in, 16)
            with sp.Fori(0, PAIRS) as i:
                S.hold(oT_ready, now(i, 2))
                sp.dma_start(oT_dram[ds(i * P, P), :], oT[:, :, :].rearrange("p b t -> p (b t)")).then_inc(oT_out, 16)
            sp.wait_ge(oT_out, (PAIRS + 1) * 16)


RC = 512
RJ = RC // P
C = 64
NCH = T // C
W_SCALE = float(np.exp(np.float32(-0.5)))
ARR = dict(r=0, v=1, nkk=2, b0=3, b1=4, kd0=5, kd1=6, L0=7, L1=8, g=9, bonus=10)
RWKV_TILES = 15


def shift_phase(nc, vecs, w_in, hT, h_in, zf_dram):
    with Phase(nc, "shift") as ph:
        U = 3
        w = ph.sb("w", [P, U, KD, P])
        zf = ph.sb("zf", [P, U, T])
        vec = ph.sb("vec", [P, VEC_N])
        keep = ph.sb("keep", [P, RWKV_TILES])
        pz = ph.ps("pz", [P, U, T])
        names = "z_psum kept shifted zf_out".split()
        z_psum, kept, shifted, zf_out = [ph.sem(n) for n in names]
        w_in_u = [ph.sem(f"w_in{u}") for u in range(U)]
        consts = ph.sem("consts")
        keep_v = ph.sem("keep_v")
        V, A, E, S = (ph.engine(e, n) for e, n in ((nc.vector, "dve"), (nc.scalar, "act"), (nc.tensor, "pe"), (nc.sync, "sp")))
        mp, mn = vec_at("mu_prev")[0], vec_at("mu_next")[0]
        w_view = w_in[0].rearrange("(k p) n -> p k n", p=P)
        zf_view = zf_dram.rearrange("(k p) t -> p k t", p=P)

        with nc.Block() as block:

            @block.sync
            def _(sp):
                for u in range(U):
                    S.open(w_in_u[u], n=16)
                sp.dma_start(vec[:, :], vecs).then_inc(consts, 16)
                with sp.Fori(0, RWKV_TILES // U) as i:
                    for u in range(U):
                        S.hold(z_psum, last(i, U, u + 1))
                        sp.dma_start(w[:, u, :, :], w_view[:, :, ds(i * (U * P) + (MLA_IN + u * P), P)]).then_inc(w_in_u[u], 16)

            @block.tensor
            def _(pe):
                E.open(z_psum, n=U)
                pe.wait_ge(h_in, KD * 16)
                with pe.Fori(0, RWKV_TILES // U) as i:
                    for u in range(U):
                        E.hold(w_in_u[u], now(i, 16))
                        E.hold(shifted, last(i, U, u + 1))
                        for half in range(2):
                            for k in range(KD):
                                m = nc.tensor.matmul(pz[:, u, half * HALF:(half + 1) * HALF], w[:, u, k, :],
                                                     hT[:, k, half * HALF:(half + 1) * HALF], start=k == 0, stop=k == KD - 1)
                        m.then_inc(z_psum, 1)

            @block.scalar
            def _(act):
                A.open(kept, n=U)
                A.open(zf_out, n=16 * U)
                act.wait_ge(keep_v, 1)
                with act.Fori(0, RWKV_TILES // U) as i:
                    for u in range(U):
                        A.hold(z_psum, now(i, U, u + 1))
                        A.hold(zf_out, last(i, 16 * U))
                        nc.scalar.activation(zf[:, u, :], pz[:, u, :], ACT.Copy, scale=keep[:, ds(i * U + u, 1)]).then_inc(kept, 1)
                    for u in range(U):
                        A.hold(shifted, now(i, U, u + 1))
                        act.dma_start(zf_view[:, ds(i * U + u, 1), :], zf[:, u:u + 1, :]).then_inc(zf_out, 16)
                act.wait_ge(zf_out, 16 * (RWKV_TILES + U))

            @block.vector
            def _(dve):
                V.open(shifted, n=U)
                dve.wait_ge(consts, 16)
                V.link(nc.vector.tensor_tensor(keep[:, :], vec[:, mp:mp + RWKV_TILES], vec[:, mn:mn + RWKV_TILES], ALU.add))
                V.link(nc.vector.tensor_scalar(keep[:, :], keep[:, :], -1.0, 1.0, ALU.mult, ALU.add))
                dve.sem_inc(keep_v, 1)
                with dve.Fori(0, RWKV_TILES // U) as i:
                    V.loop(i, U)
                    for u in range(U):
                        V.hold(kept, now(i, U, u + 1))
                        V.link(nc.vector.scalar_tensor_tensor(zf[:, u, 1:T], pz[:, u, 0:T - 1], vec[:, ds(i * U + (mp + u), 1)],
                                                              zf[:, u, 1:T], ALU.mult, ALU.add))
                        nc.vector.scalar_tensor_tensor(zf[:, u, 0:T - 1], pz[:, u, 1:T], vec[:, ds(i * U + (mn + u), 1)],
                                                       zf[:, u, 0:T - 1], ALU.mult, ALU.add).then_inc(shifted, 1)
                V.done(RWKV_TILES // U)


def prep_tables():
    t = np.arange(T)
    starts = np.stack([(t % C != 0), (t % C != C - 1)]).astype(np.float32)
    q = np.arange(P) // 64
    return np.ascontiguousarray(np.broadcast_to(starts, (P, 2, T))), (q[:, None] == q[None, :]).astype(np.float32)


def prep_phase(nc, vecs, w_up, a_up, g_up, zf_dram, starts, head_ones, arr_dram):
    with Phase(nc, "prep") as ph:
        vec = ph.sb("vec", [P, VEC_N])
        ups = ph.sb("ups", [P, 3, RC])
        up = ph.sb("up", [P, 3, P])
        go = ph.sb("go", [P, 2, T])
        ones = ph.sb("ones", [P, P])
        low = ph.sb("low", [P, 3, T])
        rkv = ph.sb("rkv", [P, 2, 3, T])
        a = ph.sb("a", [P, 2, T])
        s = ph.sb("s", [P, 2, T])
        t1 = ph.sb("t1", [P, T])
        t2 = ph.sb("t2", [P, T])
        nrm = ph.sb("nrm", [P, T])
        kmix = ph.sb("kmix", [P, 2, T])
        onek = ph.sb("onek", [P, RJ])
        out = ph.sb("out", [P, 2, 9, T])
        pw = [ph.ps(f"pw{n}", [P, T]) for n in range(4)]
        names = "up_ready sq_ready ss_psum nrm_a g_psum g_a w_psum w_a a_psum a_a d_done bt_ready bonus_psum bonus_v".split()
        (up_ready, sq_ready, ss_psum, nrm_a, g_psum, g_a, w_psum, w_a, a_psum, a_a, d_done, bt_ready,
         bonus_psum, bonus_v) = [ph.sem(n) for n in names]
        z_in = [ph.sem(f"z_in{u}") for u in range(2)]
        arr_out = [ph.sem(f"arr_out{u}") for u in range(2)]
        consts = ph.sem("consts")
        low_a = ph.sem("low_a")
        V, G, A, E, S = (ph.engine(e, n) for e, n in ((nc.vector, "dve"), (nc.gpsimd, "pool"), (nc.scalar, "act"),
                                                      (nc.tensor, "pe"), (nc.sync, "sp")))
        at = lambda n: vec_at(n)[0]
        zf_view = zf_dram.rearrange("(k p) t -> p k t", p=P)
        arr_view = arr_dram.rearrange("a (k p) t -> p a k t", p=P)
        OUT = ["nkk", "b0", "b1", "kd0", "kd1", "L0", "L1", "g", "bonus"]

        with nc.Block() as block:

            @block.sync
            def _(sp):
                S.open(*arr_out, n=16 * 11)
                for dst, src in ((vec[:, :], vecs), (go[:, :, :], starts), (ones[:, :], head_ones),
                                 (ups[:, 0, :], w_up[0].rearrange("d r c -> (d r) c")),
                                 (ups[:, 1, :], a_up[0].rearrange("d r c -> (d r) c")), (ups[:, 2, :], g_up[0]),
                                 (low[:, :, :], zf_view[:, 12:15, :])):
                    sp.dma_start(dst, src).then_inc(consts, 16)
                with sp.Fori(0, RJ // 2) as n:
                    for u in range(2):
                        j = n * 2 + u
                        S.hold(z_in[u], n * 16 + 16)
                        sp.dma_start(arr_view[:, 0, ds(j, 1), :], rkv[:, u, 0:1, :]).then_inc(arr_out[u], 16)
                        sp.dma_start(arr_view[:, 1, ds(j, 1), :], rkv[:, u, 2:3, :]).then_inc(arr_out[u], 16)
                        S.hold(bonus_v, j + 3)
                        S.hold(g_a, now(j))
                        for m, name in enumerate(OUT):
                            sp.dma_start(arr_view[:, ARR[name], ds(j, 1), :], out[:, u, m:m + 1, :]).then_inc(arr_out[u], 16)
                for u in range(2):
                    sp.wait_ge(arr_out[u], 16 * 11 * (RJ // 2 + 1))

            @block.gpsimd
            def _(pool):
                G.open(up_ready)
                pool.wait_ge(consts, 7 * 16)
                with pool.Fori(0, RJ // 2) as n:
                    for u in range(2):
                        j = n * 2 + u
                        G.hold(bonus_v, j + 1)
                        G.hold(arr_out[u], last(n, 16 * 11))
                        pool.dma_start(rkv[:, u, :, :], zf_view[:, 0:3 * RJ, :].rearrange("p (a j) t -> p a j t", j=RJ)[:, :, ds(j, 1), :].rearrange("p a o t -> p (a o) t")).then_inc(z_in[u], 16)
                        G.hold(a_psum, last(j, 2))
                        nc.gpsimd.tensor_copy(up[:, :, :], ups[:, :, ds(j * P, P)]).then_inc(up_ready, 1)

            @block.scalar
            def _(act):
                A.open(nrm_a, g_a)
                A.open(w_a, a_a, n=2)
                act.wait_ge(consts, 7 * 16)
                nc.scalar.activation(low[:, 0, :], low[:, 0, :], ACT.Tanh).then_inc(low_a, 1)
                nc.scalar.activation(low[:, 2, :], low[:, 2, :], ACT.Sigmoid).then_inc(low_a, 1)
                with act.Fori(0, RJ // 2) as n:
                    for u in range(2):
                        j = n * 2 + u
                        A.hold(ss_psum, now(j))
                        nc.scalar.activation(nrm[:, :], pw[0][:, :], ACT.Sqrt).then_inc(nrm_a, 1)
                        A.hold(g_psum, now(j))
                        A.hold(arr_out[u], last(n, 16 * 11))
                        nc.scalar.copy(out[:, u, 7, :], pw[1][:, :]).then_inc(g_a, 1)
                        for d in range(2):
                            A.hold(w_psum, now(j, 2, d + 1))
                            A.hold(d_done, last(j, 2, d + 1))
                            nc.scalar.activation(s[:, d, :], pw[2 - 2 * d][:, :], ACT.Sigmoid, bias=vec[:, ds(j + (at("w0") + 4 * d), 1)]).then_inc(w_a, 1)
                            A.hold(a_psum, now(j, 2, d + 1))
                            nc.scalar.activation(a[:, d, :], pw[3 - 2 * d][:, :], ACT.Sigmoid, bias=vec[:, ds(j + (at("a0") + 4 * d), 1)]).then_inc(a_a, 1)

            @block.tensor
            def _(pe):
                E.open(ss_psum, g_psum, bonus_psum)
                E.open(w_psum, a_psum, n=2)
                pe.wait_ge(consts, 7 * 16)
                pe.wait_ge(low_a, 2)

                def two(ps, lhsT, rhs, sem):
                    for half in range(2):
                        m = nc.tensor.matmul(ps[:, half * HALF:(half + 1) * HALF], lhsT, rhs[:, half * HALF:(half + 1) * HALF], start=True, stop=True)
                    m.then_inc(sem, 1)

                with pe.Fori(0, RJ // 2) as n:
                    for u in range(2):
                        j = n * 2 + u
                        E.hold(sq_ready, now(j))
                        E.hold(w_a, last(j, 2))
                        two(pw[0], ones[:, :], t2, ss_psum)
                        E.hold(up_ready, now(j))
                        E.hold(a_a, last(j, 2))
                        two(pw[1], up[:, 2, :], low[:, 2, :], g_psum)
                        for d in range(2):
                            lo = slice(64 * d, 64 * d + 64)
                            if d == 0:
                                E.hold(bonus_v, j + 2)
                            else:
                                E.hold(nrm_a, now(j))
                            two(pw[2 - 2 * d], up[lo, 0, :], low[lo, 0, :], w_psum)
                            if d:
                                E.hold(g_a, now(j))
                            else:
                                E.hold(a_a, last(j, 2))
                            two(pw[3 - 2 * d], up[lo, 1, :], low[lo, 1, :], a_psum)
                        E.hold(bt_ready, now(j))
                        E.hold(w_a, now(j, 2))
                        two(pw[2], ones[:, :], t1, bonus_psum)

            @block.vector
            def _(dve):
                V.open(sq_ready, bt_ready)
                V.open(bonus_v, n=2)
                V.open(d_done, n=2)
                dve.wait_ge(consts, 7 * 16)
                ka, rk, kkv = at("k_a"), at("r_k"), at("k_k")
                V.link(nc.vector.tensor_scalar(onek[:, :], vec[:, ka:ka + RJ], -1.0, 1.0, ALU.mult, ALU.add))
                with dve.Fori(0, RJ // 2) as n:
                    V.loop(n, 22)
                    for u in range(2):
                        j = n * 2 + u
                        V.hold(z_in[u], n * 16 + 16)
                        V.hold(arr_out[u], last(n, 16 * 11))
                        V.hold(bonus_psum, last(j))
                        r_, k_, v_ = (rkv[:, u, m, :] for m in range(3))
                        V.link(nc.vector.tensor_scalar(t1[:, :], k_, vec[:, ds(j + kkv, 1)], None, ALU.mult))
                        nc.vector.tensor_tensor(t2[:, :], t1[:, :], t1[:, :], ALU.mult).then_inc(sq_ready, 1)
                        V.hold(nrm_a, now(j))
                        V.link(nc.vector.tensor_scalar(nrm[:, :], nrm[:, :], 1e-12, -1.0, ALU.max, ALU.mult))
                        V.link(nc.vector.reciprocal(nrm[:, :], nrm[:, :]))
                        V.link(nc.vector.tensor_tensor(out[:, u, 0, :], t1[:, :], nrm[:, :], ALU.mult))
                        for d in range(2):
                            V.hold(w_a, now(j, 2, d + 1))
                            step = slice(None) if d == 0 else slice(None, None, -1)
                            nc.vector.tensor_tensor_scan(out[:, u, 5 + d, step], go[:, d, step], s[:, d, step], 0.0, ALU.mult, ALU.add)
                            V.hold(a_a, now(j, 2, d + 1))
                            V.link(nc.vector.tensor_scalar(kmix[:, d, :], a[:, d, :], vec[:, ds(j + ka, 1)], onek[:, ds(j, 1)], ALU.mult, ALU.add))
                            nc.vector.scalar_tensor_tensor(out[:, u, 1 + d, :], out[:, u, 0, :], -1.0, a[:, d, :], ALU.mult, ALU.mult)
                            V.link(nc.vector.tensor_tensor(out[:, u, 3 + d, :], kmix[:, d, :], k_, ALU.mult))
                            dve.sem_inc(d_done, 1)
                        V.link(nc.vector.tensor_tensor(t1[:, :], out[:, u, 3, :], out[:, u, 4, :], ALU.add))
                        V.link(nc.vector.scalar_tensor_tensor(t2[:, :], t1[:, :], vec[:, ds(j + rk, 1)], r_, ALU.mult, ALU.mult))
                        nc.vector.tensor_copy(t1[:, :], t2[:, :]).then_inc(bt_ready, 1)
                        V.hold(bonus_psum, now(j))
                        V.link(nc.vector.tensor_tensor(out[:, u, 8, :], pw[2][:, :], v_, ALU.mult))
                        dve.sem_inc(bonus_v, 1)
                V.done(RJ // 2)


LEVELS = (1, 2, 4, 8, 16, 32)


def wkv_tables():
    t = np.arange(C)
    r, c = t[:, None], t[None, :]
    masks = []
    for b in LEVELS:
        later, earlier = (r // b) % 2 == 1, (c // b) % 2 == 0
        masks.append((r // (2 * b) == c // (2 * b)) & later & earlier)
    masks.append(masks[0].T)
    masks.append(r < c)
    masks.append(r <= c)
    both = np.stack([np.stack([m, m.T]) for m in masks])
    both = both.transpose(2, 0, 1, 3).astype(np.float32)
    eye = np.broadcast_to(np.eye(C, dtype=np.float32)[:, None], (C, 2, C))
    one = np.concatenate([both.reshape(C, -1), eye.reshape(C, -1)], axis=1)
    return np.ascontiguousarray(np.concatenate([one, one]))


N_MASKS = len(LEVELS) + 3


def wkv_phase(nc, tables, arr_dram, y_dram):
    W = 2 * RJ * C
    NA = 6
    NL = len(LEVELS) - 1
    NG, NV, NK = 8, 5, 4
    IN = 16 * 2 * NA
    with Phase(nc, "wkv") as ph:
        def two(name):
            return [ph.sb(f"{name}{v}", [P, W]) for v in range(2)]

        tab = ph.sb("tab", [P, (N_MASKS + 1) * 2 * C])
        inp = [ph.sb(f"inp{v}", [P, NA, W]) for v in range(2)]
        ex = ph.sb("ex", [P, W])
        inv = ph.sb("inv", [P, W])
        at, rt, bh, kh, ak, rb, rk, bt, kt, vt, Z = (two(n) for n in "at rt bh kh ak rb rk bt kt vt Z".split())
        a_raw = ph.sb("a_raw", [P, W])
        a_l = ph.sb("a_l", [P, NL, W])
        x1 = ph.sb("x1", [P, 2, W])
        X = ph.sb("X", [P, W])
        Q = ph.sb("Q", [P, W])
        pp = ph.sb("pp", [P, W])
        uu = ph.sb("uu", [P, W])
        st = ph.sb("st", [P, W])
        st1 = ph.sb("st1", [P, W])
        dec = ph.sb("dec", [P, 2, 2 * RJ])
        yy = ph.sb("yy", [P, W])
        bX, bZ, bQ, b3, b4, b5, b6, b7 = [ph.ps(f"b{n}", [P, W]) for n in range(8)]

        names = ("exps operands g_v g_a a_masked q_psum q_kept xz_psum xz_kept p_psum p_kept u_psum u_kept "
                 "y_psum y_kept y_out s_psum s_kept grams tabs st0").split()
        (exps, operands, g_v, g_a, a_masked, q_psum, q_kept, xz_psum, xz_kept, p_psum, p_kept, u_psum, u_kept,
         y_psum, y_kept, y_out, s_psum, s_kept, grams, tabs, st0) = [ph.sem(n) for n in names]
        in_done = [ph.sem(f"in_done{v}") for v in range(2)]
        V, G, A, E, S = (ph.engine(e, n) for e, n in ((nc.vector, "dve"), (nc.gpsimd, "pool"), (nc.scalar, "act"),
                                                      (nc.tensor, "pe"), (nc.sync, "sp")))

        def mask(n):
            return tab[:, n * 2 * C:(n + 1) * 2 * C].rearrange("p (d c) -> p d c", d=2).unsqueeze(2).to_broadcast([P, 2, RJ, C])

        def grid(a):
            return a.rearrange("p (d j c) -> p d j c", d=2, j=RJ)

        def unit(t, p, n):
            return t[64 * p:64 * p + 64, n * C:(n + 1) * C]

        arr_view = arr_dram.rearrange("a (j p) t -> p a j t", p=P)
        y_view = y_dram.rearrange("d (j p) t -> p d j t", p=P)

        def turns(eng, E_, turn, links):
            turn(0, 0, 0, True, False, True)
            with eng.Fori(0, (NCH - 2) // 2) as n:
                E_.loop(n, 2 * links)
                turn(n * 2 + 1, 1, n, True, True, True)
                turn(n * 2 + 2, 0, n + 1, True, True, True)
            E_.done((NCH - 2) // 2)
            turn(NCH - 1, 1, NCH // 2 - 1, True, True, False)
            turn(NCH, 0, NCH // 2, False, True, False)

        with nc.Block() as block:

            @block.sync
            def _(sp):
                S.open(y_out, n=32)
                sp.dma_start(tab[:, :], tables).then_inc(tabs, 16)

                def load(i, v):
                    for d in range(2):
                        cols = ds(i * C, C) if d == 0 else ds(i * (-C) + (T - C), C)
                        for n, name in enumerate(("r", "v", "nkk", f"b{d}", f"kd{d}", f"L{d}")):
                            sp.dma_start(grid(inp[v][:, n, :])[:, d, :, :], arr_view[:, ARR[name], :, cols]).then_inc(in_done[v], 16)

                def turn(i, v, q, a, b, more):
                    if more:
                        if b:
                            S.hold(operands, last(i))
                            S.hold(exps, last(i))
                            S.hold(grams, last(i, NG))
                        load(i + 1, 1 - v)
                    if b:
                        S.hold(y_kept, i + 1)
                        for d in range(2):
                            cols = ds(i * C - C, C) if d == 0 else ds(i * (-C) + T, C)
                            sp.dma_start(y_view[:, d, :, cols], grid(yy[:, :])[:, d, :, :]).then_inc(y_out, 16)

                load(0, 0)
                turns(sp, S, turn, 0)
                sp.wait_ge(y_out, 32 * (NCH + 1))

            @block.gpsimd
            def _(pool):
                G.open(a_masked, n=NL)
                pool.wait_ge(tabs, 16)
                with pool.Fori(0, NCH) as i:
                    G.hold(g_a, now(i, NK, 1))
                    for n in range(NL):
                        G.hold(q_psum, last(i, NL, n + 1))
                        nc.gpsimd.tensor_tensor(grid(a_l[:, n, :]), grid(a_raw[:, :]), mask(n + 1), ALU.mult).then_inc(a_masked, 1)

            @block.scalar
            def _(act):
                A.open(exps, p_kept, u_kept, y_kept)
                A.open(g_a, n=NK)
                A.open(q_kept, n=NL)

                def turn(i, v, q, a, b, more):
                    o = 1 - v

                    def keep_q(n):
                        A.hold(q_psum, now(i, NL, n + 1))
                        A.hold(xz_psum, now(i, NL, n) if n else last(i, NL))
                        nc.scalar.copy(Q[:, :], bQ[:, :]).then_inc(q_kept, 1)

                    def keep(dst, src, gram):
                        A.hold(grams, now(i, NG, gram))
                        if b:
                            A.hold(s_psum, i)
                        nc.scalar.copy(dst[:, :], src[:, :]).then_inc(g_a, 1)

                    if a:
                        A.hold(grams, now(i, NG, 1))
                        A.hold(a_masked, last(i, NL))
                        nc.scalar.copy(a_raw[:, :], bX[:, :]).then_inc(g_a, 1)
                    if b:
                        A.hold(p_psum, i + 1)
                        A.hold(u_psum, i)
                        nc.scalar.copy(pp[:, :], b4[:, :]).then_inc(p_kept, 1)
                    if a:
                        keep_q(0)
                    if b:
                        A.hold(u_psum, i + 1)
                        A.hold(s_psum, i)
                        nc.scalar.copy(uu[:, :], b5[:, :]).then_inc(u_kept, 1)
                    if a:
                        keep_q(1)
                        keep(bt[v], b3, 6)
                    if more:
                        A.hold(in_done[o], (q + v + 1) * IN)
                        A.hold(operands, now(i))
                        nc.scalar.activation(ex[:, :], inp[o][:, 5, :], ACT.Exp, scale=-W_SCALE)
                    if a:
                        keep(kt[v], b4, 7)
                        keep_q(2)
                    if more:
                        nc.scalar.activation(inv[:, :], inp[o][:, 5, :], ACT.Exp, scale=W_SCALE).then_inc(exps, 1)
                    if b:
                        A.hold(y_psum, i + 1)
                        A.hold(y_out, i * 32)
                        nc.scalar.copy(yy[:, :], b6[:, :]).then_inc(y_kept, 1)
                    if a:
                        keep_q(3)
                        keep(vt[v], b5, 8)
                        keep_q(4)

                act.wait_ge(in_done[0], IN)
                nc.scalar.activation(ex[:, :], inp[0][:, 5, :], ACT.Exp, scale=-W_SCALE)
                nc.scalar.activation(inv[:, :], inp[0][:, 5, :], ACT.Exp, scale=W_SCALE).then_inc(exps, 1)
                turns(act, A, turn, 0)

            @block.vector
            def _(dve):
                V.open(operands, s_kept)
                V.open(g_v, n=NV)
                V.open(xz_kept, n=NL)

                def inverse_decayed(v):
                    nc.vector.tensor_tensor(bh[v][:, :], inp[v][:, 3, :], inv[:, :], ALU.mult)
                    nc.vector.tensor_tensor(kh[v][:, :], inp[v][:, 4, :], inv[:, :], ALU.mult)

                def decayed_a(v):
                    ge, ga, gi = grid(ex[:, :]), grid(at[v][:, :]), grid(inp[v][:, 2, :])
                    nc.vector.tensor_tensor(ga[:, 0, :, 1:C], gi[:, 0, :, 1:C], ge[:, 0, :, 0:C - 1], ALU.mult)
                    nc.vector.tensor_tensor(ga[:, 1, :, 0:C - 1], gi[:, 1, :, 0:C - 1], ge[:, 1, :, 1:C], ALU.mult)
                    nc.vector.tensor_copy(ga[:, 0, :, 0:1], gi[:, 0, :, 0:1])
                    nc.vector.tensor_copy(ga[:, 1, :, C - 1:C], gi[:, 1, :, C - 1:C])

                def decayed_r(v):
                    ge = grid(ex[:, :])
                    nc.vector.tensor_copy(dec[:, v, 0:RJ], ge[:, 0, :, C - 1])
                    nc.vector.tensor_copy(dec[:, v, RJ:2 * RJ], ge[:, 1, :, 0])
                    nc.vector.tensor_tensor(rt[v][:, :], inp[v][:, 0, :], ex[:, :], ALU.mult).then_inc(operands, 1)

                def turn(i, v, q, a, b, more):
                    o = 1 - v

                    def level(n):
                        V.hold(xz_psum, now(i, NL, n + 1))
                        if n < NL - 1:
                            nc.vector.tensor_tensor(X[:, :], X[:, :], bX[:, :], ALU.add)
                        nc.vector.tensor_tensor(Z[v][:, :], Z[v][:, :], bZ[:, :], ALU.add).then_inc(xz_kept, 1)
                        V.hold(xz_kept, now(i, NL, n + 1))

                    def masked(dst, src, gram, m):
                        V.hold(grams, now(i, NG, gram))
                        nc.vector.tensor_tensor(grid(dst[:, :]), grid(src[:, :]), mask(m), ALU.mult).then_inc(g_v, 1)

                    if a:
                        V.hold(g_a, now(i, NK, 1))
                        V.hold(xz_psum, last(i, NL))
                        masked(x1[:, 0, :], bX, 1, 0)
                        V.hold(grams, now(i, NG, 2))
                        V.link(nc.vector.tensor_tensor(grid(x1[:, 1, :]), grid(bZ[:, :]), mask(NL + 1), ALU.mult))
                        eye = mask(N_MASKS)
                        nc.vector.tensor_tensor(grid(X[:, :]), grid(x1[:, 0, :]), eye, ALU.add)
                        if b:
                            V.hold(u_psum, i)
                        nc.vector.tensor_tensor(grid(Z[v][:, :]), grid(x1[:, 1, :]), eye, ALU.add).then_inc(g_v, 1)
                        if b:
                            V.hold(y_psum, i)
                        masked(ak[v], b3, 3, NL + 2)
                        masked(rb[v], b6, 4, NL + 3)
                        masked(rk[v], b7, 5, NL + 3)
                        V.hold(g_v, now(i, NV, 2))
                        level(0)
                        level(1)
                        level(2)
                    if more:
                        V.hold(exps, now(i + 1))
                        if b:
                            V.hold(grams, last(i, NG))
                            V.hold(p_psum, i + 1)
                        inverse_decayed(o)
                        decayed_a(o)
                    if a:
                        level(3)
                    if b:
                        V.hold(s_psum, i + 1)
                        V.link(nc.vector.tensor_tensor(st1[:, :], st[:, :], b7[:, :], ALU.add))
                        V.link(nc.vector.tensor_tensor(st[:, :].rearrange("p (n c) -> p n c", c=C), st1[:, :].rearrange("p (n c) -> p n c", c=C),
                                                       dec[:, o, :].unsqueeze(2).to_broadcast([P, 2 * RJ, C]), ALU.mult))
                        dve.sem_inc(s_kept, 1)
                    if more:
                        if b:
                            V.hold(y_psum, i + 1)
                        decayed_r(o)
                    if a:
                        level(4)

                dve.wait_ge(tabs, 16)
                V.link(nc.vector.memset(st[:, :], 0.0))
                dve.sem_inc(st0, 1)
                dve.wait_ge(exps, 2)
                inverse_decayed(0)
                decayed_a(0)
                decayed_r(0)
                turns(dve, V, turn, 3)

            @block.tensor
            def _(pe):
                E.open(p_psum, u_psum, y_psum, s_psum)
                E.open(grams, n=NG)
                E.open(q_psum, xz_psum, n=NL)
                pe.wait_ge(tabs, 16)
                pe.wait_ge(st0, 1)
                units = [(p, n) for n in range(2 * RJ) for p in range(2)]
                eye = tab[:, N_MASKS * 2 * C:N_MASKS * 2 * C + C]

                def product(dst, pairs, some=slice(None)):
                    for p, n in units[some]:
                        for k, (lhsT, rhs) in enumerate(pairs):
                            right = rhs[64 * p:64 * p + 64, :] if rhs is eye else unit(rhs, p, n)
                            m = nc.tensor.matmul(unit(dst, p, n), unit(lhsT, p, n), right, start=k == 0, stop=k == len(pairs) - 1)
                    return m

                first, second = slice(0, 8), slice(8, 16)

                def turn(i, v, q, a, b, more):
                    o = 1 - v

                    def gram(dst, lhsT, rhs):
                        product(dst, [(lhsT, rhs)]).then_inc(grams, 1)

                    def blocks(n):
                        if a:
                            if n == 0:
                                E.hold(g_v, now(i, NV, 2))
                            else:
                                E.hold(xz_kept, now(i, NL, n))
                            E.hold(a_masked, now(i, NL, n + 1))
                            product(bQ, [(a_l[:, n, :], Z[v])]).then_inc(q_psum, 1)

                    def extend(n):
                        if a:
                            E.hold(q_kept, now(i, NL, n + 1))
                            if n < NL - 1:
                                product(bX, [(Q, X)])
                            product(bZ, [(X, Q)]).then_inc(xz_psum, 1)

                    outputs = [(st, rt[o]), (uu, rb[o]), (vt[o], rk[o])]
                    update = [(bt[o], uu), (kt[o], vt[o])]
                    if a:
                        E.hold(operands, now(i))
                        E.hold(xz_kept, last(i, NL))
                        gram(bX, at[v], bh[v])
                        gram(bZ, bh[v], at[v])
                        E.hold(g_a, last(i, NK))
                        gram(b3, kh[v], at[v])
                        if b:
                            E.hold(y_kept, i)
                        gram(b6, bh[v], rt[v])
                    if b:
                        E.hold(s_kept, i)
                        E.hold(g_v, last(i, NV))
                        E.hold(g_a, last(i, NK))
                        product(b4, [(at[o], st), (ak[o], vt[o])]).then_inc(p_psum, 1)
                    blocks(0)
                    if a:
                        gram(b7, kh[v], rt[v])
                    extend(0)
                    if b:
                        E.hold(p_kept, i + 1)
                        E.hold(xz_kept, last(i, NL))
                        product(b5, [(Z[o], pp)]).then_inc(u_psum, 1)
                    blocks(1)
                    if a:
                        E.hold(g_v, now(i, NV, 3))
                        gram(b3, bh[v], eye)
                    extend(1)
                    if a:
                        gram(b4, kh[v], eye)
                    blocks(2)
                    if b:
                        E.hold(u_kept, i + 1)
                        if a:
                            E.hold(g_v, now(i, NV, NV))
                        else:
                            E.hold(y_kept, i)
                        product(b6, outputs, first)
                    extend(2)
                    if b:
                        product(b6, outputs, second).then_inc(y_psum, 1)
                    blocks(3)
                    if b:
                        product(b7, update, first)
                    extend(3)
                    if a:
                        if b:
                            E.hold(u_kept, i + 1)
                        gram(b5, inp[v][:, 1, :], eye)
                    blocks(4)
                    if b:
                        product(b7, update, second).then_inc(s_psum, 1)
                    extend(4)

                turns(pe, E, turn, 0)


LNX_EPS = 64e-5
GATE_AT = MLA_IN + RWKV_TILES * P


def mix_phase(nc, vecs, w_in, w_br_mla, w_br_rwkv, head_ones, hT, oT_dram, arr_dram, y_dram, mixT_dram):
    with Phase(nc, "mix") as ph:
        vec = ph.sb("vec", [P, VEC_N])
        ones = ph.sb("ones", [P, P])
        oT = ph.sb("oT", [P, 2 * RJ, T])
        inp = ph.sb("inp", [P, 4, T])
        y = ph.sb("y", [P, T])
        sq = ph.sb("sq", [P, T])
        rt = ph.sb("rt", [P, T])
        wg = ph.sb("wg", [P, 2, 2, KD, P])
        wb = ph.sb("wb", [P, 2, 2, RJ, P])
        sg = ph.sb("sg", [P, 2, KD, T])
        mixed = ph.sb("mixed", [P, 2, T])
        m1 = ph.sb("m1", [P, T])
        pb = [ph.ps(f"pb{n}", [P, T]) for n in range(4)]
        names = "in_done y_sum mean_psum cent sq_ready var_psum root o_ready consts o_in rt_ready z_psum gates br_psum mixed_ready mixed_out".split()
        (in_done, y_sum, mean_psum, cent, sq_ready, var_psum, root, o_ready, consts, o_in, rt_ready, z_psum, gates, br_psum, mixed_ready,
         mixed_out) = [ph.sem(n) for n in names]
        wg_done = [ph.sem(f"wg_done{u}") for u in range(2)]
        wb_done = [ph.sem(f"wb_done{u}") for u in range(2)]
        V, A, E, S = (ph.engine(e, n) for e, n in ((nc.vector, "dve"), (nc.scalar, "act"), (nc.tensor, "pe"), (nc.sync, "sp")))
        at = lambda n: vec_at(n)[0]
        arr_view = arr_dram.rearrange("a (k p) t -> p a k t", p=P)
        y_view = y_dram.rearrange("d (k p) t -> p d k t", p=P)
        mix_view = mixT_dram.rearrange("(k p) t -> p k t", p=P)
        wi = w_in[0].rearrange("(k p) n -> p k n", p=P)
        wa = w_br_mla[0].rearrange("(k p) n -> p k n", p=P)
        wr = w_br_rwkv[0].rearrange("(k p) n -> p k n", p=P)

        with nc.Block() as block:

            @block.sync
            def _(sp):
                S.open(in_done, n=64)
                S.open(mixed_out, n=32)
                for u in range(2):
                    S.open(wg_done[u], wb_done[u], n=32)
                sp.dma_start(vec[:, :], vecs).then_inc(consts, 16)
                sp.dma_start(ones[:, :], head_ones).then_inc(consts, 16)
                with sp.Fori(0, RJ) as j:
                    for u in range(2):
                        S.hold(z_psum, last(j, 4, 2 * u + 2))
                        for b in range(2):
                            sp.dma_start(wg[:, u, b, :, :], wi[:, :, ds(j * (2 * P) + (GATE_AT + b * D + u * P), P)]).then_inc(wg_done[u], 16)
                    S.hold(o_ready, last(j))
                    for n in range(2):
                        sp.dma_start(inp[:, n:n + 1, :], y_view[:, n, ds(j, 1), :]).then_inc(in_done, 16)
                    sp.dma_start(inp[:, 2:3, :], arr_view[:, ARR["bonus"], ds(j, 1), :]).then_inc(in_done, 16)
                    sp.dma_start(inp[:, 3:4, :], arr_view[:, ARR["g"], ds(j, 1), :]).then_inc(in_done, 16)
                sp.dma_start(oT[:, 0:RJ, :], oT_dram.rearrange("(k p) t -> p k t", p=P)).then_inc(o_in, 16)
                with sp.Fori(0, KD // 2) as i:
                    for u in range(2):
                        S.hold(br_psum, last(i, 2, u + 1))
                        for b, src in enumerate((wa, wr)):
                            sp.dma_start(wb[:, u, b, :, :], src[:, :, ds(i * (2 * P) + u * P, P)]).then_inc(wb_done[u], 16)
                        if u:
                            S.hold(mixed_ready, now(i, 2, u))
                            sp.dma_start(mix_view[:, ds(i * 2, 1), :], mixed[:, 0:1, :]).then_inc(mixed_out, 16)
                    S.hold(mixed_ready, now(i, 2, 2))
                    sp.dma_start(mix_view[:, ds(i * 2 + 1, 1), :], mixed[:, 1:2, :]).then_inc(mixed_out, 16)
                sp.wait_ge(mixed_out, 16 * (KD + 2))

            @block.tensor
            def _(pe):
                E.open(mean_psum, var_psum)
                E.open(br_psum, n=2)
                E.open(z_psum, n=4)
                pe.wait_ge(consts, 32)

                def two(ps, lhsT, rhs):
                    for half in range(2):
                        m = nc.tensor.matmul(ps[:, half * HALF:(half + 1) * HALF], lhsT, rhs[:, half * HALF:(half + 1) * HALF], start=True, stop=True)
                    return m

                def many(ps, weights, n, rhs):
                    for half in range(2):
                        for k in range(n):
                            m = nc.tensor.matmul(ps[:, half * HALF:(half + 1) * HALF], weights[:, k, :],
                                                 rhs[:, k, half * HALF:(half + 1) * HALF], start=k == 0, stop=k == n - 1)
                    return m

                with pe.Fori(0, RJ) as j:

                    def gate(u, b):
                        if b == 0:
                            E.hold(wg_done[u], now(j, 32))
                        E.hold(gates, now(j, 4, 2 * u + b - 1) if u else last(j, 4, 3 + b))
                        many(pb[2 + b], wg[:, u, b, :, :], KD, hT).then_inc(z_psum, 1)

                    gate(0, 0)
                    E.hold(y_sum, now(j))
                    two(pb[0], ones[:, :], y).then_inc(mean_psum, 1)
                    gate(0, 1)
                    E.hold(sq_ready, now(j))
                    two(pb[1], ones[:, :], sq).then_inc(var_psum, 1)
                    gate(1, 0)
                    gate(1, 1)
                E.hold(o_ready, RJ + 1)
                E.hold(gates, 4 * (RJ + 1))
                pe.wait_ge(o_in, 16)
                with pe.Fori(0, KD // 2) as i:
                    for u in range(2):
                        E.hold(wb_done[u], now(i, 32))
                        E.hold(mixed_ready, last(i, 2, u + 1))
                        many(pb[2 * u], wb[:, u, 0, :, :], RJ, oT)
                        many(pb[2 * u + 1], wb[:, u, 1, :, :], RJ, oT[:, RJ:2 * RJ, :]).then_inc(br_psum, 1)

            @block.scalar
            def _(act):
                A.open(root, sq_ready)
                A.open(gates, n=4)
                act.wait_ge(consts, 32)
                with act.Fori(0, RJ) as j:

                    def gate(u, b):
                        A.hold(z_psum, now(j, 4, 2 * u + b + 1))
                        nc.scalar.activation(sg[:, b, ds(j * 2 + u, 1), :].rearrange("p o t -> p (o t)"), pb[2 + b][:, :], ACT.Sigmoid,
                                             bias=vec[:, ds(j * 2 + (at("gate_b") + b * KD + u), 1)]).then_inc(gates, 1)

                    A.hold(z_psum, now(j, 4, 1))
                    gate(0, 0)
                    A.hold(cent, now(j))
                    A.hold(var_psum, last(j))
                    nc.scalar.activation(sq[:, :], y[:, :], ACT.Square).then_inc(sq_ready, 1)
                    gate(0, 1)
                    A.hold(rt_ready, now(j))
                    nc.scalar.activation(rt[:, :], rt[:, :], ACT.Sqrt).then_inc(root, 1)
                    gate(1, 0)
                    gate(1, 1)

            @block.vector
            def _(dve):
                V.open(y_sum, cent, o_ready, rt_ready)
                V.open(mixed_ready, n=2)
                dve.wait_ge(consts, 32)
                with dve.Fori(0, RJ) as j:
                    V.loop(j, 5)
                    V.hold(in_done, now(j, 64))
                    nc.vector.tensor_tensor(y[:, :], inp[:, 0, :], inp[:, 1, :], ALU.add).then_inc(y_sum, 1)
                    V.hold(mean_psum, now(j))
                    nc.vector.scalar_tensor_tensor(y[:, :], pb[0][:, :], -1.0 / 64, y[:, :], ALU.mult, ALU.add).then_inc(cent, 1)
                    V.hold(var_psum, now(j))
                    nc.vector.tensor_scalar(rt[:, :], pb[1][:, :], 1.0 / 64, LNX_EPS, ALU.mult, ALU.add).then_inc(rt_ready, 1)
                    V.hold(root, now(j))
                    V.link(nc.vector.reciprocal(rt[:, :], rt[:, :]))
                    V.link(nc.vector.tensor_tensor(y[:, :], y[:, :], rt[:, :], ALU.mult))
                    V.link(nc.vector.tensor_scalar(y[:, :], y[:, :], vec[:, ds(j + at("lnx_g"), 1)], vec[:, ds(j + at("lnx_b"), 1)], ALU.mult, ALU.add))
                    V.link(nc.vector.tensor_tensor(y[:, :], y[:, :], inp[:, 2, :], ALU.add))
                    V.link(nc.vector.tensor_tensor(oT[:, ds(j + RJ, 1), :].rearrange("p o t -> p (o t)"), y[:, :], inp[:, 3, :], ALU.mult))
                    dve.sem_inc(o_ready, 1)
                V.done(RJ)
                dve.wait_ge(gates, 4 * (RJ + 1))
                with dve.Fori(0, KD // 2) as i:
                    V.loop(i, 4)
                    for u in range(2):
                        V.hold(br_psum, now(i, 2, u + 1))
                        V.hold(mixed_out, last(i, 32, 16 * (u + 1)))
                        for b, dst in enumerate((mixed[:, u, :], m1[:, :])):
                            r = nc.vector.tensor_tensor(dst, pb[2 * u + b][:, :], sg[:, b, ds(i * 2 + u, 1), :].rearrange("p o t -> p (o t)"), ALU.mult)
                        V.link(r)
                        V.link(nc.vector.tensor_tensor(mixed[:, u, :], mixed[:, u, :], m1[:, :], ALU.add))
                        dve.sem_inc(mixed_ready, 1)
                V.done(KD // 2)


N_GROUPS, PER_GROUP = 4, 8
N_EXP = N_GROUPS * PER_GROUP
MOE_BLOCKS = 2 * T // P + N_EXP
SLOTS = MOE_BLOCKS * P
LOGITS = N_GROUPS + N_EXP


def route_tables():
    t = np.arange(P)
    before = (t[:, None] < t[None, :]).astype(np.float32)
    row = np.concatenate([8.0 - np.arange(8), 128.0 * np.arange(8), 128.0 * np.arange(MOE_BLOCKS)])
    tok = (np.arange(NT)[None, :] * P + t[:, None])
    return np.ascontiguousarray(np.concatenate([before, np.ones((P, P)), np.broadcast_to(row, (P, row.size))], axis=1).astype(np.float32)), \
        np.ascontiguousarray(tok.astype(np.uint32))


def route_phase(nc, x, vecs, w_out, rg_w, rg_b, re_w, re_b, eye, tables, tok_ids, mixT_dram, x1_dram, h2_dram, slot_tok, keep):
    slot_u, wts, block_e, pair_used = keep
    with Phase(nc, "route") as ph:
        ident = ph.sb("ident", [P, P])
        vec = ph.sb("vec", [P, VEC_N])
        wo = ph.sb("wo", [P, KD, D])
        rw = ph.sb("rw", [P, KD, LOGITS])
        rb = ph.sb("rb", [P, LOGITS])
        mT = ph.sb("mT", [P, KD, T])
        m_t = ph.sb("m_t", [P, KD, P])
        xt = ph.sb("xt", [P, D])
        x1 = ph.sb("x1", [P, D])
        junk = ph.sb("junk", [P, D])
        h2 = ph.sb("h2", [P, D])
        h2T = ph.sb("h2T", [P, KD, P])
        small = ph.sb("small", [P, 4])
        lg = ph.sb("lg", [P, NT, LOGITS])
        tab = ph.sb("tab", [P, 2 * P + 16 + MOE_BLOCKS])
        tok = ph.sb("tok", [P, NT], U32)
        zero = ph.sb("zero", [P, MOE_BLOCKS + 1], U32)
        gdiff = ph.sb("gdiff", [P, NT, N_GROUPS])
        e21 = ph.sb("e21", [P, NT])
        mem = ph.sb("mem", [P, NT, N_EXP])
        cum = ph.sb("cum", [P, NT + 1, N_EXP])
        gmax = ph.sb("gmax", [P, NT])
        goh = ph.sb("goh", [P, NT, N_GROUPS])
        el = ph.sb("el", [P, NT, N_GROUPS, PER_GROUP])
        sel = ph.sb("sel", [P, NT, PER_GROUP])
        sel2 = ph.sb("sel2", [P, NT, PER_GROUP])
        top = ph.sb("top", [P, 2, NT])
        oh = ph.sb("oh", [P, 2, NT, PER_GROUP])
        ohe = ph.sb("ohe", [P, 2, NT, N_GROUPS, PER_GROUP])
        pref = ph.sb("pref", [P, NT, PER_GROUP])
        pmax = ph.sb("pmax", [P, NT])
        gs = ph.sb("gs", [P, NT])
        rank = ph.sb("rank", [P, NT, N_EXP])
        pick = ph.sb("pick", [P, NT, N_EXP])
        slot_f = ph.sb("slot_f", [P, 2 * NT])
        over = ph.sb("over", [P, N_EXP, PER_GROUP])
        padded = ph.sb("padded", [P, N_EXP])
        pend = ph.sb("pend", [P, N_EXP])
        pstart = ph.sb("pstart", [P, N_EXP])
        cmp = ph.sb("cmp", [P, MOE_BLOCKS, N_EXP])
        be_f = ph.sb("be_f", [P, MOE_BLOCKS])
        po = ph.ps("po", [P, D])
        pt = ph.ps("pt", [P, D])
        pl = ph.ps("pl", [P, HALF])
        pr = ph.ps("pr", [P, HALF])
        names = ("consts x_in m_in xo_psum x1_ready x1_out sq ms root h2_ready h2_out hT_psum hT_ready l_psum l_kept "
                 "members rank_psum exp_in exp_out slots scattered zeroed").split()
        (consts, x_in, m_in, xo_psum, x1_ready, x1_out, sq, ms, root, h2_ready, h2_out, hT_psum, hT_ready, l_psum, l_kept,
         members, rank_psum, exp_in, exp_out, slots, scattered, zeroed) = [ph.sem(n) for n in names]
        V, G, A, E, S = (ph.engine(e, n) for e, n in ((nc.vector, "dve"), (nc.gpsimd, "pool"), (nc.scalar, "act"),
                                                      (nc.tensor, "pe"), (nc.sync, "sp")))
        early, late = ph.sem("early"), ph.sem("late")
        wo_in = [ph.sem(f"wo_in{half}") for half in range(2)]
        g0 = vec_at("norm_ffn_g")[0]
        NCONST = 8
        EARLY = 2 * P

        with nc.Block() as block:

            @block.sync
            def _(sp):
                S.open(x_in, x1_out, h2_out, n=16)
                for dst, src in ((ident[:, :], eye), (vec[:, :], vecs), 
                                 (rw[:, :, 0:N_GROUPS], rg_w[0].rearrange("(k p) n -> p k n", p=P)),
                                 (rw[:, :, N_GROUPS:LOGITS], re_w[0].rearrange("(k p) n -> p k n", p=P)),
                                 (rb[:, 0:N_GROUPS], rg_b[0].partition_broadcast(P)), (rb[:, N_GROUPS:LOGITS], re_b[0].partition_broadcast(P)),
                                 (tab[:, :], tables), (tok[:, :], tok_ids)):
                    sp.dma_start(dst, src).then_inc(consts, 16)
                mix_view = mixT_dram.rearrange("(k p) t -> p k t", p=P)
                sp.dma_start(mT[:, :, 0:EARLY], mix_view[:, :, 0:EARLY]).then_inc(early, 16)
                for half in range(2):
                    sp.dma_start(wo[:, :, half * HALF:(half + 1) * HALF], w_out[0, :, half * HALF:(half + 1) * HALF].rearrange("(k p) n -> p k n", p=P)).then_inc(wo_in[half], 16)
                sp.dma_start(mT[:, :, EARLY:T], mix_view[:, :, EARLY:T]).then_inc(late, 16)
                with sp.Fori(0, NT) as i:
                    S.hold(x1_ready, last(i))
                    sp.dma_start(xt[:, :], x[ds(i * P, P), :]).then_inc(x_in, 16)
                    S.hold(x1_ready, now(i))
                    sp.dma_start(x1_dram[ds(i * P, P), :], x1[:, :]).then_inc(x1_out, 16)
                    S.hold(h2_ready, now(i))
                    sp.dma_start(h2_dram[ds(i * P, P), :], h2[:, :]).then_inc(h2_out, 16)
                sp.wait_ge(x1_out, 16 * (NT + 1))
                sp.wait_ge(h2_out, 16 * (NT + 1))
                sp.wait_ge(zeroed, 1)
                sp.dma_start(slot_tok.rearrange("(p b) o -> p (b o)", p=P), zero[:, :]).then_inc(zeroed, 16)

            @block.gpsimd
            def _(pool):
                G.open(m_in)
                pool.wait_ge(consts, NCONST * 16)
                nc.gpsimd.memset(zero[:, :], 0).then_inc(zeroed, 1)

                def stage(i):
                    G.hold(xo_psum, last(i))
                    nc.gpsimd.tensor_copy(m_t[:, :, :], mT[:, :, ds(i * P, P)]).then_inc(m_in, 1)

                pool.wait_ge(early, 16)
                for i in range(EARLY // P):
                    stage(i)
                pool.wait_ge(late, 16)
                with pool.Fori(EARLY // P, NT) as i:
                    stage(i)
                pool.wait_ge(slots, 1)
                pool.wait_ge(zeroed, 17)
                for n in range(2 * NT):
                    pool.indirect_dma_start(slot_tok, bass.IndirectOffsetOnAxis(ap=slot_u[:, n:n + 1], axis=0),
                                            tok[:, n % NT:n % NT + 1], None).then_inc(scattered, 16)
                pool.wait_ge(scattered, 16 * 2 * NT)

            @block.tensor
            def _(pe):
                E.open(xo_psum, hT_psum, l_psum)
                pe.wait_ge(consts, NCONST * 16)

                def product(i):
                    E.hold(m_in, now(i))
                    E.hold(x1_ready, last(i))
                    for half in range(2):
                        pe.wait_ge(wo_in[half], 16)
                        for k in range(KD):
                            m = nc.tensor.matmul(po[:, half * HALF:(half + 1) * HALF], m_t[:, k, :], wo[:, k, half * HALF:(half + 1) * HALF],
                                                 start=k == 0, stop=k == KD - 1)
                    m.then_inc(xo_psum, 1)

                def turn_h2(i):
                    E.hold(h2_ready, now(i))
                    E.hold(hT_ready, last(i))
                    for k in range(KD):
                        t = nc.tensor.transpose(pt[:, k * P:(k + 1) * P], h2[:, k * P:(k + 1) * P], ident[:, :])
                    t.then_inc(hT_psum, 1)

                def logits(i):
                    E.hold(hT_ready, now(i))
                    E.hold(l_kept, last(i))
                    for k in range(KD):
                        m = nc.tensor.matmul(pl[:, 0:LOGITS], h2T[:, k, :], rw[:, k, :], start=k == 0, stop=k == KD - 1)
                    m.then_inc(l_psum, 1)

                product(0)
                with pe.Fori(0, NT - 1) as n:
                    product(n + 1)
                    turn_h2(n)
                    logits(n)
                turn_h2(NT - 1)
                logits(NT - 1)
                pe.wait_ge(members, 1)
                nc.tensor.matmul(pr[:, 0:NT * N_EXP], tab[:, 0:P], mem[:, :, :], start=True, stop=False)
                nc.tensor.matmul(pr[:, 0:NT * N_EXP], tab[:, P:2 * P], cum[:, 0:NT, :], start=False, stop=True)
                nc.tensor.matmul(pl[:, 0:N_EXP], tab[:, P:2 * P], cum[:, NT, :], start=True, stop=True).then_inc(rank_psum, 1)

            @block.scalar
            def _(act):
                A.open(sq, root)
                with act.Fori(0, NT) as i:
                    A.hold(x1_ready, now(i))
                    nc.scalar.activation(junk[:, :], x1[:, :], ACT.Square, accum_out=small[:, 0:1]).then_inc(sq, 1)
                    A.hold(ms, now(i))
                    nc.scalar.activation(small[:, 2:3], small[:, 1:2], ACT.Sqrt).then_inc(root, 1)
                act.wait_ge(exp_in, 1)
                nc.scalar.activation(gdiff[:, :, :], gdiff[:, :, :], ACT.Exp)
                nc.scalar.activation(e21[:, :], e21[:, :], ACT.Exp).then_inc(exp_out, 1)

            @block.vector
            def _(dve):
                V.open(x1_ready, ms, h2_ready, hT_ready, l_kept)
                dve.wait_ge(consts, NCONST * 16)

                def norm(i):
                    V.hold(x_in, now(i, 16))
                    V.hold(xo_psum, now(i))
                    V.hold(x1_out, last(i, 16))
                    V.hold(sq, last(i))
                    nc.vector.tensor_tensor(x1[:, :], po[:, :], xt[:, :], ALU.add).then_inc(x1_ready, 1)
                    V.hold(sq, now(i))
                    nc.vector.tensor_scalar(small[:, 1:2], small[:, 0:1], 1.0 / D, NORM_EPS, ALU.mult, ALU.add).then_inc(ms, 1)
                    V.hold(root, now(i))
                    V.link(nc.vector.reciprocal(small[:, 3:4], small[:, 2:3]))
                    V.hold(h2_out, last(i, 16))
                    V.hold(hT_psum, last(i))
                    nc.vector.tensor_scalar(h2[:, :], x1[:, :], small[:, 3:4], None, ALU.mult).then_inc(h2_ready, 1)

                def scaled(i):
                    V.hold(hT_psum, now(i))
                    V.hold(l_psum, last(i))
                    nc.vector.tensor_tensor(h2T[:, :, :], pt[:, :].rearrange("p (k t) -> p k t", k=KD),
                                            vec[:, g0:g0 + KD].unsqueeze(2).to_broadcast([P, KD, P]), ALU.mult).then_inc(hT_ready, 1)

                def keep_logits(i):
                    V.hold(l_psum, now(i))
                    nc.vector.tensor_tensor(lg[:, ds(i, 1), :].rearrange("p o n -> p (o n)"), pl[:, 0:LOGITS], rb[:, :], ALU.add).then_inc(l_kept, 1)

                norm(0)
                with dve.Fori(0, NT - 1) as n:
                    V.loop(n, 1)
                    scaled(n)
                    keep_logits(n)
                    norm(n + 1)
                V.done(NT - 1)
                scaled(NT - 1)
                keep_logits(NT - 1)
                dve.wait_ge(l_kept, NT + 1)

                def first_of(out, vals, best, n):
                    V.link(nc.vector.tensor_tensor(out, vals, best.unsqueeze(2).to_broadcast([P, NT, n]), ALU.is_equal))
                    V.link(nc.vector.tensor_tensor(pref[:, :, 0:n], out, tab[:, 2 * P:2 * P + n].unsqueeze(1).to_broadcast([P, NT, n]), ALU.mult))
                    V.link(nc.vector.reduce_max(pmax[:, :], pref[:, :, 0:n], AX_X))
                    V.link(nc.vector.tensor_tensor(out, pref[:, :, 0:n], pmax[:, :].unsqueeze(2).to_broadcast([P, NT, n]), ALU.is_equal))

                gl = lg[:, :, 0:N_GROUPS]
                V.link(nc.vector.reduce_max(gmax[:, :], gl, AX_X))
                first_of(goh[:, :, :], gl, gmax[:, :], N_GROUPS)
                V.link(nc.vector.tensor_tensor(gdiff[:, :, :], gl, gmax[:, :].unsqueeze(2).to_broadcast([P, NT, N_GROUPS]), ALU.subtract))
                for g in range(N_GROUPS):
                    V.link(nc.vector.tensor_tensor(el[:, :, g, :], lg[:, :, N_GROUPS + g * PER_GROUP:N_GROUPS + (g + 1) * PER_GROUP],
                                                   goh[:, :, g:g + 1].to_broadcast([P, NT, PER_GROUP]), ALU.mult))
                V.link(nc.vector.tensor_reduce(sel[:, :, :], el[:, :, :, :].rearrange("p t g e -> p t e g"), AX_X, ALU.add))
                V.link(nc.vector.reduce_max(top[:, 0, :], sel[:, :, :], AX_X))
                first_of(oh[:, 0, :, :], sel[:, :, :], top[:, 0, :], PER_GROUP)
                V.link(nc.vector.scalar_tensor_tensor(sel2[:, :, :], oh[:, 0, :, :], -3e38, sel[:, :, :], ALU.mult, ALU.add))
                V.link(nc.vector.reduce_max(top[:, 1, :], sel2[:, :, :], AX_X))
                first_of(oh[:, 1, :, :], sel2[:, :, :], top[:, 1, :], PER_GROUP)
                V.link(nc.vector.tensor_tensor(e21[:, :], top[:, 1, :], top[:, 0, :], ALU.subtract))
                dve.sem_inc(exp_in, 1)
                for n in range(2):
                    for g in range(N_GROUPS):
                        V.link(nc.vector.tensor_tensor(ohe[:, n, :, g, :], oh[:, n, :, :], goh[:, :, g:g + 1].to_broadcast([P, NT, PER_GROUP]), ALU.mult))
                V.link(nc.vector.tensor_tensor(mem[:, :, :], ohe[:, 0, :, :, :].rearrange("p t g e -> p t (g e)"),
                                               ohe[:, 1, :, :, :].rearrange("p t g e -> p t (g e)"), ALU.add))
                V.link(nc.vector.memset(cum[:, 0, :], 0.0))
                for n in range(NT):
                    V.link(nc.vector.tensor_tensor(cum[:, n + 1, :], cum[:, n, :], mem[:, n, :], ALU.add))
                dve.sem_inc(members, 1)
                dve.wait_ge(exp_out, 1)
                V.link(nc.vector.tensor_reduce(gs[:, :], gdiff[:, :, :], AX_X, ALU.add))
                V.link(nc.vector.tensor_scalar(pmax[:, :], e21[:, :], 1.0, None, ALU.add))
                V.link(nc.vector.tensor_tensor(gs[:, :], gs[:, :], pmax[:, :], ALU.mult))
                V.link(nc.vector.reciprocal(wts[:, 0:NT], gs[:, :]))
                V.link(nc.vector.tensor_tensor(wts[:, NT:2 * NT], wts[:, 0:NT], e21[:, :], ALU.mult))
                dve.wait_ge(rank_psum, 1)
                V.link(nc.vector.tensor_tensor(over[:, :, :], pl[:, 0:N_EXP].unsqueeze(2).to_broadcast([P, N_EXP, 8]),
                                               tab[:, 2 * P + 8:2 * P + 16].unsqueeze(1).to_broadcast([P, N_EXP, 8]), ALU.is_gt))
                V.link(nc.vector.tensor_reduce(padded[:, :], over[:, :, :], AX_X, ALU.add))
                V.link(nc.vector.tensor_scalar(padded[:, :], padded[:, :], float(P), None, ALU.mult))
                V.link(nc.vector.tensor_tensor_scan(pend[:, :], tab[:, P:P + N_EXP], padded[:, :], 0.0, ALU.mult, ALU.add))
                V.link(nc.vector.tensor_tensor(pstart[:, :], pend[:, :], padded[:, :], ALU.subtract))
                V.link(nc.vector.tensor_tensor(rank[:, :, :], pr[:, 0:NT * N_EXP].rearrange("p (t e) -> p t e", e=N_EXP),
                                               pstart[:, :].unsqueeze(1).to_broadcast([P, NT, N_EXP]), ALU.add))
                for n in range(2):
                    V.link(nc.vector.tensor_tensor(pick[:, :, :], rank[:, :, :], ohe[:, n, :, :, :].rearrange("p t g e -> p t (g e)"), ALU.mult))
                    V.link(nc.vector.tensor_reduce(slot_f[:, n * NT:(n + 1) * NT], pick[:, :, :], AX_X, ALU.add))
                V.link(nc.vector.tensor_copy(slot_u[:, :], slot_f[:, :]))
                dve.sem_inc(slots, 1)
                V.link(nc.vector.tensor_tensor(cmp[:, :, :], pend[:, :].unsqueeze(1).to_broadcast([P, MOE_BLOCKS, N_EXP]),
                                               tab[:, 2 * P + 16:2 * P + 16 + MOE_BLOCKS].unsqueeze(2).to_broadcast([P, MOE_BLOCKS, N_EXP]), ALU.is_le))
                V.link(nc.vector.tensor_reduce(be_f[:, :], cmp[:, :, :], AX_X, ALU.add))
                V.link(nc.vector.tensor_scalar(block_e[:, :], be_f[:, :], float(N_EXP - 1), None, ALU.min))
                firsts = be_f[:, :].rearrange("p (n u) -> p n u", u=2)[:, :, 0]
                V.link(nc.vector.tensor_scalar(pair_used[:, :], firsts, float(N_EXP), None, ALU.is_lt))


D_EXP = 256


def experts_phase(nc, vecs, w1, w3, w2, eye, block_e, pair_used, slot_tok, h2_dram, yb_dram):
    with Phase(nc, "exp") as ph:
        U = 2
        ident = ph.sb("ident", [P, P])
        vec = ph.sb("vec", [P, VEC_N])
        wb = ph.sb("wb", [P, U, 2, KD, D_EXP])
        w2b = ph.sb("w2b", [P, U, 2, D])
        idx = ph.sb("idx", [P, U], U32)
        xg = ph.sb("xg", [P, U, D])
        xT = ph.sb("xT", [P, U, KD, P])
        sg = ph.sb("sg", [P, D_EXP])
        hid = ph.sb("hid", [P, D_EXP])
        hidT = ph.sb("hidT", [P, 2, P])
        y = ph.sb("y", [P, U, D])
        zero = ph.sb("zero", [P, D])
        pt = ph.ps("pt", [P, D])
        pg = ph.ps("pg", [P, HALF])
        phT = ph.ps("phT", [P, HALF])
        py = ph.ps("py", [P, D])
        names = "consts x_psum x_ready gu_psum act_done hid_ready hT_psum hT_ready y_psum y_a y_v y_out zeroed".split()
        (consts, x_psum, x_ready, gu_psum, act_done, hid_ready, hT_psum, hT_ready, y_psum, y_a, y_v, y_out, zeroed) = [ph.sem(n) for n in names]
        w_done = [ph.sem(f"w_done{u}") for u in range(U)]
        idx_done = [ph.sem(f"idx_done{u}") for u in range(U)]
        x_in = [ph.sem(f"x_in{u}") for u in range(U)]
        V, G, A, E, S = (ph.engine(e, n) for e, n in ((nc.vector, "dve"), (nc.gpsimd, "pool"), (nc.scalar, "act"),
                                                      (nc.tensor, "pe"), (nc.sync, "sp")))
        g0 = vec_at("norm_ffn_g")[0]
        NB = MOE_BLOCKS

        def in_use(eng, i):
            return eng.value_load(pair_used[0:1, ds(i, 1)], min_val=0, max_val=1)

        with nc.Block() as block:

            @block.sync
            def _(sp):
                for u in range(U):
                    S.open(w_done[u], n=48)
                    S.open(idx_done[u], n=16)
                sp.dma_start(ident[:, :], eye).then_inc(consts, 16)
                sp.dma_start(vec[:, :], vecs).then_inc(consts, 16)
                sp.dma_start(idx[:, 0:1], slot_tok[0:P, :]).then_inc(idx_done[0], 16)
                with sp.Fori(0, NB // U) as i:
                    with sp.If(in_use(sp, i) > 0):
                        for u in range(U):
                            S.hold(y_psum, last(i, U, u + 1))
                            e = sp.value_load(block_e[0:1, ds(i * U + u, 1)], min_val=0, max_val=N_EXP - 1)
                            for n, w in enumerate((w1, w3)):
                                sp.dma_start(wb[:, u, n, :, :], w[0][ds(e, 1), :, :].rearrange("o (k p) f -> p (o k) f", p=P)).then_inc(w_done[u], 16)
                            sp.dma_start(w2b[:, u, :, :], w2[0][ds(e, 1), :, :].rearrange("o (k p) f -> p (o k) f", p=P)).then_inc(w_done[u], 16)
                            S.hold(x_psum, i * U + (U + u))
                            sp.dma_start(idx[:, 1 - u:2 - u], slot_tok[ds((i * U + (u + 1)) * P, P), :]).then_inc(idx_done[1 - u], 16)

            @block.gpsimd
            def _(pool):
                def gather(u):
                    pool.indirect_dma_start(xg[:, u, :], None, h2_dram, bass.IndirectOffsetOnAxis(ap=idx[:, u:u + 1], axis=0)).then_inc(x_in[u], 16)

                nc.gpsimd.memset(zero[:, :], 0.0).then_inc(zeroed, 1)
                pool.wait_ge(idx_done[0], 32)
                gather(0)
                with pool.Fori(0, NB // U) as i:
                    with pool.If(in_use(pool, i) > 0):
                        for u in range(U):
                            v = 1 - u
                            G.hold(idx_done[v], now(i, 16) if u == 0 else now(i + 1, 16))
                            G.hold(x_psum, last(i, U, u + 1))
                            gather(v)

            @block.tensor
            def _(pe):
                E.open(gu_psum, hT_psum, y_psum, x_psum, n=U)
                pe.wait_ge(consts, 32)

                def turn_x(v):
                    for k in range(KD):
                        t = nc.tensor.transpose(pt[:, k * P:(k + 1) * P], xg[:, v, k * P:(k + 1) * P], ident[:, :])
                    t.then_inc(x_psum, 1)

                pe.wait_ge(x_in[0], 16)
                turn_x(0)
                with pe.Fori(0, NB // U) as i:
                    with pe.If(in_use(pe, i) > 0):
                        for u in range(U):
                            v = 1 - u
                            E.hold(x_ready, now(i, U, u + 1))
                            E.hold(w_done[u], now(i, 48))
                            E.hold(hid_ready, last(i, U, u + U) if u == 0 else now(i, U, u))
                            for k in range(KD):
                                m = nc.tensor.matmul(pg[:, :], xT[:, u, k, :], wb[:, u, :, k, :], start=k == 0, stop=k == KD - 1)
                            m.then_inc(gu_psum, 1)
                            E.hold(x_in[v], i * 16 + (16 if u == 0 else 32))
                            turn_x(v)
                            E.hold(hid_ready, now(i, U, u + 1))
                            for k in range(2):
                                t = nc.tensor.transpose(phT[:, k * P:(k + 1) * P], hid[:, k * P:(k + 1) * P], ident[:, :])
                            t.then_inc(hT_psum, 1)
                            E.hold(hT_ready, now(i, U, u + 1))
                            E.hold(y_a, now(i, U, u) if u else last(i, U))
                            E.hold(y_v, now(i, U, u) if u else last(i, U))
                            for half in range(2):
                                for k in range(2):
                                    m = nc.tensor.matmul(py[:, half * HALF:(half + 1) * HALF], hidT[:, k, :], w2b[:, u, k, half * HALF:(half + 1) * HALF],
                                                         start=k == 0, stop=k == 1)
                            m.then_inc(y_psum, 1)

            @block.scalar
            def _(act):
                A.open(act_done, y_a, n=U)
                A.open(y_out, n=32)
                act.wait_ge(zeroed, 1)
                with act.Fori(0, NB // U) as i:
                    with act.If(in_use(act, i) > 0):
                        for u in range(U):
                            A.hold(gu_psum, now(i, U, u + 1))
                            nc.scalar.activation(sg[:, :], pg[:, 0:D_EXP], ACT.Silu).then_inc(act_done, 1)
                            A.hold(y_psum, now(i, U, u + 1))
                            A.hold(y_out, last(i, 32))
                            nc.scalar.copy(y[:, u, 0:HALF], py[:, 0:HALF]).then_inc(y_a, 1)
                            A.hold(y_a, now(i, U, u + 1))
                            A.hold(y_v, now(i, U, u + 1))
                            act.dma_start(yb_dram[ds((i * U + u) * P, P), :], y[:, u, :]).then_inc(y_out, 16)
                    with act.Else():
                        for u in range(U):
                            act.dma_start(yb_dram[ds((i * U + u) * P, P), :], zero[:, :]).then_inc(y_out, 16)
                act.wait_ge(y_out, 16 * (NB + U))

            @block.vector
            def _(dve):
                V.open(hid_ready, hT_ready, y_v, n=U)
                V.open(x_ready, n=U)
                dve.wait_ge(consts, 32)
                gx = vec[:, g0:g0 + KD].unsqueeze(2).to_broadcast([P, KD, P])

                def keep_x(v):
                    nc.vector.tensor_tensor(xT[:, v, :, :], pt[:, :].rearrange("p (k t) -> p k t", k=KD), gx, ALU.mult).then_inc(x_ready, 1)

                dve.wait_ge(x_psum, U + 1)
                keep_x(0)
                with dve.Fori(0, NB // U) as i:
                    with dve.If(in_use(dve, i) > 0):
                        for u in range(U):
                            V.hold(act_done, now(i, U, u + 1))
                            V.hold(hT_psum, last(i, U, u + U) if u == 0 else now(i, U, u))
                            nc.vector.tensor_tensor(hid[:, :], sg[:, :], pg[:, D_EXP:HALF], ALU.mult).then_inc(hid_ready, 1)
                            V.hold(x_psum, now(i, U, u + 2))
                            keep_x(1 - u)
                            V.hold(hT_psum, now(i, U, u + 1))
                            V.hold(y_psum, last(i, U, u + U) if u == 0 else now(i, U, u))
                            nc.vector.tensor_copy(hidT[:, :, :], phT[:, 0:D_EXP].rearrange("p (k t) -> p k t", k=2)).then_inc(hT_ready, 1)
                            V.hold(y_psum, now(i, U, u + 1))
                            V.hold(y_out, last(i, 32))
                            nc.vector.tensor_copy(y[:, u, HALF:D], py[:, HALF:D]).then_inc(y_v, 1)


def combine_phase(nc, norm_final_g, slot_u, wts, x1_dram, yb_dram, x2_dram):
    with Phase(nc, "comb") as ph:
        g = ph.sb("g", [P, D])
        B = 4
        x1 = ph.sb("x1", [P, B, D])
        ya = ph.sb("ya", [P, B, 2, D])
        junk = ph.sb("junk", [P, B, D])
        small = ph.sb("small", [P, B, 4])
        out = ph.sb("out", [P, B, D])
        names = "consts summed sq ms root out_ready".split()
        consts, summed, sq, ms, root, out_ready = [ph.sem(n) for n in names]
        rows_in = [ph.sem(f"rows_in{u}") for u in range(B)]
        x_in = [ph.sem(f"x_in{u}") for u in range(B)]
        x_out = [ph.sem(f"x_out{u}") for u in range(B)]
        V = ph.engine(nc.vector, "dve")

        with nc.Block() as block:

            @block.sync
            def _(sp):
                sp.dma_start(g[:, :], norm_final_g.partition_broadcast(P)).then_inc(consts, 16)
                def load(i):
                    sp.dma_start(x1[:, i % B, :], x1_dram[i * P:(i + 1) * P, :]).then_inc(x_in[i % B], 16)

                for i in range(B):
                    load(i)
                for i in range(NT):
                    sp.wait_ge(out_ready, i + 1)
                    sp.dma_start(x2_dram[i * P:(i + 1) * P, :], out[:, i % B, :]).then_inc(x_out[i % B], 16)
                    if i + B < NT:
                        load(i + B)
                for v in range(B):
                    sp.wait_ge(x_out[v], 16 * NT // B)

            @block.gpsimd
            def _(pool):
                for i in range(NT):
                    u = i % B
                    if i >= B:
                        pool.wait_ge(summed, i - B + 1)
                    for n in range(2):
                        pool.indirect_dma_start(ya[:, u, n, :], None, yb_dram, bass.IndirectOffsetOnAxis(ap=slot_u[:, n * NT + i:n * NT + i + 1], axis=0)).then_inc(rows_in[u], 16)
                for u in range(B):
                    pool.wait_ge(rows_in[u], 32 * NT // B)

            @block.scalar
            def _(act):
                for i in range(NT):
                    u = i % B
                    act.wait_ge(summed, i + 1)
                    nc.scalar.activation(junk[:, u, :], x1[:, u, :], ACT.Square, accum_out=small[:, u, 0:1]).then_inc(sq, 1)
                    act.wait_ge(ms, i + 1)
                    if i >= B:
                        act.wait_ge(out_ready, i - B + 1)
                    nc.scalar.activation(small[:, u, 2:3], small[:, u, 1:2], ACT.Sqrt).then_inc(root, 1)

            @block.vector
            def _(dve):
                dve.wait_ge(consts, 16)

                def add(i):
                    u = i % B
                    dve.wait_ge(x_in[u], 16 * (i // B + 1))
                    dve.wait_ge(rows_in[u], 32 * (i // B + 1))
                    V.link(nc.vector.scalar_tensor_tensor(x1[:, u, :], ya[:, u, 0, :], wts[:, i:i + 1], x1[:, u, :], ALU.mult, ALU.add))
                    nc.vector.scalar_tensor_tensor(x1[:, u, :], ya[:, u, 1, :], wts[:, NT + i:NT + i + 1], x1[:, u, :], ALU.mult, ALU.add).then_inc(summed, 1)

                def mean_square(i):
                    u = i % B
                    dve.wait_ge(sq, i + 1)
                    nc.vector.tensor_scalar(small[:, u, 1:2], small[:, u, 0:1], 1.0 / D, NORM_EPS, ALU.mult, ALU.add).then_inc(ms, 1)

                add(0)
                for i in range(NT):
                    u = i % B
                    mean_square(i)
                    if i + 1 < NT:
                        add(i + 1)
                    dve.wait_ge(root, i + 1)
                    V.link(nc.vector.reciprocal(small[:, u, 3:4], small[:, u, 2:3]))
                    if i >= B:
                        dve.wait_ge(x_out[u], 16 * (i // B))
                    nc.vector.scalar_tensor_tensor(out[:, u, :], x1[:, u, :], small[:, u, 3:4], g[:, :], ALU.mult, ALU.mult).then_inc(out_ready, 1)


HD, NQ, NKV, GRP = 64, 16, 4, 4
QKV = (NQ + 2 * NKV) * HD
BAND = 3 * P
ROT = HD // 4
ALPHA = 4.0 ** 0.25
LN_EPS = 1e-5
NEG = -1e30


def gqa_tables():
    pos = np.arange(T, dtype=np.float32)
    inv = np.float32(500000.0) ** (-np.arange(0, ROT, 2, dtype=np.float32) / ROT)
    ang = (pos[:, None] * inv[None, :]).astype(np.float32)
    rope = np.concatenate([np.cos(ang), np.sin(ang)], axis=1).astype(np.float32).reshape(NT, P, ROT).transpose(1, 0, 2)
    q = np.arange(P)[:, None, None] + P * np.arange(NT)[None, :, None]
    k = P * (np.arange(NT)[None, :, None] - 1) + np.arange(BAND)[None, None, :]
    ok = (np.abs(q - k) <= P) & (k >= 0) & (k < T)
    return np.ascontiguousarray(rope), np.where(ok, 0.0, NEG).astype(np.float32)


def gqa_phase(nc, w_qkv, w_o, sink, eye, rope, masks, ln_g, ln_b, x_dram, out_dram):
    with Phase(nc, "gqa") as ph:
        ident = ph.sb("ident", [P, P])
        oT = ph.sb("oT", [P, KD, T])
        with Phase(nc, "gqak") as kept:
            qT = kept.sb("qT", [P, NQ // 2, T])
            kT = kept.sb("kT", [P, NKV, T + 2 * P])
            v = kept.sb("v", [P, NT + 2, NKV * HD])
            with Phase(nc, "gqap") as one:
                gqa_project(nc, one, w_qkv, eye, rope, x_dram, ident, qT, kT, v)
            with Phase(nc, "gqaa") as two:
                gqa_attend(nc, two, sink, masks, ident, qT, kT, v, oT)
        with Phase(nc, "gqao") as three:
            product_and_norm(nc, three, oT, w_o, ln_g, ln_b, x_dram, out_dram)


def gqa_project(nc, ph, w_qkv, eye, rope, x_dram, ident, qT, kT, v):
    w = ph.sb("w", [P, KD, QKV])
    tab = ph.sb("tab", [P, NT, ROT])
    xt = ph.sb("xt", [P, D])
    xT = ph.sb("xT", [P, KD, P])
    qs = ph.sb("qs", [P, NQ, HD])
    ks = ph.sb("ks", [P, NKV, 2, HD])
    rr = ph.sb("rr", [P, 4, NQ + NKV, 8])
    pt = ph.ps("pt", [P, D])
    pqT = ph.ps("pqT", [P, D])
    pq = ph.ps("pq", [P, 3, HALF])
    pk = ph.ps("pk", [P, HALF])
    names = "consts x_in x_psum xT_ready qkv_psum q_copied kv_copied qk_ready qT_psum qT_kept kT_psum kT_kept zeros".split()
    consts, x_in, x_psum, xT_ready, qkv_psum, q_copied, kv_copied, qk_ready, qT_psum, qT_kept, kT_psum, kT_kept, zeros = [ph.sem(n) for n in names]
    w_in = [ph.sem(f"w_in{b}") for b in range(3)]
    V, A, E, S = (ph.engine(e, n) for e, n in ((nc.vector, "dve"), (nc.scalar, "act"), (nc.tensor, "pe"), (nc.sync, "sp")))

    with nc.Block() as block:

        @block.sync
        def _(sp):
            S.open(x_in, n=16)
            sp.dma_start(ident[:, :], eye).then_inc(consts, 16)
            sp.dma_start(tab[:, :, :], rope).then_inc(consts, 16)
            sp.dma_start(xt[:, :], x_dram[0:P, :]).then_inc(x_in, 16)
            for b in range(3):
                for k in range(0, KD, 4):
                    sp.dma_start(w[:, k:k + 4, b * HALF:(b + 1) * HALF],
                                 w_qkv[0, k * P:(k + 4) * P, b * HALF:(b + 1) * HALF].rearrange("(k p) n -> p k n", p=P)).then_inc(w_in[b], 16)
            with sp.Fori(1, NT) as i:
                S.hold(x_psum, last(i))
                sp.dma_start(xt[:, :], x_dram[ds(i * P, P), :]).then_inc(x_in, 16)

        @block.gpsimd
        def _(pool):
            for b in (0, T + P):
                nc.gpsimd.memset(kT[:, :, b:b + P], 0.0)
            for b in (0, NT + 1):
                z = nc.gpsimd.memset(v[:, b, :], 0.0)
            z.then_inc(zeros, 1)

        def turns(eng, E_, turn, links):
            turn(0, False, True)
            with eng.Fori(0, NT - 2) as n:
                E_.loop(n, links)
                turn(n + 1, True, True)
            E_.done(NT - 2)
            turn(NT - 1, True, False)

        @block.tensor
        def _(pe):
            E.open(x_psum, qkv_psum, qT_psum, kT_psum)
            pe.wait_ge(consts, 2 * 16)

            def turn_x(i):
                E.hold(x_in, now(i, 16))
                E.hold(xT_ready, last(i))
                for k in range(KD):
                    t = nc.tensor.transpose(pt[:, k * P:(k + 1) * P], xt[:, k * P:(k + 1) * P], ident[:, :])
                t.then_inc(x_psum, 1)

            def turn_heads(i):
                E.hold(qk_ready, now(i))
                E.hold(qT_kept, last(i))
                for n in range(NQ // 2):
                    t = nc.tensor.transpose(pqT[:, n * P:(n + 1) * P], qs[:, 2 * n:2 * n + 2, :].rearrange("p h d -> p (h d)"), ident[:, :])
                t.then_inc(qT_psum, 1)
                E.hold(kT_kept, last(i))
                for n in range(NKV):
                    t = nc.tensor.transpose(pk[:, n * P:(n + 1) * P], ks[:, n, :, :].rearrange("p h d -> p (h d)"), ident[:, :])
                t.then_inc(kT_psum, 1)

            def turn(i, prev, more):

                def product(b):
                    pe.wait_ge(w_in[b], 2 * 16)
                    for k in range(KD):
                        m = nc.tensor.matmul(pq[:, b, :], xT[:, k, :], w[:, k, b * HALF:(b + 1) * HALF], start=k == 0, stop=k == KD - 1)
                    return m

                E.hold(xT_ready, now(i))
                E.hold(q_copied, last(i))
                product(0)
                if prev:
                    turn_heads(i - 1)
                E.hold(kv_copied, last(i))
                product(1)
                product(2).then_inc(qkv_psum, 1)
                if more:
                    turn_x(i + 1)

            turn_x(0)
            turns(pe, E, turn, 0)
            turn_heads(NT - 1)

        @block.scalar
        def _(act):
            A.open(q_copied, qT_kept)

            def keep_q(i):
                A.hold(qT_psum, now(i))
                nc.scalar.copy(qT[:, :, ds(i * P, P)], pqT[:, :].rearrange("p (k t) -> p k t", k=NQ // 2)).then_inc(qT_kept, 1)

            def turn(i, prev, more):
                if prev:
                    keep_q(i - 1)
                A.hold(qkv_psum, now(i))
                A.hold(qT_psum, last(i))
                nc.scalar.copy(qs[:, :, :].rearrange("p (b h) d -> p b (h d)", b=2), pq[:, 0:2, :]).then_inc(q_copied, 1)

            turns(act, A, turn, 0)
            keep_q(NT - 1)

        @block.vector
        def _(dve):
            V.open(xT_ready, kv_copied, qk_ready, kT_kept)
            dve.wait_ge(zeros, 1)
            dve.wait_ge(consts, 2 * 16)

            def keep_x(i):
                V.hold(x_psum, now(i))
                V.hold(qkv_psum, last(i))
                nc.vector.tensor_copy(xT[:, :, :], pt[:, :].rearrange("p (k t) -> p k t", k=KD)).then_inc(xT_ready, 1)

            def keep_k(i):
                V.hold(kT_psum, now(i))
                nc.vector.tensor_copy(kT[:, :, ds(i * P + P, P)], pk[:, :].rearrange("p (k t) -> p k t", k=NKV)).then_inc(kT_kept, 1)

            def turn(i, prev, more):
                if prev:
                    keep_k(i - 1)
                V.hold(qkv_psum, now(i))
                V.hold(kT_psum, last(i))
                for b in range(2):
                    nc.vector.tensor_copy(ks[:, :, b, :], pq[:, 2, 0:NKV * HD].rearrange("p (h d) -> p h d", d=HD))
                V.link(nc.vector.tensor_copy(v[:, ds(i + 1, 1), :].rearrange("p o n -> p (o n)"), pq[:, 2, NKV * HD:HALF]))
                dve.sem_inc(kv_copied, 1)
                if more:
                    keep_x(i + 1)
                V.hold(q_copied, now(i))
                co, si = tab[:, ds(i, 1), 0:8], tab[:, ds(i, 1), 8:16]
                for src, lo, n in ((qs[:, :, :], 0, NQ), (ks[:, :, 0, :], NQ, NKV)):
                    for m, (c, half) in enumerate(((co, 0), (si, 8), (si, 0), (co, 8))):
                        r = nc.vector.tensor_tensor(rr[:, m, lo:lo + n, :], src[:, :, half:half + 8], c.to_broadcast([P, n, 8]), ALU.mult)
                V.link(r)
                nc.vector.tensor_tensor(qs[:, :, 0:8], rr[:, 0, 0:NQ, :], rr[:, 1, 0:NQ, :], ALU.subtract)
                nc.vector.tensor_tensor(qs[:, :, 8:16], rr[:, 2, 0:NQ, :], rr[:, 3, 0:NQ, :], ALU.add)
                for b in range(2):
                    nc.vector.tensor_tensor(ks[:, :, b, 0:8], rr[:, 0, NQ:NQ + NKV, :], rr[:, 1, NQ:NQ + NKV, :], ALU.subtract)
                    r = nc.vector.tensor_tensor(ks[:, :, b, 8:16], rr[:, 2, NQ:NQ + NKV, :], rr[:, 3, NQ:NQ + NKV, :], ALU.add)
                r.then_inc(qk_ready, 1)

            keep_x(0)
            turns(dve, V, turn, 2)
            keep_k(NT - 1)


def gqa_attend(nc, ph, sink, masks, ident, qT, kT, v, oT):
    SCALE = float(HD) ** -0.5
    B, U = 2, 2 * NKV
    mask = ph.sb("mask", [P, NT, BAND])
    sk = ph.sb("sk", [P, NQ])
    q_t = [ph.sb(f"q_t{b}", [P, NQ // 2, P]) for b in range(B)]
    k_t = [ph.sb(f"k_t{b}", [P, NKV, BAND]) for b in range(B)]
    v_t = [ph.sb(f"v_t{b}", [P, 3, NKV * HD]) for b in range(B)]
    s = ph.sb("s", [P, 2, GRP, BAND])
    pr = ph.sb("pr", [P, 4, GRP, BAND])
    pT = ph.sb("pT", [P, 2, 3, GRP * P])
    mx = ph.sb("mx", [P, GRP])
    nmx = ph.sb("nmx", [P, 2, GRP])
    ex = ph.sb("ex", [P, 2, GRP])
    den = ph.sb("den", [P, 2, GRP])
    rden = ph.sb("rden", [P, 2, GRP])
    pS = ph.ps("pS", [P, GRP, HALF])
    pP = ph.ps("pP", [P, 3, HALF])
    pO = ph.ps("pO", [P, HALF])
    names = "consts qkv_in s_psum s_ready sh_ready exp_done normed p_psum p_kept o_psum o_kept".split()
    consts, qkv_in, s_psum, s_ready, sh_ready, exp_done, normed, p_psum, p_kept, o_psum, o_kept = [ph.sem(n) for n in names]
    V, G, A, E = (ph.engine(e, n) for e, n in ((nc.vector, "dve"), (nc.gpsimd, "pool"), (nc.scalar, "act"), (nc.tensor, "pe")))

    def per_unit(i, u):
        return now(i, U, u + 1) if u >= 0 else last(i, U, U + u + 1)

    def turns(eng, E_, step, links, lag):
        for u in range(U):
            step(0, u, u)
        with eng.Fori(0, NT // B - 1) as n:
            E_.loop(n, links)
            for u in range(U):
                step(n + 1, u, U)
        E_.done(NT // B - 1)
        for u in range(lag):
            step(NT // B, u, U, False)

    with nc.Block() as block:

        @block.sync
        def _(sp):
            sp.dma_start(mask[:, :, :], masks).then_inc(consts, 16)
            sp.dma_start(sk[:, :], sink[0].partition_broadcast(P)).then_inc(consts, 16)

        @block.gpsimd
        def _(pool):
            G.open(qkv_in, n=B)
            with pool.Fori(0, NT // B) as i:
                for b in range(B):
                    G.hold(o_psum, last(i, U, (b + 1) * NKV))
                    nc.gpsimd.tensor_copy(k_t[b][:, :, :], kT[:, :, ds(i * (B * P) + b * P, BAND)])
                    nc.gpsimd.tensor_copy(v_t[b][:, :, :], v[:, ds(i * B + b, 3), :])
                    nc.gpsimd.tensor_copy(q_t[b][:, :, :], qT[:, :, ds(i * (B * P) + b * P, P)]).then_inc(qkv_in, 1)

        @block.tensor
        def _(pe):
            E.open(s_psum, p_psum, o_psum, n=U)

            def scores(i, u):
                b, g = u // NKV, u % NKV
                if g == 0:
                    E.hold(qkv_in, now(i, B, b + 1))
                E.hold(s_ready, per_unit(i, u - 1))
                for h in range(GRP):
                    half = slice(64 * (h % 2), 64 * (h % 2) + 64)
                    m = nc.tensor.matmul(pS[:, h, 0:BAND], q_t[b][half, GRP // 2 * g + h // 2, :], k_t[b][half, g, :], start=True, stop=True)
                m.then_inc(s_psum, 1)

            def outputs(i, u):
                b, g = u % U // NKV, u % NKV
                E.hold(p_kept, per_unit(i, u))
                E.hold(o_kept, per_unit(i, u - 1))
                for odd in range(2):
                    for kb in range(3):
                        m = nc.tensor.matmul(pO[64 * odd:64 * odd + 64, 0:2 * P], v_t[b][:, kb, g * HD:(g + 1) * HD],
                                             pT[:, u % 2, kb, odd * 2 * P:(odd + 1) * 2 * P], start=kb == 0, stop=kb == 2)
                m.then_inc(o_psum, 1)

            def transposes(i, u):
                E.hold(normed, per_unit(i, u))
                E.hold(p_kept, per_unit(i, u - 1))
                for kb in range(3):
                    for h in range(GRP):
                        at = (h % 2 * 2 + h // 2) * P
                        t = nc.tensor.transpose(pP[:, kb, at:at + P], pr[:, u % 4, h, kb * P:(kb + 1) * P], ident[:, :])
                t.then_inc(p_psum, 1)

            def step(i, u, before, new=True):
                if new:
                    scores(i, u)
                if before >= 2 and (new or u < 2):
                    transposes(i, u - 2)
                if before >= 3:
                    outputs(i, u - 3)

            turns(pe, E, step, 0, 3)

        @block.scalar
        def _(act):
            A.open(exp_done, p_kept, o_kept, n=U)
            def keep_p(i, u):
                A.hold(p_psum, per_unit(i, u))
                A.hold(o_psum, per_unit(i, u - 2))
                nc.scalar.copy(pT[:, u % 2, :, :], pP[:, :, :]).then_inc(p_kept, 1)

            def keep_o(i, u):
                b, g = u % U // NKV, u % NKV
                at = (i if u >= 0 else i - 1) * (B * P) + b * P
                A.hold(o_psum, per_unit(i, u))
                nc.scalar.copy(oT[:, 2 * g:2 * g + 2, ds(at, P)], pO[:, 0:2 * P].rearrange("p (k t) -> p k t", k=2)).then_inc(o_kept, 1)

            def exps(i, u):
                c, n = u % 2, u % 4
                A.hold(sh_ready, per_unit(i, u))
                A.hold(p_psum, per_unit(i, u - 4))
                A.hold(normed, per_unit(i, u - 2))
                for h in range(GRP):
                    nc.scalar.activation(pr[:, n, h, :], s[:, c, h, :], ACT.Exp, bias=nmx[:, c, h:h + 1], accum_out=den[:, c, h:h + 1])
                nc.scalar.activation(ex[:, c, :], ex[:, c, :], ACT.Exp).then_inc(exp_done, 1)

            def step(i, u, before, new=True):
                if before >= 3:
                    keep_p(i, u - 3)
                if new:
                    exps(i, u)
                if before >= 3:
                    keep_o(i, u - 3)

            turns(act, A, step, 0, 3)

        @block.vector
        def _(dve):
            V.open(s_ready, sh_ready, normed, n=U)
            dve.wait_ge(consts, 32)
            def shifted(i, u):
                b, g, c = u // NKV, u % NKV, u % 2
                heads = sk[:, GRP * g:GRP * (g + 1)]
                V.hold(s_psum, per_unit(i, u))
                V.hold(exp_done, per_unit(i, u - 2))
                V.link(nc.vector.scalar_tensor_tensor(s[:, c, :, :], pS[:, :, 0:BAND], SCALE,
                                                      mask[:, ds(i * B + b, 1), :].to_broadcast([P, GRP, BAND]), ALU.mult, ALU.add))
                dve.sem_inc(s_ready, 1)
                V.link(nc.vector.reduce_max(mx[:, :], s[:, c, :, :], AX_X))
                V.link(nc.vector.tensor_tensor(mx[:, :], mx[:, :], heads, ALU.max))
                nc.vector.tensor_scalar(nmx[:, c, :], mx[:, :], -1.0, None, ALU.mult)
                nc.vector.tensor_tensor(ex[:, c, :], heads, mx[:, :], ALU.subtract).then_inc(sh_ready, 1)

            def normalised(i, u):
                c, n = u % 2, u % 4
                V.hold(exp_done, per_unit(i, u))
                V.hold(normed, per_unit(i, u - 2))
                V.link(nc.vector.tensor_tensor(den[:, c, :], den[:, c, :], ex[:, c, :], ALU.add))
                V.link(nc.vector.reciprocal(rden[:, c, :], den[:, c, :]))
                nc.vector.tensor_tensor(pr[:, n, :, :], pr[:, n, :, :], rden[:, c, :].unsqueeze(2).to_broadcast([P, GRP, BAND]), ALU.mult).then_inc(normed, 1)

            def step(i, u, before, new=True):
                if new:
                    shifted(i, u)
                if before >= 1:
                    normalised(i, u - 1)

            turns(dve, V, step, 5 * U, 1)


def product_and_norm(nc, ph, aT, w_out, ln_g, ln_b, x_dram, out_dram):
    U = 2
    wo = ph.sb("wo", [P, KD, D])
    gb = ph.sb("gb", [P, 2, D])
    a_t = ph.sb("a_t", [P, U, KD, P])
    xt = ph.sb("xt", [P, U, D])
    r = ph.sb("r", [P, U, D])
    junk = ph.sb("junk", [P, D])
    small = ph.sb("small", [P, U, 8])
    out = ph.sb("out", [P, U, D])
    po = ph.ps("po", [P, U, D])
    names = "consts staged o_psum summed mean cent sq ms root ready".split()
    consts, staged, o_psum, summed, mean, cent, sq, ms, root, ready = [ph.sem(n) for n in names]
    w_in = [ph.sem(f"w_in{half}") for half in range(2)]
    x_in = [ph.sem(f"x_in{u}") for u in range(U)]
    done = [ph.sem(f"done{u}") for u in range(U)]
    V, G, A, E, S = (ph.engine(e, n) for e, n in ((nc.vector, "dve"), (nc.gpsimd, "pool"), (nc.scalar, "act"),
                                                  (nc.tensor, "pe"), (nc.sync, "sp")))

    with nc.Block() as block:

        @block.sync
        def _(sp):
            for u in range(U):
                S.open(x_in[u], n=16)
            for half in range(2):
                for k in range(0, KD, 4):
                    sp.dma_start(wo[:, k:k + 4, half * HALF:(half + 1) * HALF],
                                 w_out[0, k * P:(k + 4) * P, half * HALF:(half + 1) * HALF].rearrange("(k p) n -> p k n", p=P)).then_inc(w_in[half], 16)
            sp.dma_start(gb[:, 0, :], ln_g.partition_broadcast(P)).then_inc(consts, 16)
            sp.dma_start(gb[:, 1, :], ln_b.partition_broadcast(P)).then_inc(consts, 16)
            with sp.Fori(0, NT // U) as i:
                for u in range(U):
                    S.hold(summed, last(i, U, u + 1))
                    sp.dma_start(xt[:, u, :], x_dram[ds((i * U + u) * P, P), :]).then_inc(x_in[u], 16)

        @block.gpsimd
        def _(pool):
            G.open(staged, n=U)
            with pool.Fori(0, NT // U) as i:
                for u in range(U):
                    G.hold(o_psum, last(i, U, u + 1))
                    nc.gpsimd.tensor_copy(a_t[:, u, :, :], aT[:, :, ds((i * U + u) * P, P)]).then_inc(staged, 1)

        @block.tensor
        def _(pe):
            E.open(o_psum, n=U)
            with pe.Fori(0, NT // U) as i:
                for u in range(U):
                    E.hold(staged, now(i, U, u + 1))
                    E.hold(summed, last(i, U, u + 1))
                    for half in range(2):
                        pe.wait_ge(w_in[half], 2 * 16)
                        for k in range(KD):
                            m = nc.tensor.matmul(po[:, u, half * HALF:(half + 1) * HALF], a_t[:, u, k, :], wo[:, k, half * HALF:(half + 1) * HALF],
                                                 start=k == 0, stop=k == KD - 1)
                    m.then_inc(o_psum, 1)

        @block.scalar
        def _(act):
            A.open(sq, root, mean, n=U)
            for u in range(U):
                A.open(done[u], n=16)
            with act.Fori(0, NT // U) as i:
                for u in range(U):
                    A.hold(summed, now(i, U, u + 1))
                    nc.scalar.activation(junk[:, :], r[:, u, :], ACT.Copy, accum_out=small[:, u, 0:1]).then_inc(mean, 1)
                    A.hold(cent, now(i, U, u + 1))
                    nc.scalar.activation(junk[:, :], r[:, u, :], ACT.Square, accum_out=small[:, u, 2:3]).then_inc(sq, 1)
                    A.hold(ms, now(i, U, u + 1))
                    nc.scalar.activation(small[:, u, 4:5], small[:, u, 3:4], ACT.Sqrt).then_inc(root, 1)
                    A.hold(ready, now(i, U, u + 1))
                    act.dma_start(out_dram[ds((i * U + u) * P, P), :], out[:, u, :]).then_inc(done[u], 16)
            for u in range(U):
                act.wait_ge(done[u], 16 * (NT // U + 1))

        @block.vector
        def _(dve):
            V.open(summed, cent, ms, ready, n=U)
            dve.wait_ge(consts, 32)
            with dve.Fori(0, NT // U) as i:
                V.loop(i, 4 * U)
                for u in range(U):
                    V.hold(x_in[u], now(i, 16))
                    V.hold(o_psum, now(i, U, u + 1))
                    nc.vector.scalar_tensor_tensor(r[:, u, :], xt[:, u, :], ALPHA, po[:, u, :], ALU.mult, ALU.add).then_inc(summed, 1)
                    V.hold(mean, now(i, U, u + 1))
                    V.link(nc.vector.tensor_scalar(small[:, u, 1:2], small[:, u, 0:1], 1.0 / D, None, ALU.mult))
                    nc.vector.tensor_scalar(r[:, u, :], r[:, u, :], small[:, u, 1:2], None, ALU.subtract).then_inc(cent, 1)
                    V.hold(sq, now(i, U, u + 1))
                    nc.vector.tensor_scalar(small[:, u, 3:4], small[:, u, 2:3], 1.0 / D, LN_EPS, ALU.mult, ALU.add).then_inc(ms, 1)
                    V.hold(root, now(i, U, u + 1))
                    V.link(nc.vector.reciprocal(small[:, u, 5:6], small[:, u, 4:5]))
                    V.hold(done[u], last(i, 16))
                    V.link(nc.vector.scalar_tensor_tensor(out[:, u, :], r[:, u, :], small[:, u, 5:6], gb[:, 0, :], ALU.mult, ALU.mult))
                    V.link(nc.vector.tensor_tensor(out[:, u, :], out[:, u, :], gb[:, 1, :], ALU.add))
                    dve.sem_inc(ready, 1)
            V.done(NT // U)


def norm_phase(nc, name, ln_g, ln_b, x_dram, add_dram, out_dram):
    with Phase(nc, name) as ph:
        gb = ph.sb("gb", [P, 2, D])
        U = 4
        xt = ph.sb("xt", [P, U, D])
        at = ph.sb("at", [P, U, D])
        r = ph.sb("r", [P, U, D])
        junk = ph.sb("junk", [P, U, D])
        small = ph.sb("small", [P, U, 8])
        out = ph.sb("out", [P, U, D])
        names = "consts summed mean cent sq ms root scaled ready".split()
        consts, summed, mean, cent, sq, ms, root, scaled, ready = [ph.sem(n) for n in names]
        x_in = [ph.sem(f"x_in{u}") for u in range(U)]
        done = [ph.sem(f"done{u}") for u in range(U)]
        V, G, A, S = (ph.engine(e, n) for e, n in ((nc.vector, "dve"), (nc.gpsimd, "pool"), (nc.scalar, "act"), (nc.sync, "sp")))

        with nc.Block() as block:

            @block.sync
            def _(sp):
                for u in range(U):
                    S.open(x_in[u], n=32)
                with sp.Fori(0, NT // U) as i:
                    for u in range(U):
                        S.hold(summed, last(i, U, u + 1))
                        sp.dma_start(xt[:, u, :], x_dram[ds((i * U + u) * P, P), :]).then_inc(x_in[u], 16)
                        sp.dma_start(at[:, u, :], add_dram[ds((i * U + u) * P, P), :]).then_inc(x_in[u], 16)

            @block.scalar
            def _(act):
                A.open(sq, root, mean, n=U)
                for u in range(U):
                    A.open(done[u], n=16)
                act.dma_start(gb[:, 0, :], ln_g.partition_broadcast(P)).then_inc(consts, 16)
                act.dma_start(gb[:, 1, :], ln_b.partition_broadcast(P)).then_inc(consts, 16)
                with act.Fori(0, NT // U) as i:
                    for u in range(U):
                        A.hold(summed, now(i, U, u + 1))
                        nc.scalar.activation(junk[:, u, :], r[:, u, :], ACT.Copy, accum_out=small[:, u, 0:1]).then_inc(mean, 1)
                    for u in range(U):
                        A.hold(cent, now(i, U, u + 1))
                        nc.scalar.activation(junk[:, u, :], r[:, u, :], ACT.Square, accum_out=small[:, u, 2:3]).then_inc(sq, 1)
                    for u in range(U):
                        A.hold(ms, now(i, U, u + 1))
                        nc.scalar.activation(small[:, u, 4:5], small[:, u, 3:4], ACT.Sqrt).then_inc(root, 1)
                    for u in range(U):
                        A.hold(ready, now(i, U, u + 1))
                        act.dma_start(out_dram[ds((i * U + u) * P, P), :], out[:, u, :]).then_inc(done[u], 16)
                for u in range(U):
                    act.wait_ge(done[u], 16 * (NT // U + 1))

            @block.gpsimd
            def _(pool):
                G.open(ready, n=U)
                pool.wait_ge(consts, 32)
                with pool.Fori(0, NT // U) as i:
                    for u in range(U):
                        G.hold(scaled, now(i, U, u + 1))
                        nc.gpsimd.tensor_tensor(out[:, u, :], out[:, u, :], gb[:, 1, :], ALU.add).then_inc(ready, 1)

            @block.vector
            def _(dve):
                V.open(summed, cent, ms, scaled, n=U)
                dve.wait_ge(consts, 32)
                with dve.Fori(0, NT // U) as i:
                    V.loop(i, 2 * U)
                    for u in range(U):
                        V.hold(x_in[u], now(i, 32))
                        V.hold(scaled, last(i, U, u + 1))
                        nc.vector.scalar_tensor_tensor(r[:, u, :], xt[:, u, :], ALPHA, at[:, u, :], ALU.mult, ALU.add).then_inc(summed, 1)
                    for u in range(U):
                        V.hold(mean, now(i, U, u + 1))
                        V.link(nc.vector.tensor_scalar(small[:, u, 1:2], small[:, u, 0:1], 1.0 / D, None, ALU.mult))
                        nc.vector.tensor_scalar(r[:, u, :], r[:, u, :], small[:, u, 1:2], None, ALU.subtract).then_inc(cent, 1)
                    for u in range(U):
                        V.hold(sq, now(i, U, u + 1))
                        nc.vector.tensor_scalar(small[:, u, 3:4], small[:, u, 2:3], 1.0 / D, LN_EPS, ALU.mult, ALU.add).then_inc(ms, 1)
                    for u in range(U):
                        V.hold(root, now(i, U, u + 1))
                        V.link(nc.vector.reciprocal(small[:, u, 5:6], small[:, u, 4:5]))
                        V.hold(done[u], last(i, 16))
                        nc.vector.scalar_tensor_tensor(out[:, u, :], r[:, u, :], small[:, u, 5:6], gb[:, 0, :], ALU.mult, ALU.mult).then_inc(scaled, 1)
                V.done(NT // U)


E2 = 16
CAP = 2 * T // E2
FF = D


class Experts:

    def __init__(self, ph, w_gu, w_dn):
        self.w_gu, self.w_dn = w_gu, w_dn
        self.wg = ph.sb("wg", [P, KD, 2 * FF])
        self.wd = ph.sb("wd", [P, KD, D])
        self.wg_in = [ph.sem(f"wg_in{k}") for k in range(KD)]
        self.wd_in = [ph.sem(f"wd_in{k}") for k in range(KD)]

    def load_g(self, sp, e, k):
        sp.dma_start(self.wg[:, k, :].unsqueeze(1), self.w_gu[ds(e, 1), k * P:(k + 1) * P, :].rearrange("o p n -> p o n")).then_inc(self.wg_in[k], 16)

    def load_d(self, sp, e, k):
        sp.dma_start(self.wd[:, k, :].unsqueeze(1), self.w_dn[ds(e, 1), k * P:(k + 1) * P, :].rearrange("o p n -> p o n")).then_inc(self.wd_in[k], 16)


def expert_choice_phase(nc, name, w_router, w_gu, w_dn, eye, x_dram, acc_dram):
    with Phase(nc, name) as ph:
        gate = ph.sb("gate", [P, E2])
        idx = ph.sb("idx", [P, E2 + 1], U32)
        weights = Experts(ph, w_gu, w_dn)
        choose_phase(nc, f"{name}c", w_router, eye, x_dram, acc_dram, gate, idx, weights)
        choice_phase(nc, f"{name}e", eye, x_dram, acc_dram, gate, idx, weights)


def choose_phase(nc, name, w_router, eye, x_dram, acc_dram, gate, idx, weights):
    with Phase(nc, name) as ph:
        ident = ph.sb("ident", [P, P])
        w = ph.sb("w", [P, KD, E2])
        xt = ph.sb("xt", [P, 2, D])
        xT = ph.sb("xT", [P, 2, KD, P])
        small = ph.sb("small", [P, 2, 4])
        ex = ph.sb("ex", [P, 2, E2])
        aff = ph.sb("aff", [P, E2])
        affT = ph.sb("affT", [E2, 2, T])
        top = ph.sb("top", [E2, CAP])
        top_i = ph.sb("top_i", [E2, CAP], U32)
        top_f = ph.sb("top_f", [E2, CAP])
        zero = ph.sb("zero", [P, D])
        pt = ph.ps("pt", [P, D])
        pl = ph.ps("pl", [P, 2, HALF])
        pa = ph.ps("pa", [P, HALF])
        names = "consts zeroed acc_out x_psum xT_ready l_psum sh_ready exp_done aff_ready a_psum a_kept tops f_psum".split()
        consts, zeroed, acc_out, x_psum, xT_ready, l_psum, sh_ready, exp_done, aff_ready, a_psum, a_kept, tops, f_psum = [ph.sem(n) for n in names]
        x_in = [ph.sem(f"x_in{u}") for u in range(2)]
        V, A, E, S = (ph.engine(e, n) for e, n in ((nc.vector, "dve"), (nc.scalar, "act"), (nc.tensor, "pe"), (nc.sync, "sp")))
        U = 2

        def turns(eng, E_, turn, links):
            turn(0, 0, 0, False, True)
            with eng.Fori(0, (NT - 2) // 2) as n:
                E_.loop(n, 2 * links)
                turn(n * 2 + 1, 1, n, True, True)
                turn(n * 2 + 2, 0, n + 1, True, True)
            E_.done((NT - 2) // 2)
            turn(NT - 1, 1, NT // 2 - 1, True, False)

        with nc.Block() as block:

            @block.sync
            def _(sp):
                for u in range(U):
                    S.open(x_in[u], n=16)
                sp.dma_start(ident[:, :], eye).then_inc(consts, 16)
                sp.dma_start(w[:, :, :], w_router.rearrange("(k p) e -> p k e", p=P)).then_inc(consts, 16)
                for u in range(U):
                    sp.dma_start(xt[:, u, :], x_dram[u * P:(u + 1) * P, :]).then_inc(x_in[u], 16)
                with sp.Fori(0, NT // U - 1) as i:
                    for u in range(U):
                        S.hold(x_psum, i * U + (U + u))
                        sp.dma_start(xt[:, u, :], x_dram[ds(i * (U * P) + (U + u) * P, P), :]).then_inc(x_in[u], 16)
                for k in range(KD):
                    S.open(weights.wg_in[k], weights.wd_in[k], n=16)
                    weights.load_g(sp, 0, k)
                for k in range(KD):
                    weights.load_d(sp, 0, k)
                sp.wait_ge(zeroed, 1)
                for n in range(NT):
                    sp.dma_start(acc_dram[n * P:(n + 1) * P, :], zero[:, :]).then_inc(acc_out, 16)
                sp.wait_ge(acc_out, 16 * NT)

            @block.gpsimd
            def _(pool):
                nc.gpsimd.memset(zero[:, :], 0.0).then_inc(zeroed, 1)

            @block.tensor
            def _(pe):
                E.open(x_psum, l_psum, a_psum)
                pe.wait_ge(consts, 32)

                def turn_x(i, v, q):
                    E.hold(x_in[v], now(q, 16))
                    E.hold(xT_ready, last(i))
                    for k in range(KD):
                        t = nc.tensor.transpose(pt[:, k * P:(k + 1) * P], xt[:, v, k * P:(k + 1) * P], ident[:, :])
                    t.then_inc(x_psum, 1)

                def turn_a(i):
                    E.hold(aff_ready, now(i))
                    E.hold(a_kept, last(i))
                    nc.tensor.transpose(pa[0:E2, 0:P], aff[:, :], ident[:, :]).then_inc(a_psum, 1)

                def turn(i, v, q, prev, more):
                    if more:
                        turn_x(i + 1, 1 - v, q + v)
                    E.hold(xT_ready, now(i))
                    if prev:
                        E.hold(exp_done, i)
                    for k in range(KD):
                        m = nc.tensor.matmul(pl[:, v, 0:E2], xT[:, v, k, :], w[:, k, :], start=k == 0, stop=k == KD - 1)
                    m.then_inc(l_psum, 1)
                    if prev:
                        turn_a(i - 1)

                turn_x(0, 0, 0)
                turns(pe, E, turn, 0)
                turn_a(NT - 1)
                pe.wait_ge(tops, 1)
                nc.tensor.transpose(pl[:, 0, 0:E2], top[:, :], ident[0:E2, 0:E2])
                nc.tensor.transpose(pl[:, 0, E2:2 * E2], top_f[:, :], ident[0:E2, 0:E2]).then_inc(f_psum, 1)

            @block.scalar
            def _(act):
                A.open(xT_ready, exp_done)

                def keep_x(i, v):
                    A.hold(x_psum, now(i))
                    nc.scalar.copy(xT[:, v, :, :], pt[:, :].rearrange("p (k t) -> p k t", k=KD)).then_inc(xT_ready, 1)

                def turn(i, v, q, prev, more):
                    if more:
                        if prev:
                            A.hold(l_psum, last(i))
                        keep_x(i + 1, 1 - v)
                    A.hold(sh_ready, now(i))
                    if prev:
                        A.hold(aff_ready, i)
                    nc.scalar.activation(ex[:, v, :], pl[:, v, 0:E2], ACT.Exp, bias=small[:, v, 1:2], accum_out=small[:, v, 2:3]).then_inc(exp_done, 1)

                keep_x(0, 0)
                turns(act, A, turn, 0)

            @block.vector
            def _(dve):
                V.open(sh_ready, aff_ready, a_kept)

                def keep_a(i):
                    V.hold(a_psum, now(i))
                    nc.vector.tensor_copy(affT[:, 0, ds(i * P, P)], pa[0:E2, 0:P]).then_inc(a_kept, 1)

                def turn(i, v, q, prev, more):
                    V.hold(l_psum, now(i))
                    V.link(nc.vector.reduce_max(small[:, v, 0:1], pl[:, v, 0:E2], AX_X))
                    nc.vector.tensor_scalar(small[:, v, 1:2], small[:, v, 0:1], -1.0, None, ALU.mult).then_inc(sh_ready, 1)
                    if prev:
                        keep_a(i - 1)
                    V.hold(exp_done, now(i))
                    V.link(nc.vector.reciprocal(small[:, v, 3:4], small[:, v, 2:3]))
                    V.hold(a_psum, last(i))
                    nc.vector.tensor_scalar(aff[:, :], ex[:, v, :], small[:, v, 3:4], None, ALU.mult).then_inc(aff_ready, 1)

                turns(dve, V, turn, 2)
                keep_a(NT - 1)
                dve.wait_ge(a_kept, NT + 1)
                for n in range(CAP // 8):
                    eight = slice(8 * n, 8 * n + 8)
                    V.link(nc.vector.max(top[:, eight], affT[:, n % 2, :]))
                    nc.vector.max_index(top_i[:, eight], top[:, eight], affT[:, n % 2, :])
                    V.link(nc.vector.match_replace(affT[:, (n + 1) % 2, :], top[:, eight], affT[:, n % 2, :], -1.0))
                V.link(nc.vector.tensor_copy(top_f[:, :], top_i[:, :]))
                dve.sem_inc(tops, 1)
                dve.wait_ge(f_psum, 1)
                nc.vector.tensor_copy(gate[:, :], pl[:, 0, 0:E2])
                nc.vector.tensor_copy(idx[:, E2:E2 + 1], pl[:, 0, E2:E2 + 1])
                V.link(nc.vector.tensor_copy(idx[:, 0:E2], pl[:, 0, E2:2 * E2]))


def choice_phase(nc, name, eye, x_dram, acc_dram, gate, idx, weights):
    with Phase(nc, name) as ph:
        ident = ph.sb("ident", [P, P])
        wg, wd, wg_in, wd_in = weights.wg, weights.wd, weights.wg_in, weights.wd_in
        ic = [ph.sb(f"ic{v}", [P, 1], U32) for v in range(2)]
        xg = ph.sb("xg", [P, D])
        xT = ph.sb("xT", [P, KD, P])
        sg = ph.sb("sg", [P, FF])
        hid = ph.sb("hid", [P, FF])
        hidT = ph.sb("hidT", [P, KD, P])
        y = ph.sb("y", [P, D])
        pg = ph.ps("pg", [P, 4, HALF])
        pt = ph.ps("pt", [P, D])
        py = ph.ps("py", [P, D])
        names = "consts ic_ready x_in x_psum x_ready g_used half_psum silu hid_ready h_psum hT_a hT_v d_used y_ready sent added".split()
        (consts, ic_ready, x_in, x_psum, x_ready, g_used, half_psum, silu, hid_ready, h_psum, hT_a, hT_v, d_used, y_ready, sent,
         added) = [ph.sem(n) for n in names]
        V, G, A, E, S = (ph.engine(e, n) for e, n in ((nc.vector, "dve"), (nc.gpsimd, "pool"), (nc.scalar, "act"),
                                                      (nc.tensor, "pe"), (nc.sync, "sp")))

        with nc.Block() as block:

            @block.sync
            def _(sp):
                sp.dma_start(ident[:, :], eye).then_inc(consts, 16)
                with sp.Fori(0, E2 - 1) as e:
                    for k in range(KD):
                        S.hold(g_used, now(e, KD, k + 1))
                        weights.load_g(sp, e + 1, k)
                    for k in range(KD):
                        S.hold(d_used, now(e, KD, k + 1))
                        weights.load_d(sp, e + 1, k)

            @block.gpsimd
            def _(pool):
                G.open(ic_ready, sent)

                def gather(v):
                    pool.indirect_dma_start(xg[:, :], None, x_dram, bass.IndirectOffsetOnAxis(ap=ic[v][:, :], axis=0)).then_inc(x_in, 16)

                nc.gpsimd.tensor_copy(ic[0][:, :], idx[:, 0:1]).then_inc(ic_ready, 1)
                pool.wait_ge(ic_ready, 2)
                gather(0)
                with pool.Fori(0, E2 // 2) as i:
                    for u in range(2):
                        v = 1 - u
                        nc.gpsimd.tensor_copy(ic[v][:, :], idx[:, ds(i * 2 + (u + 1), 1)]).then_inc(ic_ready, 1)
                        G.hold(ic_ready, i * 2 + (u + 3))
                        G.hold(x_psum, i * 2 + (u + 2))
                        gather(v)
                        G.hold(y_ready, i * 2 + (u + 2))
                        pool.indirect_dma_start(acc_dram, bass.IndirectOffsetOnAxis(ap=ic[u][:, :], axis=0), y[:, :], None, compute_op=ALU.add).then_inc(added, 16)
                        G.hold(added, i * 32 + (16 * u + 16))
                        pool.sem_inc(sent, 1)
                pool.wait_ge(x_in, 16 * (E2 + 1))

            @block.tensor
            def _(pe):
                E.open(half_psum, x_psum)
                E.open(h_psum, n=2)
                E.open(g_used, d_used, n=KD)
                pe.wait_ge(consts, 16)

                def turn_x():
                    for k in range(KD):
                        t = nc.tensor.transpose(pt[:, k * P:(k + 1) * P], xg[:, k * P:(k + 1) * P], ident[:, :])
                    t.then_inc(x_psum, 1)

                pe.wait_ge(x_in, 16)
                turn_x()
                with pe.Fori(0, E2) as e:

                    def turn_hid(half):
                        E.hold(hid_ready, now(e, 2, half + 1))
                        for k in range(4):
                            at = half * HALF + k * P
                            t = nc.tensor.transpose(pg[:, 2 * half, k * P:(k + 1) * P], hid[:, at:at + P], ident[:, :])
                        t.then_inc(h_psum, 1)

                    E.hold(x_ready, now(e))
                    E.hold(hT_a, last(e))
                    E.hold(hT_v, last(e))
                    for k in range(KD):
                        E.hold(wg_in[k], now(e, 16))
                        for b in (0, 2, 1, 3):
                            m = nc.tensor.matmul(pg[:, b, :], xT[:, k, :], wg[:, k, b * HALF:(b + 1) * HALF], start=k == 0, stop=k == KD - 1)
                            if k == KD - 1 and b == 2:
                                m.then_inc(half_psum, 1)
                        m.then_inc(g_used, 1)
                    turn_hid(0)
                    E.hold(x_in, e * 16 + 32)
                    turn_x()
                    turn_hid(1)
                    E.hold(y_ready, last(e))
                    for k in range(KD):
                        E.hold(wd_in[k], now(e, 16))
                        if k == 0:
                            E.hold(hT_a, now(e))
                        if k == KD // 2:
                            E.hold(hT_v, now(e))
                        for b in range(2):
                            m = nc.tensor.matmul(py[:, b * HALF:(b + 1) * HALF], hidT[:, k, :], wd[:, k, b * HALF:(b + 1) * HALF], start=k == 0, stop=k == KD - 1)
                        m.then_inc(d_used, 1)

            @block.scalar
            def _(act):
                A.open(hT_a)
                A.open(silu, n=2)
                with act.Fori(0, E2) as e:
                    for half in range(2):
                        if half:
                            A.hold(g_used, now(e, KD))
                        else:
                            A.hold(half_psum, now(e))
                        A.hold(hid_ready, last(e, 2, half + 1))
                        nc.scalar.activation(sg[:, half * HALF:(half + 1) * HALF], pg[:, half, :], ACT.Silu).then_inc(silu, 1)
                    A.hold(h_psum, now(e, 2, 1))
                    A.hold(d_used, last(e, KD))
                    nc.scalar.copy(hidT[:, 0:4, :], pg[:, 0, :].rearrange("p (k t) -> p k t", k=4)).then_inc(hT_a, 1)

            @block.vector
            def _(dve):
                V.open(hT_v, x_ready, y_ready)
                V.open(hid_ready, n=2)
                dve.wait_ge(x_psum, 2)

                def keep_x():
                    nc.vector.tensor_copy(xT[:, :, :], pt[:, :].rearrange("p (k t) -> p k t", k=KD)).then_inc(x_ready, 1)

                keep_x()
                with dve.Fori(0, E2) as e:
                    for half in range(2):
                        V.hold(silu, now(e, 2, half + 1))
                        V.hold(h_psum, last(e, 2, half + 1))
                        cols = slice(half * HALF, (half + 1) * HALF)
                        nc.vector.tensor_tensor(hid[:, cols], sg[:, cols], pg[:, 2 + half, :], ALU.mult).then_inc(hid_ready, 1)
                    V.hold(g_used, now(e, KD))
                    V.hold(x_psum, now(e + 1))
                    keep_x()
                    V.hold(h_psum, now(e, 2, 2))
                    V.hold(d_used, last(e, KD))
                    nc.vector.tensor_copy(hidT[:, 4:8, :], pg[:, 2, :].rearrange("p (k t) -> p k t", k=4)).then_inc(hT_v, 1)
                    V.hold(d_used, now(e, KD))
                    V.hold(sent, e + 1)
                    nc.vector.tensor_scalar(y[:, :], py[:, :], gate[:, ds(e, 1)], None, ALU.mult).then_inc(y_ready, 1)


NBLK, BW = 4, 256
GELU_C = float(np.sqrt(2.0 / np.pi))
CONV = 4


def lru_phase(nc, vecs, w_in, w_r, w_i, w_out, eye, ln_g, ln_b, x_dram, out_dram):
    with Phase(nc, "lru") as ph:
        ggT = ph.sb("ggT", [P, KD, T])
        with Phase(nc, "lruk") as kept:
            vec = kept.sb("vec", [P, VEC_N])
            xc = kept.sb("xc", [P, KD, T])
            with Phase(nc, "lrui") as one:
                lru_in(nc, one, vec, xc, vecs, w_in, eye, x_dram, ggT)
            with Phase(nc, "lrus") as two:
                lru_scan(nc, two, vec, xc, w_r, w_i, ggT)
        with Phase(nc, "lruo") as three:
            product_and_norm(nc, three, ggT, w_out, ln_g, ln_b, x_dram, out_dram)


def lru_in(nc, ph, vec, xc, vecs, w_in, eye, x_dram, ggT):
    ident = ph.sb("ident", [P, P])
    xt = ph.sb("xt", [P, 2, D])
    xT = ph.sb("xT", [P, KD, T])
    w = ph.sb("w", [P, 2, 2, KD, P])
    gx = ph.sb("gx", [P, T])
    g2 = ph.sb("g2", [P, T])
    g3 = ph.sb("g3", [P, T])
    cv = ph.sb("cv", [P, T])
    cw = ph.sb("cw", [P, CONV + 1])
    pt = ph.ps("pt", [P, D])
    pg = ph.ps("pg", [P, T])
    px = ph.ps("px", [P, T])
    U = 2
    names = "consts x_psum xT_ready g_psum b_psum g_copied cube sig gg_ready cw_ready conv_done".split()
    consts, x_psum, xT_ready, g_psum, b_psum, g_copied, cube, sig, gg_ready, cw_ready, conv_done = [ph.sem(n) for n in names]
    x_in = [ph.sem(f"x_in{u}") for u in range(U)]
    w_done = [ph.sem(f"w_done{u}") for u in range(U)]
    V, G, A, E, S = (ph.engine(e, n) for e, n in ((nc.vector, "dve"), (nc.gpsimd, "pool"), (nc.scalar, "act"),
                                                  (nc.tensor, "pe"), (nc.sync, "sp")))
    wv = w_in[0].rearrange("(k p) n -> p k n", p=P)
    c0 = vec_at("lru_conv_w_2")[0]
    cb = vec_at("lru_conv_b_2")[0]

    with nc.Block() as block:

        @block.sync
        def _(sp):
            for u in range(U):
                S.open(x_in[u], n=16)
                S.open(w_done[u], n=32)
            sp.dma_start(ident[:, :], eye).then_inc(consts, 16)
            sp.dma_start(vec[:, :], vecs).then_inc(consts, 16)
            with sp.Fori(0, NT // U) as i:
                for u in range(U):
                    S.hold(x_psum, last(i, U, u + 1))
                    sp.dma_start(xt[:, u, :], x_dram[ds((i * U + u) * P, P), :]).then_inc(x_in[u], 16)
            with sp.Fori(0, KD // U) as i:
                for u in range(U):
                    S.hold(b_psum, last(i, U, u + 1))
                    for n in range(2):
                        sp.dma_start(w[:, u, n, :, :], wv[:, :, ds(i * (U * P) + (n * D + u * P), P)]).then_inc(w_done[u], 16)

        @block.gpsimd
        def _(pool):
            G.open(cw_ready)
            pool.wait_ge(consts, 32)
            with pool.Fori(0, KD) as i:
                G.hold(conv_done, last(i))
                for j in range(CONV):
                    nc.gpsimd.tensor_copy(cw[:, j:j + 1], vec[:, ds(i + (c0 + j * KD), 1)])
                nc.gpsimd.tensor_copy(cw[:, CONV:CONV + 1], vec[:, ds(i + cb, 1)]).then_inc(cw_ready, 1)

        @block.tensor
        def _(pe):
            E.open(x_psum, g_psum, b_psum, n=U)
            pe.wait_ge(consts, 32)
            with pe.Fori(0, NT // U) as i:
                for u in range(U):
                    E.hold(x_in[u], now(i, 16))
                    E.hold(xT_ready, last(i, U, u + U) if u == 0 else now(i, U, u))
                    for k in range(KD):
                        t = nc.tensor.transpose(pt[:, k * P:(k + 1) * P], xt[:, u, k * P:(k + 1) * P], ident[:, :])
                    t.then_inc(x_psum, 1)
            pe.wait_ge(xT_ready, NT + U)
            with pe.Fori(0, KD // U) as i:
                for u in range(U):
                    E.hold(w_done[u], now(i, 32))
                    for n, ps in enumerate((pg, px)):
                        if n == 0:
                            E.hold(g_copied, i * U + (u + 1))
                        else:
                            E.hold(conv_done, i * U + (u + 1))
                        for half in range(2):
                            for k in range(KD):
                                m = nc.tensor.matmul(ps[:, half * HALF:(half + 1) * HALF], w[:, u, n, k, :], xT[:, k, half * HALF:(half + 1) * HALF],
                                                     start=k == 0, stop=k == KD - 1)
                        m.then_inc(b_psum if n else g_psum, 1)

        @block.scalar
        def _(act):
            A.open(xT_ready, n=U)
            A.open(g_copied, sig)
            with act.Fori(0, NT // U) as i:
                for u in range(U):
                    A.hold(x_psum, now(i, U, u + 1))
                    nc.scalar.copy(xT[:, :, ds((i * U + u) * P, P)], pt[:, :].rearrange("p (k t) -> p k t", k=KD)).then_inc(xT_ready, 1)
            with act.Fori(0, KD) as i:
                A.hold(g_psum, i + (U + 1))
                A.hold(gg_ready, last(i))
                nc.scalar.copy(gx[:, :], pg[:, :]).then_inc(g_copied, 1)
                A.hold(cube, now(i))
                nc.scalar.activation(g3[:, :], g3[:, :], ACT.Sigmoid, scale=2.0 * GELU_C).then_inc(sig, 1)

        @block.vector
        def _(dve):
            V.open(cube, gg_ready, conv_done)
            with dve.Fori(0, KD) as i:
                V.loop(i, 6)
                V.hold(g_copied, now(i))
                V.link(nc.vector.tensor_tensor(g2[:, :], gx[:, :], gx[:, :], ALU.mult))
                V.link(nc.vector.tensor_scalar(g2[:, :], g2[:, :], 0.044715, 1.0, ALU.mult, ALU.add))
                nc.vector.tensor_tensor(g3[:, :], g2[:, :], gx[:, :], ALU.mult).then_inc(cube, 1)
                V.hold(b_psum, i + (U + 1))
                V.hold(cw_ready, now(i))
                V.link(nc.vector.tensor_scalar(cv[:, :], px[:, :], cw[:, 2:3], cw[:, CONV:CONV + 1], ALU.mult, ALU.add))
                V.link(nc.vector.scalar_tensor_tensor(cv[:, 2:T], px[:, 0:T - 2], cw[:, 0:1], cv[:, 2:T], ALU.mult, ALU.add))
                V.link(nc.vector.scalar_tensor_tensor(cv[:, 1:T], px[:, 0:T - 1], cw[:, 1:2], cv[:, 1:T], ALU.mult, ALU.add))
                V.link(nc.vector.scalar_tensor_tensor(cv[:, 0:T - 1], px[:, 1:T], cw[:, 3:4], cv[:, 0:T - 1], ALU.mult, ALU.add))
                nc.vector.tensor_copy(xc[:, ds(i, 1), :].rearrange("p o t -> p (o t)"), cv[:, :]).then_inc(conv_done, 1)
                V.hold(sig, now(i))
                nc.vector.tensor_tensor(ggT[:, ds(i, 1), :].rearrange("p o t -> p (o t)"), gx[:, :], g3[:, :], ALU.mult).then_inc(gg_ready, 1)
            V.done(KD)


def lru_scan(nc, ph, vec, xc, w_r, w_i, ggT):
    w = ph.sb("w", [P, 2, 2, 2, 2, P])
    r, ig, th, a, m, h = ([ph.sb(f"{n}{u}", [P, 2, T]) for u in range(2)] for n in "r ig th a m h".split())
    dec = ph.sb("dec", [P, 2 * KD])
    sm = ph.sb("sm", [P, 6, 2 * KD])
    pw = ph.ps("pw", [P, 4, T])
    names = "sp_a dec_ready w_psum gates th_ready squared input_ready m2_ready mult ready".split()
    sp_a, dec_ready, w_psum, gates, th_ready, squared, input_ready, m2_ready, mult, ready = [ph.sem(n) for n in names]
    w_done = [ph.sem(f"w_done{u}") for u in range(2)]
    V, G, A, E, S = (ph.engine(e, n) for e, n in ((nc.vector, "dve"), (nc.gpsimd, "pool"), (nc.scalar, "act"),
                                                  (nc.tensor, "pe"), (nc.sync, "sp")))
    lam = vec_at("lru_lambda_2")[0]
    br, bi = vec_at("lru_b_rgate_2")[0], vec_at("lru_b_igate_2")[0]

    with nc.Block() as block:

        @block.sync
        def _(sp):
            for u in range(2):
                S.open(w_done[u], n=64)
            with sp.Fori(0, NBLK) as n:
                for u in range(2):
                    S.hold(w_psum, last(n, 8, 4 * u + 4))
                    for z in range(2):
                        for k, wt in enumerate((w_r, w_i)):
                            sp.dma_start(w[:, u, z, k, :, :], wt[0, z][ds(n, 1), :, u * P:(u + 1) * P].rearrange("o (c p) f -> p (o c) f", p=P)).then_inc(w_done[u], 16)

        @block.tensor
        def _(pe):
            E.open(w_psum, n=8)
            with pe.Fori(0, NBLK) as n:
                for u in range(2):
                    E.hold(w_done[u], now(n, 64))
                    for z in range(2):
                        for k in range(2):
                            at = 2 * z + k
                            E.hold(gates, now(n, 8, at + 1) if u else last(n, 8, 4 + at + 1))
                            for half in range(2):
                                for c in range(2):
                                    mm = nc.tensor.matmul(pw[:, at, half * HALF:(half + 1) * HALF], w[:, u, z, k, c, :],
                                                          xc[:, ds(n * 2 + c, 1), half * HALF:(half + 1) * HALF].rearrange("p o t -> p (o t)"), start=c == 0, stop=c == 1)
                            mm.then_inc(w_psum, 1)

        @block.gpsimd
        def _(pool):
            G.open(squared, input_ready, n=2)
            with pool.Fori(0, NBLK) as n:
                for u in range(2):
                    G.hold(gates, now(n, 8, 4 * u + 4))
                    nc.gpsimd.tensor_tensor(ig[u][:, :, :], ig[u][:, :, :], xc[:, ds(n * 2 + u, 1), :].to_broadcast([P, 2, T]), ALU.mult).then_inc(input_ready, 1)
                    G.hold(th_ready, now(n, 2, u + 1))
                    G.hold(ready, last(n, 2, u + 1))
                    nc.gpsimd.tensor_tensor(m[u][:, :, :], a[u][:, :, :], a[u][:, :, :], ALU.mult).then_inc(squared, 1)

        @block.scalar
        def _(act):
            A.open(gates, n=8)
            A.open(th_ready, mult, n=2)
            nc.scalar.activation(sm[:, 0, :], vec[:, lam:lam + 2 * KD], ACT.Abs).then_inc(sp_a, 1)
            act.wait_ge(sp_a, 1)
            nc.scalar.activation(sm[:, 1, :], sm[:, 0, :], ACT.Exp, scale=-1.0).then_inc(sp_a, 1)
            act.wait_ge(dec_ready, 1)
            with act.Fori(0, NBLK) as n:

                def sigmoids(u):
                    A.hold(ready, last(n, 2, u + 1))
                    for z in range(2):
                        for k, (dst, b0) in enumerate(((r[u], br), (ig[u], bi))):
                            A.hold(w_psum, now(n, 8, 4 * u + 2 * z + k + 1))
                            nc.scalar.activation(dst[:, z, :], pw[:, 2 * z + k, :], ACT.Sigmoid, bias=vec[:, ds(n * 2 + (b0 + z * KD + u), 1)]).then_inc(gates, 1)

                def decays(u):
                    A.hold(gates, now(n, 8, 4 * u + 4))
                    A.hold(squared, last(n, 2, u + 1))
                    for z in range(2):
                        nc.scalar.activation(th[u][:, z, :], r[u][:, z, :], ACT.Tanh, scale=dec[:, ds(n * 2 + (z * KD + u), 1)])
                        tt = nc.scalar.activation(a[u][:, z, :], r[u][:, z, :], ACT.Exp, scale=dec[:, ds(n * 2 + (z * KD + u), 1)])
                    tt.then_inc(th_ready, 1)

                def root(u):
                    A.hold(m2_ready, now(n, 2, u + 1))
                    nc.scalar.activation(m[u][:, :, :], m[u][:, :, :], ACT.Sqrt, scale=-1.0).then_inc(mult, 1)

                sigmoids(0)
                decays(0)
                sigmoids(1)
                root(0)
                decays(1)
                root(1)

        @block.vector
        def _(dve):
            V.open(m2_ready, ready, n=2)
            dve.wait_ge(sp_a, 2)
            y, s_, s2, acc = sm[:, 1, :], sm[:, 2, :], sm[:, 3, :], sm[:, 4, :]
            V.link(nc.vector.tensor_scalar(acc, y, 2.0, None, ALU.add))
            V.link(nc.vector.reciprocal(acc, acc))
            V.link(nc.vector.tensor_tensor(s_, y, acc, ALU.mult))
            V.link(nc.vector.tensor_tensor(s2, s_, s_, ALU.mult))
            V.link(nc.vector.memset(acc, 1.0 / 19))
            for odd in range(17, 0, -2):
                V.link(nc.vector.tensor_tensor(acc, acc, s2, ALU.mult))
                V.link(nc.vector.tensor_scalar(acc, acc, 1.0 / odd, None, ALU.add))
            V.link(nc.vector.tensor_tensor(acc, acc, s_, ALU.mult))
            V.link(nc.vector.tensor_scalar(sm[:, 5, :], vec[:, lam:lam + 2 * KD], -1.0, 0.0, ALU.mult, ALU.max))
            V.link(nc.vector.tensor_scalar(acc, acc, 2.0, None, ALU.mult))
            V.link(nc.vector.tensor_tensor(acc, acc, sm[:, 5, :], ALU.add))
            V.link(nc.vector.tensor_scalar(dec[:, :], acc, -8.0, None, ALU.mult))
            dve.sem_inc(dec_ready, 1)
            with dve.Fori(0, NBLK) as n:
                V.loop(n, 8)

                def minus_mult2(u):
                    V.hold(th_ready, now(n, 2, u + 1))
                    V.hold(squared, now(n, 2, u + 1))
                    nc.vector.scalar_tensor_tensor(m[u][:, :, :], m[u][:, :, :], 1.0, th[u][:, :, :], ALU.add, ALU.mult).then_inc(m2_ready, 1)

                def scans(u):
                    V.hold(mult, now(n, 2, u + 1))
                    V.hold(input_ready, now(n, 2, u + 1))
                    nc.vector.memset(m[u][:, 0, 0:1], 1.0)
                    V.link(nc.vector.memset(m[u][:, 1, T - 1:T], 1.0))
                    V.link(nc.vector.tensor_tensor(m[u][:, :, :], m[u][:, :, :], ig[u][:, :, :], ALU.mult))
                    nc.vector.tensor_tensor_scan(h[u][:, 0, :], a[u][:, 0, :], m[u][:, 0, :], 0.0, ALU.mult, ALU.add)
                    V.link(nc.vector.tensor_tensor_scan(h[u][:, 1, ::-1], a[u][:, 1, ::-1], m[u][:, 1, ::-1], 0.0, ALU.mult, ALU.add))

                def gated(u):
                    V.link(nc.vector.tensor_tensor(h[u][:, 0, :], h[u][:, 0, :], h[u][:, 1, :], ALU.add))
                    g = ggT[:, ds(n * 2 + u, 1), :].rearrange("p o t -> p (o t)")
                    nc.vector.tensor_tensor(g, h[u][:, 0, :], g, ALU.mult).then_inc(ready, 1)

                minus_mult2(0)
                scans(0)
                gated(0)
                minus_mult2(1)
                scans(1)
                gated(1)
            V.done(NBLK)


def moe_and_transformer_kernel(nc, I, out):
    def scratch(name, shape, dt=F32):
        return nc.dram_tensor(name, shape, dt, kind="Internal").ap()

    hT, oT = scratch("hT", [D, T]), scratch("oT", [MLA_H * V_DIM, T])
    with Phase(nc, "h") as shared:
        h_all = shared.sb("h_all", [P, KD, T])
        h_in = shared.sem("h_in")
        mla_phase(nc, I["x"], I["vecs"], I["w_in"], I["w_uq"], I["w_ukv"], I["eye"], I["mla_rope"], hT, oT, h_all, h_in)

        zfT = scratch("zfT", [RWKV_TILES * P, T])
        arrays = scratch("arrays", [len(ARR), RC, T])
        shift_phase(nc, I["vecs"], I["w_in"], h_all, h_in, zfT)
        prep_phase(nc, I["vecs"], I["w_up"], I["a_up"], I["g_up"], zfT, I["starts"], I["head_ones"], arrays)
        yT = scratch("yT", [2, RC, T])
        wkv_phase(nc, I["wkv_tables"], arrays, yT)

        mixT = scratch("mixT", [D, T])
        mix_phase(nc, I["vecs"], I["w_in"], I["w_br_mla"], I["w_br_rwkv"], I["head_ones"], h_all, oT, arrays, yT, mixT)
    x1, h2, x2 = scratch("x1", [T, D]), scratch("h2", [T, D]), scratch("x2", [T, D])
    slot_tok = scratch("slot_tok", [SLOTS + P, 1], U32)
    yb = scratch("yb", [SLOTS, D])
    with ExitStack() as routes:
        slots = routes.enter_context(nc.sbuf_tensor("slots", [P, 2 * NT], U32))
        weights = routes.enter_context(nc.sbuf_tensor("weights", [P, 2 * NT], F32))
        block_e = routes.enter_context(nc.sbuf_tensor("block_e", [P, MOE_BLOCKS], U32))
        pair_used = routes.enter_context(nc.sbuf_tensor("pair_used", [P, MOE_BLOCKS // 2], U32))
        route_phase(nc, I["x"], I["vecs"], I["w_out"], I["router_group_w"], I["router_group_b"], I["router_expert_w"],
                    I["router_expert_b"], I["eye"], I["route_tables"], I["tok_ids"], mixT, x1, h2, slot_tok,
                    (slots, weights, block_e, pair_used))
        experts_phase(nc, I["vecs"], I["w1"], I["w3"], I["w2"], I["eye"], block_e, pair_used, slot_tok, h2, yb)
        combine_phase(nc, I["norm_final_g"], slots, weights, x1, yb, x2)

    acc, x3, x4, x5 = (scratch(n, [T, D]) for n in ("acc", "x3", "x4", "x5"))
    gqa_phase(nc, I["attn_w_qkv_2"], I["attn_w_o_2"], I["attn_sink_2"], I["eye"], I["gqa_rope"], I["gqa_masks"],
              I["ln_mix_g_2"][0], I["ln_mix_b_2"][0], x2, x3)
    expert_choice_phase(nc, "ec0", I["moe_w_router_2"][0], I["moe_w_gate_up_2"][0], I["moe_w_down_2"][0], I["eye"],
                        x3, acc)
    norm_phase(nc, "norm1", I["ln_ffn_g_2"][0], I["ln_ffn_b_2"][0], x3, acc, x4)

    lru_phase(nc, I["vecs"], I["lru_w_in_2"], I["lru_w_rgate_2"], I["lru_w_igate_2"], I["lru_w_out_2"], I["eye"],
              I["ln_mix_g_2"][1], I["ln_mix_b_2"][1], x4, x5)
    expert_choice_phase(nc, "ec1", I["moe_w_router_2"][1], I["moe_w_gate_up_2"][1], I["moe_w_down_2"][1], I["eye"],
                        x5, acc)
    norm_phase(nc, "norm3", I["ln_ffn_g_2"][1], I["ln_ffn_b_2"][1], x5, acc, out)


_WHOLE = ["w_in", "w_uq", "w_ukv", "w_br_mla", "w_up", "a_up", "g_up", "w_br_rwkv", "w_out", "router_group_w",
          "router_group_b", "router_expert_w", "router_expert_b", "w1", "w3", "w2", "norm_final_g", "attn_w_qkv_2",
          "attn_w_o_2", "attn_sink_2", "lru_w_in_2", "lru_w_rgate_2", "lru_w_igate_2", "lru_w_out_2",
          "moe_w_router_2", "moe_w_gate_up_2", "moe_w_down_2", "ln_mix_g_2", "ln_mix_b_2", "ln_ffn_g_2",
          "ln_ffn_b_2"]


def kernel(**inputs):
    import concourse.bacc as _bacc
    from concourse.bass_utils import run_bass_kernel_spmd as _run

    a = {n: np.ascontiguousarray(inputs[n]) for n in _WHOLE}
    a["x"] = np.ascontiguousarray(inputs["x"]).reshape(T, D)
    a["vecs"] = np.ascontiguousarray(
        np.concatenate([np.asarray(inputs[n]).reshape(-1, P).T for n in VECS], axis=1))
    a["eye"] = np.eye(P, dtype=np.float32)
    a["mla_rope"] = mla_tables()
    a["starts"], a["head_ones"] = prep_tables()
    a["wkv_tables"] = wkv_tables()
    a["route_tables"], a["tok_ids"] = route_tables()
    a["gqa_rope"], a["gqa_masks"] = gqa_tables()
    nc = _bacc.Bacc("TRN2", target_bir_lowering=False, num_devices=1)
    arrays = {f"in_{n}_dram": v for n, v in a.items()}
    aps = {n: nc.dram_tensor(f"in_{n}_dram", v.shape, mybir.dt.from_np(v.dtype), kind="ExternalInput").ap()
           for n, v in a.items()}
    out = nc.dram_tensor("out_0_dram", (T, D), F32, kind="ExternalOutput").ap()
    moe_and_transformer_kernel(nc, aps, out)
    r = _run(nc, [arrays], core_ids=[0])
    return r.results[0]["out_0_dram"].reshape(1, T, D)
```
